# Optimizing a Trainium2 kernel written in Bass

```python
import math
import jax
import jax.numpy as jnp
from jax import lax
import numpy as np

D_MODEL = 1024
BATCH = 1
SEQ = 512
DEPTH = 2
DEC_BATCH = 8
DEC_SEQ = 8
PAST_LEN = 512
PAGE_SIZE = 128

HEAD_DIM = 64
NSA_HEADS = D_MODEL // (2 * HEAD_DIM)
NSA_KV = 2
NSA_QPG = NSA_HEADS // NSA_KV
NSA_WIDTH = NSA_HEADS * HEAD_DIM
NSA_KV_WIDTH = NSA_KV * HEAD_DIM
CMP_LEN = 32
CMP_STRIDE = 16
CMP_HIDDEN = 2 * HEAD_DIM
SEL_LEN = 64
N_SELECT = 16
WINDOW = 512
NSA_CHUNK = 64
FORCE_SCORE = 1e9
RWKV_HEADS = D_MODEL // (2 * HEAD_DIM)
RWKV_WIDTH = RWKV_HEADS * HEAD_DIM
DECAY_LORA = 64
AAA_LORA = 64
GATE_LORA = 128
RWKV_PROJ = 3 * RWKV_WIDTH + DECAY_LORA + AAA_LORA + GATE_LORA
NSA_PROJ = NSA_WIDTH + 6 * NSA_KV_WIDTH + 3 * NSA_HEADS
EVEN_PROJ = NSA_PROJ + RWKV_PROJ
MIX_WIDTH = NSA_WIDTH + RWKV_WIDTH
CONV_WIDTH = D_MODEL
CONV_K = 3
D_FF = ((8 * D_MODEL // 3 + 255) // 256) * 256
FFN_CONV_K = 3
NUM_BUCKETS = 32
MAX_DISTANCE = 128
N_EVEN = (DEPTH + 1) // 2
N_ODD = DEPTH // 2
RMS_EPS = 1e-6
GN_EPS = 64e-5

kernel_name = 'nsa_rwkv7_shortconv_convffn_decode_step'

def rms_norm(x, g):
    xf = x.astype(jnp.float32)
    y = xf * lax.rsqrt(jnp.mean(xf * xf, axis=-1, keepdims=True) + RMS_EPS)
    return (y * g.astype(jnp.float32)).astype(x.dtype)

def masked_softmax(s, mask):
    s = jnp.where(mask, s, -jnp.inf)
    m = jnp.max(s, axis=-1, keepdims=True)
    e = jnp.exp(s - jnp.where(jnp.isfinite(m), m, 0.0))
    den = jnp.sum(e, axis=-1, keepdims=True)
    return e / jnp.where(den > 0, den, 1.0)

def rel_bucket(dist):
    n = jnp.maximum(dist, 0)
    max_exact = NUM_BUCKETS // 2
    nf = jnp.maximum(n, 1).astype(jnp.float32)
    large = max_exact + (jnp.log(nf / max_exact) / math.log(MAX_DISTANCE / max_exact)
                         * (NUM_BUCKETS - max_exact)).astype(jnp.int32)
    large = jnp.minimum(large, NUM_BUCKETS - 1)
    return jnp.where(n < max_exact, n, large)

def causal_dwconv(u, prev, w):
    kw = w.shape[0]
    t = u.shape[1]
    ext = jnp.concatenate([prev.astype(u.dtype), u], axis=1)
    y = ext[:, 0:t] * w[0]
    for j in range(1, kw):
        y = y + ext[:, j:j + t] * w[j]
    return y, ext[:, t:]

def compress(k, pe, w1, w2):
    b, t = k.shape[:2]
    r_n = CMP_LEN // CMP_STRIDE
    m = t // CMP_STRIDE
    nc = m - r_n + 1
    seg = k[:, :m * CMP_STRIDE].reshape(b, m, CMP_STRIDE, NSA_KV, HEAD_DIM)
    w1r = w1.reshape(r_n, CMP_STRIDE, HEAD_DIM, CMP_HIDDEN)
    part = jnp.einsum('bmjgd,rjde->rbmge', seg, w1r)
    hid = jnp.einsum('jd,jde->e', pe, w1) + part[0, :, 0:nc]
    for r in range(1, r_n):
        hid = hid + part[r, :, r:r + nc]
    return jnp.einsum('bnge,ed->bngd', jax.nn.gelu(hid), w2)

def nsa_chunk(q, gate, qpos, kc, vc, cend, ks_blk, vs_blk, kw, vw, wpos, overlap, rel_bias):
    b, c = q.shape[:2]
    scale = HEAD_DIM ** -0.5
    tb = rel_bias.astype(jnp.float32).reshape(NUM_BUCKETS, NSA_KV, NSA_QPG)
    dist_c = qpos[:, None] - cend[None, :]
    s_c = jnp.einsum('bcgqd,bngd->bcgqn', q, kc).astype(jnp.float32) * scale
    s_c = s_c + jnp.moveaxis(tb[rel_bucket(dist_c)], 1, -1)[None]
    p_c = masked_softmax(s_c, (dist_c >= 0)[None, :, None, None, :])
    o_c = jnp.einsum('bcgqn,bngd->bcgqd', p_c.astype(vc.dtype), vc)
    ns = ks_blk.shape[2]
    imp = jnp.einsum('bcgqn,ns->bcgs', p_c, overlap)
    blk = jnp.arange(ns, dtype=jnp.int32)[None, :]
    cur = (qpos // SEL_LEN)[:, None]
    forced = (blk == 0) | (blk == cur) | (blk == cur - 1)
    future = blk * SEL_LEN > qpos[:, None]
    imp = jnp.where(forced[None, :, None], FORCE_SCORE, imp)
    imp = jnp.where(future[None, :, None], -FORCE_SCORE, imp)
    n_top = min(N_SELECT, ns)
    _, idx = lax.top_k(imp, n_top)
    bi = jnp.arange(b)[:, None, None, None]
    gi = jnp.arange(NSA_KV)[None, None, :, None]
    n_keys = n_top * SEL_LEN
    k_sel = ks_blk[bi, gi, idx].reshape(b, c, NSA_KV, n_keys, HEAD_DIM)
    v_sel = vs_blk[bi, gi, idx].reshape(b, c, NSA_KV, n_keys, HEAD_DIM)
    kpos = (idx[..., None] * SEL_LEN + jnp.arange(SEL_LEN, dtype=jnp.int32)).reshape(b, c, NSA_KV, n_keys)
    dist_s = qpos[None, :, None, None] - kpos
    s_s = jnp.einsum('bcgqd,bcgkd->bcgqk', q, k_sel).astype(jnp.float32) * scale
    s_s = s_s + jnp.swapaxes(tb[rel_bucket(dist_s), gi], -1, -2)
    p_s = masked_softmax(s_s, (dist_s >= 0)[:, :, :, None, :])
    o_s = jnp.einsum('bcgqk,bcgkd->bcgqd', p_s.astype(v_sel.dtype), v_sel)
    dist_w = qpos[:, None] - wpos[None, :]
    s_w = jnp.einsum('bcgqd,bwgd->bcgqw', q, kw).astype(jnp.float32) * scale
    s_w = s_w + jnp.moveaxis(tb[rel_bucket(dist_w)], 1, -1)[None]
    mask_w = (dist_w >= 0) & (dist_w < WINDOW) & (wpos >= 0)[None, :]
    p_w = masked_softmax(s_w, mask_w[None, :, None, None, :])
    o_w = jnp.einsum('bcgqw,bwgd->bcgqd', p_w.astype(vw.dtype), vw)
    g = jax.nn.sigmoid(gate.astype(jnp.float32))
    o = g[..., 0:1] * o_c + g[..., 1:2] * o_s + g[..., 2:3] * o_w
    return o.astype(q.dtype)

def nsa_attend(q, gates, k_cmp, v_cmp, k_slc, v_slc, k_win, v_win, q0, w0, chunk, banded, phi, rel_bias):
    b, tq = q.shape[:2]
    pe, w1, w2, kn_cmp = phi
    kc = rms_norm(compress(k_cmp, pe[0], w1[0], w2[0]), kn_cmp)
    vc = compress(v_cmp, pe[1], w1[1], w2[1])
    nc = kc.shape[1]
    cend = jnp.arange(nc, dtype=jnp.int32) * CMP_STRIDE + (CMP_LEN - 1)
    t_all = k_slc.shape[1]
    ns = -(-t_all // SEL_LEN)

    def blockify(a):
        a = jnp.pad(a, ((0, 0), (0, ns * SEL_LEN - t_all), (0, 0), (0, 0)))
        return a.reshape(b, ns, SEL_LEN, NSA_KV, HEAD_DIM).transpose(0, 3, 1, 2, 4)

    ks_blk, vs_blk = blockify(k_slc), blockify(v_slc)
    c0 = jnp.arange(nc)[:, None] * CMP_STRIDE
    s0 = jnp.arange(ns)[None, :] * SEL_LEN
    overlap = ((c0 < s0 + SEL_LEN) & (c0 + CMP_LEN > s0)).astype(jnp.float32)
    n_chunks = tq // chunk

    def to_chunks(a):
        return jnp.swapaxes(a.reshape((b, n_chunks, chunk) + a.shape[2:]), 0, 1)

    qc = to_chunks(q.reshape(b, tq, NSA_KV, NSA_QPG, HEAD_DIM))
    gc = to_chunks(gates.reshape(b, tq, NSA_KV, NSA_QPG, 3))
    if banded:
        pad = ((0, 0), (WINDOW, 0), (0, 0), (0, 0))
        kw_src, vw_src = jnp.pad(k_win, pad), jnp.pad(v_win, pad)
        span = WINDOW + chunk
    else:
        kw_src, vw_src = k_win, v_win
        span = k_win.shape[1]

    def body(args):
        q_i, g_i, c_i = args
        start = c_i * chunk
        qpos = q0 + start + jnp.arange(chunk, dtype=jnp.int32)
        if banded:
            kw_i = lax.dynamic_slice_in_dim(kw_src, start, span, axis=1)
            vw_i = lax.dynamic_slice_in_dim(vw_src, start, span, axis=1)
            wpos = w0 + start - WINDOW + jnp.arange(span, dtype=jnp.int32)
        else:
            kw_i, vw_i = kw_src, vw_src
            wpos = w0 + jnp.arange(span, dtype=jnp.int32)
        return nsa_chunk(q_i, g_i, qpos, kc, vc, cend, ks_blk, vs_blk, kw_i, vw_i, wpos, overlap, rel_bias)

    out = lax.map(body, (qc, gc, jnp.arange(n_chunks, dtype=jnp.int32)))
    return jnp.swapaxes(out, 0, 1).reshape(b, tq, NSA_WIDTH)

def rwkv_mix(z, z_prev, s0, li, P):
    b, t, _ = z.shape
    f32 = jnp.float32
    shifted = jnp.concatenate([z_prev[:, None].astype(z.dtype), z[:, :-1]], axis=1)
    zz = z + (shifted - z) * P['rwkv_mu'][li]
    offs = [RWKV_WIDTH, 2 * RWKV_WIDTH, 3 * RWKV_WIDTH, 3 * RWKV_WIDTH + DECAY_LORA,
            3 * RWKV_WIDTH + DECAY_LORA + AAA_LORA]
    r, k, v, zw, za, zg = jnp.split(zz, offs, axis=-1)
    w_log = -jax.nn.softplus(-(P['rwkv_w0'][li] + jnp.tanh(zw) @ P['rwkv_w2'][li]).astype(f32)) - 0.5
    decay = jnp.exp(-jnp.exp(w_log))
    a = jax.nn.sigmoid((P['rwkv_a0'][li] + za @ P['rwkv_a2'][li]).astype(f32))
    g = jax.nn.sigmoid(zg) @ P['rwkv_g2'][li]

    def hd(a_):
        return a_.reshape(b, t, RWKV_HEADS, HEAD_DIM)

    kk = hd((k * P['rwkv_kk'][li]).astype(f32))
    kk = kk * lax.rsqrt(jnp.maximum(jnp.sum(kk * kk, axis=-1, keepdims=True), 1e-24))
    k_mod = hd(k.astype(f32) * (1.0 + (a - 1.0) * P['rwkv_ka'][li].astype(f32)))
    r_h, v_h, a_h, w_h = hd(r.astype(f32)), hd(v.astype(f32)), hd(a), hd(decay)

    def step(S, inp):
        r_t, w_t, k_t, v_t, kk_t, a_t = inp
        sa = jnp.einsum('bhij,bhj->bhi', S, -kk_t)
        S = (S * w_t[:, :, None, :] + sa[..., None] * (kk_t * a_t)[:, :, None, :]
             + v_t[..., None] * k_t[:, :, None, :])
        return S, jnp.einsum('bhij,bhj->bhi', S, r_t)

    xs = tuple(jnp.swapaxes(a_, 0, 1) for a_ in (r_h, w_h, k_mod, v_h, kk, a_h))
    s_t, y = lax.scan(step, s0.astype(f32), xs)
    y = jnp.swapaxes(y, 0, 1)
    mu = jnp.mean(y, axis=-1, keepdims=True)
    var = jnp.mean(jnp.square(y - mu), axis=-1, keepdims=True)
    y = (y - mu) * lax.rsqrt(var + GN_EPS)
    y = (y * P['rwkv_ln_w'][li].astype(f32).reshape(RWKV_HEADS, HEAD_DIM)
         + P['rwkv_ln_b'][li].astype(f32).reshape(RWKV_HEADS, HEAD_DIM))
    y = y + jnp.sum(r_h * k_mod * P['rwkv_rk'][li].astype(f32), axis=-1, keepdims=True) * v_h
    y = y.reshape(b, t, RWKV_WIDTH).astype(z.dtype) * g
    return y, s_t, z[:, -1]

def nsa_rwkv_mixer(h, li, P, st):
    b, t, _ = h.shape
    z = jnp.einsum('btd,de->bte', h, P['w_in_even'][li])
    sizes = [NSA_WIDTH] + [NSA_KV_WIDTH] * 6 + [3 * NSA_HEADS]
    offs, acc = [], 0
    for s in sizes:
        acc += s
        offs.append(acc)
    q, k_c, v_c, k_s, v_s, k_w, v_w, gates, z_rwkv = jnp.split(z, offs, axis=-1)

    def kvh(a_):
        return a_.reshape(b, t, NSA_KV, HEAD_DIM)

    q = rms_norm(q.reshape(b, t, NSA_HEADS, HEAD_DIM), P['q_norm'][li])
    k_c, v_c, v_s, v_w = kvh(k_c), kvh(v_c), kvh(v_s), kvh(v_w)
    k_s = rms_norm(kvh(k_s), P['k_norm'][li, 1])
    k_w = rms_norm(kvh(k_w), P['k_norm'][li, 2])
    phi = (P['phi_pe'][li], P['phi_w1'][li], P['phi_w2'][li], P['k_norm'][li, 0])
    if st is None:
        nsa = nsa_attend(q, gates, k_c, v_c, k_s, v_s, k_w, v_w, 0, 0, NSA_CHUNK, True, phi, P['rel_bias'])
        win_k, win_v = k_w, v_w
        z_prev = jnp.zeros((b, RWKV_PROJ), h.dtype)
        s0 = jnp.zeros((b, RWKV_HEADS, HEAD_DIM, HEAD_DIM), jnp.float32)
    else:
        pt = st['page_table']
        past = pt.shape[1] * PAGE_SIZE

        def paged(pool):
            rows = pool[pt, li]
            return rows.reshape(b, past, 2, NSA_KV, HEAD_DIM).astype(h.dtype)

        def cat(a_, b_):
            return jnp.concatenate([a_, b_], axis=1)

        pc, ps = paged(st['cmp']), paged(st['slc'])
        buf = st['win'][:, li].astype(h.dtype)
        wb = buf.shape[1]
        win_k, win_v = cat(buf[:, :, 0], k_w), cat(buf[:, :, 1], v_w)
        nsa = nsa_attend(q, gates, cat(pc[:, :, 0], k_c), cat(pc[:, :, 1], v_c),
                         cat(ps[:, :, 0], k_s), cat(ps[:, :, 1], v_s), win_k, win_v,
                         past, past - wb, 1, False, phi, P['rel_bias'])
        z_prev = st['shift'][:, li]
        s0 = st['wkv'][:, li]
    n_keep = min(WINDOW, win_k.shape[1])
    win_rows = jnp.stack([win_k, win_v], axis=2)[:, -n_keep:]
    rw, s_t, z_last = rwkv_mix(z_rwkv, z_prev, s0, li, P)
    out = jnp.einsum('bte,ed->btd', jnp.concatenate([nsa, rw], axis=-1), P['w_out_even'][li])
    return out, (jnp.stack([k_c, v_c], axis=2), jnp.stack([k_s, v_s], axis=2), win_rows, s_t, z_last)

def conv_mixer(h, li, P, st):
    b = h.shape[0]
    z = jnp.einsum('btd,de->bte', h, P['w_in_odd'][li])
    bg, cg, xi = jnp.split(z, [CONV_WIDTH, 2 * CONV_WIDTH], axis=-1)
    prev = jnp.zeros((b, CONV_K - 1, CONV_WIDTH), h.dtype) if st is None else st['conv'][:, li]
    c, new = causal_dwconv(cg * xi, prev, P['conv_w'][li])
    return jnp.einsum('bte,ed->btd', bg * c, P['w_out_odd'][li]), new

def conv_ffn(h, l, P, st):
    b = h.shape[0]
    a, u = jnp.split(jnp.einsum('btd,df->btf', h, P['ffn_up'][l]), [D_FF], axis=-1)
    prev = jnp.zeros((b, FFN_CONV_K - 1, D_FF), h.dtype) if st is None else st['ffn'][:, l]
    ac, new = causal_dwconv(a, prev, P['ffn_conv'][l])
    return jnp.einsum('btf,fd->btd', jax.nn.silu(ac) * u, P['ffn_down'][l]), new

def trunk(x, P, st):
    cmp_r, slc_r, win_r, wkv_r, sh_r, conv_r, ffn_r = [], [], [], [], [], [], []
    for l in range(DEPTH):
        li = l // 2
        h = rms_norm(x, P['norm_mix'][l])
        if l % 2 == 0:
            o, (c_, s_, w_, S_, sh_) = nsa_rwkv_mixer(h, li, P, st)
            cmp_r.append(c_)
            slc_r.append(s_)
            win_r.append(w_)
            wkv_r.append(S_)
            sh_r.append(sh_)
        else:
            o, cs = conv_mixer(h, li, P, st)
            conv_r.append(cs)
        x = x + o
        o, fs = conv_ffn(rms_norm(x, P['norm_ffn'][l]), l, P, st)
        ffn_r.append(fs)
        x = x + o
    stk = lambda a_: jnp.stack(a_, axis=1)
    return x, (stk(cmp_r), stk(slc_r), stk(win_r), stk(wkv_r), stk(sh_r), stk(conv_r), stk(ffn_r))

def setup_inputs(seed: int = 0) -> dict:
    key = jax.random.key(seed)
    keys = jax.random.split(key, 64)
    counter = iter(range(64))

    def nk():
        return keys[next(counter)]

    def nrm(shape, scale=1.0):
        return jax.random.normal(nk(), shape, jnp.float32) * scale

    def gain(shape, base=1.0):
        return base + 0.05 * jax.random.normal(nk(), shape, jnp.float32)

    def unif(shape, lo, hi):
        return jax.random.uniform(nk(), shape, jnp.float32, lo, hi)

    n_pages = PAST_LEN // PAGE_SIZE
    used = DEC_BATCH * n_pages
    n_pool = used + max(used // 4, 1)
    wb = min(WINDOW, PAST_LEN)
    d = D_MODEL
    return {
        'x_prompt': nrm((BATCH, SEQ, d)),
        'x_sample': nrm((DEC_BATCH, DEC_SEQ, d)),
        'cache_cmp_kv': nrm((n_pool, N_EVEN, PAGE_SIZE, 2, NSA_KV, HEAD_DIM)),
        'cache_slc_kv': nrm((n_pool, N_EVEN, PAGE_SIZE, 2, NSA_KV, HEAD_DIM)),
        'cache_win_kv': nrm((DEC_BATCH, N_EVEN, wb, 2, NSA_KV, HEAD_DIM)),
        'state_rwkv_wkv': nrm((DEC_BATCH, N_EVEN, RWKV_HEADS, HEAD_DIM, HEAD_DIM), 0.3),
        'state_rwkv_shift': nrm((DEC_BATCH, N_EVEN, RWKV_PROJ)),
        'state_conv': nrm((DEC_BATCH, N_ODD, CONV_K - 1, CONV_WIDTH)),
        'state_ffn_conv': nrm((DEC_BATCH, DEPTH, FFN_CONV_K - 1, D_FF)),
        'page_table': jax.random.permutation(nk(), n_pool)[:used].reshape(DEC_BATCH, n_pages).astype(jnp.int32),
        'norm_mix': gain((DEPTH, d)),
        'norm_ffn': gain((DEPTH, d)),
        'rel_bias': nrm((NUM_BUCKETS, NSA_HEADS), 0.5),
        'w_in_even': nrm((N_EVEN, d, EVEN_PROJ), d ** -0.5),
        'w_out_even': nrm((N_EVEN, MIX_WIDTH, d), MIX_WIDTH ** -0.5),
        'q_norm': gain((N_EVEN, HEAD_DIM)),
        'k_norm': gain((N_EVEN, 3, HEAD_DIM)),
        'phi_pe': nrm((N_EVEN, 2, CMP_LEN, HEAD_DIM), 0.5),
        'phi_w1': nrm((N_EVEN, 2, CMP_LEN, HEAD_DIM, CMP_HIDDEN), (CMP_LEN * HEAD_DIM) ** -0.5),
        'phi_w2': nrm((N_EVEN, 2, CMP_HIDDEN, HEAD_DIM), CMP_HIDDEN ** -0.5),
        'rwkv_mu': unif((N_EVEN, RWKV_PROJ), 0.0, 1.0),
        'rwkv_w0': unif((N_EVEN, RWKV_WIDTH), -5.0, -0.5),
        'rwkv_w2': nrm((N_EVEN, DECAY_LORA, RWKV_WIDTH), 0.1 * DECAY_LORA ** -0.5),
        'rwkv_a0': nrm((N_EVEN, RWKV_WIDTH), 0.1),
        'rwkv_a2': nrm((N_EVEN, AAA_LORA, RWKV_WIDTH), AAA_LORA ** -0.5),
        'rwkv_g2': nrm((N_EVEN, GATE_LORA, RWKV_WIDTH), GATE_LORA ** -0.5),
        'rwkv_kk': gain((N_EVEN, RWKV_WIDTH), 0.85),
        'rwkv_ka': gain((N_EVEN, RWKV_WIDTH)),
        'rwkv_rk': nrm((N_EVEN, RWKV_HEADS, HEAD_DIM), 0.1),
        'rwkv_ln_w': gain((N_EVEN, RWKV_WIDTH)),
        'rwkv_ln_b': nrm((N_EVEN, RWKV_WIDTH), 0.02),
        'w_in_odd': nrm((N_ODD, d, 3 * CONV_WIDTH), d ** -0.5),
        'conv_w': nrm((N_ODD, CONV_K, CONV_WIDTH), CONV_K ** -0.5),
        'w_out_odd': nrm((N_ODD, CONV_WIDTH, d), CONV_WIDTH ** -0.5),
        'ffn_up': nrm((DEPTH, d, 2 * D_FF), d ** -0.5),
        'ffn_conv': nrm((DEPTH, FFN_CONV_K, D_FF), FFN_CONV_K ** -0.5),
        'ffn_down': nrm((DEPTH, D_FF, d), D_FF ** -0.5),
    }

def reference(x_prompt, x_sample, cache_cmp_kv, cache_slc_kv, cache_win_kv, state_rwkv_wkv,
              state_rwkv_shift, state_conv, state_ffn_conv, page_table, norm_mix, norm_ffn,
              rel_bias, w_in_even, w_out_even, q_norm, k_norm, phi_pe, phi_w1, phi_w2,
              rwkv_mu, rwkv_w0, rwkv_w2, rwkv_a0, rwkv_a2, rwkv_g2, rwkv_kk, rwkv_ka, rwkv_rk,
              rwkv_ln_w, rwkv_ln_b, w_in_odd, conv_w, w_out_odd, ffn_up, ffn_conv, ffn_down):
    P = dict(norm_mix=norm_mix, norm_ffn=norm_ffn, rel_bias=rel_bias, w_in_even=w_in_even,
             w_out_even=w_out_even, q_norm=q_norm, k_norm=k_norm, phi_pe=phi_pe, phi_w1=phi_w1,
             phi_w2=phi_w2, rwkv_mu=rwkv_mu, rwkv_w0=rwkv_w0, rwkv_w2=rwkv_w2, rwkv_a0=rwkv_a0,
             rwkv_a2=rwkv_a2, rwkv_g2=rwkv_g2, rwkv_kk=rwkv_kk, rwkv_ka=rwkv_ka, rwkv_rk=rwkv_rk,
             rwkv_ln_w=rwkv_ln_w, rwkv_ln_b=rwkv_ln_b, w_in_odd=w_in_odd, conv_w=conv_w,
             w_out_odd=w_out_odd, ffn_up=ffn_up, ffn_conv=ffn_conv, ffn_down=ffn_down)
    st = dict(cmp=cache_cmp_kv, slc=cache_slc_kv, win=cache_win_kv, wkv=state_rwkv_wkv,
              shift=state_rwkv_shift, conv=state_conv, ffn=state_ffn_conv, page_table=page_table)
    y_prompt, (cmp_p, slc_p, win_p, wkv_p, sh_p, conv_p, ffn_p) = trunk(x_prompt, P, None)
    y_sample, (cmp_s, slc_s, win_s, wkv_s, sh_s, conv_s, ffn_s) = trunk(x_sample, P, st)
    return (y_prompt, y_sample, cmp_p, cmp_s, slc_p, slc_s, win_p, win_s, wkv_p, wkv_s,
            sh_p, sh_s, conv_p, conv_s, ffn_p, ffn_s)


_drawn_inputs = setup_inputs


def setup_inputs(seed=0):
    import zlib

    import numpy as np

    out = dict(_drawn_inputs(seed))
    spreads = {}
    factors = {'q_norm': 8.0, 'rwkv_w2': 8.0, 'rwkv_ln_b': 4.554}
    for name, (base, spread) in spreads.items():
        noise = np.random.default_rng([zlib.crc32(name.encode()), seed]).standard_normal(out[name].shape)
        drawn = base * np.exp(spread * noise) if base else spread * noise
        out[name] = jnp.asarray(drawn.astype(out[name].dtype))
    for name, factor in factors.items():
        out[name] = (out[name] * factor).astype(out[name].dtype)
    return out
```

```python
import concourse.bass as bass
from concourse import mybir
import numpy as np
import math
from contextlib import ExitStack

F32 = mybir.dt.float32
F32R = mybir.dt.float32r
I32 = mybir.dt.int32
ALU = mybir.AluOpType
ACT = mybir.ActivationFunctionType
AX = mybir.AxisListType

D = 1024
KT = D // 128
TP = 512
NB, TS = 8, 8
NS = NB * TS
T = TP + NS
HT = T // 2
TPAD = 640
DFF = 2816
FT = DFF // 128
HD = 64
NH = 8
W_NSA = 1304
W_RW = 1792
RT = W_RW // 128
SLAB = 2048
EPS = 1e-6
GN_EPS = 64e-5
NEG = -1e30
FLOOR = -1e25
CH = 64
PAGE = 128
NBK = 32
RVL = 1168
RV0 = 638
BTW = 1040

V_MIX, V_FFN, V_CONV, V_MU, V_W0, V_A0, V_KK, V_KA, V_RK, V_ROWS = 0, 16, 32, 56, 70, 74, 78, 82, 86, 90


def tables():
    dist = RV0 - np.arange(RVL)
    n = np.maximum(dist, 0)
    nf = np.maximum(n, 1).astype(np.float32)
    large = 16 + (np.log(nf / np.float32(16)) / np.float32(math.log(8.0)) * np.float32(16)).astype(np.int32)
    bucket = np.where(n < 16, n, np.minimum(large, 31))
    onehot = (bucket[None, :] == np.arange(NBK)[:, None]).astype(np.float32)
    masked = np.broadcast_to(np.where(dist >= 0, 0.0, NEG).astype(np.float32)[None, :], (NH, RVL)).copy()
    s = np.arange(CH)
    strict, incl = s[:, None] < s[None, :], s[:, None] <= s[None, :]
    same = (s[:, None] // TS) == (s[None, :] // TS)
    def gmask(m):
        return np.block([[strict & m, incl & m], [strict & m, incl & m]])
    gm = np.stack([gmask(np.ones((CH, CH), bool)), gmask(same)], 1).astype(np.float32)
    blk = (s[:, None] // 16) == (s[None, :] // 16)
    up = np.stack([strict & blk, strict & ~blk, strict & blk & same, strict & ~blk & same], 1)
    lo = np.stack([strict.T & blk, strict.T & ~blk, strict.T & blk & same, strict.T & ~blk & same], 1)
    inv = np.stack([up, lo], 1).astype(np.float32)
    keep = np.ones((128, T), np.float32)
    keep[:, 0:TP:CH] = 0.0
    keep[:, TP::TS] = 0.0
    seq = ((np.arange(128)[:, None] % CH) // TS == np.arange(NB)[None, :]).astype(np.float32)
    head = np.zeros((128, 128), np.float32)
    head[:64, :64] = 1.0
    head[64:, 64:] = 1.0
    row = np.arange(128)
    wmask = np.where(np.arange(TS)[None, :] <= (row % TS)[:, None], NEG, 0.0).astype(np.float32)
    return dict(onehot=onehot, masked=masked, gmask=gm, invmask=inv, keep=keep, seqmask=seq,
                headones=head, ident=np.eye(128, dtype=np.float32),
                flip=np.eye(128, dtype=np.float32)[::-1].copy(), wmask=wmask)



class Chain:

    def __init__(self, sem):
        self.sem, self.n, self.loop = sem, 0, None

    def __call__(self, eng, ins):
        ins.then_inc(self.sem, 1)
        self.n += 1
        if self.loop is None:
            eng.wait_ge(self.sem, self.n)
        else:
            i, start, per, _ = self.loop
            eng.wait_ge(self.sem, i * per + self.n)
        return ins

    def begin(self, i, per, trips):
        self.loop = (i, self.n, per, trips)

    def end(self):
        i, start, per, trips = self.loop
        assert self.n - start == per, (self.n - start, per)
        self.n = start + per * trips
        self.loop = None


def build(nc, a, o, k):
    ctx = ExitStack()
    base = [nc.sbuf_base + (-nc.sbuf_base) % 64]
    names = [0]

    def at(name, shape, dt, offset):
        names[0] += 1
        return nc.alloc_sbuf_tensor_at(f"{name}_{names[0]}", shape, dt, offset=offset)

    def fixed(name, shape, dt=F32):
        size = 4 * int(np.prod(shape[1:]))
        t = at(name, shape, dt, base[0])
        base[0] += size + (-size) % 32
        return t

    sems = {}

    lasting = []

    def sem(name):
        if name not in sems:
            sems[name] = nc.alloc_semaphore(name)
        return sems[name]

    def keep_semaphores():
        lasting[:] = list(sems)

    def retire_semaphores():
        old = [sems.pop(name) for name in list(sems) if name not in lasting]
        nc.clear_and_free_semaphores(old)
        nc.all_engine_barrier()

    with ctx:
        ctx.enter_context(nc.allow_non_contiguous_dma(reason="small tables"))
        raw = [fixed(f"w_raw{s}", [128, SLAB]) for s in range(2)]
        whi = [fixed(f"w_hi{s}", [128, SLAB], F32R) for s in range(2)]
        wlo = [fixed(f"w_lo{s}", [128, SLAB], F32R) for s in range(2)]
        xT = fixed("xT", [128, KT, T])
        ident = fixed("ident", [128, 128])
        ones = fixed("ones", [128, 128])
        vec = fixed("vec", [128, V_ROWS])
        ffnw = fixed("ffnw", [128, 2, 3, FT])
        convst = fixed("convst", [128, NB, 2, KT])
        ffnst = fixed("ffnst", [128, 2, NB, 2, FT])
        newconv = fixed("newconv", [128, 9, 2, KT])
        newffn = fixed("newffn", [128, 9, 2, FT])
        zlast = fixed("zlast", [128, 9, RT])
        R = base[0]
        END = nc.sbuf_usable_end

        class Region:
            def __init__(self, start):
                self.at = start

            def take(self, name, shape, dt=F32):
                size = 4 * int(np.prod(shape[1:]))
                t = at(name, shape, dt, self.at)
                self.at += size + (-size) % 32
                assert self.at <= END, (name, self.at - END)
                return t

        ps = ctx.enter_context(nc.psum_tensor("ps", [128, 8, 512], F32))
        rv_dram = nc.dram_tensor("rv", (NH, RVL), F32, kind="Internal").ap()
        gate_dram = nc.dram_tensor("gates", (NS, 24), F32, kind="Internal").ap()

        w_in, w_out = a["w_in_even"][0], a["w_out_even"][0]
        w_in_odd, w_out_odd = a["w_in_odd"][0], a["w_out_odd"][0]

        def cols(w, kt0, kts, c0, width):
            return w.rearrange("(t p) n -> p t n", p=128)[:, kt0:kt0 + kts, bass.ds(c0, width)]

        stages = []
        n_slabs = [0]
        bank_uses = [0, 0]

        def stage(n, kts, width, src):
            st = dict(base=n_slabs[0], n=n, kts=kts, width=width, src=src, before=tuple(bank_uses))
            n_slabs[0] += n
            bank_uses[0] += (n + 1) // 2
            bank_uses[1] += n // 2
            stages.append(st)
            return st

        st_nsa = stage(5, KT, 256, lambda s: cols(w_in, 0, KT, 256 * s, 256))
        st_gate = stage(1, KT, 24, lambda s: cols(w_in, 0, KT, 1280, 24))
        st_rw = stage(7, KT, 256, lambda s: cols(w_in, 0, KT, W_NSA + 256 * s, 256))
        st_out = stage(4, KT, 256, lambda s: cols(w_out, 0, KT, 256 * s, 256))

        def ffn_stages(l):
            out = []
            up, down = a["ffn_up"][l], a["ffn_down"][l]
            for f0, nf in ((0, 12), (12, 10)):
                def src_up(s, f0=f0, side=None):
                    return cols(up, 0, KT, side * DFF + 128 * f0 + 256 * s, 256)
                out.append((stage(nf, KT, 256, src_up), stage(8, nf, 128, lambda s, f0=f0, nf=nf: cols(down, f0, nf, 128 * s, 128)), f0, nf))
            return out

        ffn0 = ffn_stages(0)
        st_odd = stage(12, KT, 256, None)
        st_oout = stage(4, KT, 256, lambda s: cols(w_out_odd, 0, KT, 256 * s, 256))
        ffn1 = ffn_stages(1)

        def stage_at(g):
            for st in stages:
                if st["base"] <= g < st["base"] + st["n"]:
                    return st
            return None

        def slab_source(st, p, q, m):
            if st is st_odd:
                return cols(w_in_odd, 0, KT, (D, 2 * D, 0)[q % 3] + 256 * (p * (m // 3) + q // 3), 256)
            if st["n"] in (12, 10) and st is not st_odd:
                return st["src"](p * (m // 2) + q // 2, side=q % 2)
            return st["src"](p * m + q)

        def slab_view(t, st):
            return t[:, 0:st["kts"] * st["width"]]

        w_loaded = [sem("w_loaded0"), sem("w_loaded1")]
        w_hi_ready, w_lo_ready, slab_done = sem("w_hi_ready"), sem("w_lo_ready"), sem("slab_done")
        banks_free = [sem("banks_free_low"), sem("banks_free_high")]

        def load_slab(sp, st, p, q, m):
            g = st["base"] + p * m + q
            slot = (st["base"] + q) % 2
            if st["base"] + q >= 2:
                sp.wait_ge(w_lo_ready, g - 1)
            view = slab_view(raw[slot], st).rearrange("p (t n) -> p t n", t=st["kts"])
            sp.dma_start(view, slab_source(st, p, q, m)).then_inc(w_loaded[slot], 16)

        def slot_count(st, p, q, m):
            return 16 * ((st["base"] + q) // 2 + 1) + p * (8 * m)

        def split_hi(act, st, p, q, m):
            g = st["base"] + p * m + q
            slot = (st["base"] + q) % 2
            act.wait_ge(w_loaded[slot], slot_count(st, p, q, m))
            if st["base"] + q >= 2:
                act.wait_ge(slab_done, g - 1)
            act.activation(slab_view(whi[slot], st), slab_view(raw[slot], st), ACT.Copy).then_inc(w_hi_ready, 1)

        def split_lo(pool, st, p, q, m):
            g = st["base"] + p * m + q
            slot = (st["base"] + q) % 2
            pool.wait_ge(w_hi_ready, g + 1)
            pool.tensor_tensor(slab_view(wlo[slot], st), slab_view(raw[slot], st),
                               slab_view(whi[slot], st).bitcast(F32), ALU.subtract).then_inc(w_lo_ready, 1)

        def follow(g):
            st = stage_at(g)
            return None if st is None else (st, 0, g - st["base"], st_period(st))

        def st_period(st):
            return 12 if st is st_odd else 16

        def loads_after(sp, g):
            for x in (g, g + 1):
                f = follow(x)
                if f is not None:
                    load_slab(sp, *f)

        def wait_banks(pe, st, p, q, m):
            pe.wait_ge(banks_free[q % 2], st["before"][q % 2] + q // 2 + 1 + p * (m // 2))

        def products(pe, st, p, q, m, bank, xs, xhi, xlo):
            g = st["base"] + p * m + q
            slot = (st["base"] + q) % 2
            wait_banks(pe, st, p, q, m)
            pe.wait_ge(w_lo_ready, g + 1)
            W = st["width"]
            for j in range(W // 128):
                for t in range(st["kts"]):
                    c = t * W + j * 128
                    for n, (w, x) in enumerate(((whi, xhi), (whi, xlo), (wlo, xhi))):
                        for half in range(2):
                            last = pe.matmul(ps[:, bank + 2 * j + half, 0:HT], w[slot][:, c:c + 128],
                                             x[:, xs + t, half * HT:(half + 1) * HT],
                                             start=(t == 0 and n == 0), stop=(t == st["kts"] - 1 and n == 2))
            last.then_inc(slab_done, 1)

        tmp = Region(R)
        xin = tmp.take("xin", [128, 5, D])
        rows = [tmp.take("rows_vec", [V_ROWS, 128]), tmp.take("rows_f0", [66, 128]), tmp.take("rows_f1", [66, 128]),
                tmp.take("rows_conv", [128, 128])]
        rows_st = [[tmp.take(f"rows_st{l}{n}", [88, 128]) for n in range(4)] for l in range(2)]
        x_in, x_tiles = sem("x_in"), sem("x_tiles")
        small_in, small_t = sem("small_in"), sem("small_t")
        start_ev, small_ev = sem("start_ev"), sem("small_ev")
        consts_in = sem("consts_in")
        dve_chain, act_chain, pool_chain = Chain(sem("dve_chain")), Chain(sem("act_chain")), Chain(sem("pool_chain"))
        ones_set = sem("ones_set")

        jobs = [(rows[0], V_ROWS, vec[:, :]), (rows[1], 66, ffnw[:, 0, :, :]), (rows[2], 66, ffnw[:, 1, :, :]),
                (rows[3], 128, convst[:, :, :, :])]
        for l in range(2):
            for n in range(4):
                jobs.append((rows_st[l][n], 88, ffnst[:, l, 2 * n:2 * n + 2, :, :]))

        def flat(t):
            n = len(t.shape)
            if n == 2:
                return t
            pat = {3: "p a b -> p (a b)", 4: "p a b c -> p (a b c)", 5: "p a b c d -> p (a b c d)"}[n]
            return t.rearrange(pat)

        ext_ready, conv_done, gate_ready = sem("ext_ready"), sem("conv_done"), sem("gate_ready")
        g_f, g_hi_ready, g_lo_ready = sem("g_f"), sem("g_hi_ready"), sem("g_lo_ready")
        with nc.Block() as block:
            @block.sync
            def _(sp):
                sp.dma_start(ident[:, :], k["ident"]).then_inc(consts_in, 16)
                for t in range(4):
                    sp.dma_start(xin[:, t, :], a["x_prompt"][0, 128 * t:128 * t + 128, :]).then_inc(x_in, 16)
                sp.dma_start(xin[0:NS, 4, :], a["x_sample"].rearrange("b t d -> (b t) d")).then_inc(x_in, 16)
                loads_after(sp, 0)

                def row_load(dst, src):
                    sp.dma_start(dst, src).then_inc(small_in, 16)
                v = rows[0]
                row_load(v[V_MIX:V_MIX + 16, :], a["norm_mix"].rearrange("l (c p) -> (l c) p", p=128))
                row_load(v[V_FFN:V_FFN + 16, :], a["norm_ffn"].rearrange("l (c p) -> (l c) p", p=128))
                row_load(v[V_CONV:V_CONV + 24, :], a["conv_w"][0].rearrange("k (c p) -> (k c) p", p=128))
                row_load(v[V_MU:V_MU + 14, :], a["rwkv_mu"].rearrange("l (c p) -> (l c) p", p=128))
                for at_, name in ((V_W0, "rwkv_w0"), (V_A0, "rwkv_a0"), (V_KK, "rwkv_kk"), (V_KA, "rwkv_ka")):
                    row_load(v[at_:at_ + 4, :], a[name].rearrange("l (c p) -> (l c) p", p=128))
                row_load(v[V_RK:V_RK + 4, :], a["rwkv_rk"][0].rearrange("(c h) d -> c (h d)", h=2))
                for l in range(2):
                    row_load(rows[1 + l][:, :], a["ffn_conv"][l].rearrange("k (c p) -> (k c) p", p=128))
                row_load(rows[3][:, :], a["state_conv"][:, 0].rearrange("b k (c p) -> (b k c) p", p=128))
                for l in range(2):
                    for n in range(4):
                        for h in range(2):
                            row_load(rows_st[l][n][44 * h:44 * h + 44, :],
                                     a["state_ffn_conv"][2 * n + h, l].rearrange("k (c p) -> (k c) p", p=128))

            @block.vector
            def _(dve):
                dve.memset(ones[:, :], 1.0).then_inc(ones_set, 1)
                for s in banks_free:
                    dve.nop().then_inc(s, 1)
                for s in (ext_ready, conv_done, gate_ready, g_f, g_hi_ready, g_lo_ready):
                    dve.nop().then_inc(s, 2)
                for n in range(10):
                    dve.wait_ge(x_tiles, n + 1)
                    t, c = n // 2, n % 2
                    w = 128 if t < 4 else NS
                    dve.tensor_copy(xT[:, 4 * c:4 * c + 4, 128 * t:128 * t + w],
                                    ps[:, n % 4, :].rearrange("p (c t) -> p c t", c=4)[:, :, 0:w]).then_inc(start_ev, 1)

            @block.scalar
            def _(act):
                split_hi(act, *follow(0))
                for n, (src, r, dst) in enumerate(jobs):
                    act.wait_ge(small_t, n + 1)
                    act.copy(flat(dst), ps[:, 4 + n % 4, 0:r]).then_inc(small_ev, 1)

            @block.gpsimd
            def _(pool):
                split_lo(pool, *follow(0))

            @block.tensor
            def _(pe):
                pe.wait_ge(consts_in, 16)
                pe.wait_ge(x_in, 80)
                for n in range(10):
                    t, c = n // 2, n % 2
                    w = 128 if t < 4 else NS
                    if n >= 4:
                        pe.wait_ge(start_ev, n - 3)
                    for q in range(4):
                        last = pe.transpose(ps[:, n % 4, 128 * q:128 * q + w],
                                            xin[0:w, t, (4 * c + q) * 128:(4 * c + q + 1) * 128], ident[0:w, 0:w])
                    last.then_inc(x_tiles, 1)
                pe.wait_ge(small_in, 16 * (9 + 2 + 1 + 16))
                for n, (src, r, dst) in enumerate(jobs):
                    if n >= 4:
                        pe.wait_ge(small_ev, n - 3)
                    pe.transpose(ps[:, 4 + n % 4, 0:r], src[:, :], ident[0:r, 0:r]).then_inc(small_t, 1)

        sq_ready, sq_used, ms_ready = sem("sq_ready"), sem("sq_used"), sem("ms_ready")
        std_ready, h_f, h_hi_ready, h_lo_ready, ms_used = sem("std_ready"), sem("h_f"), sem("h_hi_ready"), sem("h_lo_ready"), sem("ms_used")
        norms = [0]

        def norm(gain, hhi, hlo, region):
            reg = Region(region)
            sq = reg.take("sq", [128, 2, T])
            hf = reg.take("hf", [128, 2, T])
            std = reg.take("std", [128, T])
            rstd = reg.take("rstd", [128, T])
            i0 = norms[0]
            norms[0] += 1
            b0 = 8 * i0
            with nc.Block() as block:
                @block.scalar
                def _(act):
                    for c in range(KT):
                        if b0 + c >= 2:
                            act.wait_ge(sq_used, b0 + c - 1)
                        act.activation(sq[:, c % 2, :], xT[:, c, :], ACT.Square).then_inc(sq_ready, 1)
                    act.wait_ge(ms_used, i0 + 1)
                    act.activation(std[:, :], std[:, :], ACT.Sqrt).then_inc(std_ready, 1)
                    for c in range(KT):
                        act.wait_ge(h_f, b0 + c + 1)
                        act.copy(hhi[:, c, 0:T], hf[:, c % 2, :]).then_inc(h_hi_ready, 1)

                @block.tensor
                def _(pe):
                    for c in range(KT):
                        pe.wait_ge(sq_ready, b0 + c + 1)
                        for half in range(2):
                            last = pe.matmul(ps[:, half, 0:HT], ones[:, :], sq[:, c % 2, half * HT:(half + 1) * HT],
                                             start=(c == 0), stop=(c == KT - 1))
                        last.then_inc(sq_used, 1)

                @block.vector
                def _(dve):
                    dve.wait_ge(sq_used, b0 + KT)
                    dve.tensor_scalar(std[:, :].rearrange("p (a t) -> p a t", a=2), ps[:, 0:2, 0:HT],
                                      1.0 / D, EPS, ALU.mult, ALU.add).then_inc(ms_used, 1)
                    dve.wait_ge(std_ready, i0 + 1)
                    dve_chain(dve, dve.reciprocal(rstd[:, :], std[:, :]))
                    for c in range(KT):
                        if c >= 2:
                            dve.wait_ge(h_lo_ready, b0 + c - 1)
                        dve.scalar_tensor_tensor(hf[:, c % 2, :], xT[:, c, :], vec[:, gain + c:gain + c + 1], rstd[:, :],
                                                 ALU.mult, ALU.mult).then_inc(h_f, 1)

                @block.gpsimd
                def _(pool):
                    for c in range(KT):
                        pool.wait_ge(h_hi_ready, b0 + c + 1)
                        pool.tensor_tensor(hlo[:, c, 0:T], hf[:, c % 2, :], hhi[:, c, 0:T].bitcast(F32),
                                           ALU.subtract).then_inc(h_lo_ready, 1)

        def residual(st, hhi, hlo):
            n, base_g, J = st["n"], st["base"], st["width"] // 128
            with nc.Block() as block:
                @block.sync
                def _(sp):
                    with sp.Fori(0, (n - 2) // 2) as i:
                        for q in (2, 3):
                            load_slab(sp, st, i, q, 2)
                    loads_after(sp, base_g + n)

                @block.scalar
                def _(act):
                    with act.Fori(0, (n - 2) // 2) as i:
                        for q in (1, 2):
                            split_hi(act, st, i, q, 2)
                    split_hi(act, st, (n - 2) // 2, 1, 2)
                    if follow(base_g + n):
                        split_hi(act, *follow(base_g + n))

                @block.gpsimd
                def _(pool):
                    with pool.Fori(0, (n - 2) // 2) as i:
                        for q in (1, 2):
                            split_lo(pool, st, i, q, 2)
                    split_lo(pool, st, (n - 2) // 2, 1, 2)
                    if follow(base_g + n):
                        split_lo(pool, *follow(base_g + n))

                @block.tensor
                def _(pe):
                    with pe.Fori(0, n // 2) as i:
                        for q in (0, 1):
                            products(pe, st, i, q, 2, 4 * q, 0, hhi, hlo)

                @block.vector
                def _(dve):
                    with dve.Fori(0, n // 2) as i:
                        for q in (0, 1):
                            dve.wait_ge(slab_done, base_g + 2 * i + q + 1)
                            for j in range(J):
                                x = xT[:, bass.ds(2 * J * i + J * q + j, 1), :].rearrange("p o (a t) -> p (o a) t", a=2)
                                b = 4 * q + 2 * j
                                last = dve.tensor_tensor(x, ps[:, b:b + 2, 0:HT], x, ALU.add)
                            last.then_inc(banks_free[q], 1)

        EW = 2 + TP + NB * (TS + 2)
        YW = EW - 2

        def prompt_of(t):
            return t[:, 2:2 + TP]

        def sample_of(t):
            return t[:, 2 + TP:EW].rearrange("p (b t) -> p b t", b=NB)

        zeroed = sem("zeroed")
        gates_done = [2]
        tiles_done = [2]
        zero_count = [0]
        H1 = TP - HT

        def gated_mult(dve, out, y, bank):
            dve.tensor_tensor(out[:, 0:HT], y[:, 0:HT], ps[:, bank, 0:HT], ALU.mult)
            dve.tensor_tensor(out[:, HT:TP], y[:, HT:TP], ps[:, bank + 1, 0:H1], ALU.mult)
            ys = y[:, TP + 2:TP + 2 + NB * 10].rearrange("p (b t) -> p b t", b=NB)[:, :, 0:TS]
            return dve.tensor_tensor(out[:, TP:T].rearrange("p (b t) -> p b t", b=NB), ys,
                                     ps[:, bank + 1, H1:HT].rearrange("p (b t) -> p b t", b=NB), ALU.mult)

        def convolve(dve, y, ext, w):
            dve_chain(dve, dve.tensor_scalar(y[:, 0:YW], ext[:, 0:YW], w(0), None, ALU.mult))
            dve_chain(dve, dve.scalar_tensor_tensor(y[:, 0:YW], ext[:, 1:1 + YW], w(1), y[:, 0:YW], ALU.mult, ALU.add))
            return dve.scalar_tensor_tensor(y[:, 0:YW], ext[:, 2:2 + YW], w(2), y[:, 0:YW], ALU.mult, ALU.add)

        def keep_last(dve, new, f, ext):
            dve.tensor_copy(new[:, 0, :, bass.ds(f, 1)], ext[:, TP:TP + 2].rearrange("p (k o) -> p k o", o=1))
            dve.tensor_copy(new[:, 1:9, :, bass.ds(f, 1)].rearrange("p b k o -> p b (k o)"), sample_of(ext)[:, :, TS:TS + 2])

        def ffn_up(l, st, f0, hhi, hlo, ghi, glo, reg):
            ext = [reg.take("ext", [128, EW]) for _ in range(2)]
            y = [reg.take("y", [128, EW]) for _ in range(2)]
            gf = [reg.take("gf", [128, T]) for _ in range(2)]
            n, G, t0 = st["n"], st["base"], tiles_done[0]
            pairs = n // 2
            tg = gates_done[0]
            gates_done[0] += n
            tiles_done[0] += n
            zero_count[0] += 2
            zc = zero_count[0]
            with nc.Block() as block:
                @block.sync
                def _(sp):
                    with sp.Fori(0, pairs - 1) as i:
                        for q in (2, 3):
                            load_slab(sp, st, i, q, 2)
                    loads_after(sp, G + n)

                @block.gpsimd
                def _(pool):
                    def pair(i, nxt):
                        split_lo(pool, st, i, 1, 2)
                        split_lo(pool, *nxt)
                        for j in range(2):
                            pool.wait_ge(g_hi_ready, t0 + 2 * i + j + 1)
                            pool.tensor_tensor(glo[:, bass.ds(2 * i + j, 1), :], gf[j][:, :].rearrange("p (o t) -> p o t", o=1),
                                               ghi[:, bass.ds(2 * i + j, 1), :].bitcast(F32), ALU.subtract).then_inc(g_lo_ready, 1)
                    with pool.Fori(0, pairs - 1) as i:
                        pair(i, (st, i, 2, 2))
                    pair(pairs - 1, follow(G + n))

                @block.scalar
                def _(act):
                    def pair(i, nxt):
                        split_hi(act, st, i, 1, 2)
                        act.wait_ge(slab_done, G + 2 * i + 1)
                        for j in range(2):
                            act.wait_ge(conv_done, t0 + 2 * i + j - 1)
                            e = ext[j]
                            act.copy(e[:, 2:2 + HT], ps[:, 2 * j, 0:HT])
                            act.copy(e[:, 2 + HT:2 + TP], ps[:, 2 * j + 1, 0:H1])
                            act.copy(sample_of(e)[:, :, 0:2], ffnst[:, l, :, :, bass.ds(f0 + 2 * i + j, 1)].rearrange("p b k o -> p b (k o)"))
                            last = act.copy(sample_of(e)[:, :, 2:2 + TS],
                                            ps[:, 2 * j + 1, H1:HT].rearrange("p (b t) -> p b t", b=NB)).then_inc(ext_ready, 1)
                        act.wait_ge(ext_ready, tg + 2 * i + 2)
                        act.nop().then_inc(banks_free[0], 1)
                        for j in range(2):
                            act.wait_ge(conv_done, t0 + 2 * i + j + 1)
                            act.activation(y[j][:, 0:YW], y[j][:, 0:YW], ACT.Silu).then_inc(gate_ready, 1)
                        split_hi(act, *nxt)
                        for j in range(2):
                            act.wait_ge(g_f, t0 + 2 * i + j + 1)
                            act.copy(ghi[:, bass.ds(2 * i + j, 1), :], gf[j][:, :].rearrange("p (o t) -> p o t", o=1)).then_inc(g_hi_ready, 1)
                    act.wait_ge(zeroed, zc)
                    with act.Fori(0, pairs - 1) as i:
                        pair(i, (st, i, 2, 2))
                    pair(pairs - 1, follow(G + n))

                @block.tensor
                def _(pe):
                    with pe.Fori(0, pairs) as i:
                        for q in (0, 1):
                            products(pe, st, i, q, 2, 4 * q, 0, hhi, hlo)

                @block.vector
                def _(dve):
                    for e in ext:
                        dve.memset(e[:, 0:2], 0.0).then_inc(zeroed, 1)
                    with dve.Fori(0, pairs) as i:
                        dve_chain.begin(i, 4, pairs)
                        for j in range(2):
                            dve.wait_ge(ext_ready, tg + 2 * i + j + 1)
                            f = f0 + 2 * i + j
                            keep_last(dve, newffn, f, ext[j])
                            convolve(dve, y[j], ext[j], lambda kk: ffnw[:, l, kk, bass.ds(f, 1)]).then_inc(conv_done, 1)
                        dve.wait_ge(slab_done, G + 2 * i + 2)
                        for j in range(2):
                            dve.wait_ge(gate_ready, tg + 2 * i + j + 1)
                            dve.wait_ge(g_lo_ready, t0 + 2 * i + j - 1)
                            last = gated_mult(dve, gf[j], y[j], 4 + 2 * j)
                            last.then_inc(g_f, 1)
                        dve.wait_ge(g_f, t0 + 2 * i + 2)
                        dve.nop().then_inc(banks_free[1], 1)
                        dve_chain.end()

        st_out_sem, st_t, st_ev = sem("state_out"), sem("state_t"), sem("state_ev")
        st_n, st_dma = [0], [0]

        def flush(groups, reg):
            bufs = [reg.take("rows", [128, 128]) for _ in groups]
            n0 = st_n[0]
            st_n[0] += len(groups)
            with nc.Block() as block:
                @block.tensor
                def _(pe):
                    for n, (src, r, _) in enumerate(groups):
                        if n >= 4:
                            pe.wait_ge(st_ev, n0 + n - 3)
                        pe.transpose(ps[0:r, n % 4, 0:128], src, ident[:, :]).then_inc(st_t, 1)

                @block.scalar
                def _(act):
                    for n, (src, r, _) in enumerate(groups):
                        act.wait_ge(st_t, n0 + n + 1)
                        act.copy(bufs[n][0:r, :], ps[0:r, n % 4, 0:128]).then_inc(st_ev, 1)

                @block.sync
                def _(sp):
                    for n, (src, r, outs) in enumerate(groups):
                        sp.wait_ge(st_ev, n0 + n + 1)
                        for lo, hi, dst in outs:
                            sp.dma_start(dst, bufs[n][lo:hi, :]).then_inc(st_out_sem, 16)
                            st_dma[0] += 16
                    sp.wait_ge(st_out_sem, st_dma[0])

        def ffn(l, stages_l, gain):
            reg = Region(R)
            hhi, hlo = reg.take("h_hi", [128, KT, T], F32R), reg.take("h_lo", [128, KT, T], F32R)
            ghi, glo = reg.take("g_hi", [128, 12, T], F32R), reg.take("g_lo", [128, 12, T], F32R)
            norm(gain, hhi, hlo, reg.at)
            for up, down, f0, nf in stages_l:
                r2 = Region(reg.at)
                ffn_up(l, up, f0, hhi, hlo, ghi, glo, r2)
                residual(down, ghi, glo)
            groups = [(flat(newffn[:, 0, :, :]), 44, [(0, 44, o["ffn_p"][0, l].rearrange("k (c p) -> (k c) p", p=128))])]
            for n in range(4):
                groups.append((flat(newffn[:, 1 + 2 * n:3 + 2 * n, :, :]), 88,
                               [(44 * h, 44 * h + 44, o["ffn_s"][2 * n + h, l].rearrange("k (c p) -> (k c) p", p=128)) for h in range(2)]))
            flush(groups, Region(reg.at))

        def conv_mixer():
            reg = Region(R)
            hhi, hlo = reg.take("h_hi", [128, KT, T], F32R), reg.take("h_lo", [128, KT, T], F32R)
            mhi, mlo = reg.take("m_hi", [128, KT, T], F32R), reg.take("m_lo", [128, KT, T], F32R)
            norm(V_MIX + 8, hhi, hlo, reg.at)
            cg = [reg.take("cg", [128, T]) for _ in range(2)]
            ext = [reg.take("ext", [128, EW]) for _ in range(2)]
            y = [reg.take("y", [128, EW]) for _ in range(2)]
            gf = [reg.take("gf", [128, T]) for _ in range(2)]
            st, G, t0 = st_odd, st_odd["base"], tiles_done[0]
            tiles_done[0] += 8
            zero_count[0] += 2
            zc = zero_count[0]
            cg_ready, u_done = sem("cg_ready"), sem("u_done")
            def tile(i, h, j):
                return 4 * i + 2 * h + j
            with nc.Block() as block:
                @block.sync
                def _(sp):
                    for q in range(2, 6):
                        load_slab(sp, st, 0, q, 6)
                    for q in range(6):
                        load_slab(sp, st, 1, q, 6)
                    loads_after(sp, G + 12)

                @block.gpsimd
                def _(pool):
                    def trip(i, last):
                        for h in range(2):
                            for q in range(3):
                                qq = 3 * h + q + 1
                                split_lo(pool, *(last if qq == 6 else (st, i, qq, 6)))
                            for j in range(2):
                                tt = tile(i, h, j)
                                pool.wait_ge(g_hi_ready, t0 + tt + 1)
                                pool.tensor_tensor(mlo[:, tt, :], gf[j][:, :], mhi[:, tt, :].bitcast(F32),
                                                   ALU.subtract).then_inc(g_lo_ready, 1)
                    trip(0, (st, 1, 0, 6))
                    trip(1, follow(G + 12))

                @block.scalar
                def _(act):
                    def trip(i, last):
                        for h in range(2):
                            qb = 6 * i + 3 * h
                            bank = [4 * ((3 * h + q) % 2) for q in range(3)]
                            split_hi(act, st, i, 3 * h + 1, 6)
                            act.wait_ge(slab_done, G + qb + 1)
                            if t0 + tile(i, h, 0) > t0:
                                act.wait_ge(u_done, tile(i, h, 0))
                            for j in range(2):
                                act.copy(cg[j][:, :].rearrange("p (a t) -> p a t", a=2),
                                         ps[:, bank[0] + 2 * j:bank[0] + 2 * j + 2, 0:HT]).then_inc(cg_ready, 1)
                            act.wait_ge(cg_ready, tile(i, h, 0) + 2)
                            act.nop().then_inc(banks_free[(3 * h) % 2], 1)
                            split_hi(act, st, i, 3 * h + 2, 6)
                            split_hi(act, *(last if h == 1 else (st, i, 3, 6)))
                            for j in range(2):
                                tt = tile(i, h, j)
                                act.wait_ge(g_f, t0 + tt + 1)
                                act.copy(mhi[:, tt, :], gf[j][:, :]).then_inc(g_hi_ready, 1)
                    trip(0, (st, 1, 0, 6))
                    trip(1, follow(G + 12))

                @block.tensor
                def _(pe):
                    for i in range(2):
                        for q in range(6):
                            products(pe, st, i, q, 6, 4 * (q % 2), 0, hhi, hlo)

                @block.vector
                def _(dve):
                    for e in ext:
                        dve.memset(e[:, 0:2], 0.0).then_inc(zeroed, 1)
                    dve.wait_ge(zeroed, zc)
                    for i in range(2):
                        for h in range(2):
                            b = [4 * ((3 * h + q) % 2) for q in range(3)]
                            dve.wait_ge(cg_ready, tile(i, h, 0) + 2)
                            dve.wait_ge(slab_done, G + 6 * i + 3 * h + 2)
                            for j in range(2):
                                f = tile(i, h, j)
                                e, bk = ext[j], b[1] + 2 * j
                                dve.tensor_tensor(e[:, 2:2 + HT], cg[j][:, 0:HT], ps[:, bk, 0:HT], ALU.mult)
                                dve.tensor_tensor(e[:, 2 + HT:2 + TP], cg[j][:, HT:TP], ps[:, bk + 1, 0:H1], ALU.mult)
                                dve.tensor_copy(sample_of(e)[:, :, 0:2], convst[:, :, :, f])
                                dve.tensor_tensor(sample_of(e)[:, :, 2:2 + TS], cg[j][:, TP:T].rearrange("p (b t) -> p b t", b=NB),
                                                  ps[:, bk + 1, H1:HT].rearrange("p (b t) -> p b t", b=NB), ALU.mult).then_inc(u_done, 1)
                            dve.wait_ge(u_done, tile(i, h, 0) + 2)
                            dve.nop().then_inc(banks_free[(3 * h + 1) % 2], 1)
                            for j in range(2):
                                f = tile(i, h, j)
                                keep_last(dve, newconv, f, ext[j])
                                convolve(dve, y[j], ext[j], lambda kk: vec[:, V_CONV + 8 * kk + f:V_CONV + 8 * kk + f + 1]).then_inc(conv_done, 1)
                            dve.wait_ge(conv_done, t0 + tile(i, h, 0) + 2)
                            dve.wait_ge(slab_done, G + 6 * i + 3 * h + 3)
                            for j in range(2):
                                f = tile(i, h, j)
                                dve.wait_ge(g_lo_ready, t0 + f - 1)
                                gated_mult(dve, gf[j], y[j], b[2] + 2 * j).then_inc(g_f, 1)
                            dve.wait_ge(g_f, t0 + tile(i, h, 0) + 2)
                            dve.nop().then_inc(banks_free[(3 * h + 2) % 2], 1)
            residual(st_oout, mhi, mlo)
            groups = [(flat(newconv[:, 0, :, :]), 16, [(0, 16, o["conv_p"][0, 0].rearrange("k (c p) -> (k c) p", p=128))]),
                      (flat(newconv[:, 1:9, :, :]), 128, [(0, 128, o["conv_s"][:, 0].rearrange("b k (c p) -> (b k c) p", p=128))])]
            flush(groups, Region(reg.at))

        def store_y():
            reg = Region(R)
            yt = reg.take("yt", [128, 5, D])
            yt_t, yt_ev, y_out = sem("yt_t"), sem("yt_ev"), sem("y_out")
            with nc.Block() as block:
                @block.tensor
                def _(pe):
                    for n in range(10):
                        t, c = n // 2, n % 2
                        w = 128 if t < 4 else NS
                        if n >= 8:
                            pe.wait_ge(yt_ev, n - 7)
                        for q in range(4):
                            last = pe.transpose(ps[0:w, n % 8, 128 * q:128 * q + 128],
                                                xT[:, 4 * c + q, 128 * t:128 * t + w], ident[:, :])
                        last.then_inc(yt_t, 1)

                @block.vector
                def _(dve):
                    for n in range(10):
                        t, c = n // 2, n % 2
                        w = 128 if t < 4 else NS
                        dve.wait_ge(yt_t, n + 1)
                        dve.tensor_copy(yt[0:w, t, 512 * c:512 * c + 512], ps[0:w, n % 8, :]).then_inc(yt_ev, 1)

                @block.sync
                def _(sp):
                    for t in range(4):
                        sp.wait_ge(yt_ev, 2 * t + 2)
                        sp.dma_start(o["y_prompt"][0, 128 * t:128 * t + 128, :], yt[:, t, :]).then_inc(y_out, 16)
                    sp.wait_ge(yt_ev, 10)
                    sp.dma_start(o["y_sample"].rearrange("b t d -> (b t) d"), yt[0:NS, 4, :]).then_inc(y_out, 16)
                    sp.wait_ge(y_out, 80)

        def even_mixer():
            reg = Region(R)
            hhi, hlo = reg.take("h_hi", [128, KT, TPAD], F32R), reg.take("h_lo", [128, KT, TPAD], F32R)
            MIX = reg.at
            mixf = reg.take("mixf", [128, KT, T])
            zq = reg.take("zq", [128, 5, W_NSA])
            E0 = reg.at
            pad_zero = sem("pad_zero")
            with nc.Block() as block:
                @block.vector
                def _(dve):
                    dve.memset(hhi[:, :, T:TPAD].bitcast(F32), 0.0).then_inc(pad_zero, 1)
                    dve.memset(hlo[:, :, T:TPAD].bitcast(F32), 0.0).then_inc(pad_zero, 1)
            norm(V_MIX, hhi, hlo, E0)

            def products_tok(pe, st, p, q, m):
                g = st["base"] + p * m + q
                slot = (st["base"] + q) % 2
                wait_banks(pe, st, p, q, m)
                pe.wait_ge(w_lo_ready, g + 1)
                W = st["width"]
                for tok in range(5):
                    out = ps[:, 4 * (q % 2) + tok // 2, 256 * (tok % 2):256 * (tok % 2) + W]
                    for t in range(KT):
                        for n, (w, x) in enumerate(((whi, hhi), (whi, hlo), (wlo, hhi))):
                            last = pe.matmul(out, x[:, t, 128 * tok:128 * tok + 128], w[slot][:, t * W:t * W + W],
                                             start=(t == 0 and n == 0), stop=(t == KT - 1 and n == 2))
                last.then_inc(slab_done, 1)

            def take_tok(dve, st, p, q, m, c0):
                g = st["base"] + p * m + q
                W, b = st["width"], 4 * (q % 2)
                dve.wait_ge(slab_done, g + 1)
                dve.tensor_copy(zq[:, 0:4, bass.ds(c0, W)].rearrange("p (b u) c -> p b u c", u=2),
                                ps[:, b:b + 2, :].rearrange("p b (u c) -> p b u c", u=2)[:, :, :, 0:W])
                dve.tensor_copy(zq[:, 4, bass.ds(c0, W)], ps[:, b + 2, 0:W]).then_inc(banks_free[q % 2], 1)

            raw_out, zq_done = sem("raw_out"), sem("zq_done")
            with nc.Block() as block:
                @block.sync
                def _(sp):
                    for q in range(2, 5):
                        load_slab(sp, st_nsa, 0, q, 2)
                    load_slab(sp, st_gate, 0, 0, 2)
                    loads_after(sp, 6)

                @block.scalar
                def _(act):
                    for g in range(1, 7):
                        split_hi(act, *follow(g))

                @block.gpsimd
                def _(pool):
                    for g in range(1, 7):
                        split_lo(pool, *follow(g))

                @block.tensor
                def _(pe):
                    with pe.Fori(0, 2) as i:
                        for q in range(2):
                            products_tok(pe, st_nsa, i, q, 2)
                    products_tok(pe, st_nsa, 2, 0, 2)
                    products_tok(pe, st_gate, 0, 0, 2)

                @block.vector
                def _(dve):
                    with dve.Fori(0, 2) as i:
                        for q in range(2):
                            take_tok(dve, st_nsa, i, q, 2, 512 * i + 256 * q)
                    take_tok(dve, st_nsa, 2, 0, 2, 1024)
                    take_tok(dve, st_gate, 0, 0, 2, 1280)

            def kv_out(sp, c0, dst_p, dst_s, s):
                sp.dma_start(dst_p.rearrange("(t p) k g d -> p t (k g d)", p=128), zq[:, 0:4, c0:c0 + 256]).then_inc(s, 16)
                for b in range(NB):
                    sp.dma_start(dst_s[b], zq[TS * b:TS * b + TS, 4, c0:c0 + 256]).then_inc(s, 16)

            r = Region(E0)
            kcT = r.take("kcT", [128, 288])
            vc = r.take("vc", [128, 3, 128])
            E1 = r.at
            seg = [r.take("seg", [128, 16, 128]) for _ in range(2)]
            segr = at("seg_by_group", [128, 2, 16, HD], F32, MIX)
            KTc = r.take("segT", [128, 2, 8, 290])
            w1 = r.take("phi_w1", [128, 16, 128])
            w2 = r.take("phi_w2", [128, 2, HD])
            hid = r.take("hid", [128, 2, 288])
            pe_rows = r.take("pe_rows", [16, 2, 128])
            peT = r.take("peT", [128, 2, 16])
            pe_bias = r.take("pe_bias", [128, 2])
            kcn = r.take("kcn", [128, 3, 128])
            kcs = r.take("kcs", [128, 3, 2])
            gain_c = r.take("gain_c", [128, HD])
            pt = r.take("pt", [1, 32], I32)
            c_in, seg_in, seg_t, seg_ev, w1_in = sem("c_in"), [sem("seg_in0"), sem("seg_in1")], sem("seg_t"), sem("seg_ev"), sem("w1_in")
            hid_done, hid_ready, c_done, peb_ps, peb_ready, kc_ready, kc_t = (sem(x) for x in (
                "hid_done", "hid_ready", "c_done", "peb_ps", "peb_ready", "kc_ready", "kc_t"))
            n_pool = a["cache_cmp_kv"].shape[0]
            seg_r, kc_copied = sem("seg_r"), sem("kc_copied")
            kc_taken, vc_done, kc_sq, kc_ms = sem("kc_taken"), sem("vc_done"), sem("kc_sq"), sem("kc_ms")
            rows_of = (128, 128, 32)
            with nc.Block() as block:
                @block.sync
                def _(sp):
                    kv_out(sp, 512, o["cmp_p"][0, 0], o["cmp_s"][:, 0].rearrange("b t k g d -> b t (k g d)"), raw_out)
                    sp.dma_start(pt[:, :], a["page_table"].rearrange("(o b) n -> o (b n)", o=1)).then_inc(c_in, 16)
                    for kv in range(2):
                        sp.dma_start(w2[:, kv, :], a["phi_w2"][0, kv]).then_inc(c_in, 16)
                        sp.dma_start(pe_rows[:, kv, :], a["phi_pe"][0, kv].rearrange("(i j) d -> i (j d)", j=2)).then_inc(c_in, 16)
                    sp.dma_start(gain_c[:, :], bass.AP(a["k_norm"].tensor, a["k_norm"].offset, [[0, 128], [1, HD]])).then_inc(c_in, 16)
                    sp.wait_ge(c_in, 96)
                    for kv in range(2):
                        if kv == 1:
                            sp.wait_ge(hid_done, 2)
                        sp.dma_start(w1[:, :, :], a["phi_w1"][0, kv].rearrange("(i j) d e -> (j d) i e", j=2)).then_inc(w1_in, 16)
                        for st in range(3):
                            n = 3 * kv + st
                            if n >= 2:
                                sp.wait_ge(seg_r, n - 1)
                            if st == 2:
                                sp.wait_ge(raw_out, 16 * 9)
                                src = o["cmp_p"][0, 0, :, kv].rearrange("(m j) g d -> m j (g d)", j=16)
                                sp.dma_start(seg[n % 2][0:32, :, :], src).then_inc(seg_in[n % 2], 16)
                            else:
                                for b in range(16):
                                    page = sp.value_load(pt[0:1, 16 * st + b:16 * st + b + 1], min_val=0, max_val=n_pool - 1)
                                    src = a["cache_cmp_kv"][bass.ds(page, 1), 0, :, kv].rearrange("o (m j) g d -> (o m) j (g d)", j=16)
                                    sp.dma_start(seg[n % 2][8 * b:8 * b + 8, :, :], src).then_inc(seg_in[n % 2], 16)

                @block.tensor
                def _(pe):
                    pe.wait_ge(c_in, 96)
                    for kv in range(2):
                        pe.transpose(ps[:, 7, 16 * kv:16 * kv + 16], pe_rows[:, kv, :], ident[0:16, 0:16]).then_inc(peb_ps, 1)
                    for kv in range(2):
                        pe.wait_ge(w1_in, 16 * (kv + 1))
                        pe.wait_ge(peb_ready, 1)
                        if kv == 1:
                            pe.wait_ge(kc_copied, 1)
                        for i in range(16):
                            last = pe.matmul(ps[:, 7, 64 + kv:65 + kv], w1[:, i, :], peT[:, kv, i:i + 1], start=(i == 0), stop=(i == 15))
                        last.then_inc(peb_ps, 1)
                        for st in range(3):
                            n, rws = 3 * kv + st, rows_of[st]
                            pe.wait_ge(seg_r, n + 1)
                            for u in range(4):
                                e = 4 * n + u
                                if e >= 4:
                                    pe.wait_ge(seg_ev, e - 3)
                                gg, j0 = u // 2, 4 * (u % 2)
                                for jj in range(4):
                                    src = segr[0:rws, gg, 2 * (j0 + jj):2 * (j0 + jj) + 2, :].rearrange("p j d -> p (j d)")
                                    last = pe.transpose(ps[:, e % 4, 128 * jj:128 * jj + rws], src, ident[0:rws, 0:rws])
                                last.then_inc(seg_t, 1)
                        pe.wait_ge(seg_ev, 12 * (kv + 1))
                        for gg in range(2):
                            if kv == 1:
                                pe.wait_ge(hid_ready, gg + 1)
                            for i in range(16):
                                last = pe.matmul(ps[:, 4 + gg, 0:288], w1[:, i, :], KTc[:, gg, i % 8, i // 8:i // 8 + 288],
                                                 start=(i == 0), stop=(i == 15))
                            last.then_inc(hid_done, 1)
                        pe.wait_ge(hid_ready, 2 * (kv + 1))
                        if kv == 1:
                            pe.wait_ge(kc_taken, 1)
                        for nt in range(3):
                            for gg in range(2):
                                rws = rows_of[nt]
                                last = pe.matmul(ps[0:rws, 6, 128 * nt + 64 * gg:128 * nt + 64 * gg + 64],
                                                 hid[:, gg, 128 * nt:128 * nt + rws], w2[:, kv, :], start=True, stop=True)
                        last.then_inc(c_done, 1)
                        if kv == 0:
                            pe.wait_ge(kc_ready, 2)
                            for nt in range(3):
                                rws = rows_of[nt]
                                last = pe.transpose(ps[:, 7, 128 + 128 * nt:128 + 128 * nt + rws], kcn[0:rws, nt, :], ident[0:rws, 0:rws])
                            last.then_inc(kc_t, 1)

                @block.gpsimd
                def _(pool):
                    for kv in range(2):
                        for st in range(3):
                            n, rws = 3 * kv + st, rows_of[st]
                            loads = (16, 16, 1, 16, 16, 1)
                            pool.wait_ge(seg_in[n % 2], 16 * sum(loads[n % 2:n + 1:2]))
                            if n >= 1:
                                pool.wait_ge(seg_t, 4 * n)
                            pool.tensor_copy(segr[0:rws, :, :, :], seg[n % 2][0:rws, :, :].rearrange("p j (g d) -> p g j d", g=2)).then_inc(seg_r, 1)

                @block.scalar
                def _(act):
                    act.wait_ge(peb_ps, 2)
                    act.copy(peT[:, :, :], ps[:, 7, 0:32].rearrange("p (a b) -> p a b", a=2)).then_inc(peb_ready, 1)
                    for kv in range(2):
                        act.wait_ge(peb_ps, 3 + kv)
                        act.copy(pe_bias[:, kv:kv + 1], ps[:, 7, 64 + kv:65 + kv]).then_inc(act_chain.sem, 1)
                        act_chain.n += 1
                        act.wait_ge(act_chain.sem, act_chain.n)
                        for gg in range(2):
                            act.wait_ge(hid_done, 2 * kv + gg + 1)
                            if kv == 1:
                                act.wait_ge(c_done, 1)
                            act.activation(hid[:, gg, :], ps[:, 4 + gg, 0:288], ACT.Gelu_apprx_tanh, bias=pe_bias[:, kv:kv + 1]).then_inc(hid_ready, 1)
                        if kv == 0:
                            act.wait_ge(c_done, 1)
                            act.activation(kcn[:, 0:2, :], ps[:, 6, 0:256].rearrange("p (a b) -> p a b", a=2), ACT.Square)
                            act.activation(kcn[0:32, 2, :], ps[0:32, 6, 256:384], ACT.Square).then_inc(kc_sq, 1)
                            act.wait_ge(kc_ms, 1)
                            act.activation(kcs[:, 0:2, :], kcs[:, 0:2, :], ACT.Sqrt)
                            act.activation(kcs[0:32, 2, :], kcs[0:32, 2, :], ACT.Sqrt).then_inc(kc_sq, 1)

                @block.vector
                def _(dve):
                    dve.memset(KTc[:, :, :, 288:290], 0.0)
                    for kv in range(2):
                        for st in range(3):
                            rws = rows_of[st]
                            for u in range(4):
                                e = 12 * kv + 4 * st + u
                                dve.wait_ge(seg_t, e + 1)
                                if kv == 1 and st == 0 and u == 0:
                                    dve.wait_ge(hid_done, 2)
                                gg, j0 = u // 2, 4 * (u % 2)
                                dve.tensor_copy(KTc[:, gg, j0:j0 + 4, 128 * st:128 * st + rws],
                                                ps[:, e % 4, :].rearrange("p (j n) -> p j n", j=4)[:, :, 0:rws]).then_inc(seg_ev, 1)
                        dve.wait_ge(c_done, kv + 1)
                        if kv == 0:
                            dve.wait_ge(kc_sq, 1)
                            dve.tensor_reduce(kcs[:, 0:2, :], kcn[:, 0:2, :].rearrange("p n (g d) -> p n g d", g=2), AX.X, ALU.add)
                            dve_chain(dve, dve.tensor_reduce(kcs[0:32, 2, :], kcn[0:32, 2, :].rearrange("p (g d) -> p g d", g=2), AX.X, ALU.add))
                            dve.tensor_scalar(kcs[:, 0:2, :], kcs[:, 0:2, :], 1.0 / HD, EPS, ALU.mult, ALU.add)
                            dve.tensor_scalar(kcs[0:32, 2, :], kcs[0:32, 2, :], 1.0 / HD, EPS, ALU.mult, ALU.add).then_inc(kc_ms, 1)
                            dve.wait_ge(kc_sq, 2)
                            dve.reciprocal(kcs[:, 0:2, :], kcs[:, 0:2, :])
                            dve_chain(dve, dve.reciprocal(kcs[0:32, 2, :], kcs[0:32, 2, :]))
                            def scaled(rr, lo, hi):
                                nn = hi - lo
                                out = kcn[0:rr, lo:hi, :].rearrange("p n (g d) -> p (n g) d", g=2)
                                src = ps[0:rr, 6, 128 * lo:128 * hi].rearrange("p (n d) -> p n d", d=HD)
                                fac = kcs[0:rr, lo:hi, :].rearrange("p n (g o) -> p (n g) o", o=1).to_broadcast([rr, 2 * nn, HD])
                                dve_chain(dve, dve.tensor_tensor(out, src, fac, ALU.mult))
                                gn = gain_c[0:rr, :].rearrange("p (o d) -> p o d", o=1).to_broadcast([rr, 2 * nn, HD])
                                return dve.tensor_tensor(out, out, gn, ALU.mult)
                            scaled(128, 0, 2).then_inc(kc_ready, 1)
                            scaled(32, 2, 3).then_inc(kc_ready, 1)
                            dve.wait_ge(kc_ready, 2)
                            dve.nop().then_inc(kc_taken, 1)
                            dve.wait_ge(kc_t, 1)
                            dve.tensor_copy(kcT[:, :], ps[:, 7, 128:128 + 288]).then_inc(kc_copied, 1)
                        else:
                            dve.tensor_copy(vc[:, 0:2, :], ps[:, 6, 0:256].rearrange("p (a b) -> p a b", a=2))
                            dve.tensor_copy(vc[0:32, 2, :], ps[0:32, 6, 256:384]).then_inc(vc_done, 1)

            r = Region(E1)
            gs = r.take("gate_s", [128, 4, 3])
            gp = r.take("gate_p", [128, 5, 24])
            gpr = r.take("gate_prompt_rev", [128, 4, 24])
            flip = r.take("flip", [128, 128])
            qbd = r.take("qbd", [128, NB, 64])
            kTs = r.take("kTs", [128, T])
            kTw = r.take("kTw", [128, T])
            EQ = r.at
            qT = r.take("qT", [128, 4, TP])
            E2 = r.at
            sqs = r.take("sqs", [128, 5, 12, HD])
            qn = sqs[:, :, 0:8, :].rearrange("p t (h g) d -> p t h g d", g=2)
            rs = r.take("rs", [128, 5, 12])
            gains = r.take("gains", [128, 3, HD])
            n_in, n_sq, n_ms, n_std, n_done, g_sig, q_t, q_ev = (sem(x) for x in ("n_in", "n_sq", "n_ms", "n_std", "n_done", "g_sig", "q_t", "q_ev"))
            q_ev2, gpr_ps = sem("q_ev2"), sem("gpr_ps")
            gate_out, gate_in, slc_out, rel_in = sem("gate_out"), sem("gate_in"), sem("slc_out"), sem("rel_in")
            onehot = r.take("onehot", [NBK, RVL])
            masked = r.take("masked", [NH, RVL])
            relb = r.take("rel_bias", [NBK, NH])
            rv = r.take("rv_sb", [NH, RVL])
            rv_ps, rv_sb, rv_out = sem("rv_ps"), sem("rv_ready"), sem("rv_out")
            RC = RVL // 4
            heads = ((0, 8, 0, 0), (768, 2, 8, 1), (1024, 2, 10, 2))
            with nc.Block() as block:
                @block.sync
                def _(sp):
                    def bcast(dst, src, off, n):
                        sp.dma_start(dst, bass.AP(src.tensor, off, [[0, 128], [1, n]])).then_inc(n_in, 16)
                    bcast(gains[:, 0, :], a["q_norm"], 0, HD)
                    bcast(gains[:, 1, :], a["k_norm"], HD, HD)
                    bcast(gains[:, 2, :], a["k_norm"], 2 * HD, HD)
                    sp.dma_start(flip[:, :], k["flip"]).then_inc(n_in, 16)
                    sp.dma_start(onehot[:, :], k["onehot"]).then_inc(rel_in, 16)
                    sp.dma_start(masked[:, :], k["masked"]).then_inc(rel_in, 16)
                    sp.dma_start(relb[:, :], a["rel_bias"]).then_inc(rel_in, 16)
                    sp.wait_ge(rv_sb, 4)
                    sp.dma_start(rv_dram, rv[:, :]).then_inc(rv_out, 16)
                    sp.wait_ge(g_sig, 1)
                    sp.dma_start(gate_dram, gp[0:NS, 4, :]).then_inc(gate_out, 16)
                    sp.wait_ge(gate_out, 16)
                    for grp in range(4):
                        for s2 in range(2):
                            src = bass.AP(gate_dram.tensor, (2 * grp + s2) * TS * 24, [[3, NH], [24, TS], [1, 3]])
                            sp.dma_start(gs[64 * s2:64 * s2 + 64, grp, :], src).then_inc(gate_in, 16)
                    sp.wait_ge(n_done, 3)
                    kv_out(sp, 768, o["slc_p"][0, 0], o["slc_s"][:, 0].rearrange("b t k g d -> b t (k g d)"), slc_out)
                    kv_out(sp, 1024, o["win_p"][0, 0], o["win_s"][:, 0, 504:512].rearrange("b t k g d -> b t (k g d)"), slc_out)
                    for b in range(NB):
                        sp.dma_start(o["win_s"][b, 0, 0:504].rearrange("t k g d -> t (k g d)"),
                                     a["cache_win_kv"][b, 0, 8:512].rearrange("t k g d -> t (k g d)")).then_inc(slc_out, 16)
                    sp.wait_ge(slc_out, 16 * 26)
                    sp.wait_ge(raw_out, 16 * 9)
                    sp.wait_ge(gate_in, 128)
                    sp.wait_ge(rv_out, 16)

                @block.scalar
                def _(act):
                    for c0, nh, s0, _ in heads:
                        act.activation(sqs[:, :, s0:s0 + nh, :], zq[:, :, c0:c0 + 64 * nh].rearrange("p t (h d) -> p t h d", d=HD), ACT.Square).then_inc(n_sq, 1)
                    act.activation(gp[:, :, :], zq[:, :, 1280:1304], ACT.Sigmoid).then_inc(g_sig, 1)
                    act.wait_ge(n_ms, 1)
                    act.activation(rs[:, :, :], rs[:, :, :], ACT.Sqrt).then_inc(n_std, 1)
                    for n in range(4):
                        act.wait_ge(q_t, n + 1)
                        act.copy(qT[:, n, :], ps[:, n, :]).then_inc(q_ev, 1)

                @block.vector
                def _(dve):
                    dve.memset(qbd[:, :, :], 0.0)
                    dve.wait_ge(n_sq, 3)
                    dve_chain(dve, dve.tensor_reduce(rs[:, :, :], sqs[:, :, :, :], AX.X, ALU.add))
                    dve.tensor_scalar(rs[:, :, :], rs[:, :, :], 1.0 / HD, EPS, ALU.mult, ALU.add).then_inc(n_ms, 1)
                    dve.wait_ge(n_std, 1)
                    dve_chain(dve, dve.reciprocal(rs[:, :, :], rs[:, :, :]))
                    dve_chain(dve, dve.tensor_scalar(rs[:, :, 0:8], rs[:, :, 0:8], HD ** -0.5, None, ALU.mult))
                    dve.wait_ge(n_in, 64)
                    for c0, nh, s0, gi in heads:
                        z = zq[:, :, c0:c0 + 64 * nh].rearrange("p t (h d) -> p t h d", d=HD)
                        dve_chain(dve, dve.tensor_tensor(z, z, rs[:, :, s0:s0 + nh].rearrange("p t (h o) -> p t h o", o=1).to_broadcast([128, 5, nh, HD]), ALU.mult))
                        gb = gains[:, gi, :].rearrange("p (a b d) -> p a b d", a=1, b=1).to_broadcast([128, 5, nh, HD])
                        if gi == 0:
                            for g in range(2):
                                last = dve.tensor_tensor(qn[:, :, :, g, :], z[:, :, 4 * g:4 * g + 4, :], gb[:, :, 0:4, :], ALU.mult)
                            last.then_inc(n_done, 1)
                        else:
                            dve.tensor_tensor(z, z, gb, ALU.mult).then_inc(n_done, 1)
                    dve.wait_ge(rel_in, 48)
                    for n in range(4):
                        dve.wait_ge(rv_ps, n + 1)
                        dve.tensor_tensor(rv[:, RC * n:RC * n + RC], ps[0:NH, 7, 0:RC], masked[:, RC * n:RC * n + RC], ALU.add).then_inc(rv_sb, 1)
                    dve.wait_ge(gpr_ps, 1)
                    dve.tensor_copy(flat(gpr[:, :, :]), ps[:, 7, 0:96])
                    dve.wait_ge(q_t, 5)
                    for g in range(2):
                        dve.tensor_copy(qbd[64 * g:64 * g + 64, :, 32 * g:32 * g + 32].rearrange("p s (h t) -> p s h t", h=4),
                                        ps[64 * g:64 * g + 64, 4, 0:256].rearrange("p (h s t) -> p s h t", h=4, s=NB))
                    for n, kT in enumerate((kTs, kTw)):
                        dve.wait_ge(q_t, 6 + n)
                        dve.tensor_copy(kT[:, 0:TP], ps[:, 5 + n, :])
                        last = dve.tensor_copy(kT[:, TP:T], ps[:, 4, 256 + 64 * n:320 + 64 * n])
                    last.then_inc(q_ev2, 1)

                @block.tensor
                def _(pe):
                    pe.wait_ge(rel_in, 48)
                    for n in range(4):
                        if n >= 1:
                            pe.wait_ge(rv_sb, n)
                        pe.matmul(ps[0:NH, 7, 0:RC], relb[:, :], onehot[:, RC * n:RC * n + RC], start=True, stop=True).then_inc(rv_ps, 1)
                    pe.wait_ge(g_sig, 1)
                    pe.wait_ge(n_in, 64)
                    pe.wait_ge(rv_sb, 4)
                    pe.matmul(ps[:, 7, 0:96], flip[:, :], gp[:, 0:4, :].rearrange("p t n -> p (t n)"), start=True, stop=True).then_inc(gpr_ps, 1)
                    pe.wait_ge(n_done, 3)

                    def q_of(tok, hh, rws):
                        return qn[0:rws, tok, hh].rearrange("p g d -> p (g d)")
                    for hh in range(4):
                        for tok in range(4):
                            last = pe.matmul(ps[:, hh, 128 * tok:128 * tok + 128], q_of(tok, hh, 128), flip[:, :], start=True, stop=True)
                        last.then_inc(q_t, 1)
                    for hh in range(4):
                        last = pe.transpose(ps[:, 4, 64 * hh:64 * hh + 64], q_of(4, hh, NS), ident[0:NS, 0:NS])
                    for n, c0 in enumerate((768, 1024)):
                        last = pe.transpose(ps[:, 4, 256 + 64 * n:320 + 64 * n], zq[0:NS, 4, c0:c0 + 128], ident[0:NS, 0:NS])
                    last.then_inc(q_t, 1)
                    for n, c0 in enumerate((768, 1024)):
                        for tok in range(4):
                            last = pe.transpose(ps[:, 5 + n, 128 * tok:128 * tok + 128], zq[:, tok, c0:c0 + 128], ident[:, :])
                        last.then_inc(q_t, 1)

            r = Region(E2)
            onat = r.take("onat", [128, 4, 512])
            BT = [r.take("BT", [128, BTW]) for _ in range(2)]
            sS = [r.take("s_slc", [128, TP]) for _ in range(2)]
            sW = [r.take("s_win", [128, TP]) for _ in range(2)]
            sC = [r.take("s_cmp", [128, 32]) for _ in range(2)]
            PTs = r.take("PTs", [128, 4, 128])
            PTw = r.take("PTw", [128, 4, 128])
            PTc = r.take("PTc", [32, 128])
            mx = r.take("mx", [128, 2, 3])
            den = r.take("den", [128, 2, 3])
            bt_in, s_ready, s_taken, p_ready, pt_ready, pt_act, pt_dve, o_ready, o_taken, m_ready = (sem(x) for x in (
                "bt_in", "s_ready", "s_taken", "p_ready", "pt_ready", "pt_act", "pt_dve", "o_ready", "o_taken", "m_ready"))
            on_t, on_ev = sem("on_t"), sem("on_ev")
            U = 4 * NH
            with nc.Block() as block:
                @block.sync
                def _(sp):
                    for h in range(NH):
                        if h >= 2:
                            sp.wait_ge(s_taken, 4 * (h - 1))
                        src = bass.AP(rv_dram.tensor, h * RVL, [[1, 128], [1, BTW]])
                        sp.dma_start(BT[h % 2][:, :], src).then_inc(bt_in, 16)
                        sp.wait_ge(bt_in, 16 * (h + 1))

                @block.tensor
                def _(pe):
                    def scores(u):
                        h, qt, s = u // 4, u % 4, u % 2
                        g, hh = h // 4, h % 4
                        if u >= 1:
                            pe.wait_ge(s_taken, u)
                        q = qT[64 * g:64 * g + 64, hh, 128 * qt:128 * qt + 128]
                        nk = 128 * (qt + 1)
                        pe.matmul(ps[:, s, 0:nk], q, kTs[64 * g:64 * g + 64, 0:nk], start=True, stop=True)
                        pe.matmul(ps[:, 2 + s, 0:nk], q, kTw[64 * g:64 * g + 64, 0:nk], start=True, stop=True)
                        pe.matmul(ps[:, 4, 0:32], q, kcT[64 * g:64 * g + 64, 256:288], start=True, stop=True).then_inc(s_ready, 1)
                    scores(0)
                    for u in range(U):
                        h, qt, s = u // 4, u % 4, u % 2
                        g = h // 4
                        if u + 1 < U:
                            scores(u + 1)
                        pe.wait_ge(p_ready, u + 1)
                        if u >= 1:
                            pe.wait_ge(pt_act, u)
                            pe.wait_ge(pt_dve, u)
                        for kt in range(qt + 1):
                            pe.transpose(ps[:, 5, 128 * kt:128 * kt + 128], sS[s][:, 128 * kt:128 * kt + 128], ident[:, :])
                            pe.transpose(ps[:, 6, 128 * kt:128 * kt + 128], sW[s][:, 128 * kt:128 * kt + 128], ident[:, :])
                        if u >= 1:
                            pe.wait_ge(o_taken, u)
                        pe.transpose(ps[0:32, 7, 256:384], sC[s][:, :], ident[:, :]).then_inc(pt_ready, 1)
                        pe.wait_ge(pt_act, u + 1)
                        pe.wait_ge(pt_dve, u + 1)
                        O = ps[:, 7, 0:192]
                        pe.matmul(O[:, 0:64], PTc[:, :], vc[0:32, 2, 64 * g:64 * g + 64], start=True, stop=True)
                        for n, (PT, c0) in enumerate(((PTs, 896), (PTw, 1152))):
                            for kt in range(qt + 1):
                                last = pe.matmul(O[:, 64 * (n + 1):64 * (n + 2)], PT[:, kt, :], zq[:, kt, c0 + 64 * g:c0 + 64 * g + 64],
                                                 start=(kt == 0), stop=(kt == qt))
                        last.then_inc(o_ready, 1)
                    for qt in range(4):
                        pe.wait_ge(o_taken, U)
                        for c in range(4):
                            last = pe.matmul(ps[:, qt, 128 * c:128 * c + 128], onat[:, qt, 128 * c:128 * c + 128], flip[:, :], start=True, stop=True)
                        last.then_inc(on_t, 1)

                @block.vector
                def _(dve):
                    def masked_max(u):
                        h, qt, s = u // 4, u % 4, u % 2
                        nk = 128 * (qt + 1)
                        dve.wait_ge(s_ready, u + 1)
                        dve.wait_ge(bt_in, 16 * (h + 1))
                        if u >= 2:
                            dve.wait_ge(pt_ready, u - 1)
                        y0 = 511 - 128 * qt
                        B = BT[h % 2]
                        dve.tensor_tensor_reduce(sC[s][:, :], ps[:, 4, 0:32], B[:, y0 + 31:y0 + 31 + 16 * 31 + 1:16], 1.0, FLOOR,
                                                 ALU.add, ALU.max, mx[:, s, 0:1])
                        dve.tensor_tensor_reduce(sS[s][:, 0:nk], ps[:, s, 0:nk], B[:, y0:y0 + nk], 1.0, FLOOR, ALU.add, ALU.max, mx[:, s, 1:2])
                        dve.tensor_tensor_reduce(sW[s][:, 0:nk], ps[:, 2 + s, 0:nk], B[:, y0:y0 + nk], 1.0, FLOOR, ALU.add, ALU.max,
                                                 mx[:, s, 2:3]).then_inc(s_taken, 1)
                        dve.wait_ge(s_taken, u + 1)
                        dve.tensor_scalar(mx[:, s, :], mx[:, s, :], -1.0, None, ALU.mult).then_inc(m_ready, 1)
                    masked_max(0)
                    for u in range(U):
                        h, qt, s = u // 4, u % 4, u % 2
                        if u + 1 < U:
                            masked_max(u + 1)
                        dve.wait_ge(pt_ready, u + 1)
                        if u >= 1:
                            dve.wait_ge(o_ready, u)
                        dve.tensor_copy(PTw[:, 0:qt + 1, :], ps[:, 6, 0:128 * (qt + 1)].rearrange("p (a b) -> p a b", b=128)).then_inc(pt_dve, 1)
                        dve_chain(dve, dve.tensor_scalar(den[:, s, :], den[:, s, :], 1e-30, None, ALU.max))
                        dve_chain(dve, dve.reciprocal(den[:, s, :], den[:, s, :]))
                        dve_chain(dve, dve.tensor_tensor(den[:, s, :], den[:, s, :], gpr[:, qt, 3 * h:3 * h + 3], ALU.mult))
                        dve.wait_ge(o_ready, u + 1)
                        O, out = ps[:, 7, 0:192], onat[:, qt, 64 * h:64 * h + 64]
                        dve_chain(dve, dve.tensor_scalar(out, O[:, 0:64], den[:, s, 0:1], None, ALU.mult))
                        dve_chain(dve, dve.scalar_tensor_tensor(out, O[:, 64:128], den[:, s, 1:2], out, ALU.mult, ALU.add))
                        dve.scalar_tensor_tensor(out, O[:, 128:192], den[:, s, 2:3], out, ALU.mult, ALU.add).then_inc(o_taken, 1)

                @block.scalar
                def _(act):
                    def exps(u):
                        qt, s = u % 4, u % 2
                        nk = 128 * (qt + 1)
                        act.wait_ge(m_ready, u + 1)
                        if u >= 2:
                            act.wait_ge(o_taken, u - 1)
                        act.activation(sC[s][:, :], sC[s][:, :], ACT.Exp, bias=mx[:, s, 0:1], accum_out=den[:, s, 0:1])
                        act.activation(sS[s][:, 0:nk], sS[s][:, 0:nk], ACT.Exp, bias=mx[:, s, 1:2], accum_out=den[:, s, 1:2])
                        act.activation(sW[s][:, 0:nk], sW[s][:, 0:nk], ACT.Exp, bias=mx[:, s, 2:3], accum_out=den[:, s, 2:3]).then_inc(p_ready, 1)
                    exps(0)
                    for u in range(U):
                        qt = u % 4
                        if u + 1 < U:
                            exps(u + 1)
                        act.wait_ge(pt_ready, u + 1)
                        if u >= 1:
                            act.wait_ge(o_ready, u)
                        act.copy(PTc[:, :], ps[0:32, 7, 256:384])
                        act.copy(PTs[:, 0:qt + 1, :], ps[:, 5, 0:128 * (qt + 1)].rearrange("p (a b) -> p a b", b=128)).then_inc(pt_act, 1)
                    for qt in range(4):
                        act.wait_ge(on_t, qt + 1)
                        act.copy(mixf[:, 0:4, 128 * qt:128 * qt + 128], ps[:, qt, :].rearrange("p (c t) -> p c t", c=4)).then_inc(on_ev, 1)

            r = Region(EQ)
            KV = [[r.take("kv_rows", [128, 4, 256]) for _ in range(2)] for _ in range(2)]
            SBs = r.take("bias_past", [128, TP])
            SBw = r.take("bias_win", [128, TP])
            SBn = r.take("bias_new", [128, 4, NS])
            SBc = r.take("bias_cmp", [128, 2, 128])
            wm = r.take("wmask", [128, TS])
            S2 = [r.take("s_past", [128, TP + NS]) for _ in range(2)]
            Sc = r.take("s_cmps", [128, 128])
            kT = [r.take("kT", [128, TP]) for _ in range(2)]
            PT2 = [r.take("PT2", [128, 4, 128]) for _ in range(2)]
            PTn = r.take("PTn", [64, 2, 128])
            PTcs = r.take("PTcs", [128, 128])
            mx2 = r.take("mx2", [128, 3])
            den2 = r.take("den2", [128, 3])
            acc = r.take("acc", [128, HD])
            tab_zero, tab_in = sem("tab_zero"), sem("tab_in")
            kvp_in, kvw_in = [sem("kvp_in0"), sem("kvp_in1")], [sem("kvw_in0"), sem("kvw_in1")]
            kT_ps, kT_sb, ss_ready, ss_taken, sm_ready, sp_ready = (sem(x) for x in ("kT_ps", "kT_sb", "ss_ready", "ss_taken", "sm_ready", "sp_ready"))
            spt_ready, spt_a, spt_d, so_ready, so_acc, so_t, so_ev = (sem(x) for x in (
                "spt_ready", "spt_act", "spt_dve", "so_ready", "so_acc", "so_t", "so_ev"))
            pt2 = r.take("pt2", [1, 32], I32)
            NTAB = 2 + 8 + 8 + 1 + 1
            with nc.Block() as block:
                @block.sync
                def _(sp):
                    sp.dma_start(pt2[:, :], a["page_table"].rearrange("(o b) n -> o (b n)", o=1)).then_inc(tab_in, 16)
                    sp.dma_start(wm[:, :], k["wmask"]).then_inc(tab_in, 16)
                    sp.wait_ge(tab_in, 32)
                    for s2 in range(2):
                        sp.dma_start(SBs[64 * s2:64 * s2 + 64, :],
                                     bass.AP(rv_dram.tensor, RV0 - TP, [[RVL, NH], [-1, TS], [1, TP]])).then_inc(tab_in, 16)
                    sp.wait_ge(tab_zero, 1)
                    for s2 in range(2):
                        for grp in range(4):
                            c0 = TS * (2 * grp + s2)
                            sp.dma_start(SBn[64 * s2:64 * s2 + 64, grp, c0:c0 + TS],
                                         bass.AP(rv_dram.tensor, RV0, [[RVL, NH], [-1, TS], [1, TS]])).then_inc(tab_in, 16)
                    for grp in range(4):
                        if grp >= 1:
                            sp.wait_ge(so_ready, grp)
                        for s2 in range(2):
                            b = 2 * grp + s2
                            for pg in range(4):
                                page = sp.value_load(pt2[0:1, 4 * b + pg:4 * b + pg + 1], min_val=0, max_val=n_pool - 1)
                                src = a["cache_slc_kv"][bass.ds(page, 1), 0].rearrange("o t k g d -> (o t) (k g d)")
                                sp.dma_start(KV[0][s2][:, pg, :], src).then_inc(kvp_in[s2], 16)
                            sp.dma_start(KV[1][s2][:, :, :], a["cache_win_kv"][b, 0].rearrange("(t p) k g d -> p t (k g d)", p=128)).then_inc(kvw_in[s2], 16)

                @block.tensor
                def _(pe):
                    pe.wait_ge(tab_in, 32)
                    for grp in range(4):
                        for s2 in range(2):
                            b = 2 * grp + s2
                            pe.wait_ge(kvp_in[s2], 64 * (grp + 1))
                            pe.wait_ge(kvw_in[s2], 16 * (grp + 1))
                            for br in range(2):
                                n = 4 * grp + 2 * s2 + br
                                if n >= 1:
                                    pe.wait_ge(kT_sb, n)
                                if s2 == 0 and br == 0 and grp >= 1:
                                    pe.wait_ge(so_acc, grp)
                                for pg in range(4):
                                    last = pe.transpose(ps[:, br, 128 * pg:128 * pg + 128], KV[br][s2][:, pg, 0:128], ident[:, :])
                                last.then_inc(kT_ps, 1)
                                pe.wait_ge(kT_sb, n + 1)
                                if n >= 2 and s2 == 0 and br == 0:
                                    pe.wait_ge(ss_taken, grp)
                                rows = slice(64 * s2, 64 * s2 + 64)
                                pe.matmul(ps[rows, 2 + br, :], qbd[:, b, :], kT[br][:, :], start=True, stop=True)
                                last = pe.matmul(ps[rows, 4, 64 * br:64 * br + 64], qbd[:, b, :], (kTs, kTw)[br][:, TP:T], start=True, stop=True)
                            last = pe.matmul(ps[rows, 4, 128:256], qbd[:, b, :], kcT[:, 128 * (b // 4):128 * (b // 4) + 128], start=True, stop=True)
                        last.then_inc(ss_ready, 1)
                        pe.wait_ge(sp_ready, grp + 1)
                        for br in range(2):
                            for kt in range(4):
                                pe.transpose(ps[:, 5 + br, 128 * kt:128 * kt + 128], S2[br][:, 128 * kt:128 * kt + 128], ident[:, :])
                            pe.transpose(ps[0:64, 7, 128 * br:128 * br + 128], S2[br][:, TP:TP + NS], ident[:, :])
                        pe.transpose(ps[:, 7, 256:384], Sc[:, :], ident[:, :]).then_inc(spt_ready, 1)
                        pe.wait_ge(spt_a, grp + 1)
                        pe.wait_ge(spt_d, grp + 1)
                        for s2 in range(2):
                            rows = slice(64 * s2, 64 * s2 + 64)
                            b = 2 * grp + s2
                            for br, c0 in ((0, 896), (1, 1152)):
                                out = ps[rows, 0, 128 * (br + 1):128 * (br + 2)]
                                for kt in range(4):
                                    pe.matmul(out, PT2[br][:, kt, rows], KV[br][s2][:, kt, 128:256], start=(kt == 0), stop=False)
                                pe.matmul(out, PTn[:, br, rows], zq[0:64, 4, c0:c0 + 128], start=False, stop=True)
                            last = pe.matmul(ps[rows, 0, 0:128], PTcs[:, rows], vc[:, b // 4, :], start=True, stop=True)
                        last.then_inc(so_ready, 1)
                        pe.wait_ge(so_acc, grp + 1)
                        pe.transpose(ps[0:64, 1, 0:128], acc[:, :], ident[:, :]).then_inc(so_t, 1)
                        pe.wait_ge(so_ev, grp + 1)

                @block.scalar
                def _(act):
                    for grp in range(4):
                        for n in range(4):
                            if n % 2 == 0:
                                act.wait_ge(kT_ps, 4 * grp + n + 1)
                                if grp or n:
                                    act.wait_ge(kT_sb, 4 * grp + n)
                                act.copy(kT[0][:, :], ps[:, 0, :]).then_inc(kT_sb, 1)
                            else:
                                act.wait_ge(kT_ps, 4 * grp + n + 1)
                                act.copy(kT[1][:, :], ps[:, 1, :]).then_inc(kT_sb, 1)
                        act.wait_ge(sm_ready, grp + 1)
                        act.activation(S2[0][:, :], S2[0][:, :], ACT.Exp, bias=mx2[:, 0:1], accum_out=den2[:, 0:1])
                        act.activation(S2[1][:, :], S2[1][:, :], ACT.Exp, bias=mx2[:, 1:2], accum_out=den2[:, 1:2])
                        act.activation(Sc[:, :], Sc[:, :], ACT.Exp, bias=mx2[:, 2:3], accum_out=den2[:, 2:3]).then_inc(sp_ready, 1)
                        act.wait_ge(spt_ready, grp + 1)
                        act.copy(PT2[0][:, :, :], ps[:, 5, :].rearrange("p (a b) -> p a b", a=4)).then_inc(spt_a, 1)
                        act.wait_ge(so_t, grp + 1)
                        for par in range(2):
                            src = ps[0:64, 1, 0:128].rearrange("p (s c r t) -> p s c r t", s=2, c=4, r=2)[:, :, :, par, :]
                            dst = mixf[64 * par:64 * par + 64, 0:4, TP + 16 * grp:TP + 16 * grp + 16].rearrange("p c (s t) -> p s c t", s=2)
                            for s2 in range(2):
                                last = act.copy(dst[:, s2], src[:, s2])
                        last.then_inc(so_ev, 1)

                @block.vector
                def _(dve):
                    dve.memset(SBn[:, :, :], NEG)
                    dve.memset(SBc[:, :, :], NEG).then_inc(tab_zero, 1)
                    dve.wait_ge(tab_in, 16 * 12)
                    dve.wait_ge(tab_zero, 1)
                    for par in range(2):
                        for s2 in range(2):
                            c0 = 64 * par + 32 * s2
                            dve.tensor_copy(SBc[64 * s2:64 * s2 + 64, par, c0:c0 + 31], SBs[64 * s2:64 * s2 + 64, 31:31 + 16 * 30 + 1:16])
                    dve.tensor_copy(SBw[:, TS:TP], SBs[:, TS:TP])
                    dve_chain(dve, dve.tensor_tensor(SBw[:, 0:TS], SBs[:, 0:TS], wm[:, :], ALU.add))
                    for grp in range(4):
                        dve.wait_ge(ss_ready, grp + 1)
                        for br in range(2):
                            dve.tensor_tensor(S2[br][:, 0:TP], ps[:, 2 + br, :], (SBs, SBw)[br][:, :], ALU.add)
                            dve.tensor_tensor(S2[br][:, TP:TP + NS], ps[:, 4, 64 * br:64 * br + 64], SBn[:, grp, :], ALU.add)
                        dve.tensor_tensor(Sc[:, :], ps[:, 4, 128:256], SBc[:, grp % 2, :], ALU.add).then_inc(ss_taken, 1)
                        dve.wait_ge(ss_taken, grp + 1)
                        for n, S in enumerate((S2[0], S2[1], Sc)):
                            last = dve.tensor_reduce(mx2[:, n:n + 1], S[:, :], AX.X, ALU.max)
                        dve_chain(dve, last)
                        dve.tensor_scalar(mx2[:, :], mx2[:, :], FLOOR, -1.0, ALU.max, ALU.mult).then_inc(sm_ready, 1)
                        dve.wait_ge(spt_ready, grp + 1)
                        dve.tensor_copy(PT2[1][:, :, :], ps[:, 6, :].rearrange("p (a b) -> p a b", a=4))
                        dve.tensor_copy(PTcs[:, :], ps[:, 7, 256:384])
                        dve.tensor_copy(PTn[:, :, :], ps[0:64, 7, 0:256].rearrange("p (a b) -> p a b", a=2)).then_inc(spt_d, 1)
                        dve_chain(dve, dve.tensor_scalar(den2[:, :], den2[:, :], 1e-30, None, ALU.max))
                        dve_chain(dve, dve.reciprocal(den2[:, :], den2[:, :]))
                        dve.tensor_tensor(den2[:, 0:2], den2[:, 0:2], gs[:, grp, 1:3], ALU.mult)
                        dve_chain(dve, dve.tensor_tensor(den2[:, 2:3], den2[:, 2:3], gs[:, grp, 0:1], ALU.mult))
                        dve.wait_ge(so_ready, grp + 1)
                        for n, (cc, slot) in enumerate(((2, 0), (0, 1), (1, 2))):
                            for blk in range(4):
                                rr = slice(32 * blk, 32 * blk + 32)
                                g = blk % 2
                                O = ps[rr, 0, 128 * slot + 64 * g:128 * slot + 64 * g + 64]
                                if n == 0:
                                    last = dve.tensor_scalar(acc[rr, :], O, den2[rr, cc:cc + 1], None, ALU.mult)
                                else:
                                    last = dve.scalar_tensor_tensor(acc[rr, :], O, den2[rr, cc:cc + 1], acc[rr, :], ALU.mult, ALU.add)
                            if n < 2:
                                dve_chain(dve, last)
                        last.then_inc(so_acc, 1)

            retire_semaphores()
            RZ = MIX + 4 * KT * T
            r = Region(RZ)
            zz = r.take("zz", [128, RT, T])
            AB = r.take("ab_hat", [128, 2, 4, T])
            pc = r.take("p_end", [64, NH, 16])
            bonus = r.take("bonus", [128, 5, NH])
            lnw = r.take("ln_w", [128, 512])
            lnb = r.take("ln_b", [128, 512])
            w2 = r.take("rwkv_w2", [128, 512])
            g2 = r.take("rwkv_g2", [128, 512])
            R2 = r.at
            shT = r.take("shiftT", [128, NB, RT])
            ext = [r.take("z_ext", [128, 1 + TP + NB * (TS + 1)]) for _ in range(2)]
            df = [r.take("z_diff", [128, TP + NB * (TS + 1)]) for _ in range(2)]
            sh_rows = r.take("sh_rows", [NB * RT, 128])
            rw_in, sh_t, sh_ev, rx_ready, rx_used = (sem(x) for x in ("rw_in", "sh_t", "sh_ev", "rx_ready", "rx_used"))
            with nc.Block() as block:
                @block.sync
                def _(sp):
                    sp.dma_start(sh_rows[:, :], a["state_rwkv_shift"].rearrange("b o (c p) -> (b o c) p", p=128)).then_inc(rw_in, 16)
                    for dst, name in ((lnw, "rwkv_ln_w"), (lnb, "rwkv_ln_b")):
                        sp.dma_start(dst[:, :], bass.AP(a[name].tensor, 0, [[0, 128], [1, 512]])).then_inc(rw_in, 16)
                    sp.dma_start(w2[0:64, :], a["rwkv_w2"][0]).then_inc(rw_in, 16)
                    sp.dma_start(w2[64:128, :], a["rwkv_a2"][0]).then_inc(rw_in, 16)
                    sp.dma_start(g2[:, :], a["rwkv_g2"][0]).then_inc(rw_in, 16)
                    sp.wait_ge(rw_in, 96)

                @block.tensor
                def _(pe):
                    pe.wait_ge(rw_in, 96)
                    pe.transpose(ps[:, 0, 0:NB * RT], sh_rows[:, :], ident[0:NB * RT, 0:NB * RT]).then_inc(sh_t, 1)

                @block.scalar
                def _(act):
                    act.wait_ge(sh_t, 1)
                    act.copy(flat(shT[:, :, :]), ps[:, 0, 0:NB * RT]).then_inc(sh_ev, 1)

            def z_sample(e):
                return e[:, 1 + TP:].rearrange("p (b t) -> p b t", b=NB)

            with nc.Block() as block:
                @block.sync
                def _(sp):
                    with sp.Fori(0, 2) as i:
                        for q in (2, 3):
                            load_slab(sp, st_rw, i, q, 2)
                    load_slab(sp, st_rw, 3, 0, 2)
                    loads_after(sp, st_rw["base"] + 7)

                @block.scalar
                def _(act):
                    def slab(i, q, nxt):
                        split_hi(act, *nxt)
                        act.wait_ge(slab_done, st_rw["base"] + 2 * i + q + 1)
                        for j in range(2):
                            kk = 4 * i + 2 * q + j
                            act.wait_ge(rx_used, kk + 1)
                            e, b = ext[j], 4 * q + 2 * j
                            act.copy(e[:, 1:1 + HT], ps[:, b, 0:HT])
                            act.copy(e[:, 1 + HT:1 + TP], ps[:, b + 1, 0:H1])
                            act.copy(z_sample(e)[:, :, 0:1], shT[:, :, bass.ds(kk, 1)])
                            act.copy(z_sample(e)[:, :, 1:1 + TS], ps[:, b + 1, H1:HT].rearrange("p (b t) -> p b t", b=NB)).then_inc(rx_ready, 1)
                        act.wait_ge(rx_ready, 4 * i + 2 * q + 2)
                        act.nop().then_inc(banks_free[q], 1)
                    with act.Fori(0, 3) as i:
                        slab(i, 0, (st_rw, i, 1, 2))
                        slab(i, 1, (st_rw, i, 2, 2))
                    slab(3, 0, follow(st_rw["base"] + 7))

                @block.gpsimd
                def _(pool):
                    with pool.Fori(0, 3) as i:
                        split_lo(pool, st_rw, i, 1, 2)
                        split_lo(pool, st_rw, i, 2, 2)
                    split_lo(pool, *follow(st_rw["base"] + 7))

                @block.tensor
                def _(pe):
                    with pe.Fori(0, 3) as i:
                        for q in range(2):
                            products(pe, st_rw, i, q, 2, 4 * q, 0, hhi, hlo)
                    products(pe, st_rw, 3, 0, 2, 0, 0, hhi, hlo)

                @block.vector
                def _(dve):
                    for e in ext:
                        dve.memset(e[:, 0:1], 0.0).then_inc(rx_used, 1)

                    def tile(kk, j):
                        e, d = ext[j], df[j]
                        dve.wait_ge(rx_ready, kk + 1)
                        dve.tensor_copy(zlast[:, 0:1, bass.ds(kk, 1)], e[:, TP:TP + 1].rearrange("p (a b) -> p a b", a=1))
                        dve.tensor_copy(zlast[:, 1:9, bass.ds(kk, 1)], z_sample(e)[:, :, TS:TS + 1])
                        n = TP + NB * (TS + 1)
                        dve_chain(dve, dve.tensor_tensor(d[:, :], e[:, 0:n], e[:, 1:1 + n], ALU.subtract))
                        mu = vec[:, bass.ds(V_MU + kk, 1)]
                        dve.scalar_tensor_tensor(zz[:, bass.ds(kk, 1), 0:TP].rearrange("p o t -> p (o t)"), d[:, 0:TP], mu, e[:, 1:1 + TP], ALU.mult, ALU.add)
                        dd = d[:, TP:TP + NB * (TS + 1)].rearrange("p (b t) -> p b t", b=NB)[:, :, 1:1 + TS]
                        dve.scalar_tensor_tensor(zz[:, bass.ds(kk, 1), TP:T].rearrange("p o (b t) -> p (o b) t", b=NB), dd, mu,
                                                 z_sample(e)[:, :, 1:1 + TS], ALU.mult, ALU.add).then_inc(rx_used, 1)

                    with dve.Fori(0, 3) as i:
                        dve_chain.begin(i, 4, 3)
                        for q in range(2):
                            for j in range(2):
                                tile(4 * i + 2 * q + j, j)
                        dve_chain.end()
                    for j in range(2):
                        tile(12 + j, j)

            r = Region(R)
            sg, aa, CL, CM, Pp, PI, PM, kk_, km, tt_ = (r.take(x, [128, T]) for x in
                                                      ("sg", "aa", "CL", "CM", "P", "PI", "PM", "kk", "km", "tt"))
            keep = r.take("keep", [128, T])
            hones = r.take("headones", [128, 128])
            omka = r.take("omka", [128, 4])
            assert r.at <= MIX
            k_in, act_lora, wa_ps, sig_ready, cl_ready, cm_ready, exp_ready, kk_ready, sq2_ready, ss_ps, ss_m, ss_std, rk_ready, bo_ps, c_free = (
                sem(x) for x in ("k_in", "act_lora", "wa_ps", "sig_ready", "cl_ready", "cm_ready", "exp_ready", "kk_ready", "sq2_ready",
                                 "ss_ps", "ss_m", "ss_std", "rk_ready", "bo_ps", "c_free"))
            halves = lambda t: t.rearrange("p (a t) -> p a t", a=2)
            with nc.Block() as block:
                @block.sync
                def _(sp):
                    sp.dma_start(keep[:, :], k["keep"]).then_inc(k_in, 16)
                    sp.dma_start(hones[:, :], k["headones"]).then_inc(k_in, 16)
                    sp.wait_ge(k_in, 32)

                @block.scalar
                def _(act):
                    act.activation(zz[0:64, 12, :], zz[0:64, 12, :], ACT.Tanh)
                    act.activation(zz[:, 13, :], zz[:, 13, :], ACT.Sigmoid).then_inc(act_lora, 1)
                    for c in range(4):
                        act.wait_ge(wa_ps, c + 1)
                        if c >= 1:
                            act.wait_ge(c_free, c)
                        act.activation(halves(sg[:, :]), ps[:, 0:2, 0:HT], ACT.Sigmoid, bias=vec[:, V_W0 + c:V_W0 + c + 1])
                        act.activation(halves(aa[:, :]), ps[:, 2:4, 0:HT], ACT.Sigmoid, bias=vec[:, V_A0 + c:V_A0 + c + 1]).then_inc(sig_ready, 1)
                        act.wait_ge(kk_ready, c + 1)
                        act.activation(tt_[:, :], kk_[:, :], ACT.Square).then_inc(sq2_ready, 1)
                        act.wait_ge(cm_ready, c + 1)
                        act.activation(Pp[:, :], CL[:, :], ACT.Exp)
                        act.activation(PI[:, :], CL[:, :], ACT.Exp, scale=-1.0)
                        act.activation(PM[:, :], CM[:, :], ACT.Exp).then_inc(exp_ready, 1)
                        act.wait_ge(ss_m, c + 1)
                        act.activation(tt_[:, :], tt_[:, :], ACT.Sqrt).then_inc(ss_std, 1)

                @block.tensor
                def _(pe):
                    pe.wait_ge(act_lora, 1)
                    pe.wait_ge(k_in, 32)
                    for c in range(4):
                        if c >= 1:
                            pe.wait_ge(sig_ready, c)
                        for half in range(2):
                            cols_ = slice(half * HT, (half + 1) * HT)
                            pe.matmul(ps[:, half, 0:HT], w2[0:64, 128 * c:128 * c + 128], zz[0:64, 12, cols_], start=True, stop=True)
                            last = pe.matmul(ps[:, 2 + half, 0:HT], w2[64:128, 128 * c:128 * c + 128], zz[64:128, 12, cols_], start=True, stop=True)
                        last.then_inc(wa_ps, 1)
                        pe.wait_ge(sq2_ready, c + 1)
                        for half in range(2):
                            last = pe.matmul(ps[:, 4 + half, 0:HT], hones[:, :], tt_[:, half * HT:(half + 1) * HT], start=True, stop=True)
                        last.then_inc(ss_ps, 1)
                        pe.wait_ge(rk_ready, c + 1)
                        for tok in range(5):
                            w = 128 if tok < 4 else NS
                            last = pe.matmul(ps[0:w, 6, 8 * tok + 2 * c:8 * tok + 2 * c + 2], CM[:, 128 * tok:128 * tok + w], hones[:, 0:128:64],
                                             start=True, stop=True)
                        last.then_inc(bo_ps, 1)

                @block.vector
                def _(dve):
                    L = lambda ins: dve_chain(dve, ins)
                    ka = vec[:, V_KA:V_KA + 4]
                    L(dve.tensor_scalar(omka[:, :], ka, -1.0, 1.0, ALU.mult, ALU.add))
                    dve.wait_ge(k_in, 32)
                    for c in range(4):
                        col = lambda v: vec[:, v + c:v + c + 1]
                        if c >= 1:
                            dve.wait_ge(bo_ps, c)
                        dve.tensor_scalar(kk_[:, :], zz[:, 4 + c, :], col(V_KK), None, ALU.mult).then_inc(kk_ready, 1)
                        dve.wait_ge(sig_ready, c + 1)
                        L(dve.tensor_scalar(sg[:, :], sg[:, :], -math.exp(-0.5), None, ALU.mult))
                        L(dve.tensor_tensor_scan(CL[:, :], keep[:, :], sg[:, :], 0.0, ALU.mult, ALU.add))
                        dve.tensor_tensor(CM[:, :], CL[:, :], sg[:, :], ALU.subtract).then_inc(cm_ready, 1)
                        L(dve.tensor_scalar(km[:, :], aa[:, :], col(V_KA), omka[:, c:c + 1], ALU.mult, ALU.add))
                        L(dve.tensor_tensor(km[:, :], km[:, :], zz[:, 4 + c, :], ALU.mult))
                        dve.wait_ge(ss_ps, c + 1)
                        dve.tensor_scalar(halves(tt_[:, :]), ps[:, 4:6, 0:HT], 1e-24, None, ALU.max).then_inc(ss_m, 1)
                        dve.wait_ge(ss_std, c + 1)
                        L(dve.reciprocal(tt_[:, :], tt_[:, :]))
                        L(dve.tensor_tensor(kk_[:, :], kk_[:, :], tt_[:, :], ALU.mult))
                        dve.wait_ge(exp_ready, c + 1)
                        dve.scalar_tensor_tensor(AB[:, 0, c, :], kk_[:, :], -1.0, PM[:, :], ALU.mult, ALU.mult)
                        L(dve.tensor_tensor(tt_[:, :], kk_[:, :], aa[:, :], ALU.mult))
                        dve.tensor_tensor(AB[:, 1, c, :], tt_[:, :], PI[:, :], ALU.mult)
                        dve.scalar_tensor_tensor(CM[:, :], zz[:, c, :], col(V_RK), km[:, :], ALU.mult, ALU.mult).then_inc(rk_ready, 1)
                        dve.tensor_tensor(zz[:, 4 + c, :], km[:, :], PI[:, :], ALU.mult)
                        dve.tensor_tensor(zz[:, c, :], zz[:, c, :], Pp[:, :], ALU.mult)
                        for hb in range(2):
                            rows_ = slice(64 * hb, 64 * hb + 64)
                            dve.tensor_copy(pc[:, 2 * c + hb, 0:8], Pp[rows_, CH - 1:TP:CH])
                            last = dve.tensor_copy(pc[:, 2 * c + hb, 8:16], Pp[rows_, TP + TS - 1:T:TS])
                        last.then_inc(c_free, 1)
                    dve.wait_ge(bo_ps, 4)
                    dve.tensor_copy(bonus[:, 0:4, :], ps[:, 6, 0:32].rearrange("p (a b) -> p a b", a=4))
                    dve.tensor_copy(bonus[0:NS, 4, :], ps[0:NS, 6, 32:40])

            r = Region(R)
            AR = r.take("a_r", [64, 2, NH, 2, CH])
            BK = r.take("b_k", [64, 2, NH, 2, CH])
            gm = r.take("gm", [128, 2, NH, 128])
            Sv = [r.take("sv", [128, 512]) for _ in range(2)]
            Uv = [r.take("uv", [128, 512]) for _ in range(2)]
            Zs = r.take("zs", [64, 512])
            gmask = r.take("gmask", [128, 2, 128])
            imask = r.take("imask", [64, 2, 4, CH])
            smask = r.take("smask", [128, NB])
            assert r.at <= MIX, r.at - MIX
            r = Region(R2)
            assert st_out["base"] % 2 == 1
            w_at = nc.sbuf_base + (-nc.sbuf_base) % 64 + 2 * 4 * SLAB
            SL = [at("inv", [64, 2, 512], F32, w_at + 4096 * (n % 2) + 4 * 4 * SLAB // 2 * (n // 2)) for n in range(4)]
            y2_at = r.at
            SL += [r.take("inv", [64, 2, 512]) for _ in range(2)]
            ysq_v = at("y_sq", [128, 512], F32, y2_at)
            BKt = r.take("bkt", [128, 2, 512])
            yb = r.take("yb", [128, 512])
            SpO = r.take("sp", [128, 4, CH])
            st8 = r.take("stats", [128, 2, NH])
            D_, DT, E_, Y_, P4, P5 = range(6)
            STEPS = [[(P4, DT, D_, 0), (P5, D_, DT, 0)],
                     [(Y_, P5, Y_, 1), (D_, P5, P4, 0), (DT, P4, P5, 0)],
                     [(Y_, DT, Y_, 1), (P4, D_, DT, 0)],
                     [(Y_, P4, Y_, 1)],
                     [(P5, Y_, None, 0)],
                     [(D_, P5, E_, 0), (DT, E_, P5, 0)],
                     [(P4, D_, DT, 0)],
                     [(Y_, P4, Y_, 1)],
                     [(Y_, DT, Y_, 1)]]
            TILES = 5
            chunks_of = lambda t: 2 if t < 4 else 1
            units = []
            for t in range(TILES):
                for s, step in enumerate(STEPS):
                    for ch in range(chunks_of(t)):
                        for n, pr in enumerate(step):
                            units.append((t, s, ch, n, "dve" if pr[3] or (len(units) % 2) else "act"))

            def taken(engine, t, s, ch):
                return sum(1 for u in units if u[4] == engine and u[:3] <= (t, s, ch))
            m_in, cp_a, cp_d, gg_ps, gg_sb, zst, inv_ps, inv_a, inv_d, bkt_ps, bkt_sb, v_ps, v_sb = (sem(x) for x in (
                "m_in", "cp_ar", "cp_bk", "gg_ps", "gg_sb", "zstack", "inv_ps", "inv_act", "inv_dve", "bkt_ps", "bkt_sb", "v_ps", "v_sb"))
            z_ps, z_sb, u_ps, u_sb, n_ps, n_sb, y_ps, gv_ps, yn_a, yn_b, yn_c, yo, yt_ps2, yt_sb2, s_zero = (sem(x) for x in (
                "z_ps", "z_sb", "u_ps", "u_sb", "n_ps", "n_sb", "y_ps", "gv_ps", "yn_mean", "yn_sq", "yn_std", "y_out_ready", "ymix_ps", "ymix_sb", "s_zero"))
            sT_ps, sT_sb, zsT_ps, zsT_sb, um_ready, sn_ps, sn_sb, so_ps, so_sb, st_in, wkv_out, pT_ps, pT_sb = (sem(x) for x in (
                "sT_ps", "sT_sb", "zsT_ps", "zsT_sb", "um_ready", "sn_ps", "sn_sb", "sO_ps", "sO_sb", "st_in", "wkv_out", "pT_ps", "pT_sb"))
            q = Region(RZ)
            S0T = q.take("s0T", [64, NB, 512])
            assert q.at <= RZ + 4 * 8 * T
            ZST = gm[0:64, 1].rearrange("p h (x t) -> p h x t", x=2)
            q = Region(RZ + 4 * RT * T)
            S0n = q.take("s0", [128, NB, 4, CH])
            Um = [q.take("um", [128, NB, CH]) for _ in range(2)]
            Sn = [q.take("sn", [64, NB, CH]) for _ in range(2)]
            assert q.at <= RZ + 4 * RT * T + 4 * 8 * T
            So = at("so", [128, NH, 4, CH], F32, R)
            chunk_no = lambda t, ch: 2 * t + ch
            ntok = lambda t: 128 if t < 4 else NS
            flatv = zz[:, :, :].rearrange("p c t -> p (c t)")

            def inverse_units(t, engine):
                for idx, u in enumerate(units):
                    if u[0] == t and u[4] == engine:
                        yield idx + 1, u[2], u[3], STEPS[u[1]][u[3]]

            with nc.Block() as block:
                @block.sync
                def _(sp):
                    sp.dma_start(gmask[:, :, :], k["gmask"]).then_inc(m_in, 16)
                    sp.dma_start(imask[:, :, :, :], k["invmask"]).then_inc(m_in, 16)
                    sp.dma_start(smask[:, :], k["seqmask"]).then_inc(m_in, 16)
                    sp.wait_ge(cp_a, TILES)
                    sp.wait_ge(cp_d, TILES)
                    for b in range(NB):
                        for h2 in range(2):
                            sp.dma_start(S0n[64 * h2:64 * h2 + 64, b, :, :],
                                         a["state_rwkv_wkv"][b, 0].rearrange("(c h) i j -> h i c j", h=2)[h2]).then_inc(st_in, 16)
                    sp.wait_ge(pT_sb, 1)
                    for h2 in range(2):
                        sp.dma_start(o["wkv_p"][0, 0].rearrange("(c h) i j -> h i c j", h=2)[h2], SpO[64 * h2:64 * h2 + 64, :, :]).then_inc(wkv_out, 16)
                    sp.wait_ge(so_sb, NH)
                    for qq in range(4):
                        for b2 in range(2):
                            sp.dma_start(o["wkv_s"][2 * qq + b2, 0].rearrange("h i j -> i h j"), So[64 * b2:64 * b2 + 64, :, qq, :]).then_inc(wkv_out, 16)
                    sp.wait_ge(wkv_out, 160)

                @block.tensor
                def _(pe):
                    for t in range(TILES):
                        C = chunks_of(t)
                        pe.wait_ge(cp_a, t + 1)
                        pe.wait_ge(cp_d, t + 1)
                        if t >= 1:
                            pe.wait_ge(yt_sb2, t)
                        for ch in range(C):
                            for h in range(NH):
                                pe.matmul(ps[:, 2 * ch + h // 4, 128 * (h % 4):128 * (h % 4) + 128],
                                          BK[:, ch, h].rearrange("p x t -> p (x t)"), AR[:, ch, h].rearrange("p x t -> p (x t)"), start=True, stop=True)
                                last = pe.matmul(ps[0:64, 4 + ch, 64 * h:64 * h + 64], AR[:, ch, h, 0, :], BK[:, ch, h, 0, :], start=True, stop=True)
                            last.then_inc(gg_ps, 1)
                        for ch in range(C):
                            for h in range(NH):
                                last = pe.transpose(ps[:, 6 + ch, 64 * h:64 * h + 64], BK[:, ch, h].rearrange("p x t -> p (x t)"), ident[0:64, 0:64])
                        last.then_inc(bkt_ps, 1)
                        if t == 4:
                            pe.wait_ge(st_in, 256)
                            for b in range(NB):
                                if b >= 1:
                                    pe.wait_ge(sT_sb, b)
                                for c in range(4):
                                    last = pe.transpose(ps[0:64, 5, 128 * c:128 * c + 128], S0n[:, b, c, :], ident[:, :])
                                last.then_inc(sT_ps, 1)
                            pe.wait_ge(sT_sb, NB)
                            for h in range(NH):
                                for b in range(NB):
                                    last = pe.matmul(ps[0:64, 2 + h // 4, 128 * (h % 4):128 * (h % 4) + 128].rearrange("p (x t) -> p x t", x=2)[:, :, 8 * b:8 * b + 8],
                                                     S0T[:, b, 64 * h:64 * h + 64], AR[:, 0, h, :, 8 * b:8 * b + 8], start=True, stop=True)
                            last.then_inc(zsT_ps, 1)
                        for ch in range(C):
                            n = chunk_no(t, ch)
                            pe.wait_ge(bkt_sb, t + 1)
                            for c in range(4):
                                at_ = (8 + c) * T + CH * n - CH
                                last = pe.transpose(ps[:, 6 + ch, 128 * c:128 * c + 128], flatv[:, at_:at_ + 128], ident[:, :])
                            last.then_inc(v_ps, 1)
                        if t == 4:
                            pe.wait_ge(zsT_sb, 1)
                        for s, step in enumerate(STEPS):
                            for ch in range(C):
                                if s == 0:
                                    pe.wait_ge(gg_sb, 2 * t + ch + 1)
                                    pe.wait_ge(gg_sb, 2 * t + C)
                                else:
                                    pe.wait_ge(inv_a, taken("act", t, s - 1, ch))
                                    pe.wait_ge(inv_d, taken("dve", t, s - 1, ch))
                                for n, (dst, l, rr, add) in enumerate(step):
                                    for h in range(NH):
                                        hs = slice(64 * h, 64 * h + 64)
                                        out = ps[0:64, 3 * ch + n, hs]
                                        if rr is None:
                                            last = pe.transpose(out, SL[l][:, ch, hs], ident[0:64, 0:64])
                                        else:
                                            last = pe.matmul(out, SL[l][:, ch, hs], SL[rr][:, ch, hs], start=True, stop=True)
                                    last.then_inc(inv_ps, 1)
                        pe.wait_ge(inv_a, taken("act", t, len(STEPS) - 1, C - 1))
                        pe.wait_ge(inv_d, taken("dve", t, len(STEPS) - 1, C - 1))
                        for ch in range(C):
                            n = chunk_no(t, ch)
                            S, Un = Sv[n % 2], Uv[n % 2]
                            pe.wait_ge(v_sb, n + 1)
                            pe.wait_ge(zst, n + 1)
                            pe.wait_ge(n_sb, n + 1)
                            for h in range(NH):
                                hs = slice(64 * h, 64 * h + 64)
                                last = pe.matmul(ps[0:64, 0, hs], gm[:, ch, h, 0:64], S[:, hs], start=True, stop=True)
                            last.then_inc(z_ps, 1)
                            pe.wait_ge(z_sb, n + 1)
                            for h in range(NH):
                                hs = slice(64 * h, 64 * h + 64)
                                last = pe.matmul(ps[0:64, 1, hs], SL[Y_][:, ch, hs], Zs[:, hs], start=True, stop=True)
                            last.then_inc(u_ps, 1)
                            pe.wait_ge(u_sb, n + 1)
                            if t < 4:
                                for h in range(NH):
                                    hs = slice(64 * h, 64 * h + 64)
                                    last = pe.matmul(ps[0:64, 2, hs], BKt[:, ch, hs], Un[:, hs], start=True, stop=True)
                                last.then_inc(n_ps, 1)
                            for h in range(NH):
                                hs = slice(64 * h, 64 * h + 64)
                                r_of = AR[:, ch, h, 1, :] if t < 4 else ZST[:, h, 1, :]
                                pe.matmul(ps[64 * ch:64 * ch + 64, 3, hs], gm[:, ch, h, 64:128], Un[:, hs], start=True, stop=False)
                                last = pe.matmul(ps[64 * ch:64 * ch + 64, 3, hs], r_of, S[0:64, hs], start=False, stop=True)
                        last.then_inc(y_ps, 1)
                        w = ntok(t)
                        pe.matmul(ps[0:w, 4, :], zz[:, 13, 128 * t:128 * t + w], g2[:, :], start=True, stop=True)
                        for c in range(4):
                            last = pe.transpose(ps[0:w, 5, 128 * c:128 * c + 128], zz[:, 8 + c, 128 * t:128 * t + w], ident[:, :])
                        last.then_inc(gv_ps, 1)
                        if t == 3:
                            pe.wait_ge(n_sb, 9)
                            for c in range(4):
                                last = pe.transpose(ps[:, 6, 64 * c:64 * c + 64], Sv[0][0:64, 128 * c:128 * c + 128], ident[0:64, 0:64])
                            last.then_inc(pT_ps, 1)
                            pe.wait_ge(pT_sb, 1)
                        pe.wait_ge(yo, t + 1)
                        for c in range(4):
                            last = pe.transpose(ps[:, 7, 128 * c:128 * c + w], yb[0:w, 128 * c:128 * c + 128], ident[0:w, 0:w])
                        last.then_inc(yt_ps2, 1)
                    for h in range(NH):
                        pe.wait_ge(um_ready, h + 1)
                        if h >= 2:
                            pe.wait_ge(sn_sb, h - 1)
                        pe.matmul(ps[0:64, h % 2, :], BKt[:, 0, 64 * h:64 * h + 64], Um[h % 2][:, :, :].rearrange("p b i -> p (b i)"), start=True, stop=True).then_inc(sn_ps, 1)
                        pe.wait_ge(sn_sb, h + 1)
                        if h >= 2:
                            pe.wait_ge(so_sb, h - 1)
                        for qq in range(4):
                            last = pe.transpose(ps[:, 2 + h % 2, 64 * qq:64 * qq + 64], Sn[h % 2][:, 2 * qq:2 * qq + 2, :].rearrange("p b i -> p (b i)"), ident[0:64, 0:64])
                        last.then_inc(so_ps, 1)

                @block.scalar
                def _(act):
                    for t in range(TILES):
                        C, w = chunks_of(t), ntok(t)
                        if t >= 1:
                            act.wait_ge(yt_ps2, t)
                        for x, src in ((0, AB[:, 0]), (1, zz[:, 0:4])):
                            for hb in range(2):
                                last = act.copy(AR[:, 0:C, hb::2, x, :].rearrange("p n c t -> p c n t"),
                                                src[64 * hb:64 * hb + 64, :, 128 * t:128 * t + w].rearrange("p c (n t) -> p c n t", n=C))
                        last.then_inc(cp_a, 1)
                        act.wait_ge(bkt_ps, t + 1)
                        act.copy(BKt[:, 0:C, :], ps[:, 6:6 + C, :]).then_inc(bkt_sb, 1)
                        if t == 4:
                            for b in range(NB):
                                act.wait_ge(sT_ps, b + 1)
                                act.copy(S0T[:, b, :], ps[0:64, 5, :]).then_inc(sT_sb, 1)
                            act.wait_ge(zsT_ps, 1)
                            act.copy(gm[0:64, 1].rearrange("p (b h) w -> p b (h w)", b=2), ps[0:64, 2:4, :]).then_inc(zsT_sb, 1)
                            act.wait_ge(zsT_sb, 1)
                        for ch in range(C):
                            n = chunk_no(t, ch)
                            act.wait_ge(gg_sb, 2 * t + C)
                            src = AR[:, ch, :, 0, :] if t < 4 else ZST[:, :, 0, :]
                            act.copy(gm[0:64, ch, :, 0:64], src).then_inc(zst, 1)
                            act.wait_ge(v_ps, n + 1)
                            act.copy(Sv[n % 2][64:128, :], ps[64:128, 6 + ch, :])
                            act.copy(Uv[n % 2][64:128, :], ps[64:128, 6 + ch, :]).then_inc(v_sb, 1)
                        for count, ch, n, (dst, l, rr, add) in inverse_units(t, "act"):
                            act.wait_ge(inv_ps, count)
                            act.copy(SL[dst][:, ch, :], ps[0:64, 3 * ch + n, :]).then_inc(inv_a, 1)
                        act.wait_ge(yn_a, t + 1)
                        act.activation(ysq_v[0:w, :], yb[0:w, :], ACT.Square).then_inc(yn_b, 1)
                        act.wait_ge(yn_c, 2 * t + 1)
                        act.activation(st8[0:w, 1, :], st8[0:w, 1, :], ACT.Sqrt).then_inc(yn_b, 1)
                        if t == 3:
                            act.wait_ge(pT_ps, 1)
                            act.copy(SpO[:, :, :], ps[:, 6, 0:256].rearrange("p (c j) -> p c j", c=4)).then_inc(pT_sb, 1)
                        act.wait_ge(yt_ps2, t + 1)
                        act.copy(mixf[:, 4:8, 128 * t:128 * t + w], ps[:, 7, :].rearrange("p (c t) -> p c t", c=4)[:, :, 0:w]).then_inc(yt_sb2, 1)
                    for h in range(NH):
                        act.wait_ge(so_ps, h + 1)
                        act.copy(So[:, h, :, :], ps[:, 2 + h % 2, 0:256].rearrange("p (q j) -> p q j", q=4)).then_inc(so_sb, 1)

                @block.vector
                def _(dve):
                    L = lambda ins: dve_chain(dve, ins)
                    dve.wait_ge(m_in, 48)
                    dve.memset(Sv[0][0:64, :], 0.0).then_inc(n_sb, 1)
                    for t in range(TILES):
                        C, w, ms = chunks_of(t), ntok(t), int(t == 4)
                        if t >= 1:
                            dve.wait_ge(yt_ps2, t)
                        for x, src in ((0, AB[:, 1]), (1, zz[:, 4:8])):
                            for hb in range(2):
                                last = dve.tensor_copy(BK[:, 0:C, hb::2, x, :].rearrange("p n c t -> p c n t"),
                                                       src[64 * hb:64 * hb + 64, :, 128 * t:128 * t + w].rearrange("p c (n t) -> p c n t", n=C))
                        last.then_inc(cp_d, 1)
                        for ch in range(C):
                            dve.wait_ge(gg_ps, 2 * t + ch + 1)
                            for half in range(2):
                                g4 = ps[:, 2 * ch + half, :].rearrange("p (h t) -> p h t", h=4)
                                L(dve.tensor_tensor(gm[:, ch, 4 * half:4 * half + 4, :], g4,
                                                    gmask[:, ms:ms + 1, :].to_broadcast([128, 4, 128]), ALU.mult))
                            up = gm[0:64, ch, :, 0:64]
                            hv = lambda s: SL[s][:, ch, :].rearrange("p (h t) -> p h t", h=NH)
                            bm = lambda m_, x: imask[:, m_, 2 * ms + x:2 * ms + x + 1, :].to_broadcast([64, NH, CH])
                            dve.tensor_tensor(hv(E_), up, bm(0, 1), ALU.mult)
                            dve.tensor_tensor(hv(DT), ps[0:64, 4 + ch, :].rearrange("p (h t) -> p h t", h=NH), bm(1, 0), ALU.mult)
                            L(dve.tensor_tensor(hv(D_), up, bm(0, 0), ALU.mult))
                            idb = ident[0:64, 0:64].rearrange("p (o t) -> p o t", o=1).to_broadcast([64, NH, CH])
                            dve.tensor_tensor(hv(Y_), hv(D_), idb, ALU.add).then_inc(gg_sb, 1)
                        if t == 4:
                            dve.tensor_copy(Sv[0][0:64, :].rearrange("p (h t) -> p h t", h=NH),
                                            ident[0:64, 0:64].rearrange("p (o t) -> p o t", o=1).to_broadcast([64, NH, CH]))
                        for count, ch, n, (dst, l, rr, add) in inverse_units(t, "dve"):
                            dve.wait_ge(inv_ps, count)
                            if add:
                                dve.tensor_tensor(SL[dst][:, ch, :], ps[0:64, 3 * ch + n, :], SL[dst][:, ch, :], ALU.add).then_inc(inv_d, 1)
                            else:
                                dve.tensor_copy(SL[dst][:, ch, :], ps[0:64, 3 * ch + n, :]).then_inc(inv_d, 1)
                        for ch in range(C):
                            n = chunk_no(t, ch)
                            S, Nx, Un = Sv[n % 2], Sv[(n + 1) % 2], Uv[n % 2]
                            dve.wait_ge(z_ps, n + 1)
                            dve.tensor_copy(Zs[:, :], ps[0:64, 0, :]).then_inc(z_sb, 1)
                            dve.wait_ge(u_ps, n + 1)
                            dve.tensor_copy(Un[0:64, :], ps[0:64, 1, :]).then_inc(u_sb, 1)
                            if t < 4:
                                dve.wait_ge(n_ps, n + 1)
                                L(dve.tensor_tensor(Nx[0:64, :], ps[0:64, 2, :], S[0:64, :], ALU.add))
                                nx = Nx[0:64, :].rearrange("p (h i) -> p h i", h=NH)
                                L(dve.tensor_tensor(nx, nx, pc[:, :, n:n + 1].to_broadcast([64, NH, CH]), ALU.mult))
                                dve.nop().then_inc(n_sb, 1)
                        dve.wait_ge(y_ps, t + 1)
                        hv = lambda x: x.rearrange("p (h i) -> p h i", h=NH)
                        per = lambda x: x.rearrange("p (h o) -> p h o", o=1).to_broadcast([w, NH, CH])
                        L(dve.tensor_reduce(st8[0:w, 0, :], hv(ps[0:w, 3, :]), AX.X, ALU.add))
                        L(dve.tensor_scalar(st8[0:w, 0, :], st8[0:w, 0, :], 1.0 / HD, None, ALU.mult))
                        dve.tensor_tensor(hv(yb[0:w, :]), hv(ps[0:w, 3, :]), per(st8[0:w, 0, :]), ALU.subtract).then_inc(yn_a, 1)
                        dve.wait_ge(yn_b, 2 * t + 1)
                        L(dve.tensor_reduce(st8[0:w, 1, :], hv(ysq_v[0:w, :]), AX.X, ALU.add))
                        dve.tensor_scalar(st8[0:w, 1, :], st8[0:w, 1, :], 1.0 / HD, GN_EPS, ALU.mult, ALU.add).then_inc(yn_c, 1)
                        dve.wait_ge(yn_b, 2 * t + 2)
                        dve.nop().then_inc(yn_c, 1)
                        L(dve.reciprocal(st8[0:w, 1, :], st8[0:w, 1, :]))
                        L(dve.tensor_tensor(hv(yb[0:w, :]), hv(yb[0:w, :]), per(st8[0:w, 1, :]), ALU.mult))
                        L(dve.tensor_tensor(yb[0:w, :], yb[0:w, :], lnw[0:w, :], ALU.mult))
                        L(dve.tensor_tensor(yb[0:w, :], yb[0:w, :], lnb[0:w, :], ALU.add))
                        dve.wait_ge(gv_ps, t + 1)
                        L(dve.tensor_tensor(hv(ysq_v[0:w, :]), hv(ps[0:w, 5, :]), per(bonus[0:w, t, :]), ALU.mult))
                        L(dve.tensor_tensor(yb[0:w, :], yb[0:w, :], ysq_v[0:w, :], ALU.add))
                        dve.tensor_tensor(yb[0:w, :], yb[0:w, :], ps[0:w, 4, :], ALU.mult).then_inc(yo, 1)
                    dve.wait_ge(yt_ps2, TILES)
                    for h in range(NH):
                        if h >= 2:
                            dve.wait_ge(sn_ps, h - 1)
                        hs = slice(64 * h, 64 * h + 64)
                        dve.tensor_tensor(Um[h % 2][:, :, :], Uv[0][:, hs].rearrange("p (o i) -> p o i", o=1).to_broadcast([128, NB, CH]),
                                          smask[:, :].rearrange("p (b o) -> p b o", o=1).to_broadcast([128, NB, CH]), ALU.mult).then_inc(um_ready, 1)
                        dve.wait_ge(sn_ps, h + 1)
                        if h >= 2:
                            dve.wait_ge(so_ps, h - 1)
                        L(dve.tensor_tensor(Sn[h % 2][:, :, :], ps[0:64, h % 2, :].rearrange("p (b i) -> p b i", b=NB), S0T[:, :, hs], ALU.add))
                        dve.tensor_tensor(Sn[h % 2][:, :, :], Sn[h % 2][:, :, :],
                                          pc[:, h, 8:16].rearrange("p (b o) -> p b o", o=1).to_broadcast([64, NB, CH]), ALU.mult).then_inc(sn_sb, 1)

            flush([(flat(zlast[:, :, :]), 9 * RT, [(0, RT, o["shift_p"].rearrange("b o (c p) -> (b o c) p", p=128)),
                                                   (RT, 9 * RT, o["shift_s"].rearrange("b o (c p) -> (b o c) p", p=128))])], Region(RZ))
            mix_out(mixf)

        def mix_out(mixf):
            reg = Region(R + 8 * T * 4 + 2 * KT * TPAD * 4)
            mhi, mlo = reg.take("mix_hi", [128, KT, T], F32R), reg.take("mix_lo", [128, KT, T], F32R)
            mix_hi_ready, mix_lo_ready = sem("mix_hi_ready"), sem("mix_lo_ready")
            with nc.Block() as block:
                @block.scalar
                def _(act):
                    for c in range(KT):
                        act.copy(mhi[:, c, :], mixf[:, c, :]).then_inc(mix_hi_ready, 1)

                @block.vector
                def _(dve):
                    for c in range(KT):
                        dve.wait_ge(mix_hi_ready, c + 1)
                        dve.tensor_tensor(mlo[:, c, :], mixf[:, c, :], mhi[:, c, :].bitcast(F32), ALU.subtract)
            residual(st_out, mhi, mlo)

        keep_semaphores()
        even_mixer()
        retire_semaphores()
        ffn(0, ffn0, V_FFN)
        conv_mixer()
        ffn(1, ffn1, V_FFN + 8)
        store_y()


_INS = ["x_prompt", "x_sample", "cache_cmp_kv", "cache_slc_kv", "cache_win_kv", "state_rwkv_wkv",
        "state_rwkv_shift", "state_conv", "state_ffn_conv", "page_table", "norm_mix", "norm_ffn",
        "rel_bias", "w_in_even", "w_out_even", "q_norm", "k_norm", "phi_pe", "phi_w1", "phi_w2",
        "rwkv_mu", "rwkv_w0", "rwkv_w2", "rwkv_a0", "rwkv_a2", "rwkv_g2", "rwkv_kk", "rwkv_ka", "rwkv_rk",
        "rwkv_ln_w", "rwkv_ln_b", "w_in_odd", "conv_w", "w_out_odd", "ffn_up", "ffn_conv", "ffn_down"]
_OUTS = [("y_prompt", (1, TP, D)), ("y_sample", (NB, TS, D)),
         ("cmp_p", (1, 1, TP, 2, 2, HD)), ("cmp_s", (NB, 1, TS, 2, 2, HD)),
         ("slc_p", (1, 1, TP, 2, 2, HD)), ("slc_s", (NB, 1, TS, 2, 2, HD)),
         ("win_p", (1, 1, TP, 2, 2, HD)), ("win_s", (NB, 1, 512, 2, 2, HD)),
         ("wkv_p", (1, 1, NH, HD, HD)), ("wkv_s", (NB, 1, NH, HD, HD)),
         ("shift_p", (1, 1, W_RW)), ("shift_s", (NB, 1, W_RW)),
         ("conv_p", (1, 1, 2, D)), ("conv_s", (NB, 1, 2, D)),
         ("ffn_p", (1, 2, 2, DFF)), ("ffn_s", (NB, 2, 2, DFF))]


def kernel(**inputs):
    import concourse.bacc as bacc
    from concourse.bass_utils import run_bass_kernel_spmd

    nc = bacc.Bacc("TRN2", target_bir_lowering=False, num_devices=1)
    arrays, ins, outs, consts = {}, {}, {}, {}
    for name in _INS:
        a = np.ascontiguousarray(inputs[name])
        arrays[f"in_{name}"] = a
        ins[name] = nc.dram_tensor(f"in_{name}", a.shape, mybir.dt.from_np(a.dtype), kind="ExternalInput").ap()
    for name, a in tables().items():
        arrays[f"const_{name}"] = a
        consts[name] = nc.dram_tensor(f"const_{name}", a.shape, F32, kind="ExternalInput").ap()
    for name, shape in _OUTS:
        outs[name] = nc.dram_tensor(f"out_{name}", shape, F32, kind="ExternalOutput").ap()
    build(nc, ins, outs, consts)
    r = run_bass_kernel_spmd(nc, [arrays], core_ids=[0])
    return tuple(r.results[0][f"out_{name}"] for name, _ in _OUTS)
```

```python
import concourse.bass as bass
from concourse import mybir
import numpy as np
import math
from contextlib import ExitStack

F32 = mybir.dt.float32
F32R = mybir.dt.float32r
I32 = mybir.dt.int32
ALU = mybir.AluOpType
ACT = mybir.ActivationFunctionType
AX = mybir.AxisListType

D = 1024
KT = D // 128
TP = 512
NB, TS = 8, 8
NS = NB * TS
T = TP + NS
HT = T // 2
TPAD = 640
DFF = 2816
FT = DFF // 128
HD = 64
NH = 8
W_NSA = 1304
W_RW = 1792
RT = W_RW // 128
SLAB = 2048
EPS = 1e-6
GN_EPS = 64e-5
NEG = -1e30
FLOOR = -1e25
CH = 64
PAGE = 128
NBK = 32
RVL = 1168
RV0 = 638
BTW = 1040

V_MIX, V_FFN, V_CONV, V_MU, V_W0, V_A0, V_KK, V_KA, V_RK, V_ROWS = 0, 16, 32, 56, 70, 74, 78, 82, 86, 90


def tables():
    dist = RV0 - np.arange(RVL)
    n = np.maximum(dist, 0)
    nf = np.maximum(n, 1).astype(np.float32)
    large = 16 + (np.log(nf / np.float32(16)) / np.float32(math.log(8.0)) * np.float32(16)).astype(np.int32)
    bucket = np.where(n < 16, n, np.minimum(large, 31))
    onehot = (bucket[None, :] == np.arange(NBK)[:, None]).astype(np.float32)
    masked = np.broadcast_to(np.where(dist >= 0, 0.0, NEG).astype(np.float32)[None, :], (NH, RVL)).copy()
    s = np.arange(CH)
    strict, incl = s[:, None] < s[None, :], s[:, None] <= s[None, :]
    same = (s[:, None] // TS) == (s[None, :] // TS)
    def gmask(m):
        return np.block([[strict & m, incl & m], [strict & m, incl & m]])
    gm = np.stack([gmask(np.ones((CH, CH), bool)), gmask(same)], 1).astype(np.float32)
    blk = (s[:, None] // 16) == (s[None, :] // 16)
    up = np.stack([strict & blk, strict & ~blk, strict & blk & same, strict & ~blk & same], 1)
    lo = np.stack([strict.T & blk, strict.T & ~blk, strict.T & blk & same, strict.T & ~blk & same], 1)
    inv = np.tile(np.stack([up, lo], 1).astype(np.float32), (2, 1, 1, 1))
    keep = np.ones((128, T), np.float32)
    keep[:, 0:TP:CH] = 0.0
    keep[:, TP::TS] = 0.0
    seq = ((np.arange(128)[:, None] % CH) // TS == np.arange(NB)[None, :]).astype(np.float32)
    head = np.zeros((128, 128), np.float32)
    head[:64, :64] = 1.0
    head[64:, 64:] = 1.0
    row = np.arange(128)
    wmask = np.where(np.arange(TS)[None, :] <= (row % TS)[:, None], NEG, 0.0).astype(np.float32)
    return dict(onehot=onehot, masked=masked, gmask=gm, invmask=inv, keep=keep, seqmask=seq,
                headones=head, ident=np.eye(128, dtype=np.float32),
                flip=np.eye(128, dtype=np.float32)[::-1].copy(), wmask=wmask)



class Chain:

    def __init__(self, sem):
        self.sem, self.n, self.loop = sem, 0, None

    def __call__(self, eng, ins):
        ins.then_inc(self.sem, 1)
        self.n += 1
        if self.loop is None:
            eng.wait_ge(self.sem, self.n)
        else:
            i, start, per, _ = self.loop
            eng.wait_ge(self.sem, i * per + self.n)
        return ins

    def begin(self, i, per, trips):
        self.loop = (i, self.n, per, trips)

    def end(self):
        i, start, per, trips = self.loop
        assert self.n - start == per, (self.n - start, per)
        self.n = start + per * trips
        self.loop = None


def build(nc, a, o, k):
    ctx = ExitStack()
    base = [nc.sbuf_base + (-nc.sbuf_base) % 64]
    names = [0]

    def at(name, shape, dt, offset):
        names[0] += 1
        return nc.alloc_sbuf_tensor_at(f"{name}_{names[0]}", shape, dt, offset=offset)

    def fixed(name, shape, dt=F32):
        size = 4 * int(np.prod(shape[1:]))
        t = at(name, shape, dt, base[0])
        base[0] += size + (-size) % 32
        return t

    sems = {}

    lasting = []

    def sem(name):
        if name not in sems:
            sems[name] = nc.alloc_semaphore(name)
        return sems[name]

    def keep_semaphores():
        lasting[:] = list(sems)

    def retire_semaphores():
        old = [sems.pop(name) for name in list(sems) if name not in lasting]
        nc.clear_and_free_semaphores(old)
        nc.all_engine_barrier()

    with ctx:
        ctx.enter_context(nc.allow_non_contiguous_dma(reason="small tables"))
        raw = [fixed(f"w_raw{s}", [128, SLAB]) for s in range(2)]
        whi = [fixed(f"w_hi{s}", [128, SLAB], F32R) for s in range(2)]
        wlo = [fixed(f"w_lo{s}", [128, SLAB], F32R) for s in range(2)]
        xT = fixed("xT", [128, KT, T])
        ident = fixed("ident", [128, 128])
        ones = fixed("ones", [128, 128])
        vec = fixed("vec", [128, V_ROWS])
        ffnw = fixed("ffnw", [128, 2, 3, FT])
        convst = fixed("convst", [128, NB, 2, KT])
        ffnst = fixed("ffnst", [128, 2, NB, 2, FT])
        newconv = fixed("newconv", [128, 9, 2, KT])
        newffn = fixed("newffn", [128, 9, 2, FT])
        zlast = fixed("zlast", [128, 9, RT])
        R = base[0]
        END = nc.sbuf_usable_end

        class Region:
            def __init__(self, start):
                self.at = start + (-start) % 32

            def take(self, name, shape, dt=F32):
                size = 4 * int(np.prod(shape[1:]))
                t = at(name, shape, dt, self.at)
                self.at += size + (-size) % 32
                assert self.at <= END, (name, self.at - END)
                return t

        ps = ctx.enter_context(nc.psum_tensor("ps", [128, 8, 512], F32))
        rv_dram = nc.dram_tensor("rv", (NH, RVL), F32, kind="Internal").ap()
        gate_dram = nc.dram_tensor("gates", (NS, 24), F32, kind="Internal").ap()

        w_in, w_out = a["w_in_even"][0], a["w_out_even"][0]
        w_in_odd, w_out_odd = a["w_in_odd"][0], a["w_out_odd"][0]

        def cols(w, kt0, kts, c0, width):
            return w.rearrange("(t p) n -> p t n", p=128)[:, kt0:kt0 + kts, bass.ds(c0, width)]

        stages = []
        n_slabs = [0]
        bank_uses = [0, 0]

        def stage(n, kts, width, src):
            st = dict(base=n_slabs[0], n=n, kts=kts, width=width, src=src, before=tuple(bank_uses))
            n_slabs[0] += n
            bank_uses[0] += (n + 1) // 2
            bank_uses[1] += n // 2
            stages.append(st)
            return st

        st_nsa = stage(5, KT, 256, lambda s: cols(w_in, 0, KT, 256 * s, 256))
        st_gate = stage(1, KT, 24, lambda s: cols(w_in, 0, KT, 1280, 24))
        st_rw = stage(7, KT, 256, lambda s: cols(w_in, 0, KT, W_NSA + 256 * s, 256))
        st_out = stage(4, KT, 256, lambda s: cols(w_out, 0, KT, 256 * s, 256))

        def ffn_stages(l):
            out = []
            up, down = a["ffn_up"][l], a["ffn_down"][l]
            for f0, nf in ((0, 12), (12, 10)):
                def src_up(s, f0=f0, side=None):
                    return cols(up, 0, KT, side * DFF + 128 * f0 + 256 * s, 256)
                out.append((stage(nf, KT, 256, src_up), stage(8, nf, 128, lambda s, f0=f0, nf=nf: cols(down, f0, nf, 128 * s, 128)), f0, nf))
            return out

        ffn0 = ffn_stages(0)
        st_odd = stage(12, KT, 256, None)
        st_oout = stage(4, KT, 256, lambda s: cols(w_out_odd, 0, KT, 256 * s, 256))
        ffn1 = ffn_stages(1)

        def stage_at(g):
            for st in stages:
                if st["base"] <= g < st["base"] + st["n"]:
                    return st
            return None

        def slab_source(st, p, q, m):
            if st is st_odd:
                return cols(w_in_odd, 0, KT, (D, 2 * D, 0)[q % 3] + 256 * (p * (m // 3) + q // 3), 256)
            if st["n"] in (12, 10) and st is not st_odd:
                return st["src"](p * (m // 2) + q // 2, side=q % 2)
            return st["src"](p * m + q)

        def slab_view(t, st):
            return t[:, 0:st["kts"] * st["width"]]

        w_loaded = [sem("w_loaded0"), sem("w_loaded1")]
        w_hi_ready, w_lo_ready, slab_done = sem("w_hi_ready"), sem("w_lo_ready"), sem("slab_done")
        banks_free = [sem("banks_free_low"), sem("banks_free_high")]

        def load_slab(sp, st, p, q, m):
            g = st["base"] + p * m + q
            slot = (st["base"] + q) % 2
            if st["base"] + q >= 2:
                sp.wait_ge(w_lo_ready, g - 1)
            view = slab_view(raw[slot], st).rearrange("p (t n) -> p t n", t=st["kts"])
            sp.dma_start(view, slab_source(st, p, q, m)).then_inc(w_loaded[slot], 16)

        def slot_count(st, p, q, m):
            return 16 * ((st["base"] + q) // 2 + 1) + p * (8 * m)

        def split_hi(act, st, p, q, m):
            g = st["base"] + p * m + q
            slot = (st["base"] + q) % 2
            act.wait_ge(w_loaded[slot], slot_count(st, p, q, m))
            if st["base"] + q >= 2:
                act.wait_ge(slab_done, g - 1)
            act.activation(slab_view(whi[slot], st), slab_view(raw[slot], st), ACT.Copy).then_inc(w_hi_ready, 1)

        def split_lo(pool, st, p, q, m):
            g = st["base"] + p * m + q
            slot = (st["base"] + q) % 2
            pool.wait_ge(w_hi_ready, g + 1)
            pool.tensor_tensor(slab_view(wlo[slot], st), slab_view(raw[slot], st),
                               slab_view(whi[slot], st).bitcast(F32), ALU.subtract).then_inc(w_lo_ready, 1)

        def follow(g):
            st = stage_at(g)
            return None if st is None else (st, 0, g - st["base"], st_period(st))

        def st_period(st):
            return 12 if st is st_odd else 16

        def loads_after(sp, g):
            for x in (g, g + 1):
                f = follow(x)
                if f is not None:
                    load_slab(sp, *f)

        def wait_banks(pe, st, p, q, m):
            pe.wait_ge(banks_free[q % 2], st["before"][q % 2] + q // 2 + 1 + p * (m // 2))

        def products(pe, st, p, q, m, bank, xs, xhi, xlo, ready=None):
            g = st["base"] + p * m + q
            slot = (st["base"] + q) % 2
            wait_banks(pe, st, p, q, m)
            pe.wait_ge(w_lo_ready, g + 1)
            W = st["width"]
            for j in range(W // 128):
                for t in range(st["kts"]):
                    if ready is not None and j == 0:
                        ready(pe, t)
                    c = t * W + j * 128
                    for n, (w, x) in enumerate(((whi, xhi), (whi, xlo), (wlo, xhi))):
                        for half in range(2):
                            last = pe.matmul(ps[:, bank + 2 * j + half, 0:HT], w[slot][:, c:c + 128],
                                             x[:, xs + t, half * HT:(half + 1) * HT],
                                             start=(t == 0 and n == 0), stop=(t == st["kts"] - 1 and n == 2))
            last.then_inc(slab_done, 1)

        tmp = Region(R)
        xin = tmp.take("xin", [128, 5, D])
        rows = [tmp.take("rows_vec", [V_ROWS, 128]), tmp.take("rows_f0", [66, 128]), tmp.take("rows_f1", [66, 128]),
                tmp.take("rows_conv", [128, 128])]
        rows_st = [[tmp.take(f"rows_st{l}{n}", [88, 128]) for n in range(4)] for l in range(2)]
        x_in, x_tiles = sem("x_in"), sem("x_tiles")
        small_in, small_t = sem("small_in"), sem("small_t")
        start_ev, small_ev = sem("start_ev"), sem("small_ev")
        consts_in = sem("consts_in")
        dve_chain, act_chain, pool_chain = Chain(sem("dve_chain")), Chain(sem("act_chain")), Chain(sem("pool_chain"))
        ones_set = sem("ones_set")

        jobs = [(rows[0], V_ROWS, vec[:, :]), (rows[1], 66, ffnw[:, 0, :, :]), (rows[2], 66, ffnw[:, 1, :, :]),
                (rows[3], 128, convst[:, :, :, :])]
        for l in range(2):
            for n in range(4):
                jobs.append((rows_st[l][n], 88, ffnst[:, l, 2 * n:2 * n + 2, :, :]))

        def flat(t):
            n = len(t.shape)
            if n == 2:
                return t
            pat = {3: "p a b -> p (a b)", 4: "p a b c -> p (a b c)", 5: "p a b c d -> p (a b c d)"}[n]
            return t.rearrange(pat)

        ext_ready, conv_done, gate_ready = sem("ext_ready"), sem("conv_done"), sem("gate_ready")
        g_f, g_hi_ready, g_lo_ready = sem("g_f"), sem("g_hi_ready"), sem("g_lo_ready")
        with nc.Block() as block:
            @block.sync
            def _(sp):
                sp.dma_start(ident[:, :], k["ident"]).then_inc(consts_in, 16)
                for t in range(4):
                    sp.dma_start(xin[:, t, :], a["x_prompt"][0, 128 * t:128 * t + 128, :]).then_inc(x_in, 16)
                sp.dma_start(xin[0:NS, 4, :], a["x_sample"].rearrange("b t d -> (b t) d")).then_inc(x_in, 16)
                loads_after(sp, 0)

                def row_load(dst, src):
                    sp.dma_start(dst, src).then_inc(small_in, 16)
                v = rows[0]
                row_load(v[V_MIX:V_MIX + 16, :], a["norm_mix"].rearrange("l (c p) -> (l c) p", p=128))
                row_load(v[V_FFN:V_FFN + 16, :], a["norm_ffn"].rearrange("l (c p) -> (l c) p", p=128))
                row_load(v[V_CONV:V_CONV + 24, :], a["conv_w"][0].rearrange("k (c p) -> (k c) p", p=128))
                row_load(v[V_MU:V_MU + 14, :], a["rwkv_mu"].rearrange("l (c p) -> (l c) p", p=128))
                for at_, name in ((V_W0, "rwkv_w0"), (V_A0, "rwkv_a0"), (V_KK, "rwkv_kk"), (V_KA, "rwkv_ka")):
                    row_load(v[at_:at_ + 4, :], a[name].rearrange("l (c p) -> (l c) p", p=128))
                row_load(v[V_RK:V_RK + 4, :], a["rwkv_rk"][0].rearrange("(c h) d -> c (h d)", h=2))
                for l in range(2):
                    row_load(rows[1 + l][:, :], a["ffn_conv"][l].rearrange("k (c p) -> (k c) p", p=128))
                row_load(rows[3][:, :], a["state_conv"][:, 0].rearrange("b k (c p) -> (b k c) p", p=128))
                for l in range(2):
                    for n in range(4):
                        for h in range(2):
                            row_load(rows_st[l][n][44 * h:44 * h + 44, :],
                                     a["state_ffn_conv"][2 * n + h, l].rearrange("k (c p) -> (k c) p", p=128))

            @block.vector
            def _(dve):
                dve.memset(ones[:, :], 1.0).then_inc(ones_set, 1)
                for s in banks_free:
                    dve.nop().then_inc(s, 1)
                for s in (ext_ready, conv_done, gate_ready, g_f, g_hi_ready, g_lo_ready):
                    dve.nop().then_inc(s, 2)
                for n in range(10):
                    dve.wait_ge(x_tiles, n + 1)
                    t, c = n // 2, n % 2
                    w = 128 if t < 4 else NS
                    dve.tensor_copy(xT[:, 4 * c:4 * c + 4, 128 * t:128 * t + w],
                                    ps[:, n % 4, :].rearrange("p (c t) -> p c t", c=4)[:, :, 0:w]).then_inc(start_ev, 1)

            @block.scalar
            def _(act):
                split_hi(act, *follow(0))
                for n, (src, r, dst) in enumerate(jobs):
                    act.wait_ge(small_t, n + 1)
                    act.copy(flat(dst), ps[:, 4 + n % 4, 0:r]).then_inc(small_ev, 1)

            @block.gpsimd
            def _(pool):
                split_lo(pool, *follow(0))

            @block.tensor
            def _(pe):
                pe.wait_ge(consts_in, 16)
                pe.wait_ge(x_in, 80)
                for n in range(10):
                    t, c = n // 2, n % 2
                    w = 128 if t < 4 else NS
                    if n >= 4:
                        pe.wait_ge(start_ev, n - 3)
                    for q in range(4):
                        last = pe.transpose(ps[:, n % 4, 128 * q:128 * q + w],
                                            xin[0:w, t, (4 * c + q) * 128:(4 * c + q + 1) * 128], ident[0:w, 0:w])
                    last.then_inc(x_tiles, 1)
                pe.wait_ge(small_in, 16 * (9 + 2 + 1 + 16))
                for n, (src, r, dst) in enumerate(jobs):
                    if n >= 4:
                        pe.wait_ge(small_ev, n - 3)
                    pe.transpose(ps[:, 4 + n % 4, 0:r], src[:, :], ident[0:r, 0:r]).then_inc(small_t, 1)

        sq_ready, sq_used, ms_ready = sem("sq_ready"), sem("sq_used"), sem("ms_ready")
        std_ready, h_f, h_hi_ready, h_lo_ready, ms_used = sem("std_ready"), sem("h_f"), sem("h_hi_ready"), sem("h_lo_ready"), sem("ms_used")
        norms = [0]

        TOP = END - END % 32
        sq_sum = at("sq_sum", [128, T], F32, TOP - 4 * T)
        sq_slot = [at("sq_slot", [128, T], F32, TOP - 4 * T * (2 + n)) for n in range(2)]
        x_done, sq_set, sq_added = sem("x_done"), sem("sq_set"), sem("sq_added")
        h_lo_dve = sem("h_lo_dve")
        DVE_LO = (2, 5)
        squares = [0]

        def norm(gain, hhi, hlo, region, summed=True):
            reg = Region(region)
            sq = None if summed else reg.take("sq", [128, 2, T])
            hf = reg.take("hf", [128, 3, T])
            std = reg.take("std", [128, T])
            rstd = reg.take("rstd", [128, T])
            i0 = norms[0]
            norms[0] += 1
            b0, n_pool, n_dve = 8 * i0, (KT - len(DVE_LO)) * i0, len(DVE_LO) * i0

            def lo_ready(eng, c):
                if c in DVE_LO:
                    eng.wait_ge(h_lo_dve, n_dve + DVE_LO.index(c) + 1)
                else:
                    eng.wait_ge(h_lo_ready, n_pool + sum(x not in DVE_LO for x in range(c + 1)))

            def act_part(act):
                if not summed:
                    for c in range(KT):
                        if c >= 2:
                            act.wait_ge(sq_used, c - 1)
                        act.activation(sq[:, c % 2, :], xT[:, c, :], ACT.Square).then_inc(sq_ready, 1)
                act.wait_ge(ms_used, i0 + 1)
                act.activation(std[:, :], std[:, :], ACT.Sqrt).then_inc(std_ready, 1)
                for c in range(KT):
                    act.wait_ge(h_f, b0 + c + 1)
                    act.copy(hhi[:, c, 0:T], hf[:, c % 3, :]).then_inc(h_hi_ready, 1)

            def pe_part(pe):
                if summed:
                    pe.wait_ge(sq_added, 8 * squares[0])
                    for half in range(2):
                        last = pe.matmul(ps[:, half, 0:HT], ones[:, :], sq_sum[:, half * HT:(half + 1) * HT], start=True, stop=True)
                    last.then_inc(ms_ready, 1)
                    return
                for c in range(KT):
                    pe.wait_ge(sq_ready, c + 1)
                    for half in range(2):
                        last = pe.matmul(ps[:, half, 0:HT], ones[:, :], sq[:, c % 2, half * HT:(half + 1) * HT],
                                         start=(c == 0), stop=(c == KT - 1))
                    last.then_inc(sq_used, 1)
                pe.nop().then_inc(ms_ready, 1)

            def dve_part(dve):
                if not summed:
                    dve.wait_ge(sq_used, KT)
                dve.wait_ge(ms_ready, i0 + 1)
                dve.tensor_scalar(std[:, :].rearrange("p (a t) -> p a t", a=2), ps[:, 0:2, 0:HT],
                                  1.0 / D, EPS, ALU.mult, ALU.add).then_inc(ms_used, 1)
                dve.wait_ge(std_ready, i0 + 1)
                dve_chain(dve, dve.reciprocal(rstd[:, :], std[:, :]))
                for c in range(KT + 1):
                    if c < KT:
                        if c >= 3:
                            lo_ready(dve, c - 3)
                        dve.scalar_tensor_tensor(hf[:, c % 3, :], xT[:, c, :], vec[:, gain + c:gain + c + 1], rstd[:, :],
                                                 ALU.mult, ALU.mult).then_inc(h_f, 1)
                    if c - 1 in DVE_LO:
                        dve.wait_ge(h_hi_ready, b0 + c)
                        dve.tensor_tensor(hlo[:, c - 1, 0:T], hf[:, (c - 1) % 3, :], hhi[:, c - 1, 0:T].bitcast(F32),
                                          ALU.subtract).then_inc(h_lo_dve, 1)

            def pool_part(pool):
                for c in range(KT):
                    if c not in DVE_LO:
                        pool.wait_ge(h_hi_ready, b0 + c + 1)
                        pool.tensor_tensor(hlo[:, c, 0:T], hf[:, c % 3, :], hhi[:, c, 0:T].bitcast(F32),
                                           ALU.subtract).then_inc(h_lo_ready, 1)
            return dict(act=act_part, pe=pe_part, dve=dve_part, pool=pool_part, ready=lo_ready)

        def residual(st, hhi, hlo, sum_squares=True):
            n, base_g, J = st["n"], st["base"], st["width"] // 128
            s0 = 8 * squares[0]
            if sum_squares:
                squares[0] += 1

            def squares_of(act, f, f0):
                act.wait_ge(x_done, s0 + f + 1)
                if f0 >= 2:
                    act.wait_ge(sq_added, s0 + f - 1)
                act.activation(sq_slot[f0 % 2][:, :], xT[:, f, :], ACT.Square).then_inc(sq_set, 1)

            def add_square(pool, f):
                pool.wait_ge(sq_set, s0 + f + 1)
                if f == 0:
                    pool.tensor_copy(sq_sum[:, :], sq_slot[0][:, :]).then_inc(sq_added, 1)
                else:
                    pool.wait_ge(sq_added, s0 + f)
                    pool.tensor_tensor(sq_sum[:, :], sq_sum[:, :], sq_slot[f % 2][:, :], ALU.add).then_inc(sq_added, 1)
            with nc.Block() as block:
                @block.sync
                def _(sp):
                    with sp.Fori(0, (n - 2) // 2) as i:
                        for q in (2, 3):
                            load_slab(sp, st, i, q, 2)
                    loads_after(sp, base_g + n)

                @block.scalar
                def _(act):
                    for g in range(1, n + 2):
                        if g < n:
                            split_hi(act, st, 0, g, 16)
                        elif g == n and follow(base_g + n):
                            split_hi(act, *follow(base_g + n))
                        if sum_squares and g >= 2:
                            for j in range(J):
                                squares_of(act, J * (g - 2) + j, J * (g - 2) + j)

                @block.gpsimd
                def _(pool):
                    for g in range(1, n + 2):
                        if g < n:
                            split_lo(pool, st, 0, g, 16)
                        elif g == n and follow(base_g + n):
                            split_lo(pool, *follow(base_g + n))
                        if sum_squares and g >= 2:
                            for j in range(J):
                                add_square(pool, J * (g - 2) + j)

                @block.tensor
                def _(pe):
                    for i in range(n // 2):
                        for q in (0, 1):
                            products(pe, st, i, q, 2, 4 * q, 0, hhi, hlo)

                @block.vector
                def _(dve):
                    with dve.Fori(0, n // 2) as i:
                        for q in (0, 1):
                            dve.wait_ge(slab_done, base_g + 2 * i + q + 1)
                            for j in range(J):
                                x = xT[:, bass.ds(2 * J * i + J * q + j, 1), :].rearrange("p o (a t) -> p (o a) t", a=2)
                                b = 4 * q + 2 * j
                                last = dve.tensor_tensor(x, ps[:, b:b + 2, 0:HT], x, ALU.add)
                                if sum_squares:
                                    last.then_inc(x_done, 1)
                            if sum_squares:
                                dve.wait_ge(x_done, s0 + J * (2 * i + q + 1))
                                dve.nop().then_inc(banks_free[q], 1)
                            else:
                                last.then_inc(banks_free[q], 1)

        EW = 2 + TP + NB * (TS + 2)
        YW = EW - 2

        def prompt_of(t):
            return t[:, 2:2 + TP]

        def sample_of(t):
            return t[:, 2 + TP:EW].rearrange("p (b t) -> p b t", b=NB)

        zeroed = sem("zeroed")
        gates_done = [2]
        tiles_done = [2]
        zero_count = [0]
        H1 = TP - HT

        def gated_mult(dve, out, y, bank):
            dve.tensor_tensor(out[:, 0:HT], y[:, 0:HT], ps[:, bank, 0:HT], ALU.mult)
            dve.tensor_tensor(out[:, HT:TP], y[:, HT:TP], ps[:, bank + 1, 0:H1], ALU.mult)
            ys = y[:, TP + 2:TP + 2 + NB * 10].rearrange("p (b t) -> p b t", b=NB)[:, :, 0:TS]
            return dve.tensor_tensor(out[:, TP:T].rearrange("p (b t) -> p b t", b=NB), ys,
                                     ps[:, bank + 1, H1:HT].rearrange("p (b t) -> p b t", b=NB), ALU.mult)

        def convolve(dve, y, ext, w):
            dve_chain(dve, dve.tensor_scalar(y[:, 0:YW], ext[:, 0:YW], w(0), None, ALU.mult))
            dve_chain(dve, dve.scalar_tensor_tensor(y[:, 0:YW], ext[:, 1:1 + YW], w(1), y[:, 0:YW], ALU.mult, ALU.add))
            return dve.scalar_tensor_tensor(y[:, 0:YW], ext[:, 2:2 + YW], w(2), y[:, 0:YW], ALU.mult, ALU.add)

        def keep_last(dve, new, f, ext):
            dve.tensor_copy(new[:, 0, :, bass.ds(f, 1)], ext[:, TP:TP + 2].rearrange("p (k o) -> p k o", o=1))
            dve.tensor_copy(new[:, 1:9, :, bass.ds(f, 1)].rearrange("p b k o -> p b (k o)"), sample_of(ext)[:, :, TS:TS + 2])

        def ffn_up(l, st, f0, hhi, hlo, ghi, glo, reg, norm_parts):
            ext = [reg.take("ext", [128, EW]) for _ in range(2)]
            y = [reg.take("y", [128, EW]) for _ in range(2)]
            gf = [reg.take("gf", [128, T]) for _ in range(2)]
            n, G, t0 = st["n"], st["base"], tiles_done[0]
            pairs = n // 2
            tg = gates_done[0]
            gates_done[0] += n
            tiles_done[0] += n
            zero_count[0] += 2
            zc = zero_count[0]
            with nc.Block() as block:
                @block.sync
                def _(sp):
                    with sp.Fori(0, pairs - 1) as i:
                        for q in (2, 3):
                            load_slab(sp, st, i, q, 2)
                    loads_after(sp, G + n)

                @block.gpsimd
                def _(pool):
                    if norm_parts:
                        norm_parts["pool"](pool)

                    def pair(i, nxt):
                        split_lo(pool, st, i, 1, 2)
                        split_lo(pool, *nxt)
                        for j in range(2):
                            pool.wait_ge(g_hi_ready, t0 + 2 * i + j + 1)
                            pool.tensor_tensor(glo[:, bass.ds(2 * i + j, 1), :], gf[j][:, :].rearrange("p (o t) -> p o t", o=1),
                                               ghi[:, bass.ds(2 * i + j, 1), :].bitcast(F32), ALU.subtract).then_inc(g_lo_ready, 1)
                    with pool.Fori(0, pairs - 1) as i:
                        pair(i, (st, i, 2, 2))
                    pair(pairs - 1, follow(G + n))

                @block.scalar
                def _(act):
                    if norm_parts:
                        norm_parts["act"](act)

                    def pair(i, nxt):
                        split_hi(act, st, i, 1, 2)
                        act.wait_ge(slab_done, G + 2 * i + 1)
                        for j in range(2):
                            act.wait_ge(conv_done, t0 + 2 * i + j - 1)
                            e = ext[j]
                            act.copy(e[:, 2:2 + HT], ps[:, 2 * j, 0:HT])
                            act.copy(e[:, 2 + HT:2 + TP], ps[:, 2 * j + 1, 0:H1])
                            act.copy(sample_of(e)[:, :, 0:2], ffnst[:, l, :, :, bass.ds(f0 + 2 * i + j, 1)].rearrange("p b k o -> p b (k o)"))
                            last = act.copy(sample_of(e)[:, :, 2:2 + TS],
                                            ps[:, 2 * j + 1, H1:HT].rearrange("p (b t) -> p b t", b=NB)).then_inc(ext_ready, 1)
                        act.wait_ge(ext_ready, tg + 2 * i + 2)
                        act.nop().then_inc(banks_free[0], 1)
                        split_hi(act, *nxt)
                        for j in range(2):
                            act.wait_ge(conv_done, t0 + 2 * i + j + 1)
                            act.activation(y[j][:, 0:YW], y[j][:, 0:YW], ACT.Silu).then_inc(gate_ready, 1)
                        for j in range(2):
                            act.wait_ge(g_f, t0 + 2 * i + j + 1)
                            act.copy(ghi[:, bass.ds(2 * i + j, 1), :], gf[j][:, :].rearrange("p (o t) -> p o t", o=1)).then_inc(g_hi_ready, 1)
                    act.wait_ge(zeroed, zc)
                    with act.Fori(0, pairs - 1) as i:
                        pair(i, (st, i, 2, 2))
                    pair(pairs - 1, follow(G + n))

                @block.tensor
                def _(pe):
                    if norm_parts:
                        norm_parts["pe"](pe)
                    for i in range(pairs):
                        for q in (0, 1):
                            products(pe, st, i, q, 2, 4 * q, 0, hhi, hlo, norm_parts["ready"] if norm_parts and i == q == 0 else None)

                @block.vector
                def _(dve):
                    if norm_parts:
                        norm_parts["dve"](dve)
                    for e in ext:
                        dve.memset(e[:, 0:2], 0.0).then_inc(zeroed, 1)
                    with dve.Fori(0, pairs) as i:
                        dve_chain.begin(i, 4, pairs)
                        for j in range(2):
                            dve.wait_ge(ext_ready, tg + 2 * i + j + 1)
                            f = f0 + 2 * i + j
                            keep_last(dve, newffn, f, ext[j])
                            convolve(dve, y[j], ext[j], lambda kk: ffnw[:, l, kk, bass.ds(f, 1)]).then_inc(conv_done, 1)
                        dve.wait_ge(slab_done, G + 2 * i + 2)
                        for j in range(2):
                            dve.wait_ge(gate_ready, tg + 2 * i + j + 1)
                            dve.wait_ge(g_lo_ready, t0 + 2 * i + j - 1)
                            last = gated_mult(dve, gf[j], y[j], 4 + 2 * j)
                            last.then_inc(g_f, 1)
                        dve.wait_ge(g_f, t0 + 2 * i + 2)
                        dve.nop().then_inc(banks_free[1], 1)
                        dve_chain.end()

        st_out_sem, st_t, st_ev = sem("state_out"), sem("state_t"), sem("state_ev")
        st_n, st_dma = [0], [0]

        def flush(groups, reg):
            bufs = [reg.take("rows", [128, 128]) for _ in groups]
            n0 = st_n[0]
            st_n[0] += len(groups)
            with nc.Block() as block:
                @block.tensor
                def _(pe):
                    for n, (src, r, _) in enumerate(groups):
                        if n >= 4:
                            pe.wait_ge(st_ev, n0 + n - 3)
                        pe.transpose(ps[0:r, n % 4, 0:128], src, ident[:, :]).then_inc(st_t, 1)

                @block.scalar
                def _(act):
                    for n, (src, r, _) in enumerate(groups):
                        act.wait_ge(st_t, n0 + n + 1)
                        act.copy(bufs[n][0:r, :], ps[0:r, n % 4, 0:128]).then_inc(st_ev, 1)

                @block.sync
                def _(sp):
                    for n, (src, r, outs) in enumerate(groups):
                        sp.wait_ge(st_ev, n0 + n + 1)
                        for lo, hi, dst in outs:
                            sp.dma_start(dst, bufs[n][lo:hi, :]).then_inc(st_out_sem, 16)
                            st_dma[0] += 16
                    sp.wait_ge(st_out_sem, st_dma[0])

        def ffn(l, stages_l, gain):
            reg = Region(R)
            hhi, hlo = reg.take("h_hi", [128, KT, T], F32R), reg.take("h_lo", [128, KT, T], F32R)
            ghi, glo = reg.take("g_hi", [128, 12, T], F32R), reg.take("g_lo", [128, 12, T], F32R)
            for up, down, f0, nf in stages_l:
                r2 = Region(reg.at)
                scratch = r2.at + 4 * (4 * EW + 2 * T) + 192
                ffn_up(l, up, f0, hhi, hlo, ghi, glo, r2, norm(gain, hhi, hlo, scratch) if f0 == 0 else None)
                residual(down, ghi, glo, sum_squares=(f0 > 0 and l == 0))
            groups = [(flat(newffn[:, 0, :, :]), 44, [(0, 44, o["ffn_p"][0, l].rearrange("k (c p) -> (k c) p", p=128))])]
            for n in range(4):
                groups.append((flat(newffn[:, 1 + 2 * n:3 + 2 * n, :, :]), 88,
                               [(44 * h, 44 * h + 44, o["ffn_s"][2 * n + h, l].rearrange("k (c p) -> (k c) p", p=128)) for h in range(2)]))
            flush(groups, Region(reg.at))

        def conv_mixer():
            reg = Region(R)
            hhi, hlo = reg.take("h_hi", [128, KT, T], F32R), reg.take("h_lo", [128, KT, T], F32R)
            mhi, mlo = reg.take("m_hi", [128, KT, T], F32R), reg.take("m_lo", [128, KT, T], F32R)
            nrm = norm(V_MIX + 8, hhi, hlo, reg.at + 4 * (4 * T + 4 * EW) + 256)
            cg = [reg.take("cg", [128, T]) for _ in range(2)]
            ext = [reg.take("ext", [128, EW]) for _ in range(2)]
            y = [reg.take("y", [128, EW]) for _ in range(2)]
            gf = [reg.take("gf", [128, T]) for _ in range(2)]
            st, G, t0 = st_odd, st_odd["base"], tiles_done[0]
            tiles_done[0] += 8
            zero_count[0] += 2
            zc = zero_count[0]
            cg_ready, u_done = sem("cg_ready"), sem("u_done")
            def tile(i, h, j):
                return 4 * i + 2 * h + j
            with nc.Block() as block:
                @block.sync
                def _(sp):
                    for q in range(2, 6):
                        load_slab(sp, st, 0, q, 6)
                    for q in range(6):
                        load_slab(sp, st, 1, q, 6)
                    loads_after(sp, G + 12)

                @block.gpsimd
                def _(pool):
                    nrm["pool"](pool)

                    def trip(i, last):
                        for h in range(2):
                            for q in range(3):
                                qq = 3 * h + q + 1
                                split_lo(pool, *(last if qq == 6 else (st, i, qq, 6)))
                            for j in range(2):
                                tt = tile(i, h, j)
                                pool.wait_ge(g_hi_ready, t0 + tt + 1)
                                pool.tensor_tensor(mlo[:, tt, :], gf[j][:, :], mhi[:, tt, :].bitcast(F32),
                                                   ALU.subtract).then_inc(g_lo_ready, 1)
                    trip(0, (st, 1, 0, 6))
                    trip(1, follow(G + 12))

                @block.scalar
                def _(act):
                    nrm["act"](act)

                    def trip(i, last):
                        for h in range(2):
                            qb = 6 * i + 3 * h
                            bank = [4 * ((3 * h + q) % 2) for q in range(3)]
                            split_hi(act, st, i, 3 * h + 1, 6)
                            act.wait_ge(slab_done, G + qb + 1)
                            if t0 + tile(i, h, 0) > t0:
                                act.wait_ge(u_done, tile(i, h, 0))
                            for j in range(2):
                                act.copy(cg[j][:, :].rearrange("p (a t) -> p a t", a=2),
                                         ps[:, bank[0] + 2 * j:bank[0] + 2 * j + 2, 0:HT]).then_inc(cg_ready, 1)
                            act.wait_ge(cg_ready, tile(i, h, 0) + 2)
                            act.nop().then_inc(banks_free[(3 * h) % 2], 1)
                            split_hi(act, st, i, 3 * h + 2, 6)
                            split_hi(act, *(last if h == 1 else (st, i, 3, 6)))
                            for j in range(2):
                                tt = tile(i, h, j)
                                act.wait_ge(g_f, t0 + tt + 1)
                                act.copy(mhi[:, tt, :], gf[j][:, :]).then_inc(g_hi_ready, 1)
                    trip(0, (st, 1, 0, 6))
                    trip(1, follow(G + 12))

                @block.tensor
                def _(pe):
                    nrm["pe"](pe)
                    for i in range(2):
                        for q in range(6):
                            products(pe, st, i, q, 6, 4 * (q % 2), 0, hhi, hlo, nrm["ready"] if i == q == 0 else None)

                @block.vector
                def _(dve):
                    nrm["dve"](dve)
                    for e in ext:
                        dve.memset(e[:, 0:2], 0.0).then_inc(zeroed, 1)
                    dve.wait_ge(zeroed, zc)
                    for i in range(2):
                        for h in range(2):
                            b = [4 * ((3 * h + q) % 2) for q in range(3)]
                            dve.wait_ge(cg_ready, tile(i, h, 0) + 2)
                            dve.wait_ge(slab_done, G + 6 * i + 3 * h + 2)
                            for j in range(2):
                                f = tile(i, h, j)
                                e, bk = ext[j], b[1] + 2 * j
                                dve.tensor_tensor(e[:, 2:2 + HT], cg[j][:, 0:HT], ps[:, bk, 0:HT], ALU.mult)
                                dve.tensor_tensor(e[:, 2 + HT:2 + TP], cg[j][:, HT:TP], ps[:, bk + 1, 0:H1], ALU.mult)
                                dve.tensor_copy(sample_of(e)[:, :, 0:2], convst[:, :, :, f])
                                dve.tensor_tensor(sample_of(e)[:, :, 2:2 + TS], cg[j][:, TP:T].rearrange("p (b t) -> p b t", b=NB),
                                                  ps[:, bk + 1, H1:HT].rearrange("p (b t) -> p b t", b=NB), ALU.mult).then_inc(u_done, 1)
                            dve.wait_ge(u_done, tile(i, h, 0) + 2)
                            dve.nop().then_inc(banks_free[(3 * h + 1) % 2], 1)
                            for j in range(2):
                                f = tile(i, h, j)
                                keep_last(dve, newconv, f, ext[j])
                                convolve(dve, y[j], ext[j], lambda kk: vec[:, V_CONV + 8 * kk + f:V_CONV + 8 * kk + f + 1]).then_inc(conv_done, 1)
                            dve.wait_ge(conv_done, t0 + tile(i, h, 0) + 2)
                            dve.wait_ge(slab_done, G + 6 * i + 3 * h + 3)
                            for j in range(2):
                                f = tile(i, h, j)
                                dve.wait_ge(g_lo_ready, t0 + f - 1)
                                gated_mult(dve, gf[j], y[j], b[2] + 2 * j).then_inc(g_f, 1)
                            dve.wait_ge(g_f, t0 + tile(i, h, 0) + 2)
                            dve.nop().then_inc(banks_free[(3 * h + 2) % 2], 1)
            residual(st_oout, mhi, mlo)
            groups = [(flat(newconv[:, 0, :, :]), 16, [(0, 16, o["conv_p"][0, 0].rearrange("k (c p) -> (k c) p", p=128))]),
                      (flat(newconv[:, 1:9, :, :]), 128, [(0, 128, o["conv_s"][:, 0].rearrange("b k (c p) -> (b k c) p", p=128))])]
            flush(groups, Region(reg.at))

        def store_y():
            reg = Region(R)
            yt = reg.take("yt", [128, 5, D])
            yt_t, yt_ev, y_out = sem("yt_t"), sem("yt_ev"), sem("y_out")
            with nc.Block() as block:
                @block.tensor
                def _(pe):
                    for n in range(10):
                        t, c = n // 2, n % 2
                        w = 128 if t < 4 else NS
                        if n >= 8:
                            pe.wait_ge(yt_ev, n - 7)
                        for q in range(4):
                            last = pe.transpose(ps[0:w, n % 8, 128 * q:128 * q + 128],
                                                xT[:, 4 * c + q, 128 * t:128 * t + w], ident[:, :])
                        last.then_inc(yt_t, 1)

                @block.vector
                def _(dve):
                    for n in range(10):
                        t, c = n // 2, n % 2
                        w = 128 if t < 4 else NS
                        dve.wait_ge(yt_t, n + 1)
                        dve.tensor_copy(yt[0:w, t, 512 * c:512 * c + 512], ps[0:w, n % 8, :]).then_inc(yt_ev, 1)

                @block.sync
                def _(sp):
                    for t in range(4):
                        sp.wait_ge(yt_ev, 2 * t + 2)
                        sp.dma_start(o["y_prompt"][0, 128 * t:128 * t + 128, :], yt[:, t, :]).then_inc(y_out, 16)
                    sp.wait_ge(yt_ev, 10)
                    sp.dma_start(o["y_sample"].rearrange("b t d -> (b t) d"), yt[0:NS, 4, :]).then_inc(y_out, 16)
                    sp.wait_ge(y_out, 80)

        def even_mixer():
            reg = Region(R)
            hhi, hlo = reg.take("h_hi", [128, KT, TPAD], F32R), reg.take("h_lo", [128, KT, TPAD], F32R)
            MIX = reg.at
            mixf = reg.take("mixf", [128, KT, T])
            zq = reg.take("zq", [128, 5, W_NSA])
            E0 = reg.at
            pad_zero = sem("pad_zero")
            with nc.Block() as block:
                @block.vector
                def _(dve):
                    dve.memset(hhi[:, :, T:TPAD].bitcast(F32), 0.0).then_inc(pad_zero, 1)
                    dve.memset(hlo[:, :, T:TPAD].bitcast(F32), 0.0).then_inc(pad_zero, 1)

            def products_tok(pe, st, p, q, m, ready=None):
                g = st["base"] + p * m + q
                slot = (st["base"] + q) % 2
                wait_banks(pe, st, p, q, m)
                pe.wait_ge(w_lo_ready, g + 1)
                W = st["width"]
                for tok in range(5):
                    out = ps[:, 4 * (q % 2) + tok // 2, 256 * (tok % 2):256 * (tok % 2) + W]
                    for t in range(KT):
                        if ready is not None and tok == 0:
                            ready(pe, t)
                        for n, (w, x) in enumerate(((whi, hhi), (whi, hlo), (wlo, hhi))):
                            last = pe.matmul(out, x[:, t, 128 * tok:128 * tok + 128], w[slot][:, t * W:t * W + W],
                                             start=(t == 0 and n == 0), stop=(t == KT - 1 and n == 2))
                last.then_inc(slab_done, 1)

            def take_tok(dve, st, p, q, m, c0):
                g = st["base"] + p * m + q
                W, b = st["width"], 4 * (q % 2)
                dve.wait_ge(slab_done, g + 1)
                dve.tensor_copy(zq[:, 0:4, bass.ds(c0, W)].rearrange("p (b u) c -> p b u c", u=2),
                                ps[:, b:b + 2, :].rearrange("p b (u c) -> p b u c", u=2)[:, :, :, 0:W])
                dve.tensor_copy(zq[:, 4, bass.ds(c0, W)], ps[:, b + 2, 0:W]).then_inc(banks_free[q % 2], 1)

            r = Region(E0)
            kcT = r.take("kcT", [128, 288])
            vc = r.take("vc", [128, 3, 128])
            E1 = r.at
            seg = [r.take("seg", [128, 16, 128]) for _ in range(2)]
            segr = at("seg_by_group", [128, 2, 16, HD], F32, MIX)
            KTc = r.take("segT", [128, 2, 8, 290])
            w1 = r.take("phi_w1", [128, 16, 128])
            w2 = r.take("phi_w2", [128, 2, HD])
            hid = r.take("hid", [128, 2, 288])
            pe_rows = r.take("pe_rows", [16, 2, 128])
            peT = r.take("peT", [128, 2, 16])
            pe_bias = r.take("pe_bias", [128, 2])
            kcn = r.take("kcn", [128, 3, 128])
            kcs = r.take("kcs", [128, 3, 2])
            gain_c = r.take("gain_c", [128, HD])
            pt = r.take("pt", [1, 32], I32)
            c_in, seg_in, seg_t, seg_ev, w1_in = sem("c_in"), [sem("seg_in0"), sem("seg_in1")], sem("seg_t"), sem("seg_ev"), sem("w1_in")
            hid_done, hid_ready, c_done, peb_ps, peb_ready, kc_ready, kc_t = (sem(x) for x in (
                "hid_done", "hid_ready", "c_done", "peb_ps", "peb_ready", "kc_ready", "kc_t"))
            n_pool = a["cache_cmp_kv"].shape[0]
            seg_a, seg_d, kc_copied = sem("seg_act"), sem("seg_dve"), sem("kc_copied")
            pt_in = sem("pt_in")
            kc_taken, vc_done, kc_sq, kc_ms = sem("kc_taken"), sem("vc_done"), sem("kc_sq"), sem("kc_ms")
            rows_of = (128, 128, 32)

            def load_pages(sp, n, lo, hi):
                kv, st = n // 3, n % 3
                for b in range(lo, hi):
                    page = sp.value_load(pt[0:1, 16 * st + b:16 * st + b + 1], min_val=0, max_val=n_pool - 1)
                    src = a["cache_cmp_kv"][bass.ds(page, 1), 0, :, kv].rearrange("o (m j) g d -> (o m) j (g d)", j=16)
                    sp.dma_start(seg[n % 2][8 * b:8 * b + 8, :, :], src).then_inc(seg_in[n % 2], 16)

            def regroup(copy, eng, n, g, done):
                rws, loads = rows_of[n % 3], (16, 16, 1, 16, 16, 1)
                eng.wait_ge(seg_in[n % 2], 16 * sum(loads[n % 2:n + 1:2]))
                if n >= 1:
                    eng.wait_ge(seg_t, 4 * n)
                copy(segr[0:rws, g, :, :], seg[n % 2][0:rws, :, 64 * g:64 * g + 64]).then_inc(done, 1)

            def load_w1(sp, kv):
                sp.dma_start(w1[:, :, :], a["phi_w1"][0, kv].rearrange("(i j) d e -> (j d) i e", j=2)).then_inc(w1_in, 16)

            raw_out = sem("raw_out")
            nrm = norm(V_MIX, hhi, hlo, MIX, summed=False)
            with nc.Block() as block:
                @block.sync
                def _(sp):
                    sp.dma_start(pt[:, :], a["page_table"].rearrange("(o b) n -> o (b n)", o=1)).then_inc(pt_in, 16)
                    for q in range(2, 5):
                        load_slab(sp, st_nsa, 0, q, 2)
                        sp.wait_ge(pt_in, 16)
                        load_pages(sp, (q - 2) // 2, 8 * ((q - 2) % 2), 8 * ((q - 2) % 2) + 8)
                    load_slab(sp, st_gate, 0, 0, 2)
                    load_pages(sp, 1, 8, 16)
                    for kv in range(2):
                        sp.dma_start(w2[:, kv, :], a["phi_w2"][0, kv]).then_inc(c_in, 16)
                        sp.dma_start(pe_rows[:, kv, :], a["phi_pe"][0, kv].rearrange("(i j) d -> i (j d)", j=2)).then_inc(c_in, 16)
                    sp.dma_start(gain_c[:, :], bass.AP(a["k_norm"].tensor, a["k_norm"].offset, [[0, 128], [1, HD]])).then_inc(c_in, 16)
                    load_w1(sp, 0)
                    loads_after(sp, 6)

                @block.scalar
                def _(act):
                    nrm["act"](act)
                    for g in range(1, 7):
                        split_hi(act, *follow(g))

                @block.gpsimd
                def _(pool):
                    nrm["pool"](pool)
                    for g in range(1, 7):
                        split_lo(pool, *follow(g))

                @block.tensor
                def _(pe):
                    nrm["pe"](pe)
                    for i in range(2):
                        for q in range(2):
                            products_tok(pe, st_nsa, i, q, 2, nrm["ready"] if i == q == 0 else None)
                    products_tok(pe, st_nsa, 2, 0, 2)
                    products_tok(pe, st_gate, 0, 0, 2)

                @block.vector
                def _(dve):
                    nrm["dve"](dve)
                    with dve.Fori(0, 2) as i:
                        for q in range(2):
                            take_tok(dve, st_nsa, i, q, 2, 512 * i + 256 * q)
                    take_tok(dve, st_nsa, 2, 0, 2, 1024)
                    take_tok(dve, st_gate, 0, 0, 2, 1280)

            def kv_out(sp, c0, dst_p, dst_s, s):
                sp.dma_start(dst_p.rearrange("(t p) k g d -> p t (k g d)", p=128), zq[:, 0:4, c0:c0 + 256]).then_inc(s, 16)
                for b in range(NB):
                    sp.dma_start(dst_s[b], zq[TS * b:TS * b + TS, 4, c0:c0 + 256]).then_inc(s, 16)

            with nc.Block() as block:
                @block.sync
                def _(sp):
                    kv_out(sp, 512, o["cmp_p"][0, 0], o["cmp_s"][:, 0].rearrange("b t k g d -> b t (k g d)"), raw_out)
                    for n in range(2, 6):
                        if n == 3:
                            sp.wait_ge(hid_done, 2)
                            load_w1(sp, 1)
                        sp.wait_ge(seg_a, n - 1)
                        sp.wait_ge(seg_d, n - 1)
                        if n % 3 == 2:
                            sp.wait_ge(raw_out, 16 * 9)
                            src = o["cmp_p"][0, 0, :, n // 3].rearrange("(m j) g d -> m j (g d)", j=16)
                            sp.dma_start(seg[n % 2][0:32, :, :], src).then_inc(seg_in[n % 2], 16)
                        else:
                            load_pages(sp, n, 0, 16)

                @block.tensor
                def _(pe):
                    pe.wait_ge(c_in, 80)
                    for kv in range(2):
                        pe.transpose(ps[:, 7, 16 * kv:16 * kv + 16], pe_rows[:, kv, :], ident[0:16, 0:16]).then_inc(peb_ps, 1)
                    for kv in range(2):
                        pe.wait_ge(w1_in, 16 * (kv + 1))
                        pe.wait_ge(peb_ready, 1)
                        if kv == 1:
                            pe.wait_ge(kc_copied, 1)
                        for i in range(16):
                            last = pe.matmul(ps[:, 7, 64 + kv:65 + kv], w1[:, i, :], peT[:, kv, i:i + 1], start=(i == 0), stop=(i == 15))
                        last.then_inc(peb_ps, 1)
                        for st in range(3):
                            n, rws = 3 * kv + st, rows_of[st]
                            pe.wait_ge(seg_a, n + 1)
                            pe.wait_ge(seg_d, n + 1)
                            for u in range(4):
                                e = 4 * n + u
                                if e >= 4:
                                    pe.wait_ge(seg_ev, e - 3)
                                gg, j0 = u // 2, 4 * (u % 2)
                                for jj in range(4):
                                    src = segr[0:rws, gg, 2 * (j0 + jj):2 * (j0 + jj) + 2, :].rearrange("p j d -> p (j d)")
                                    last = pe.transpose(ps[:, e % 4, 128 * jj:128 * jj + rws], src, ident[0:rws, 0:rws])
                                last.then_inc(seg_t, 1)
                        pe.wait_ge(seg_ev, 12 * (kv + 1))
                        for gg in range(2):
                            if kv == 1:
                                pe.wait_ge(hid_ready, gg + 1)
                            for i in range(16):
                                last = pe.matmul(ps[:, 4 + gg, 0:288], w1[:, i, :], KTc[:, gg, i % 8, i // 8:i // 8 + 288],
                                                 start=(i == 0), stop=(i == 15))
                            last.then_inc(hid_done, 1)
                        pe.wait_ge(hid_ready, 2 * (kv + 1))
                        if kv == 1:
                            pe.wait_ge(kc_taken, 1)
                        for nt in range(3):
                            for gg in range(2):
                                rws = rows_of[nt]
                                last = pe.matmul(ps[0:rws, 6, 128 * nt + 64 * gg:128 * nt + 64 * gg + 64],
                                                 hid[:, gg, 128 * nt:128 * nt + rws], w2[:, kv, :], start=True, stop=True)
                        last.then_inc(c_done, 1)
                        if kv == 0:
                            pe.wait_ge(kc_ready, 2)
                            for nt in range(3):
                                rws = rows_of[nt]
                                last = pe.transpose(ps[:, 7, 128 + 128 * nt:128 + 128 * nt + rws], kcn[0:rws, nt, :], ident[0:rws, 0:rws])
                            last.then_inc(kc_t, 1)

                @block.scalar
                def _(act):
                    act.wait_ge(peb_ps, 2)
                    act.copy(peT[:, :, :], ps[:, 7, 0:32].rearrange("p (a b) -> p a b", a=2)).then_inc(peb_ready, 1)
                    for kv in range(2):
                        for st in range(3):
                            regroup(act.copy, act, 3 * kv + st, 0, seg_a)
                        act.wait_ge(peb_ps, 3 + kv)
                        act.copy(pe_bias[:, kv:kv + 1], ps[:, 7, 64 + kv:65 + kv]).then_inc(act_chain.sem, 1)
                        act_chain.n += 1
                        act.wait_ge(act_chain.sem, act_chain.n)
                        for gg in range(2):
                            act.wait_ge(hid_done, 2 * kv + gg + 1)
                            if kv == 1:
                                act.wait_ge(c_done, 1)
                            act.activation(hid[:, gg, :], ps[:, 4 + gg, 0:288], ACT.Gelu_apprx_tanh, bias=pe_bias[:, kv:kv + 1]).then_inc(hid_ready, 1)
                        if kv == 0:
                            act.wait_ge(c_done, 1)
                            act.activation(kcn[:, 0:2, :], ps[:, 6, 0:256].rearrange("p (a b) -> p a b", a=2), ACT.Square)
                            act.activation(kcn[0:32, 2, :], ps[0:32, 6, 256:384], ACT.Square).then_inc(kc_sq, 1)
                            act.wait_ge(kc_ms, 1)
                            act.activation(kcs[:, 0:2, :], kcs[:, 0:2, :], ACT.Sqrt)
                            act.activation(kcs[0:32, 2, :], kcs[0:32, 2, :], ACT.Sqrt).then_inc(kc_sq, 1)

                @block.vector
                def _(dve):
                    dve.memset(KTc[:, :, :, 288:290], 0.0)
                    for kv in range(2):
                        for st in range(3):
                            rws = rows_of[st]
                            regroup(dve.tensor_copy, dve, 3 * kv + st, 1, seg_d)
                            for u in range(4):
                                e = 12 * kv + 4 * st + u
                                dve.wait_ge(seg_t, e + 1)
                                if kv == 1 and st == 0 and u == 0:
                                    dve.wait_ge(hid_done, 2)
                                gg, j0 = u // 2, 4 * (u % 2)
                                dve.tensor_copy(KTc[:, gg, j0:j0 + 4, 128 * st:128 * st + rws],
                                                ps[:, e % 4, :].rearrange("p (j n) -> p j n", j=4)[:, :, 0:rws]).then_inc(seg_ev, 1)
                        dve.wait_ge(c_done, kv + 1)
                        if kv == 0:
                            dve.wait_ge(kc_sq, 1)
                            dve.tensor_reduce(kcs[:, 0:2, :], kcn[:, 0:2, :].rearrange("p n (g d) -> p n g d", g=2), AX.X, ALU.add)
                            dve_chain(dve, dve.tensor_reduce(kcs[0:32, 2, :], kcn[0:32, 2, :].rearrange("p (g d) -> p g d", g=2), AX.X, ALU.add))
                            dve.tensor_scalar(kcs[:, 0:2, :], kcs[:, 0:2, :], 1.0 / HD, EPS, ALU.mult, ALU.add)
                            dve.tensor_scalar(kcs[0:32, 2, :], kcs[0:32, 2, :], 1.0 / HD, EPS, ALU.mult, ALU.add).then_inc(kc_ms, 1)
                            dve.wait_ge(kc_sq, 2)
                            dve.reciprocal(kcs[:, 0:2, :], kcs[:, 0:2, :])
                            dve_chain(dve, dve.reciprocal(kcs[0:32, 2, :], kcs[0:32, 2, :]))
                            def scaled(rr, lo, hi):
                                nn = hi - lo
                                out = kcn[0:rr, lo:hi, :].rearrange("p n (g d) -> p (n g) d", g=2)
                                src = ps[0:rr, 6, 128 * lo:128 * hi].rearrange("p (n d) -> p n d", d=HD)
                                fac = kcs[0:rr, lo:hi, :].rearrange("p n (g o) -> p (n g) o", o=1).to_broadcast([rr, 2 * nn, HD])
                                dve_chain(dve, dve.tensor_tensor(out, src, fac, ALU.mult))
                                gn = gain_c[0:rr, :].rearrange("p (o d) -> p o d", o=1).to_broadcast([rr, 2 * nn, HD])
                                return dve.tensor_tensor(out, out, gn, ALU.mult)
                            scaled(128, 0, 2).then_inc(kc_ready, 1)
                            scaled(32, 2, 3).then_inc(kc_ready, 1)
                            dve.wait_ge(kc_ready, 2)
                            dve.nop().then_inc(kc_taken, 1)
                            dve.wait_ge(kc_t, 1)
                            dve.tensor_copy(kcT[:, :], ps[:, 7, 128:128 + 288]).then_inc(kc_copied, 1)
                        else:
                            dve.tensor_copy(vc[:, 0:2, :], ps[:, 6, 0:256].rearrange("p (a b) -> p a b", a=2))
                            dve.tensor_copy(vc[0:32, 2, :], ps[0:32, 6, 256:384]).then_inc(vc_done, 1)

            r = Region(E1)
            gs = r.take("gate_s", [128, 4, 3])
            gp = r.take("gate_p", [128, 5, 24])
            gpr = r.take("gate_prompt_rev", [128, 4, 24])
            flip = r.take("flip", [128, 128])
            qbd = r.take("qbd", [128, NB, 64])
            kTs = r.take("kTs", [128, T])
            kTw = r.take("kTw", [128, T])
            EQ = r.at
            qT = r.take("qT", [128, 4, TP])
            E2 = r.at
            sqs = r.take("sqs", [128, 5, 12, HD])
            qn = sqs[:, :, 0:8, :].rearrange("p t (h g) d -> p t h g d", g=2)
            rs = r.take("rs", [128, 5, 12])
            gains = r.take("gains", [128, 3, HD])
            n_in, n_sq, n_ms, n_std, n_done, g_sig, q_t, q_ev = (sem(x) for x in ("n_in", "n_sq", "n_ms", "n_std", "n_done", "g_sig", "q_t", "q_ev"))
            q_ev2, gpr_ps = sem("q_ev2"), sem("gpr_ps")
            gate_out, gate_in, slc_out, rel_in = sem("gate_out"), sem("gate_in"), sem("slc_out"), sem("rel_in")
            onehot = r.take("onehot", [NBK, RVL])
            masked = r.take("masked", [NH, RVL])
            relb = r.take("rel_bias", [NBK, NH])
            rv = r.take("rv_sb", [NH, RVL])
            rv_ps, rv_sb, rv_out = sem("rv_ps"), sem("rv_ready"), sem("rv_out")
            RC = RVL // 4
            heads = ((0, 8, 0, 0), (768, 2, 8, 1), (1024, 2, 10, 2))
            with nc.Block() as block:
                @block.sync
                def _(sp):
                    def bcast(dst, src, off, n):
                        sp.dma_start(dst, bass.AP(src.tensor, off, [[0, 128], [1, n]])).then_inc(n_in, 16)
                    bcast(gains[:, 0, :], a["q_norm"], 0, HD)
                    bcast(gains[:, 1, :], a["k_norm"], HD, HD)
                    bcast(gains[:, 2, :], a["k_norm"], 2 * HD, HD)
                    sp.dma_start(flip[:, :], k["flip"]).then_inc(n_in, 16)
                    sp.dma_start(onehot[:, :], k["onehot"]).then_inc(rel_in, 16)
                    sp.dma_start(masked[:, :], k["masked"]).then_inc(rel_in, 16)
                    sp.dma_start(relb[:, :], a["rel_bias"]).then_inc(rel_in, 16)
                    sp.wait_ge(rv_sb, 4)
                    sp.dma_start(rv_dram, rv[:, :]).then_inc(rv_out, 16)
                    sp.wait_ge(g_sig, 1)
                    sp.dma_start(gate_dram, gp[0:NS, 4, :]).then_inc(gate_out, 16)
                    sp.wait_ge(gate_out, 16)
                    for grp in range(4):
                        for s2 in range(2):
                            src = bass.AP(gate_dram.tensor, (2 * grp + s2) * TS * 24, [[3, NH], [24, TS], [1, 3]])
                            sp.dma_start(gs[64 * s2:64 * s2 + 64, grp, :], src).then_inc(gate_in, 16)
                    sp.wait_ge(n_done, 3)
                    kv_out(sp, 768, o["slc_p"][0, 0], o["slc_s"][:, 0].rearrange("b t k g d -> b t (k g d)"), slc_out)
                    kv_out(sp, 1024, o["win_p"][0, 0], o["win_s"][:, 0, 504:512].rearrange("b t k g d -> b t (k g d)"), slc_out)
                    for b in range(NB):
                        sp.dma_start(o["win_s"][b, 0, 0:504].rearrange("t k g d -> t (k g d)"),
                                     a["cache_win_kv"][b, 0, 8:512].rearrange("t k g d -> t (k g d)")).then_inc(slc_out, 16)
                    sp.wait_ge(slc_out, 16 * 26)
                    sp.wait_ge(raw_out, 16 * 9)
                    sp.wait_ge(gate_in, 128)
                    sp.wait_ge(rv_out, 16)

                @block.scalar
                def _(act):
                    for c0, nh, s0, _ in heads:
                        act.activation(sqs[:, :, s0:s0 + nh, :], zq[:, :, c0:c0 + 64 * nh].rearrange("p t (h d) -> p t h d", d=HD), ACT.Square).then_inc(n_sq, 1)
                    act.activation(gp[:, :, :], zq[:, :, 1280:1304], ACT.Sigmoid).then_inc(g_sig, 1)
                    act.wait_ge(n_ms, 1)
                    act.activation(rs[:, :, :], rs[:, :, :], ACT.Sqrt).then_inc(n_std, 1)
                    for n in range(4):
                        act.wait_ge(q_t, n + 1)
                        act.copy(qT[:, n, :], ps[:, n, :]).then_inc(q_ev, 1)

                @block.vector
                def _(dve):
                    dve.memset(qbd[:, :, :], 0.0)
                    dve.wait_ge(n_sq, 3)
                    dve_chain(dve, dve.tensor_reduce(rs[:, :, :], sqs[:, :, :, :], AX.X, ALU.add))
                    dve.tensor_scalar(rs[:, :, :], rs[:, :, :], 1.0 / HD, EPS, ALU.mult, ALU.add).then_inc(n_ms, 1)
                    dve.wait_ge(n_std, 1)
                    dve_chain(dve, dve.reciprocal(rs[:, :, :], rs[:, :, :]))
                    dve_chain(dve, dve.tensor_scalar(rs[:, :, 0:8], rs[:, :, 0:8], HD ** -0.5, None, ALU.mult))
                    dve.wait_ge(n_in, 64)
                    for c0, nh, s0, gi in heads:
                        z = zq[:, :, c0:c0 + 64 * nh].rearrange("p t (h d) -> p t h d", d=HD)
                        dve_chain(dve, dve.tensor_tensor(z, z, rs[:, :, s0:s0 + nh].rearrange("p t (h o) -> p t h o", o=1).to_broadcast([128, 5, nh, HD]), ALU.mult))
                        gb = gains[:, gi, :].rearrange("p (a b d) -> p a b d", a=1, b=1).to_broadcast([128, 5, nh, HD])
                        if gi == 0:
                            for g in range(2):
                                last = dve.tensor_tensor(qn[:, :, :, g, :], z[:, :, 4 * g:4 * g + 4, :], gb[:, :, 0:4, :], ALU.mult)
                            last.then_inc(n_done, 1)
                        else:
                            dve.tensor_tensor(z, z, gb, ALU.mult).then_inc(n_done, 1)
                    dve.wait_ge(rel_in, 48)
                    for n in range(4):
                        dve.wait_ge(rv_ps, n + 1)
                        dve.tensor_tensor(rv[:, RC * n:RC * n + RC], ps[0:NH, 7, 0:RC], masked[:, RC * n:RC * n + RC], ALU.add).then_inc(rv_sb, 1)
                    dve.wait_ge(gpr_ps, 1)
                    dve.tensor_copy(flat(gpr[:, :, :]), ps[:, 7, 0:96])
                    dve.wait_ge(q_t, 5)
                    for g in range(2):
                        dve.tensor_copy(qbd[64 * g:64 * g + 64, :, 32 * g:32 * g + 32].rearrange("p s (h t) -> p s h t", h=4),
                                        ps[64 * g:64 * g + 64, 4, 0:256].rearrange("p (h s t) -> p s h t", h=4, s=NB))
                    for n, kT in enumerate((kTs, kTw)):
                        dve.wait_ge(q_t, 6 + n)
                        dve.tensor_copy(kT[:, 0:TP], ps[:, 5 + n, :])
                        last = dve.tensor_copy(kT[:, TP:T], ps[:, 4, 256 + 64 * n:320 + 64 * n])
                    last.then_inc(q_ev2, 1)

                @block.tensor
                def _(pe):
                    pe.wait_ge(rel_in, 48)
                    for n in range(4):
                        if n >= 1:
                            pe.wait_ge(rv_sb, n)
                        pe.matmul(ps[0:NH, 7, 0:RC], relb[:, :], onehot[:, RC * n:RC * n + RC], start=True, stop=True).then_inc(rv_ps, 1)
                    pe.wait_ge(g_sig, 1)
                    pe.wait_ge(n_in, 64)
                    pe.wait_ge(rv_sb, 4)
                    pe.matmul(ps[:, 7, 0:96], flip[:, :], gp[:, 0:4, :].rearrange("p t n -> p (t n)"), start=True, stop=True).then_inc(gpr_ps, 1)
                    pe.wait_ge(n_done, 3)

                    def q_of(tok, hh, rws):
                        return qn[0:rws, tok, hh].rearrange("p g d -> p (g d)")
                    for hh in range(4):
                        for tok in range(4):
                            last = pe.matmul(ps[:, hh, 128 * tok:128 * tok + 128], q_of(tok, hh, 128), flip[:, :], start=True, stop=True)
                        last.then_inc(q_t, 1)
                    for hh in range(4):
                        last = pe.transpose(ps[:, 4, 64 * hh:64 * hh + 64], q_of(4, hh, NS), ident[0:NS, 0:NS])
                    for n, c0 in enumerate((768, 1024)):
                        last = pe.transpose(ps[:, 4, 256 + 64 * n:320 + 64 * n], zq[0:NS, 4, c0:c0 + 128], ident[0:NS, 0:NS])
                    last.then_inc(q_t, 1)
                    for n, c0 in enumerate((768, 1024)):
                        for tok in range(4):
                            last = pe.transpose(ps[:, 5 + n, 128 * tok:128 * tok + 128], zq[:, tok, c0:c0 + 128], ident[:, :])
                        last.then_inc(q_t, 1)

            r = Region(E2)
            onat = r.take("onat", [128, 4, 512])
            BT = [r.take("BT", [128, BTW]) for _ in range(2)]
            sS = [r.take("s_slc", [128, TP]) for _ in range(2)]
            sW = [r.take("s_win", [128, TP]) for _ in range(2)]
            sC = [r.take("s_cmp", [128, 32]) for _ in range(2)]
            PTs = r.take("PTs", [128, 4, 128])
            PTw = r.take("PTw", [128, 4, 128])
            PTc = r.take("PTc", [32, 128])
            mx = r.take("mx", [128, 2, 3])
            den = r.take("den", [128, 2, 3])
            bt_in, s_ready, s_taken, p_ready, pt_ready, pt_act, pt_dve, o_ready, o_taken, m_ready = (sem(x) for x in (
                "bt_in", "s_ready", "s_taken", "p_ready", "pt_ready", "pt_act", "pt_dve", "o_ready", "o_taken", "m_ready"))
            on_t, on_ev = sem("on_t"), sem("on_ev")
            U = 4 * NH
            with nc.Block() as block:
                @block.sync
                def _(sp):
                    for h in range(NH):
                        if h >= 2:
                            sp.wait_ge(s_taken, 4 * (h - 1))
                        src = bass.AP(rv_dram.tensor, h * RVL, [[1, 128], [1, BTW]])
                        sp.dma_start(BT[h % 2][:, :], src).then_inc(bt_in, 16)
                        sp.wait_ge(bt_in, 16 * (h + 1))

                @block.tensor
                def _(pe):
                    def scores(u):
                        h, qt, s = u // 4, u % 4, u % 2
                        g, hh = h // 4, h % 4
                        if u >= 1:
                            pe.wait_ge(s_taken, u)
                        q = qT[64 * g:64 * g + 64, hh, 128 * qt:128 * qt + 128]
                        nk = 128 * (qt + 1)
                        pe.matmul(ps[:, s, 0:nk], q, kTs[64 * g:64 * g + 64, 0:nk], start=True, stop=True)
                        pe.matmul(ps[:, 2 + s, 0:nk], q, kTw[64 * g:64 * g + 64, 0:nk], start=True, stop=True)
                        pe.matmul(ps[:, 4, 0:32], q, kcT[64 * g:64 * g + 64, 256:288], start=True, stop=True).then_inc(s_ready, 1)
                    scores(0)
                    scores(1)
                    for u in range(U):
                        h, qt, s = u // 4, u % 4, u % 2
                        g = h // 4
                        pe.wait_ge(p_ready, u + 1)
                        if u >= 1:
                            pe.wait_ge(pt_act, u)
                            pe.wait_ge(pt_dve, u)
                        for kt in range(qt + 1):
                            pe.transpose(ps[:, 5, 128 * kt:128 * kt + 128], sS[s][:, 128 * kt:128 * kt + 128], ident[:, :])
                            pe.transpose(ps[:, 6, 128 * kt:128 * kt + 128], sW[s][:, 128 * kt:128 * kt + 128], ident[:, :])
                        if u >= 1:
                            pe.wait_ge(o_taken, u)
                        pe.transpose(ps[0:32, 7, 256:384], sC[s][:, :], ident[:, :]).then_inc(pt_ready, 1)
                        if u + 2 < U:
                            scores(u + 2)
                        pe.wait_ge(pt_act, u + 1)
                        pe.wait_ge(pt_dve, u + 1)
                        O = ps[:, 7, 0:192]
                        pe.matmul(O[:, 0:64], PTc[:, :], vc[0:32, 2, 64 * g:64 * g + 64], start=True, stop=True)
                        for n, (PT, c0) in enumerate(((PTs, 896), (PTw, 1152))):
                            for kt in range(qt + 1):
                                last = pe.matmul(O[:, 64 * (n + 1):64 * (n + 2)], PT[:, kt, :], zq[:, kt, c0 + 64 * g:c0 + 64 * g + 64],
                                                 start=(kt == 0), stop=(kt == qt))
                        last.then_inc(o_ready, 1)
                    for qt in range(4):
                        pe.wait_ge(o_taken, U)
                        for c in range(4):
                            last = pe.matmul(ps[:, qt, 128 * c:128 * c + 128], onat[:, qt, 128 * c:128 * c + 128], flip[:, :], start=True, stop=True)
                        last.then_inc(on_t, 1)

                @block.vector
                def _(dve):
                    def masked_max(u):
                        h, qt, s = u // 4, u % 4, u % 2
                        nk = 128 * (qt + 1)
                        dve.wait_ge(s_ready, u + 1)
                        dve.wait_ge(bt_in, 16 * (h + 1))
                        if u >= 2:
                            dve.wait_ge(pt_ready, u - 1)
                        y0 = 511 - 128 * qt
                        B = BT[h % 2]
                        dve.tensor_tensor_reduce(sC[s][:, :], ps[:, 4, 0:32], B[:, y0 + 31:y0 + 31 + 16 * 31 + 1:16], 1.0, FLOOR,
                                                 ALU.add, ALU.max, mx[:, s, 0:1])
                        dve.tensor_tensor_reduce(sS[s][:, 0:nk], ps[:, s, 0:nk], B[:, y0:y0 + nk], 1.0, FLOOR, ALU.add, ALU.max, mx[:, s, 1:2])
                        dve.tensor_tensor_reduce(sW[s][:, 0:nk], ps[:, 2 + s, 0:nk], B[:, y0:y0 + nk], 1.0, FLOOR, ALU.add, ALU.max,
                                                 mx[:, s, 2:3]).then_inc(s_taken, 1)
                        dve.wait_ge(s_taken, u + 1)
                        dve.tensor_scalar(mx[:, s, :], mx[:, s, :], -1.0, None, ALU.mult).then_inc(m_ready, 1)
                    masked_max(0)
                    masked_max(1)
                    for u in range(U):
                        h, qt, s = u // 4, u % 4, u % 2
                        dve.wait_ge(pt_ready, u + 1)
                        if u >= 1:
                            dve.wait_ge(o_ready, u)
                        dve.tensor_copy(PTw[:, 0:qt + 1, :], ps[:, 6, 0:128 * (qt + 1)].rearrange("p (a b) -> p a b", b=128)).then_inc(pt_dve, 1)
                        dve.wait_ge(p_ready, u + 1)
                        dve_chain(dve, dve.tensor_scalar(den[:, s, :], den[:, s, :], 1e-30, None, ALU.max))
                        dve_chain(dve, dve.reciprocal(den[:, s, :], den[:, s, :]))
                        dve_chain(dve, dve.tensor_tensor(den[:, s, :], den[:, s, :], gpr[:, qt, 3 * h:3 * h + 3], ALU.mult))
                        if u + 2 < U:
                            masked_max(u + 2)
                        dve.wait_ge(o_ready, u + 1)
                        O, out = ps[:, 7, 0:192], onat[:, qt, 64 * h:64 * h + 64]
                        dve_chain(dve, dve.tensor_scalar(out, O[:, 0:64], den[:, s, 0:1], None, ALU.mult))
                        dve_chain(dve, dve.scalar_tensor_tensor(out, O[:, 64:128], den[:, s, 1:2], out, ALU.mult, ALU.add))
                        dve.scalar_tensor_tensor(out, O[:, 128:192], den[:, s, 2:3], out, ALU.mult, ALU.add).then_inc(o_taken, 1)

                @block.scalar
                def _(act):
                    def exps(u):
                        qt, s = u % 4, u % 2
                        nk = 128 * (qt + 1)
                        act.wait_ge(m_ready, u + 1)
                        if u >= 2:
                            act.wait_ge(o_taken, u - 1)
                        act.activation(sC[s][:, :], sC[s][:, :], ACT.Exp, bias=mx[:, s, 0:1], accum_out=den[:, s, 0:1])
                        act.activation(sS[s][:, 0:nk], sS[s][:, 0:nk], ACT.Exp, bias=mx[:, s, 1:2], accum_out=den[:, s, 1:2])
                        act.activation(sW[s][:, 0:nk], sW[s][:, 0:nk], ACT.Exp, bias=mx[:, s, 2:3], accum_out=den[:, s, 2:3]).then_inc(p_ready, 1)
                    exps(0)
                    for u in range(U):
                        qt = u % 4
                        act.wait_ge(pt_ready, u + 1)
                        if u >= 1:
                            act.wait_ge(o_ready, u)
                        act.copy(PTc[:, :], ps[0:32, 7, 256:384])
                        act.copy(PTs[:, 0:qt + 1, :], ps[:, 5, 0:128 * (qt + 1)].rearrange("p (a b) -> p a b", b=128)).then_inc(pt_act, 1)
                        if u + 1 < U:
                            exps(u + 1)
                    for qt in range(4):
                        act.wait_ge(on_t, qt + 1)
                        act.copy(mixf[:, 0:4, 128 * qt:128 * qt + 128], ps[:, qt, :].rearrange("p (c t) -> p c t", c=4)).then_inc(on_ev, 1)

            r = Region(EQ)
            KV = [[r.take("kv_rows", [128, 4, 256]) for _ in range(2)] for _ in range(2)]
            SBs = r.take("bias_past", [128, TP])
            SBw = r.take("bias_win", [128, TP])
            SBn = r.take("bias_new", [128, 4, NS])
            SBc = r.take("bias_cmp", [128, 2, 128])
            wm = r.take("wmask", [128, TS])
            S2 = [r.take("s_past", [128, TP + NS]) for _ in range(2)]
            Sc = r.take("s_cmps", [128, 128])
            kT = [r.take("kT", [128, TP]) for _ in range(2)]
            PT2 = [r.take("PT2", [128, 4, 128]) for _ in range(2)]
            PTn = r.take("PTn", [64, 2, 128])
            PTcs = r.take("PTcs", [128, 128])
            mx2 = r.take("mx2", [128, 3])
            den2 = r.take("den2", [128, 3])
            acc = r.take("acc", [128, HD])
            tab_zero, tab_in = sem("tab_zero"), sem("tab_in")
            kvp_in, kvw_in = [sem("kvp_in0"), sem("kvp_in1")], [sem("kvw_in0"), sem("kvw_in1")]
            kT_ps, kT_sb, ss_ready, ss_taken, sm_ready, sp_ready = (sem(x) for x in ("kT_ps", "kT_sb", "ss_ready", "ss_taken", "sm_ready", "sp_ready"))
            spt_ready, spt_a, spt_d, so_ready, so_acc, so_t, so_ev = (sem(x) for x in (
                "spt_ready", "spt_act", "spt_dve", "so_ready", "so_acc", "so_t", "so_ev"))
            pt2 = r.take("pt2", [1, 32], I32)
            NTAB = 2 + 8 + 8 + 1 + 1
            with nc.Block() as block:
                @block.sync
                def _(sp):
                    sp.dma_start(pt2[:, :], a["page_table"].rearrange("(o b) n -> o (b n)", o=1)).then_inc(tab_in, 16)
                    sp.dma_start(wm[:, :], k["wmask"]).then_inc(tab_in, 16)
                    sp.wait_ge(tab_in, 32)
                    for s2 in range(2):
                        sp.dma_start(SBs[64 * s2:64 * s2 + 64, :],
                                     bass.AP(rv_dram.tensor, RV0 - TP, [[RVL, NH], [-1, TS], [1, TP]])).then_inc(tab_in, 16)
                    sp.wait_ge(tab_zero, 1)
                    for s2 in range(2):
                        for grp in range(4):
                            c0 = TS * (2 * grp + s2)
                            sp.dma_start(SBn[64 * s2:64 * s2 + 64, grp, c0:c0 + TS],
                                         bass.AP(rv_dram.tensor, RV0, [[RVL, NH], [-1, TS], [1, TS]])).then_inc(tab_in, 16)
                    for grp in range(4):
                        if grp >= 1:
                            sp.wait_ge(so_ready, grp)
                        for s2 in range(2):
                            b = 2 * grp + s2
                            for pg in range(4):
                                page = sp.value_load(pt2[0:1, 4 * b + pg:4 * b + pg + 1], min_val=0, max_val=n_pool - 1)
                                src = a["cache_slc_kv"][bass.ds(page, 1), 0].rearrange("o t k g d -> (o t) (k g d)")
                                sp.dma_start(KV[0][s2][:, pg, :], src).then_inc(kvp_in[s2], 16)
                            sp.dma_start(KV[1][s2][:, :, :], a["cache_win_kv"][b, 0].rearrange("(t p) k g d -> p t (k g d)", p=128)).then_inc(kvw_in[s2], 16)

                @block.tensor
                def _(pe):
                    pe.wait_ge(tab_in, 32)
                    for grp in range(4):
                        for s2 in range(2):
                            b = 2 * grp + s2
                            pe.wait_ge(kvp_in[s2], 64 * (grp + 1))
                            pe.wait_ge(kvw_in[s2], 16 * (grp + 1))
                            for br in range(2):
                                n = 4 * grp + 2 * s2 + br
                                if n >= 1:
                                    pe.wait_ge(kT_sb, n)
                                if s2 == 0 and br == 0 and grp >= 1:
                                    pe.wait_ge(so_acc, grp)
                                for pg in range(4):
                                    last = pe.transpose(ps[:, br, 128 * pg:128 * pg + 128], KV[br][s2][:, pg, 0:128], ident[:, :])
                                last.then_inc(kT_ps, 1)
                                pe.wait_ge(kT_sb, n + 1)
                                if n >= 2 and s2 == 0 and br == 0:
                                    pe.wait_ge(ss_taken, grp)
                                rows = slice(64 * s2, 64 * s2 + 64)
                                pe.matmul(ps[rows, 2 + br, :], qbd[:, b, :], kT[br][:, :], start=True, stop=True)
                                last = pe.matmul(ps[rows, 4, 64 * br:64 * br + 64], qbd[:, b, :], (kTs, kTw)[br][:, TP:T], start=True, stop=True)
                            last = pe.matmul(ps[rows, 4, 128:256], qbd[:, b, :], kcT[:, 128 * (b // 4):128 * (b // 4) + 128], start=True, stop=True)
                        last.then_inc(ss_ready, 1)
                        pe.wait_ge(sp_ready, grp + 1)
                        for br in range(2):
                            for kt in range(4):
                                pe.transpose(ps[:, 5 + br, 128 * kt:128 * kt + 128], S2[br][:, 128 * kt:128 * kt + 128], ident[:, :])
                            pe.transpose(ps[0:64, 7, 128 * br:128 * br + 128], S2[br][:, TP:TP + NS], ident[:, :])
                        pe.transpose(ps[:, 7, 256:384], Sc[:, :], ident[:, :]).then_inc(spt_ready, 1)
                        pe.wait_ge(spt_a, grp + 1)
                        pe.wait_ge(spt_d, grp + 1)
                        for s2 in range(2):
                            rows = slice(64 * s2, 64 * s2 + 64)
                            b = 2 * grp + s2
                            for br, c0 in ((0, 896), (1, 1152)):
                                out = ps[rows, 0, 128 * (br + 1):128 * (br + 2)]
                                for kt in range(4):
                                    pe.matmul(out, PT2[br][:, kt, rows], KV[br][s2][:, kt, 128:256], start=(kt == 0), stop=False)
                                pe.matmul(out, PTn[:, br, rows], zq[0:64, 4, c0:c0 + 128], start=False, stop=True)
                            last = pe.matmul(ps[rows, 0, 0:128], PTcs[:, rows], vc[:, b // 4, :], start=True, stop=True)
                        last.then_inc(so_ready, 1)
                        pe.wait_ge(so_acc, grp + 1)
                        pe.transpose(ps[0:64, 1, 0:128], acc[:, :], ident[:, :]).then_inc(so_t, 1)
                        pe.wait_ge(so_ev, grp + 1)

                @block.scalar
                def _(act):
                    for grp in range(4):
                        for n in range(4):
                            if n % 2 == 0:
                                act.wait_ge(kT_ps, 4 * grp + n + 1)
                                if grp or n:
                                    act.wait_ge(kT_sb, 4 * grp + n)
                                act.copy(kT[0][:, :], ps[:, 0, :]).then_inc(kT_sb, 1)
                            else:
                                act.wait_ge(kT_ps, 4 * grp + n + 1)
                                act.copy(kT[1][:, :], ps[:, 1, :]).then_inc(kT_sb, 1)
                        act.wait_ge(sm_ready, grp + 1)
                        act.activation(S2[0][:, :], S2[0][:, :], ACT.Exp, bias=mx2[:, 0:1], accum_out=den2[:, 0:1])
                        act.activation(S2[1][:, :], S2[1][:, :], ACT.Exp, bias=mx2[:, 1:2], accum_out=den2[:, 1:2])
                        act.activation(Sc[:, :], Sc[:, :], ACT.Exp, bias=mx2[:, 2:3], accum_out=den2[:, 2:3]).then_inc(sp_ready, 1)
                        act.wait_ge(spt_ready, grp + 1)
                        act.copy(PT2[0][:, :, :], ps[:, 5, :].rearrange("p (a b) -> p a b", a=4)).then_inc(spt_a, 1)
                        act.wait_ge(so_t, grp + 1)
                        for par in range(2):
                            src = ps[0:64, 1, 0:128].rearrange("p (s c r t) -> p s c r t", s=2, c=4, r=2)[:, :, :, par, :]
                            dst = mixf[64 * par:64 * par + 64, 0:4, TP + 16 * grp:TP + 16 * grp + 16].rearrange("p c (s t) -> p s c t", s=2)
                            for s2 in range(2):
                                last = act.copy(dst[:, s2], src[:, s2])
                        last.then_inc(so_ev, 1)

                @block.vector
                def _(dve):
                    dve.memset(SBn[:, :, :], NEG)
                    dve.memset(SBc[:, :, :], NEG).then_inc(tab_zero, 1)
                    dve.wait_ge(tab_in, 16 * 12)
                    dve.wait_ge(tab_zero, 1)
                    for par in range(2):
                        for s2 in range(2):
                            c0 = 64 * par + 32 * s2
                            dve.tensor_copy(SBc[64 * s2:64 * s2 + 64, par, c0:c0 + 31], SBs[64 * s2:64 * s2 + 64, 31:31 + 16 * 30 + 1:16])
                    dve.tensor_copy(SBw[:, TS:TP], SBs[:, TS:TP])
                    dve_chain(dve, dve.tensor_tensor(SBw[:, 0:TS], SBs[:, 0:TS], wm[:, :], ALU.add))
                    for grp in range(4):
                        dve.wait_ge(ss_ready, grp + 1)
                        for br in range(2):
                            dve.tensor_tensor(S2[br][:, 0:TP], ps[:, 2 + br, :], (SBs, SBw)[br][:, :], ALU.add)
                            dve.tensor_tensor(S2[br][:, TP:TP + NS], ps[:, 4, 64 * br:64 * br + 64], SBn[:, grp, :], ALU.add)
                        dve.tensor_tensor(Sc[:, :], ps[:, 4, 128:256], SBc[:, grp % 2, :], ALU.add).then_inc(ss_taken, 1)
                        dve.wait_ge(ss_taken, grp + 1)
                        for n, S in enumerate((S2[0], S2[1], Sc)):
                            last = dve.tensor_reduce(mx2[:, n:n + 1], S[:, :], AX.X, ALU.max)
                        dve_chain(dve, last)
                        dve.tensor_scalar(mx2[:, :], mx2[:, :], FLOOR, -1.0, ALU.max, ALU.mult).then_inc(sm_ready, 1)
                        dve.wait_ge(spt_ready, grp + 1)
                        dve.tensor_copy(PT2[1][:, :, :], ps[:, 6, :].rearrange("p (a b) -> p a b", a=4))
                        dve.tensor_copy(PTcs[:, :], ps[:, 7, 256:384])
                        dve.tensor_copy(PTn[:, :, :], ps[0:64, 7, 0:256].rearrange("p (a b) -> p a b", a=2)).then_inc(spt_d, 1)
                        dve_chain(dve, dve.tensor_scalar(den2[:, :], den2[:, :], 1e-30, None, ALU.max))
                        dve_chain(dve, dve.reciprocal(den2[:, :], den2[:, :]))
                        dve.tensor_tensor(den2[:, 0:2], den2[:, 0:2], gs[:, grp, 1:3], ALU.mult)
                        dve_chain(dve, dve.tensor_tensor(den2[:, 2:3], den2[:, 2:3], gs[:, grp, 0:1], ALU.mult))
                        dve.wait_ge(so_ready, grp + 1)
                        for n, (cc, slot) in enumerate(((2, 0), (0, 1), (1, 2))):
                            for blk in range(4):
                                rr = slice(32 * blk, 32 * blk + 32)
                                g = blk % 2
                                O = ps[rr, 0, 128 * slot + 64 * g:128 * slot + 64 * g + 64]
                                if n == 0:
                                    last = dve.tensor_scalar(acc[rr, :], O, den2[rr, cc:cc + 1], None, ALU.mult)
                                else:
                                    last = dve.scalar_tensor_tensor(acc[rr, :], O, den2[rr, cc:cc + 1], acc[rr, :], ALU.mult, ALU.add)
                            if n < 2:
                                dve_chain(dve, last)
                        last.then_inc(so_acc, 1)

            retire_semaphores()
            RZ = MIX + 4 * KT * T
            r = Region(RZ)
            zz = r.take("zz", [128, RT, T])
            AB = r.take("ab_hat", [128, 2, 4, T])
            pc = r.take("p_end", [64, NH, 16])
            bonus = r.take("bonus", [128, 5, NH])
            lnw = r.take("ln_w", [128, 512])
            lnb = r.take("ln_b", [128, 512])
            w2 = r.take("rwkv_w2", [128, 512])
            g2 = r.take("rwkv_g2", [128, 512])
            R2 = r.at
            shT = r.take("shiftT", [128, NB, RT])
            ext = [r.take("z_ext", [128, 1 + TP + NB * (TS + 1)]) for _ in range(2)]
            df = [r.take("z_diff", [128, TP + NB * (TS + 1)]) for _ in range(2)]
            sh_rows = r.take("sh_rows", [NB * RT, 128])
            rw_in, sh_t, sh_ev, rx_ready, rx_used = (sem(x) for x in ("rw_in", "sh_t", "sh_ev", "rx_ready", "rx_used"))
            with nc.Block() as block:
                @block.sync
                def _(sp):
                    sp.dma_start(sh_rows[:, :], a["state_rwkv_shift"].rearrange("b o (c p) -> (b o c) p", p=128)).then_inc(rw_in, 16)
                    for dst, name in ((lnw, "rwkv_ln_w"), (lnb, "rwkv_ln_b")):
                        sp.dma_start(dst[:, :], bass.AP(a[name].tensor, 0, [[0, 128], [1, 512]])).then_inc(rw_in, 16)
                    sp.dma_start(w2[0:64, :], a["rwkv_w2"][0]).then_inc(rw_in, 16)
                    sp.dma_start(w2[64:128, :], a["rwkv_a2"][0]).then_inc(rw_in, 16)
                    sp.dma_start(g2[:, :], a["rwkv_g2"][0]).then_inc(rw_in, 16)
                    sp.wait_ge(rw_in, 96)

                @block.tensor
                def _(pe):
                    pe.wait_ge(rw_in, 96)
                    pe.transpose(ps[:, 0, 0:NB * RT], sh_rows[:, :], ident[0:NB * RT, 0:NB * RT]).then_inc(sh_t, 1)

                @block.scalar
                def _(act):
                    act.wait_ge(sh_t, 1)
                    act.copy(flat(shT[:, :, :]), ps[:, 0, 0:NB * RT]).then_inc(sh_ev, 1)

            def z_sample(e):
                return e[:, 1 + TP:].rearrange("p (b t) -> p b t", b=NB)

            with nc.Block() as block:
                @block.sync
                def _(sp):
                    with sp.Fori(0, 2) as i:
                        for q in (2, 3):
                            load_slab(sp, st_rw, i, q, 2)
                    load_slab(sp, st_rw, 3, 0, 2)
                    loads_after(sp, st_rw["base"] + 7)

                @block.scalar
                def _(act):
                    def slab(i, q, nxt):
                        split_hi(act, *nxt)
                        act.wait_ge(slab_done, st_rw["base"] + 2 * i + q + 1)
                        for j in range(2):
                            kk = 4 * i + 2 * q + j
                            act.wait_ge(rx_used, kk + 1)
                            e, b = ext[j], 4 * q + 2 * j
                            act.copy(e[:, 1:1 + HT], ps[:, b, 0:HT])
                            act.copy(e[:, 1 + HT:1 + TP], ps[:, b + 1, 0:H1])
                            act.copy(z_sample(e)[:, :, 0:1], shT[:, :, bass.ds(kk, 1)])
                            act.copy(z_sample(e)[:, :, 1:1 + TS], ps[:, b + 1, H1:HT].rearrange("p (b t) -> p b t", b=NB)).then_inc(rx_ready, 1)
                        act.wait_ge(rx_ready, 4 * i + 2 * q + 2)
                        act.nop().then_inc(banks_free[q], 1)
                    with act.Fori(0, 3) as i:
                        slab(i, 0, (st_rw, i, 1, 2))
                        slab(i, 1, (st_rw, i, 2, 2))
                    slab(3, 0, follow(st_rw["base"] + 7))

                @block.gpsimd
                def _(pool):
                    with pool.Fori(0, 3) as i:
                        split_lo(pool, st_rw, i, 1, 2)
                        split_lo(pool, st_rw, i, 2, 2)
                    split_lo(pool, *follow(st_rw["base"] + 7))

                @block.tensor
                def _(pe):
                    for i in range(3):
                        for q in range(2):
                            products(pe, st_rw, i, q, 2, 4 * q, 0, hhi, hlo)
                    products(pe, st_rw, 3, 0, 2, 0, 0, hhi, hlo)

                @block.vector
                def _(dve):
                    for e in ext:
                        dve.memset(e[:, 0:1], 0.0).then_inc(rx_used, 1)

                    def tile(kk, j):
                        e, d = ext[j], df[j]
                        dve.wait_ge(rx_ready, kk + 1)
                        dve.tensor_copy(zlast[:, 0:1, bass.ds(kk, 1)], e[:, TP:TP + 1].rearrange("p (a b) -> p a b", a=1))
                        dve.tensor_copy(zlast[:, 1:9, bass.ds(kk, 1)], z_sample(e)[:, :, TS:TS + 1])
                        n = TP + NB * (TS + 1)
                        dve_chain(dve, dve.tensor_tensor(d[:, :], e[:, 0:n], e[:, 1:1 + n], ALU.subtract))
                        mu = vec[:, bass.ds(V_MU + kk, 1)]
                        dve.scalar_tensor_tensor(zz[:, bass.ds(kk, 1), 0:TP].rearrange("p o t -> p (o t)"), d[:, 0:TP], mu, e[:, 1:1 + TP], ALU.mult, ALU.add)
                        dd = d[:, TP:TP + NB * (TS + 1)].rearrange("p (b t) -> p b t", b=NB)[:, :, 1:1 + TS]
                        dve.scalar_tensor_tensor(zz[:, bass.ds(kk, 1), TP:T].rearrange("p o (b t) -> p (o b) t", b=NB), dd, mu,
                                                 z_sample(e)[:, :, 1:1 + TS], ALU.mult, ALU.add).then_inc(rx_used, 1)

                    with dve.Fori(0, 3) as i:
                        dve_chain.begin(i, 4, 3)
                        for q in range(2):
                            for j in range(2):
                                tile(4 * i + 2 * q + j, j)
                        dve_chain.end()
                    for j in range(2):
                        tile(12 + j, j)

            r = Region(R)
            sg, aa, CL, CM, Pp, PI, PM, kk_, km, tt_ = (r.take(x, [128, T]) for x in
                                                      ("sg", "aa", "CL", "CM", "P", "PI", "PM", "kk", "km", "tt"))
            keep = r.take("keep", [128, T])
            hones = r.take("headones", [128, 128])
            omka = r.take("omka", [128, 4])
            assert r.at <= MIX
            k_in, act_lora, wa_ps, sig_ready, cl_ready, cm_ready, exp_ready, kk_ready, sq2_ready, ss_ps, ss_m, ss_std, rk_ready, bo_ps, c_free = (
                sem(x) for x in ("k_in", "act_lora", "wa_ps", "sig_ready", "cl_ready", "cm_ready", "exp_ready", "kk_ready", "sq2_ready",
                                 "ss_ps", "ss_m", "ss_std", "rk_ready", "bo_ps", "c_free"))
            halves = lambda t: t.rearrange("p (a t) -> p a t", a=2)
            with nc.Block() as block:
                @block.sync
                def _(sp):
                    sp.dma_start(keep[:, :], k["keep"]).then_inc(k_in, 16)
                    sp.dma_start(hones[:, :], k["headones"]).then_inc(k_in, 16)
                    sp.wait_ge(k_in, 32)

                @block.scalar
                def _(act):
                    act.activation(zz[0:64, 12, :], zz[0:64, 12, :], ACT.Tanh)
                    act.activation(zz[:, 13, :], zz[:, 13, :], ACT.Sigmoid).then_inc(act_lora, 1)
                    for c in range(4):
                        act.wait_ge(wa_ps, c + 1)
                        if c >= 1:
                            act.wait_ge(c_free, c)
                        act.activation(halves(sg[:, :]), ps[:, 0:2, 0:HT], ACT.Sigmoid, bias=vec[:, V_W0 + c:V_W0 + c + 1])
                        act.activation(halves(aa[:, :]), ps[:, 2:4, 0:HT], ACT.Sigmoid, bias=vec[:, V_A0 + c:V_A0 + c + 1]).then_inc(sig_ready, 1)
                        act.wait_ge(kk_ready, c + 1)
                        act.activation(tt_[:, :], kk_[:, :], ACT.Square).then_inc(sq2_ready, 1)
                        act.wait_ge(cm_ready, c + 1)
                        act.activation(Pp[:, :], CL[:, :], ACT.Exp)
                        act.activation(PI[:, :], CL[:, :], ACT.Exp, scale=-1.0)
                        act.activation(PM[:, :], CM[:, :], ACT.Exp).then_inc(exp_ready, 1)
                        act.wait_ge(ss_m, c + 1)
                        act.activation(tt_[:, :], tt_[:, :], ACT.Sqrt).then_inc(ss_std, 1)

                @block.tensor
                def _(pe):
                    pe.wait_ge(act_lora, 1)
                    pe.wait_ge(k_in, 32)
                    for c in range(4):
                        if c >= 1:
                            pe.wait_ge(sig_ready, c)
                        for half in range(2):
                            cols_ = slice(half * HT, (half + 1) * HT)
                            pe.matmul(ps[:, half, 0:HT], w2[0:64, 128 * c:128 * c + 128], zz[0:64, 12, cols_], start=True, stop=True)
                            last = pe.matmul(ps[:, 2 + half, 0:HT], w2[64:128, 128 * c:128 * c + 128], zz[64:128, 12, cols_], start=True, stop=True)
                        last.then_inc(wa_ps, 1)
                        pe.wait_ge(sq2_ready, c + 1)
                        for half in range(2):
                            last = pe.matmul(ps[:, 4 + half, 0:HT], hones[:, :], tt_[:, half * HT:(half + 1) * HT], start=True, stop=True)
                        last.then_inc(ss_ps, 1)
                        pe.wait_ge(rk_ready, c + 1)
                        for tok in range(5):
                            w = 128 if tok < 4 else NS
                            last = pe.matmul(ps[0:w, 6, 8 * tok + 2 * c:8 * tok + 2 * c + 2], CM[:, 128 * tok:128 * tok + w], hones[:, 0:128:64],
                                             start=True, stop=True)
                        last.then_inc(bo_ps, 1)

                @block.vector
                def _(dve):
                    L = lambda ins: dve_chain(dve, ins)
                    ka = vec[:, V_KA:V_KA + 4]
                    L(dve.tensor_scalar(omka[:, :], ka, -1.0, 1.0, ALU.mult, ALU.add))
                    dve.wait_ge(k_in, 32)
                    for c in range(4):
                        col = lambda v: vec[:, v + c:v + c + 1]
                        if c >= 1:
                            dve.wait_ge(bo_ps, c)
                        dve.tensor_scalar(kk_[:, :], zz[:, 4 + c, :], col(V_KK), None, ALU.mult).then_inc(kk_ready, 1)
                        dve.wait_ge(sig_ready, c + 1)
                        L(dve.tensor_scalar(sg[:, :], sg[:, :], -math.exp(-0.5), None, ALU.mult))
                        L(dve.tensor_tensor_scan(CL[:, :], keep[:, :], sg[:, :], 0.0, ALU.mult, ALU.add))
                        dve.tensor_tensor(CM[:, :], CL[:, :], sg[:, :], ALU.subtract).then_inc(cm_ready, 1)
                        L(dve.tensor_scalar(km[:, :], aa[:, :], col(V_KA), omka[:, c:c + 1], ALU.mult, ALU.add))
                        L(dve.tensor_tensor(km[:, :], km[:, :], zz[:, 4 + c, :], ALU.mult))
                        dve.wait_ge(ss_ps, c + 1)
                        dve.tensor_scalar(halves(tt_[:, :]), ps[:, 4:6, 0:HT], 1e-24, None, ALU.max).then_inc(ss_m, 1)
                        dve.wait_ge(ss_std, c + 1)
                        L(dve.reciprocal(tt_[:, :], tt_[:, :]))
                        L(dve.tensor_tensor(kk_[:, :], kk_[:, :], tt_[:, :], ALU.mult))
                        dve.wait_ge(exp_ready, c + 1)
                        dve.scalar_tensor_tensor(AB[:, 0, c, :], kk_[:, :], -1.0, PM[:, :], ALU.mult, ALU.mult)
                        L(dve.tensor_tensor(tt_[:, :], kk_[:, :], aa[:, :], ALU.mult))
                        dve.tensor_tensor(AB[:, 1, c, :], tt_[:, :], PI[:, :], ALU.mult)
                        dve.scalar_tensor_tensor(CM[:, :], zz[:, c, :], col(V_RK), km[:, :], ALU.mult, ALU.mult).then_inc(rk_ready, 1)
                        dve.tensor_tensor(zz[:, 4 + c, :], km[:, :], PI[:, :], ALU.mult)
                        dve.tensor_tensor(zz[:, c, :], zz[:, c, :], Pp[:, :], ALU.mult)
                        for hb in range(2):
                            rows_ = slice(64 * hb, 64 * hb + 64)
                            dve.tensor_copy(pc[:, 2 * c + hb, 0:8], Pp[rows_, CH - 1:TP:CH])
                            last = dve.tensor_copy(pc[:, 2 * c + hb, 8:16], Pp[rows_, TP + TS - 1:T:TS])
                        last.then_inc(c_free, 1)
                    dve.wait_ge(bo_ps, 4)
                    dve.tensor_copy(bonus[:, 0:4, :], ps[:, 6, 0:32].rearrange("p (a b) -> p a b", a=4))
                    dve.tensor_copy(bonus[0:NS, 4, :], ps[0:NS, 6, 32:40])

            r = Region(R)
            G1 = r.take("state_in", [128, 2, NH, 128])
            G2 = r.take("state_out", [128, 2, NH, 128])
            BK = r.take("b_k", [64, 2, NH, 2, CH])
            Sv = [r.take("sv", [128, 512]) for _ in range(2)]
            Uv = [r.take("uv", [128, 512]) for _ in range(2)]
            Zs = r.take("zs", [128, 512])
            yb = r.take("yb", [128, 512])
            gmask = r.take("gmask", [128, 2, 128])
            imask = r.take("imask", [128, 2, 4, CH])
            smask = r.take("smask", [128, NB])
            assert r.at <= MIX, r.at - MIX
            AR = G1[0:64]
            r = Region(R2)
            STK = [r.take("stacked", [128, 512]) for _ in range(6)]
            assert st_out["base"] % 2 == 1
            w_at = nc.sbuf_base + (-nc.sbuf_base) % 64 + 2 * 4 * SLAB
            DIA = [at("diagonal", [128, NH, 128], F32, w_at + 4096 * (n % 2) + 4 * 4 * SLAB // 2 * (n // 2)) for n in range(4)]
            DIA.append(r.take("diagonal", [128, NH, 128]))
            SpO = r.take("sp", [128, 4, CH])
            st8 = r.take("stats", [128, 2, NH])
            sA, sB, sC_, sF, sE, sY = range(6)
            ysq_v = STK[sA]
            STEPS = [(0, [(1, sA, sC_, 2), (0, sB, sF, 3)]),
                     (3, [(3, sC_, None, 0), (2, sF, sA, 1)]),
                     (1, [(0, sA, None, 2)]),
                     (2, []),
                     (0, None),
                     (0, [(3, sE, None, 0), (4, sC_, sA, 1)]),
                     (0, [(0, sA, None, 2)]),
                     (2, []),
                     (1, [])]
            ADDS = (1, 2, 3, 7, 8)
            NSTEP = len(STEPS)
            MOVES = [s for s in range(NSTEP) if STEPS[s][1] is None or STEPS[s][1]]
            TILES = 5
            chunks_of = lambda t: 2 if t < 4 else 1
            ntok = lambda t: 128 if t < 4 else NS
            chunk_no = lambda t, ch: 2 * t + ch
            slot1 = lambda t, ch: ch if t < 4 else 1
            chunks_to = lambda t: 2 * t + chunks_of(t)
            m_in, cp_a, cp_d, gg_ps, dd_sb, gg_sb, bd_a, y_set, e_bd, bkt_ps, bkt_sb, v_ps, v_sb, g_zero = (sem(x) for x in (
                "m_in", "cp_ar", "cp_bk", "gg_ps", "dd_sb", "gg_sb", "diag_act", "y_set", "diag_e", "bkt_ps", "bkt_sb", "v_ps", "v_sb", "g_zero"))
            inv_ps = [sem("inv_ps0"), sem("inv_ps1")]
            inv_0, inv_m1, inv_y1 = sem("inv_taken0"), sem("inv_moved1"), sem("inv_added1")
            z_ps, z_sb, u_ps, u_sb, n_ps, n_sb, yc_sb, gate_ps, yn_a, yn_b, yn_c, yo, yt_ps2, yt_sb2 = (sem(x) for x in (
                "z_ps", "z_sb", "u_ps", "u_sb", "n_ps", "n_sb", "yc_sb", "gate_ps", "yn_mean", "yn_sq", "yn_std", "y_out_ready", "ymix_ps", "ymix_sb"))
            sT_ps, sT_sb, zsT_ps, zsT_sb, um_ready, sn_ps, sn_sb, so_ps, so_sb, st_in, wkv_out, pT_ps, pT_sb = (sem(x) for x in (
                "sT_ps", "sT_sb", "zsT_ps", "zsT_sb", "um_ready", "sn_ps", "sn_sb", "sO_ps", "sO_sb", "st_in", "wkv_out", "pT_ps", "pT_sb"))
            q = Region(RZ)
            S0T = q.take("s0T", [64, NB, 512])
            assert q.at <= RZ + 4 * 8 * T
            q = Region(RZ + 4 * RT * T)
            S0n = q.take("s0", [128, NB, 4, CH])
            Um = [q.take("um", [128, NB, CH]) for _ in range(2)]
            Sn = [q.take("sn", [64, NB, CH]) for _ in range(2)]
            assert q.at <= RZ + 4 * RT * T + 4 * 8 * T
            So = at("so", [128, NH, 4, CH], F32, R)

            def heads4(x, half):
                return x[:, 256 * half:256 * half + 256].rearrange("p (h t) -> p h t", h=4)

            def move_out(copy, t, s, half):
                C, P = chunks_of(t), 64 * chunks_of(t)
                b = 2 * half
                hs = slice(4 * half, 4 * half + 4)
                if STEPS[s][1] is None:
                    for ch in range(C):
                        src = ps[0:64, b, :].rearrange("p (h x t) -> p h x t", h=4, x=2)[:, :, ch, :]
                        rows = slice(64 * ch, 64 * ch + 64)
                        copy(heads4(STK[sC_][rows], half), src)
                        last = copy(DIA[3][rows, hs, 64 * ch:64 * ch + 64], src)
                    return last
                for n, (_, _, stk, dia) in enumerate(STEPS[s][1]):
                    src = ps[:, b, 256 * n:256 * n + 256].rearrange("p (h t) -> p h t", h=4)
                    if stk is not None:
                        copy(heads4(STK[stk][0:P], half), src[0:P])
                    for ch in range(C):
                        rows = slice(64 * ch, 64 * ch + 64)
                        last = copy(DIA[dia][rows, hs, 64 * ch:64 * ch + 64], src[rows])
                return last

            with nc.Block() as block:
                @block.sync
                def _(sp):
                    sp.dma_start(gmask[:, :, :], k["gmask"]).then_inc(m_in, 16)
                    sp.dma_start(imask[:, :, :, :], k["invmask"]).then_inc(m_in, 16)
                    sp.dma_start(smask[:, :], k["seqmask"]).then_inc(m_in, 16)
                    sp.wait_ge(cp_a, TILES)
                    sp.wait_ge(cp_d, TILES)
                    for b in range(NB):
                        for h2 in range(2):
                            sp.dma_start(S0n[64 * h2:64 * h2 + 64, b, :, :],
                                         a["state_rwkv_wkv"][b, 0].rearrange("(c h) i j -> h i c j", h=2)[h2]).then_inc(st_in, 16)
                    sp.wait_ge(pT_sb, 1)
                    for h2 in range(2):
                        sp.dma_start(o["wkv_p"][0, 0].rearrange("(c h) i j -> h i c j", h=2)[h2], SpO[64 * h2:64 * h2 + 64, :, :]).then_inc(wkv_out, 16)
                    sp.wait_ge(so_sb, NH)
                    for qq in range(4):
                        for b2 in range(2):
                            sp.dma_start(o["wkv_s"][2 * qq + b2, 0].rearrange("h i j -> i h j"), So[64 * b2:64 * b2 + 64, :, qq, :]).then_inc(wkv_out, 16)
                    sp.wait_ge(wkv_out, 160)

                @block.tensor
                def _(pe):
                    for t in range(TILES):
                        C, P, w = chunks_of(t), 64 * chunks_of(t), ntok(t)
                        pe.wait_ge(cp_a, t + 1)
                        pe.wait_ge(cp_d, t + 1)
                        if t >= 1:
                            pe.wait_ge(yt_sb2, t)
                        for ch in range(C):
                            for h in range(NH):
                                pe.matmul(ps[:, 2 * ch + h // 4, 128 * (h % 4):128 * (h % 4) + 128],
                                          BK[:, ch, h].rearrange("p x t -> p (x t)"), AR[:, ch, h, :], start=True, stop=True)
                                last = pe.matmul(ps[64 * ch:64 * ch + 64, 4, 64 * h:64 * h + 64], AR[:, ch, h, 0:64], BK[:, ch, h, 0, :], start=True, stop=True)
                        last.then_inc(gg_ps, 1)
                        for ch in range(C):
                            for h in range(NH):
                                last = pe.transpose(ps[:, 5 + ch, 64 * h:64 * h + 64], BK[:, ch, h].rearrange("p x t -> p (x t)"), ident[0:64, 0:64])
                        last.then_inc(bkt_ps, 1)
                        for c in range(4):
                            last = pe.transpose(ps[0:w, 7, 128 * c:128 * c + 128], zz[:, 8 + c, 128 * t:128 * t + w], ident[:, :])
                        last.then_inc(v_ps, 1)
                        if t == 4:
                            pe.wait_ge(st_in, 256)
                            for b in range(NB):
                                if b >= 1:
                                    pe.wait_ge(sT_sb, b)
                                for c in range(4):
                                    last = pe.transpose(ps[0:64, 6, 128 * c:128 * c + 128], S0n[:, b, c, :], ident[:, :])
                                last.then_inc(sT_ps, 1)
                            pe.wait_ge(sT_sb, NB)
                            for h in range(NH):
                                for b in range(NB):
                                    last = pe.matmul(ps[0:64, 2 + h // 4, 128 * (h % 4):128 * (h % 4) + 128].rearrange("p (x t) -> p x t", x=2)[:, :, 8 * b:8 * b + 8],
                                                     S0T[:, b, 64 * h:64 * h + 64], AR[:, 0, h, :].rearrange("p (x t) -> p x t", x=2)[:, :, 8 * b:8 * b + 8],
                                                     start=True, stop=True)
                            last.then_inc(zsT_ps, 1)
                            pe.wait_ge(zsT_sb, 1)
                        pe.wait_ge(gg_sb, t + 1)
                        pe.wait_ge(bd_a, t + 1)
                        for s, (stat, prods) in enumerate(STEPS):
                            if s == 1:
                                pe.wait_ge(y_set, t + 1)
                            if s == 5:
                                pe.wait_ge(e_bd, t + 1)
                            for half in range(2):
                                if s >= 1:
                                    if half == 0:
                                        pe.wait_ge(inv_0, NSTEP * t + s)
                                    else:
                                        pe.wait_ge(inv_m1, len(MOVES) * t + sum(m < s for m in MOVES))
                                        if t or sum(m < s for m in ADDS):
                                            pe.wait_ge(inv_y1, len(ADDS) * t + sum(m < s for m in ADDS))
                                for h4 in range(4):
                                    h = 4 * half + h4
                                    hs = slice(64 * h, 64 * h + 64)
                                    if prods is None:
                                        last = pe.transpose(ps[0:64, 2 * half, 128 * h4:128 * h4 + P], STK[sY][0:P, hs], ident[0:P, 0:P])
                                        continue
                                    for n, (l, rr, _, _) in enumerate(prods):
                                        last = pe.matmul(ps[0:P, 2 * half, 256 * n + 64 * h4:256 * n + 64 * h4 + 64], DIA[l][0:P, h, 0:P], STK[rr][0:P, hs],
                                                         start=True, stop=True)
                                    if s in ADDS:
                                        last = pe.matmul(ps[0:P, 2 * half + 1, 64 * h4:64 * h4 + 64], DIA[stat][0:P, h, 0:P], STK[sY][0:P, hs],
                                                         start=True, stop=True)
                                last.then_inc(inv_ps[half], 1)
                        pe.wait_ge(inv_0, NSTEP * (t + 1))
                        pe.wait_ge(inv_m1, len(MOVES) * (t + 1))
                        pe.wait_ge(inv_y1, len(ADDS) * (t + 1))
                        pe.wait_ge(bkt_sb, t + 1)
                        for ch in range(C):
                            n = chunk_no(t, ch)
                            S, Un = Sv[n % 2], Uv[n % 2]
                            pe.wait_ge(v_sb, n + 1)
                            pe.wait_ge(n_sb, n + 1)
                            for h in range(NH):
                                hs = slice(64 * h, 64 * h + 64)
                                last = pe.matmul(ps[:, 4 - ch, hs], G1[:, slot1(t, ch), h, :], S[:, hs], start=True, stop=True)
                            last.then_inc(z_ps, 1)
                            pe.wait_ge(z_sb, n + 1)
                            rows = slice(64 * ch, 64 * ch + 64)
                            for h in range(NH):
                                hs = slice(64 * h, 64 * h + 64)
                                last = pe.matmul(ps[0:64, 5, hs], STK[sY][rows, hs], Zs[rows, hs], start=True, stop=True)
                            last.then_inc(u_ps, 1)
                            pe.wait_ge(u_sb, n + 1)
                            for h in range(NH):
                                hs = slice(64 * h, 64 * h + 64)
                                last = pe.matmul(ps[:, 6 - 4 * ch, hs], G2[:, ch, h, :], Un[:, hs], start=True, stop=True)
                            last.then_inc(n_ps, 1)
                        pe.matmul(ps[0:w, 0, :], zz[:, 13, 128 * t:128 * t + w], g2[:, :], start=True, stop=True).then_inc(gate_ps, 1)
                        if t == 3:
                            pe.wait_ge(n_sb, 9)
                            for c in range(4):
                                last = pe.transpose(ps[:, 5, 64 * c:64 * c + 64], Sv[0][0:64, 128 * c:128 * c + 128], ident[0:64, 0:64])
                            last.then_inc(pT_ps, 1)
                            pe.wait_ge(pT_sb, 1)
                        pe.wait_ge(yo, t + 1)
                        for c in range(4):
                            last = pe.transpose(ps[:, 1, 128 * c:128 * c + w], yb[0:w, 128 * c:128 * c + 128], ident[0:w, 0:w])
                        last.then_inc(yt_ps2, 1)
                    for h in range(NH):
                        pe.wait_ge(um_ready, h + 1)
                        if h >= 2:
                            pe.wait_ge(sn_sb, h - 1)
                        if h == 0:
                            pe.wait_ge(yt_sb2, TILES)
                        pe.matmul(ps[0:64, h % 2, :], G2[:, 0, h, 0:64], Um[h % 2][:, :, :].rearrange("p b i -> p (b i)"), start=True, stop=True).then_inc(sn_ps, 1)
                        pe.wait_ge(sn_sb, h + 1)
                        if h >= 2:
                            pe.wait_ge(so_sb, h - 1)
                        for qq in range(4):
                            last = pe.transpose(ps[:, 2 + h % 2, 64 * qq:64 * qq + 64], Sn[h % 2][:, 2 * qq:2 * qq + 2, :].rearrange("p b i -> p (b i)"), ident[0:64, 0:64])
                        last.then_inc(so_ps, 1)

                @block.gpsimd
                def _(pool):
                    for n in range(3):
                        pool.memset(DIA[n][:, :, :], 0.0)
                    pool.memset(DIA[3][:, :, :], 0.0).then_inc(g_zero, 1)
                    pool.memset(DIA[4][:, :, :], 0.0).then_inc(g_zero, 1)
                    pool.wait_ge(g_zero, 2)
                    for t in range(TILES):
                        P = 64 * chunks_of(t)
                        pool.wait_ge(dd_sb, t + 1)
                        for ch in range(chunks_of(t)):
                            rows = slice(64 * ch, 64 * ch + 64)
                            idb = ident[rows, rows].rearrange("p (o t) -> p o t", o=1).to_broadcast([64, NH, CH])
                            last = pool.tensor_tensor(STK[sY][rows].rearrange("p (h t) -> p h t", h=NH), STK[sA][rows].rearrange("p (h t) -> p h t", h=NH),
                                                      idb, ALU.add)
                        last.then_inc(y_set, 1)
                        pool.wait_ge(gg_sb, t + 1)
                        for ch in range(chunks_of(t)):
                            rows = slice(64 * ch, 64 * ch + 64)
                            last = pool.tensor_copy(DIA[4][rows, :, 64 * ch:64 * ch + 64], STK[sE][rows].rearrange("p (h t) -> p h t", h=NH))
                        last.then_inc(e_bd, 1)

                @block.scalar
                def _(act):
                    act.wait_ge(g_zero, 1)
                    for t in range(TILES):
                        C, P, w = chunks_of(t), 64 * chunks_of(t), ntok(t)
                        if t >= 1:
                            act.wait_ge(yt_ps2, t)
                        for x, src in ((0, AB[:, 0]), (1, zz[:, 0:4])):
                            for hb in range(2):
                                last = act.copy(AR[:, 0:C, hb::2, 64 * x:64 * x + 64].rearrange("p n c t -> p c n t"),
                                                src[64 * hb:64 * hb + 64, :, 128 * t:128 * t + w].rearrange("p c (n t) -> p c n t", n=C))
                        last.then_inc(cp_a, 1)
                        act.wait_ge(dd_sb, t + 1)
                        for stk, dia in ((sA, 0), (sB, 1)):
                            for ch in range(C):
                                rows = slice(64 * ch, 64 * ch + 64)
                                last = act.copy(DIA[dia][rows, :, 64 * ch:64 * ch + 64], STK[stk][rows].rearrange("p (h t) -> p h t", h=NH))
                        last.then_inc(bd_a, 1)
                        act.wait_ge(bkt_ps, t + 1)
                        act.copy(G2[:, 0:C, :, 0:64], ps[:, 5:5 + C, :].rearrange("p c (h j) -> p c h j", h=NH)).then_inc(bkt_sb, 1)
                        act.wait_ge(v_ps, t + 1)
                        for ch in range(C):
                            n = chunk_no(t, ch)
                            rows = slice(64 * ch, 64 * ch + 64)
                            act.copy(Sv[n % 2][64:128, :], ps[rows, 7, :])
                            act.copy(Uv[n % 2][64:128, :], ps[rows, 7, :]).then_inc(v_sb, 1)
                        if t == 4:
                            for b in range(NB):
                                act.wait_ge(sT_ps, b + 1)
                                act.copy(S0T[:, b, :], ps[0:64, 6, :]).then_inc(sT_sb, 1)
                            act.wait_ge(zsT_ps, 1)
                            act.copy(G1[0:64, 1].rearrange("p (b h) w -> p b (h w)", b=2), ps[0:64, 2:4, :]).then_inc(zsT_sb, 1)
                        for s in MOVES:
                            act.wait_ge(inv_ps[1], NSTEP * t + s + 1)
                            move_out(act.copy, t, s, 1).then_inc(inv_m1, 1)
                        act.wait_ge(yn_a, t + 1)
                        act.activation(ysq_v[0:w, :], yb[0:w, :], ACT.Square).then_inc(yn_b, 1)
                        act.wait_ge(yn_c, 2 * t + 1)
                        act.activation(st8[0:w, 1, :], st8[0:w, 1, :], ACT.Sqrt).then_inc(yn_b, 1)
                        if t == 3:
                            act.wait_ge(pT_ps, 1)
                            act.copy(SpO[:, :, :], ps[:, 5, 0:256].rearrange("p (c j) -> p c j", c=4)).then_inc(pT_sb, 1)
                        act.wait_ge(yt_ps2, t + 1)
                        act.copy(mixf[:, 4:8, 128 * t:128 * t + w], ps[:, 1, :].rearrange("p (c t) -> p c t", c=4)[:, :, 0:w]).then_inc(yt_sb2, 1)
                    for h in range(NH):
                        act.wait_ge(so_ps, h + 1)
                        act.copy(So[:, h, :, :], ps[:, 2 + h % 2, 0:256].rearrange("p (q j) -> p q j", q=4)).then_inc(so_sb, 1)

                @block.vector
                def _(dve):
                    L = lambda ins: dve_chain(dve, ins)
                    dve.memset(G1[64:128, :, :, 64:128], 0.0)
                    dve.memset(Sv[0][0:64, :], 0.0).then_inc(n_sb, 1)
                    dve.wait_ge(m_in, 48)
                    for t in range(TILES):
                        C, P, w, ms = chunks_of(t), 64 * chunks_of(t), ntok(t), int(t == 4)
                        if t >= 1:
                            dve.wait_ge(yt_ps2, t)
                        for x, src in ((0, AB[:, 1]), (1, zz[:, 4:8])):
                            for hb in range(2):
                                last = dve.tensor_copy(BK[:, 0:C, hb::2, x, :].rearrange("p n c t -> p c n t"),
                                                       src[64 * hb:64 * hb + 64, :, 128 * t:128 * t + w].rearrange("p c (n t) -> p c n t", n=C))
                        last.then_inc(cp_d, 1)
                        dve.wait_ge(gg_ps, t + 1)
                        hv = lambda x: x.rearrange("p (h t) -> p h t", h=NH)
                        bm = lambda rows, m_, x: imask[rows, m_, 2 * ms + x:2 * ms + x + 1, :].to_broadcast([rows.stop - rows.start, NH, CH])
                        prod = lambda rows, ch, x: ps[rows, 2 * ch:2 * ch + 2, :].rearrange("p b (h x t) -> p (b h) x t", h=4, x=2)[:, :, x, :]
                        low = slice(0, 64)
                        for ch in range(C):
                            dve.tensor_tensor(hv(STK[sA][64 * ch:64 * ch + 64]), prod(low, ch, 0), bm(low, 0, 0), ALU.mult)
                        dve.tensor_tensor(hv(STK[sB][0:P]), hv(ps[0:P, 4, :]), bm(slice(0, P), 1, 0), ALU.mult).then_inc(dd_sb, 1)
                        for ch in range(C):
                            dve.tensor_tensor(hv(STK[sE][64 * ch:64 * ch + 64]), prod(low, ch, 0), bm(low, 0, 1), ALU.mult)
                            mk = lambda rows, x: gmask[rows, ms:ms + 1, 64 * x:64 * x + 64].to_broadcast([rows.stop - rows.start, NH, CH])
                            dve.tensor_tensor(G1[64:128, slot1(t, ch), :, 0:64], prod(slice(64, 128), ch, 0), mk(slice(64, 128), 0), ALU.mult)
                            last = dve.tensor_tensor(G2[:, ch, :, 64:128], prod(slice(0, 128), ch, 1), mk(slice(0, 128), 1), ALU.mult)
                        last.then_inc(gg_sb, 1)
                        if t == 4:
                            dve.tensor_copy(hv(Sv[0][0:64, :]), ident[0:64, 0:64].rearrange("p (o t) -> p o t", o=1).to_broadcast([64, NH, CH]))
                        for s in range(NSTEP):
                            dve.wait_ge(inv_ps[0], NSTEP * t + s + 1)
                            if s in MOVES:
                                last = move_out(dve.tensor_copy, t, s, 0)
                            if s in ADDS:
                                last = dve.tensor_tensor(STK[sY][0:P, 0:256], ps[0:P, 1, 0:256], STK[sY][0:P, 0:256], ALU.add)
                            last.then_inc(inv_0, 1)
                            if s in ADDS:
                                dve.wait_ge(inv_ps[1], NSTEP * t + s + 1)
                                dve.tensor_tensor(STK[sY][0:P, 256:512], ps[0:P, 3, 0:256], STK[sY][0:P, 256:512], ALU.add).then_inc(inv_y1, 1)
                        for ch in range(C):
                            n = chunk_no(t, ch)
                            S, Nx, Un = Sv[n % 2], Sv[(n + 1) % 2], Uv[n % 2]
                            rows = slice(64 * ch, 64 * ch + 64)
                            dve.wait_ge(z_ps, n + 1)
                            dve.tensor_copy(Zs[rows, :], ps[0:64, 4 - ch, :]).then_inc(z_sb, 1)
                            dve.wait_ge(u_ps, n + 1)
                            dve.tensor_copy(Un[0:64, :], ps[0:64, 5, :]).then_inc(u_sb, 1)
                            dve.wait_ge(n_ps, n + 1)
                            if t < 4:
                                L(dve.tensor_tensor(Nx[0:64, :], ps[0:64, 6 - 4 * ch, :], S[0:64, :], ALU.add))
                                nx = Nx[0:64, :].rearrange("p (h i) -> p h i", h=NH)
                                dve.tensor_tensor(nx, nx, pc[:, :, n:n + 1].to_broadcast([64, NH, CH]), ALU.mult).then_inc(n_sb, 1)
                            dve.tensor_copy(yb[rows, :], ps[64:128, 4 - ch, :]).then_inc(yc_sb, 1)
                            dve.wait_ge(yc_sb, 2 * n + 1)
                            dve.tensor_tensor(yb[rows, :], yb[rows, :], ps[64:128, 6 - 4 * ch, :], ALU.add).then_inc(yc_sb, 1)
                        dve.wait_ge(yc_sb, 2 * chunks_to(t))
                        per = lambda x: x.rearrange("p (h o) -> p h o", o=1).to_broadcast([w, NH, CH])
                        L(dve.tensor_reduce(st8[0:w, 0, :], hv(yb[0:w, :]), AX.X, ALU.add))
                        L(dve.tensor_scalar(st8[0:w, 0, :], st8[0:w, 0, :], 1.0 / HD, None, ALU.mult))
                        dve.tensor_tensor(hv(yb[0:w, :]), hv(yb[0:w, :]), per(st8[0:w, 0, :]), ALU.subtract).then_inc(yn_a, 1)
                        dve.wait_ge(yn_b, 2 * t + 1)
                        L(dve.tensor_reduce(st8[0:w, 1, :], hv(ysq_v[0:w, :]), AX.X, ALU.add))
                        dve.tensor_scalar(st8[0:w, 1, :], st8[0:w, 1, :], 1.0 / HD, GN_EPS, ALU.mult, ALU.add).then_inc(yn_c, 1)
                        dve.wait_ge(yn_b, 2 * t + 2)
                        dve.nop().then_inc(yn_c, 1)
                        L(dve.reciprocal(st8[0:w, 1, :], st8[0:w, 1, :]))
                        L(dve.tensor_tensor(hv(yb[0:w, :]), hv(yb[0:w, :]), per(st8[0:w, 1, :]), ALU.mult))
                        L(dve.tensor_tensor(yb[0:w, :], yb[0:w, :], lnw[0:w, :], ALU.mult))
                        L(dve.tensor_tensor(yb[0:w, :], yb[0:w, :], lnb[0:w, :], ALU.add))
                        L(dve.tensor_tensor(hv(ysq_v[0:w, :]), hv(ps[0:w, 7, :]), per(bonus[0:w, t, :]), ALU.mult))
                        L(dve.tensor_tensor(yb[0:w, :], yb[0:w, :], ysq_v[0:w, :], ALU.add))
                        dve.wait_ge(gate_ps, t + 1)
                        dve.tensor_tensor(yb[0:w, :], yb[0:w, :], ps[0:w, 0, :], ALU.mult).then_inc(yo, 1)
                    dve.wait_ge(yt_ps2, TILES)
                    for h in range(NH):
                        if h >= 2:
                            dve.wait_ge(sn_ps, h - 1)
                        hs = slice(64 * h, 64 * h + 64)
                        dve.tensor_tensor(Um[h % 2][:, :, :], Uv[0][:, hs].rearrange("p (o i) -> p o i", o=1).to_broadcast([128, NB, CH]),
                                          smask[:, :].rearrange("p (b o) -> p b o", o=1).to_broadcast([128, NB, CH]), ALU.mult).then_inc(um_ready, 1)
                        dve.wait_ge(sn_ps, h + 1)
                        if h >= 2:
                            dve.wait_ge(so_ps, h - 1)
                        L(dve.tensor_tensor(Sn[h % 2][:, :, :], ps[0:64, h % 2, :].rearrange("p (b i) -> p b i", b=NB), S0T[:, :, hs], ALU.add))
                        dve.tensor_tensor(Sn[h % 2][:, :, :], Sn[h % 2][:, :, :],
                                          pc[:, h, 8:16].rearrange("p (b o) -> p b o", o=1).to_broadcast([64, NB, CH]), ALU.mult).then_inc(sn_sb, 1)

            flush([(flat(zlast[:, :, :]), 9 * RT, [(0, RT, o["shift_p"].rearrange("b o (c p) -> (b o c) p", p=128)),
                                                   (RT, 9 * RT, o["shift_s"].rearrange("b o (c p) -> (b o c) p", p=128))])], Region(RZ))
            mix_out(mixf)

        def mix_out(mixf):
            reg = Region(R + 8 * T * 4 + 2 * KT * TPAD * 4)
            mhi, mlo = reg.take("mix_hi", [128, KT, T], F32R), reg.take("mix_lo", [128, KT, T], F32R)
            mix_hi_ready, mix_lo_ready = sem("mix_hi_ready"), sem("mix_lo_ready")
            with nc.Block() as block:
                @block.scalar
                def _(act):
                    for c in range(KT):
                        act.copy(mhi[:, c, :], mixf[:, c, :]).then_inc(mix_hi_ready, 1)

                @block.vector
                def _(dve):
                    for c in range(KT):
                        dve.wait_ge(mix_hi_ready, c + 1)
                        dve.tensor_tensor(mlo[:, c, :], mixf[:, c, :], mhi[:, c, :].bitcast(F32), ALU.subtract)
            residual(st_out, mhi, mlo)

        keep_semaphores()
        even_mixer()
        retire_semaphores()
        ffn(0, ffn0, V_FFN)
        conv_mixer()
        ffn(1, ffn1, V_FFN + 8)
        store_y()


_INS = ["x_prompt", "x_sample", "cache_cmp_kv", "cache_slc_kv", "cache_win_kv", "state_rwkv_wkv",
        "state_rwkv_shift", "state_conv", "state_ffn_conv", "page_table", "norm_mix", "norm_ffn",
        "rel_bias", "w_in_even", "w_out_even", "q_norm", "k_norm", "phi_pe", "phi_w1", "phi_w2",
        "rwkv_mu", "rwkv_w0", "rwkv_w2", "rwkv_a0", "rwkv_a2", "rwkv_g2", "rwkv_kk", "rwkv_ka", "rwkv_rk",
        "rwkv_ln_w", "rwkv_ln_b", "w_in_odd", "conv_w", "w_out_odd", "ffn_up", "ffn_conv", "ffn_down"]
_OUTS = [("y_prompt", (1, TP, D)), ("y_sample", (NB, TS, D)),
         ("cmp_p", (1, 1, TP, 2, 2, HD)), ("cmp_s", (NB, 1, TS, 2, 2, HD)),
         ("slc_p", (1, 1, TP, 2, 2, HD)), ("slc_s", (NB, 1, TS, 2, 2, HD)),
         ("win_p", (1, 1, TP, 2, 2, HD)), ("win_s", (NB, 1, 512, 2, 2, HD)),
         ("wkv_p", (1, 1, NH, HD, HD)), ("wkv_s", (NB, 1, NH, HD, HD)),
         ("shift_p", (1, 1, W_RW)), ("shift_s", (NB, 1, W_RW)),
         ("conv_p", (1, 1, 2, D)), ("conv_s", (NB, 1, 2, D)),
         ("ffn_p", (1, 2, 2, DFF)), ("ffn_s", (NB, 2, 2, DFF))]


def kernel(**inputs):
    import concourse.bacc as bacc
    from concourse.bass_utils import run_bass_kernel_spmd

    nc = bacc.Bacc("TRN2", target_bir_lowering=False, num_devices=1)
    arrays, ins, outs, consts = {}, {}, {}, {}
    for name in _INS:
        a = np.ascontiguousarray(inputs[name])
        arrays[f"in_{name}"] = a
        ins[name] = nc.dram_tensor(f"in_{name}", a.shape, mybir.dt.from_np(a.dtype), kind="ExternalInput").ap()
    for name, a in tables().items():
        arrays[f"const_{name}"] = a
        consts[name] = nc.dram_tensor(f"const_{name}", a.shape, F32, kind="ExternalInput").ap()
    for name, shape in _OUTS:
        outs[name] = nc.dram_tensor(f"out_{name}", shape, F32, kind="ExternalOutput").ap()
    build(nc, ins, outs, consts)
    r = run_bass_kernel_spmd(nc, [arrays], core_ids=[0])
    return tuple(r.results[0][f"out_{name}"] for name, _ in _OUTS)
```

```python
import concourse.bass as bass
from concourse import mybir
import numpy as np
import math
from contextlib import ExitStack

F32 = mybir.dt.float32
F32R = mybir.dt.float32r
I32 = mybir.dt.int32
ALU = mybir.AluOpType
ACT = mybir.ActivationFunctionType
AX = mybir.AxisListType

D = 1024
KT = D // 128
TP = 512
NB, TS = 8, 8
NS = NB * TS
T = TP + NS
HT = T // 2
TPAD = 640
DFF = 2816
FT = DFF // 128
HD = 64
NH = 8
W_NSA = 1304
W_RW = 1792
RT = W_RW // 128
SLAB = 2048
EPS = 1e-6
GN_EPS = 64e-5
NEG = -1e30
FLOOR = -1e25
CH = 64
PAGE = 128
NBK = 32
RVL = 1168
RV0 = 638
BTW = 1040

V_MIX, V_FFN, V_CONV, V_MU, V_W0, V_A0, V_KK, V_KA, V_RK, V_ROWS = 0, 16, 32, 56, 70, 74, 78, 82, 86, 90


def tables():
    dist = RV0 - np.arange(RVL)
    n = np.maximum(dist, 0)
    nf = np.maximum(n, 1).astype(np.float32)
    large = 16 + (np.log(nf / np.float32(16)) / np.float32(math.log(8.0)) * np.float32(16)).astype(np.int32)
    bucket = np.where(n < 16, n, np.minimum(large, 31))
    onehot = (bucket[None, :] == np.arange(NBK)[:, None]).astype(np.float32)
    masked = np.broadcast_to(np.where(dist >= 0, 0.0, NEG).astype(np.float32)[None, :], (NH, RVL)).copy()
    s = np.arange(CH)
    strict, incl = s[:, None] < s[None, :], s[:, None] <= s[None, :]
    same = (s[:, None] // TS) == (s[None, :] // TS)
    def gmask(m):
        return np.block([[strict & m, incl & m], [strict & m, incl & m]])
    gm = np.stack([gmask(np.ones((CH, CH), bool)), gmask(same)], 1).astype(np.float32)
    blk = (s[:, None] // 16) == (s[None, :] // 16)
    up = np.stack([strict & blk, strict & ~blk, strict & blk & same, strict & ~blk & same], 1)
    lo = np.stack([strict.T & blk, strict.T & ~blk, strict.T & blk & same, strict.T & ~blk & same], 1)
    inv = np.tile(np.stack([up, lo], 1).astype(np.float32), (2, 1, 1, 1))
    keep = np.ones((128, T), np.float32)
    keep[:, 0:TP:CH] = 0.0
    keep[:, TP::TS] = 0.0
    seq = ((np.arange(128)[:, None] % CH) // TS == np.arange(NB)[None, :]).astype(np.float32)
    head = np.zeros((128, 128), np.float32)
    head[:64, :64] = 1.0
    head[64:, 64:] = 1.0
    row = np.arange(128)
    wmask = np.where(np.arange(TS)[None, :] <= (row % TS)[:, None], NEG, 0.0).astype(np.float32)
    return dict(onehot=onehot, masked=masked, gmask=gm, invmask=inv, keep=keep, seqmask=seq,
                headones=head, ident=np.eye(128, dtype=np.float32),
                flip=np.eye(128, dtype=np.float32)[::-1].copy(), wmask=wmask)



class Chain:

    def __init__(self, sem):
        self.sem, self.n, self.loop = sem, 0, None

    def __call__(self, eng, ins):
        ins.then_inc(self.sem, 1)
        self.n += 1
        if self.loop is None:
            eng.wait_ge(self.sem, self.n)
        else:
            i, start, per, _ = self.loop
            eng.wait_ge(self.sem, i * per + self.n)
        return ins

    def begin(self, i, per, trips):
        self.loop = (i, self.n, per, trips)

    def end(self):
        i, start, per, trips = self.loop
        assert self.n - start == per, (self.n - start, per)
        self.n = start + per * trips
        self.loop = None


def build(nc, a, o, k):
    ctx = ExitStack()
    base = [nc.sbuf_base + (-nc.sbuf_base) % 64]
    names = [0]

    def at(name, shape, dt, offset):
        names[0] += 1
        return nc.alloc_sbuf_tensor_at(f"{name}_{names[0]}", shape, dt, offset=offset)

    def fixed(name, shape, dt=F32):
        size = 4 * int(np.prod(shape[1:]))
        t = at(name, shape, dt, base[0])
        base[0] += size + (-size) % 32
        return t

    sems = {}

    lasting = []

    def sem(name):
        if name not in sems:
            sems[name] = nc.alloc_semaphore(name)
        return sems[name]

    def keep_semaphores():
        lasting[:] = list(sems)

    def retire_semaphores():
        old = [sems.pop(name) for name in list(sems) if name not in lasting]
        nc.clear_and_free_semaphores(old)
        nc.all_engine_barrier()

    with ctx:
        ctx.enter_context(nc.allow_non_contiguous_dma(reason="small tables"))
        raw = [fixed(f"w_raw{s}", [128, SLAB]) for s in range(2)]
        whi = [fixed(f"w_hi{s}", [128, SLAB], F32R) for s in range(2)]
        wlo = [fixed(f"w_lo{s}", [128, SLAB], F32R) for s in range(2)]
        xT = fixed("xT", [128, KT, T])
        ident = fixed("ident", [128, 128])
        ones = fixed("ones", [128, 128])
        vec = fixed("vec", [128, V_ROWS])
        ffnw = fixed("ffnw", [128, 2, 3, FT])
        convst = fixed("convst", [128, NB, 2, KT])
        ffnst = fixed("ffnst", [128, 2, NB, 2, FT])
        newconv = fixed("newconv", [128, 9, 2, KT])
        newffn = fixed("newffn", [128, 2, 9, 2, FT])
        zlast = fixed("zlast", [128, 9, RT])
        R = base[0]
        END = nc.sbuf_usable_end

        class Region:
            def __init__(self, start):
                self.at = start + (-start) % 32

            def take(self, name, shape, dt=F32):
                size = 4 * int(np.prod(shape[1:]))
                t = at(name, shape, dt, self.at)
                self.at += size + (-size) % 32
                assert self.at <= END, (name, self.at - END)
                return t

        ps = ctx.enter_context(nc.psum_tensor("ps", [128, 8, 512], F32))
        rv_dram = nc.dram_tensor("rv", (NH, RVL), F32, kind="Internal").ap()
        gate_dram = nc.dram_tensor("gates", (NS, 24), F32, kind="Internal").ap()

        w_in, w_out = a["w_in_even"][0], a["w_out_even"][0]
        w_in_odd, w_out_odd = a["w_in_odd"][0], a["w_out_odd"][0]

        def cols(w, kt0, kts, c0, width):
            return w.rearrange("(t p) n -> p t n", p=128)[:, kt0:kt0 + kts, bass.ds(c0, width)]

        stages = []
        n_slabs = [0]
        bank_uses = [0, 0]

        def stage(n, kts, width, src):
            st = dict(base=n_slabs[0], n=n, kts=kts, width=width, src=src, before=tuple(bank_uses))
            n_slabs[0] += n
            bank_uses[0] += (n + 1) // 2
            bank_uses[1] += n // 2
            stages.append(st)
            return st

        st_nsa = stage(5, KT, 256, lambda s: cols(w_in, 0, KT, 256 * s, 256))
        st_gate = stage(1, KT, 24, lambda s: cols(w_in, 0, KT, 1280, 24))
        st_rw = stage(7, KT, 256, lambda s: cols(w_in, 0, KT, W_NSA + 256 * s, 256))
        st_out = stage(4, KT, 256, lambda s: cols(w_out, 0, KT, 256 * s, 256))

        def ffn_stages(l):
            out = []
            up, down = a["ffn_up"][l], a["ffn_down"][l]
            for f0, nf in ((0, 12), (12, 10)):
                def src_up(s, f0=f0, side=None):
                    return cols(up, 0, KT, side * DFF + 128 * f0 + 256 * s, 256)
                out.append((stage(nf, KT, 256, src_up), stage(8, nf, 128, lambda s, f0=f0, nf=nf: cols(down, f0, nf, 128 * s, 128)), f0, nf))
            return out

        ffn0 = ffn_stages(0)
        st_odd = stage(12, KT, 256, None)
        st_oout = stage(4, KT, 256, lambda s: cols(w_out_odd, 0, KT, 256 * s, 256))
        ffn1 = ffn_stages(1)

        def stage_at(g):
            for st in stages:
                if st["base"] <= g < st["base"] + st["n"]:
                    return st
            return None

        def slab_source(st, p, q, m):
            if st is st_odd:
                return cols(w_in_odd, 0, KT, (D, 2 * D, 0)[q % 3] + 256 * (p * (m // 3) + q // 3), 256)
            if st["n"] in (12, 10) and st is not st_odd:
                return st["src"](p * (m // 2) + q // 2, side=q % 2)
            return st["src"](p * m + q)

        def slab_view(t, st):
            return t[:, 0:st["kts"] * st["width"]]

        w_loaded = [sem("w_loaded0"), sem("w_loaded1")]
        w_hi_ready, w_lo_ready, slab_done = sem("w_hi_ready"), sem("w_lo_ready"), sem("slab_done")
        banks_free = [sem("banks_free_low"), sem("banks_free_high")]

        def load_slab(sp, st, p, q, m):
            g = st["base"] + p * m + q
            slot = (st["base"] + q) % 2
            if st["base"] + q >= 2:
                sp.wait_ge(w_lo_ready, g - 1)
            view = slab_view(raw[slot], st).rearrange("p (t n) -> p t n", t=st["kts"])
            sp.dma_start(view, slab_source(st, p, q, m)).then_inc(w_loaded[slot], 16)

        def slot_count(st, p, q, m):
            return 16 * ((st["base"] + q) // 2 + 1) + p * (8 * m)

        def split_hi(act, st, p, q, m):
            g = st["base"] + p * m + q
            slot = (st["base"] + q) % 2
            act.wait_ge(w_loaded[slot], slot_count(st, p, q, m))
            if st["base"] + q >= 2:
                act.wait_ge(slab_done, g - 1)
            act.activation(slab_view(whi[slot], st), slab_view(raw[slot], st), ACT.Copy).then_inc(w_hi_ready, 1)

        def split_lo(pool, st, p, q, m):
            g = st["base"] + p * m + q
            slot = (st["base"] + q) % 2
            pool.wait_ge(w_hi_ready, g + 1)
            pool.tensor_tensor(slab_view(wlo[slot], st), slab_view(raw[slot], st),
                               slab_view(whi[slot], st).bitcast(F32), ALU.subtract).then_inc(w_lo_ready, 1)

        def follow(g):
            st = stage_at(g)
            return None if st is None else (st, 0, g - st["base"], st_period(st))

        def st_period(st):
            return 12 if st is st_odd else 16

        def loads_after(sp, g):
            for x in (g, g + 1):
                f = follow(x)
                if f is not None:
                    load_slab(sp, *f)

        def wait_banks(pe, st, p, q, m):
            pe.wait_ge(banks_free[q % 2], st["before"][q % 2] + q // 2 + 1 + p * (m // 2))

        def products(pe, st, p, q, m, bank, xs, xhi, xlo, ready=None):
            g = st["base"] + p * m + q
            slot = (st["base"] + q) % 2
            wait_banks(pe, st, p, q, m)
            pe.wait_ge(w_lo_ready, g + 1)
            W = st["width"]
            for j in range(W // 128):
                for t in range(st["kts"]):
                    if ready is not None and j == 0:
                        ready(pe, t)
                    c = t * W + j * 128
                    for n, (w, x) in enumerate(((whi, xhi), (whi, xlo), (wlo, xhi))):
                        for half in range(2):
                            last = pe.matmul(ps[:, bank + 2 * j + half, 0:HT], w[slot][:, c:c + 128],
                                             x[:, xs + t, half * HT:(half + 1) * HT],
                                             start=(t == 0 and n == 0), stop=(t == st["kts"] - 1 and n == 2))
            last.then_inc(slab_done, 1)

        tmp = Region(R)
        xin = tmp.take("xin", [128, 5, D])
        rows = [tmp.take("rows_vec", [V_ROWS, 128]), tmp.take("rows_f0", [66, 128]), tmp.take("rows_f1", [66, 128]),
                tmp.take("rows_conv", [128, 128])]
        rows_st = [[tmp.take(f"rows_st{l}{n}", [88, 128]) for n in range(4)] for l in range(2)]
        x_in, x_tiles = sem("x_in"), sem("x_tiles")
        small_in, small_t = sem("small_in"), sem("small_t")
        start_ev, small_ev = sem("start_ev"), sem("small_ev")
        consts_in = sem("consts_in")
        dve_chain, act_chain = Chain(sem("dve_chain")), Chain(sem("act_chain"))
        ones_set = sem("ones_set")

        jobs = [(rows[0], V_ROWS, vec[:, :]), (rows[1], 66, ffnw[:, 0, :, :]), (rows[2], 66, ffnw[:, 1, :, :]),
                (rows[3], 128, convst[:, :, :, :])]
        for l in range(2):
            for n in range(4):
                jobs.append((rows_st[l][n], 88, ffnst[:, l, 2 * n:2 * n + 2, :, :]))

        def flat(t):
            n = len(t.shape)
            if n == 2:
                return t
            pat = {3: "p a b -> p (a b)", 4: "p a b c -> p (a b c)", 5: "p a b c d -> p (a b c d)"}[n]
            return t.rearrange(pat)

        ext_ready, conv_done, gate_ready = sem("ext_ready"), sem("conv_done"), sem("gate_ready")
        g_f, g_hi_ready, g_lo_ready = sem("g_f"), sem("g_hi_ready"), sem("g_lo_ready")
        with nc.Block() as block:
            @block.sync
            def _(sp):
                sp.dma_start(ident[:, :], k["ident"]).then_inc(consts_in, 16)
                for t in range(4):
                    sp.dma_start(xin[:, t, :], a["x_prompt"][0, 128 * t:128 * t + 128, :]).then_inc(x_in, 16)
                sp.dma_start(xin[0:NS, 4, :], a["x_sample"].rearrange("b t d -> (b t) d")).then_inc(x_in, 16)
                loads_after(sp, 0)

                def row_load(dst, src):
                    sp.dma_start(dst, src).then_inc(small_in, 16)
                v = rows[0]
                row_load(v[V_MIX:V_MIX + 16, :], a["norm_mix"].rearrange("l (c p) -> (l c) p", p=128))
                row_load(v[V_FFN:V_FFN + 16, :], a["norm_ffn"].rearrange("l (c p) -> (l c) p", p=128))
                row_load(v[V_CONV:V_CONV + 24, :], a["conv_w"][0].rearrange("k (c p) -> (k c) p", p=128))
                row_load(v[V_MU:V_MU + 14, :], a["rwkv_mu"].rearrange("l (c p) -> (l c) p", p=128))
                for at_, name in ((V_W0, "rwkv_w0"), (V_A0, "rwkv_a0"), (V_KK, "rwkv_kk"), (V_KA, "rwkv_ka")):
                    row_load(v[at_:at_ + 4, :], a[name].rearrange("l (c p) -> (l c) p", p=128))
                row_load(v[V_RK:V_RK + 4, :], a["rwkv_rk"][0].rearrange("(c h) d -> c (h d)", h=2))
                for l in range(2):
                    row_load(rows[1 + l][:, :], a["ffn_conv"][l].rearrange("k (c p) -> (k c) p", p=128))
                row_load(rows[3][:, :], a["state_conv"][:, 0].rearrange("b k (c p) -> (b k c) p", p=128))
                for l in range(2):
                    for n in range(4):
                        for h in range(2):
                            row_load(rows_st[l][n][44 * h:44 * h + 44, :],
                                     a["state_ffn_conv"][2 * n + h, l].rearrange("k (c p) -> (k c) p", p=128))

            @block.vector
            def _(dve):
                dve.memset(ones[:, :], 1.0).then_inc(ones_set, 1)
                for s in banks_free:
                    dve.nop().then_inc(s, 1)
                for s in (ext_ready, conv_done, gate_ready, g_f, g_hi_ready, g_lo_ready):
                    dve.nop().then_inc(s, 2)
                for n in range(10):
                    dve.wait_ge(x_tiles, n + 1)
                    t, c = n // 2, n % 2
                    w = 128 if t < 4 else NS
                    dve.tensor_copy(xT[:, 4 * c:4 * c + 4, 128 * t:128 * t + w],
                                    ps[:, n % 4, :].rearrange("p (c t) -> p c t", c=4)[:, :, 0:w]).then_inc(start_ev, 1)

            @block.scalar
            def _(act):
                split_hi(act, *follow(0))
                for n, (src, r, dst) in enumerate(jobs):
                    act.wait_ge(small_t, n + 1)
                    act.copy(flat(dst), ps[:, 4 + n % 4, 0:r]).then_inc(small_ev, 1)

            @block.gpsimd
            def _(pool):
                split_lo(pool, *follow(0))

            @block.tensor
            def _(pe):
                pe.wait_ge(consts_in, 16)
                pe.wait_ge(x_in, 80)
                for n in range(10):
                    t, c = n // 2, n % 2
                    w = 128 if t < 4 else NS
                    if n >= 4:
                        pe.wait_ge(start_ev, n - 3)
                    for q in range(4):
                        last = pe.transpose(ps[:, n % 4, 128 * q:128 * q + w],
                                            xin[0:w, t, (4 * c + q) * 128:(4 * c + q + 1) * 128], ident[0:w, 0:w])
                    last.then_inc(x_tiles, 1)
                pe.wait_ge(small_in, 16 * (9 + 2 + 1 + 16))
                for n, (src, r, dst) in enumerate(jobs):
                    if n >= 4:
                        pe.wait_ge(small_ev, n - 3)
                    pe.transpose(ps[:, 4 + n % 4, 0:r], src[:, :], ident[0:r, 0:r]).then_inc(small_t, 1)

        sq_ready, sq_used, ms_ready = sem("sq_ready"), sem("sq_used"), sem("ms_ready")
        std_ready, h_f, h_hi_ready, h_lo_ready, ms_used = sem("std_ready"), sem("h_f"), sem("h_hi_ready"), sem("h_lo_ready"), sem("ms_used")
        norms = [0]

        TOP = END - END % 32
        sq_sum = at("sq_sum", [128, T], F32, TOP - 4 * T)
        sq_slot = [at("sq_slot", [128, T], F32, TOP - 4 * T * (2 + n)) for n in range(2)]
        x_done, sq_set, sq_added = sem("x_done"), sem("sq_set"), sem("sq_added")
        h_lo_dve = sem("h_lo_dve")
        DVE_LO = (2, 5)
        squares = [0]

        def norm(gain, hhi, hlo, region, summed=True):
            reg = Region(region)
            sq = None if summed else reg.take("sq", [128, 2, T])
            hf = reg.take("hf", [128, 3, T])
            std = reg.take("std", [128, T])
            rstd = reg.take("rstd", [128, T])
            i0 = norms[0]
            norms[0] += 1
            b0, n_pool, n_dve = 8 * i0, (KT - len(DVE_LO)) * i0, len(DVE_LO) * i0

            def lo_ready(eng, c):
                if c in DVE_LO:
                    eng.wait_ge(h_lo_dve, n_dve + DVE_LO.index(c) + 1)
                else:
                    eng.wait_ge(h_lo_ready, n_pool + sum(x not in DVE_LO for x in range(c + 1)))

            def act_part(act):
                if not summed:
                    for c in range(KT):
                        if c >= 2:
                            act.wait_ge(sq_used, c - 1)
                        act.activation(sq[:, c % 2, :], xT[:, c, :], ACT.Square).then_inc(sq_ready, 1)
                act.wait_ge(ms_used, i0 + 1)
                act.activation(std[:, :], std[:, :], ACT.Sqrt).then_inc(std_ready, 1)
                for c in range(KT):
                    act.wait_ge(h_f, b0 + c + 1)
                    act.copy(hhi[:, c, 0:T], hf[:, c % 3, :]).then_inc(h_hi_ready, 1)

            def pe_part(pe):
                if summed:
                    pe.wait_ge(sq_added, 8 * squares[0])
                    for half in range(2):
                        last = pe.matmul(ps[:, half, 0:HT], ones[:, :], sq_sum[:, half * HT:(half + 1) * HT], start=True, stop=True)
                    last.then_inc(ms_ready, 1)
                    return
                for c in range(KT):
                    pe.wait_ge(sq_ready, c + 1)
                    for half in range(2):
                        last = pe.matmul(ps[:, half, 0:HT], ones[:, :], sq[:, c % 2, half * HT:(half + 1) * HT],
                                         start=(c == 0), stop=(c == KT - 1))
                    last.then_inc(sq_used, 1)
                pe.nop().then_inc(ms_ready, 1)

            def dve_part(dve):
                if not summed:
                    dve.wait_ge(sq_used, KT)
                dve.wait_ge(ms_ready, i0 + 1)
                dve.tensor_scalar(std[:, :].rearrange("p (a t) -> p a t", a=2), ps[:, 0:2, 0:HT],
                                  1.0 / D, EPS, ALU.mult, ALU.add).then_inc(ms_used, 1)
                dve.wait_ge(std_ready, i0 + 1)
                dve_chain(dve, dve.reciprocal(rstd[:, :], std[:, :]))
                for c in range(KT + 1):
                    if c < KT:
                        if c >= 3:
                            lo_ready(dve, c - 3)
                        dve.scalar_tensor_tensor(hf[:, c % 3, :], xT[:, c, :], vec[:, gain + c:gain + c + 1], rstd[:, :],
                                                 ALU.mult, ALU.mult).then_inc(h_f, 1)
                    if c - 1 in DVE_LO:
                        dve.wait_ge(h_hi_ready, b0 + c)
                        dve.tensor_tensor(hlo[:, c - 1, 0:T], hf[:, (c - 1) % 3, :], hhi[:, c - 1, 0:T].bitcast(F32),
                                          ALU.subtract).then_inc(h_lo_dve, 1)

            def pool_part(pool):
                for c in range(KT):
                    if c not in DVE_LO:
                        pool.wait_ge(h_hi_ready, b0 + c + 1)
                        pool.tensor_tensor(hlo[:, c, 0:T], hf[:, c % 3, :], hhi[:, c, 0:T].bitcast(F32),
                                           ALU.subtract).then_inc(h_lo_ready, 1)
            return dict(act=act_part, pe=pe_part, dve=dve_part, pool=pool_part, ready=lo_ready)

        def residual(st, hhi, hlo, sum_squares=True, first=None):
            n, base_g, J = st["n"], st["base"], st["width"] // 128
            s0 = 8 * squares[0]
            if sum_squares:
                squares[0] += 1

            def squares_of(act, f, f0):
                act.wait_ge(x_done, s0 + f + 1)
                if f0 >= 2:
                    act.wait_ge(sq_added, s0 + f - 1)
                act.activation(sq_slot[f0 % 2][:, :], xT[:, f, :], ACT.Square).then_inc(sq_set, 1)

            def add_square(pool, f):
                pool.wait_ge(sq_set, s0 + f + 1)
                if f == 0:
                    pool.tensor_copy(sq_sum[:, :], sq_slot[0][:, :]).then_inc(sq_added, 1)
                else:
                    pool.wait_ge(sq_added, s0 + f)
                    pool.tensor_tensor(sq_sum[:, :], sq_sum[:, :], sq_slot[f % 2][:, :], ALU.add).then_inc(sq_added, 1)
            with nc.Block() as block:
                @block.sync
                def _(sp):
                    with sp.Fori(0, (n - 2) // 2) as i:
                        for q in (2, 3):
                            load_slab(sp, st, i, q, 2)
                    loads_after(sp, base_g + n)

                @block.scalar
                def _(act):
                    if first:
                        first["act"](act)
                    for g in range(1, n + 2):
                        if g < n:
                            split_hi(act, st, 0, g, 16)
                        elif g == n and follow(base_g + n):
                            split_hi(act, *follow(base_g + n))
                        if sum_squares and g >= 2:
                            for j in range(J):
                                squares_of(act, J * (g - 2) + j, J * (g - 2) + j)

                @block.gpsimd
                def _(pool):
                    for g in range(1, n + 2):
                        if g < n:
                            split_lo(pool, st, 0, g, 16)
                        elif g == n and follow(base_g + n):
                            split_lo(pool, *follow(base_g + n))
                        if sum_squares and g >= 2:
                            for j in range(J):
                                add_square(pool, J * (g - 2) + j)

                @block.tensor
                def _(pe):
                    for i in range(n // 2):
                        for q in (0, 1):
                            products(pe, st, i, q, 2, 4 * q, 0, hhi, hlo, first["ready"] if first and i == q == 0 else None)

                @block.vector
                def _(dve):
                    if first:
                        first["dve"](dve)
                    with dve.Fori(0, n // 2) as i:
                        for q in (0, 1):
                            dve.wait_ge(slab_done, base_g + 2 * i + q + 1)
                            for j in range(J):
                                x = xT[:, bass.ds(2 * J * i + J * q + j, 1), :].rearrange("p o (a t) -> p (o a) t", a=2)
                                b = 4 * q + 2 * j
                                last = dve.tensor_tensor(x, ps[:, b:b + 2, 0:HT], x, ALU.add)
                                if sum_squares:
                                    last.then_inc(x_done, 1)
                            if sum_squares:
                                dve.wait_ge(x_done, s0 + J * (2 * i + q + 1))
                                dve.nop().then_inc(banks_free[q], 1)
                            else:
                                last.then_inc(banks_free[q], 1)

        EW = 2 + TP + NB * (TS + 2)
        YW = EW - 2

        def prompt_of(t):
            return t[:, 2:2 + TP]

        def sample_of(t):
            return t[:, 2 + TP:EW].rearrange("p (b t) -> p b t", b=NB)

        zeroed = sem("zeroed")
        gates_done = [2]
        tiles_done = [2]
        zero_count = [0]
        H1 = TP - HT

        def gated_mult(dve, out, y, bank):
            dve.tensor_tensor(out[:, 0:HT], y[:, 0:HT], ps[:, bank, 0:HT], ALU.mult)
            dve.tensor_tensor(out[:, HT:TP], y[:, HT:TP], ps[:, bank + 1, 0:H1], ALU.mult)
            ys = y[:, TP + 2:TP + 2 + NB * 10].rearrange("p (b t) -> p b t", b=NB)[:, :, 0:TS]
            return dve.tensor_tensor(out[:, TP:T].rearrange("p (b t) -> p b t", b=NB), ys,
                                     ps[:, bank + 1, H1:HT].rearrange("p (b t) -> p b t", b=NB), ALU.mult)

        def convolve(dve, y, ext, w):
            dve_chain(dve, dve.tensor_scalar(y[:, 0:YW], ext[:, 0:YW], w(0), None, ALU.mult))
            dve_chain(dve, dve.scalar_tensor_tensor(y[:, 0:YW], ext[:, 1:1 + YW], w(1), y[:, 0:YW], ALU.mult, ALU.add))
            return dve.scalar_tensor_tensor(y[:, 0:YW], ext[:, 2:2 + YW], w(2), y[:, 0:YW], ALU.mult, ALU.add)

        def keep_last(dve, new, f, ext):
            dve.tensor_copy(new[:, 0, :, bass.ds(f, 1)], ext[:, TP:TP + 2].rearrange("p (k o) -> p k o", o=1))
            dve.tensor_copy(new[:, 1:9, :, bass.ds(f, 1)].rearrange("p b k o -> p b (k o)"), sample_of(ext)[:, :, TS:TS + 2])

        def ffn_up(l, st, f0, hhi, hlo, ghi, glo, reg, norm_parts):
            ext = [reg.take("ext", [128, EW]) for _ in range(2)]
            y = [reg.take("y", [128, EW]) for _ in range(2)]
            gf = [reg.take("gf", [128, T]) for _ in range(2)]
            n, G, t0 = st["n"], st["base"], tiles_done[0]
            pairs = n // 2
            tg = gates_done[0]
            gates_done[0] += n
            tiles_done[0] += n
            zero_count[0] += 2
            zc = zero_count[0]
            with nc.Block() as block:
                @block.sync
                def _(sp):
                    with sp.Fori(0, pairs - 1) as i:
                        for q in (2, 3):
                            load_slab(sp, st, i, q, 2)
                    loads_after(sp, G + n)

                @block.gpsimd
                def _(pool):
                    if norm_parts:
                        norm_parts["pool"](pool)

                    def pair(i, nxt):
                        split_lo(pool, st, i, 1, 2)
                        split_lo(pool, *nxt)
                        for j in range(2):
                            pool.wait_ge(g_hi_ready, t0 + 2 * i + j + 1)
                            pool.tensor_tensor(glo[:, bass.ds(2 * i + j, 1), :], gf[j][:, :].rearrange("p (o t) -> p o t", o=1),
                                               ghi[:, bass.ds(2 * i + j, 1), :].bitcast(F32), ALU.subtract).then_inc(g_lo_ready, 1)
                    with pool.Fori(0, pairs - 1) as i:
                        pair(i, (st, i, 2, 2))
                    pair(pairs - 1, follow(G + n))

                @block.scalar
                def _(act):
                    if norm_parts:
                        norm_parts["act"](act)

                    def pair(i, nxt):
                        split_hi(act, st, i, 1, 2)
                        act.wait_ge(slab_done, G + 2 * i + 1)
                        for j in range(2):
                            act.wait_ge(conv_done, t0 + 2 * i + j - 1)
                            e = ext[j]
                            act.copy(e[:, 2:2 + HT], ps[:, 2 * j, 0:HT])
                            act.copy(e[:, 2 + HT:2 + TP], ps[:, 2 * j + 1, 0:H1])
                            act.copy(sample_of(e)[:, :, 0:2], ffnst[:, l, :, :, bass.ds(f0 + 2 * i + j, 1)].rearrange("p b k o -> p b (k o)"))
                            act.copy(sample_of(e)[:, :, 2:2 + TS],
                                     ps[:, 2 * j + 1, H1:HT].rearrange("p (b t) -> p b t", b=NB)).then_inc(ext_ready, 1)
                        act.wait_ge(ext_ready, tg + 2 * i + 2)
                        act.nop().then_inc(banks_free[0], 1)
                        split_hi(act, *nxt)
                        for j in range(2):
                            act.wait_ge(conv_done, t0 + 2 * i + j + 1)
                            act.activation(y[j][:, 0:YW], y[j][:, 0:YW], ACT.Silu).then_inc(gate_ready, 1)
                        for j in range(2):
                            act.wait_ge(g_f, t0 + 2 * i + j + 1)
                            act.copy(ghi[:, bass.ds(2 * i + j, 1), :], gf[j][:, :].rearrange("p (o t) -> p o t", o=1)).then_inc(g_hi_ready, 1)
                    act.wait_ge(zeroed, zc)
                    with act.Fori(0, pairs - 1) as i:
                        pair(i, (st, i, 2, 2))
                    pair(pairs - 1, follow(G + n))

                @block.tensor
                def _(pe):
                    if norm_parts:
                        norm_parts["pe"](pe)
                    for i in range(pairs):
                        for q in (0, 1):
                            products(pe, st, i, q, 2, 4 * q, 0, hhi, hlo, norm_parts["ready"] if norm_parts and i == q == 0 else None)

                @block.vector
                def _(dve):
                    if norm_parts:
                        norm_parts["dve"](dve)
                    for e in ext:
                        dve.memset(e[:, 0:2], 0.0).then_inc(zeroed, 1)
                    with dve.Fori(0, pairs) as i:
                        dve_chain.begin(i, 4, pairs)
                        for j in range(2):
                            dve.wait_ge(ext_ready, tg + 2 * i + j + 1)
                            f = f0 + 2 * i + j
                            keep_last(dve, newffn[:, l], f, ext[j])
                            convolve(dve, y[j], ext[j], lambda kk: ffnw[:, l, kk, bass.ds(f, 1)]).then_inc(conv_done, 1)
                        dve.wait_ge(slab_done, G + 2 * i + 2)
                        for j in range(2):
                            dve.wait_ge(gate_ready, tg + 2 * i + j + 1)
                            dve.wait_ge(g_lo_ready, t0 + 2 * i + j - 1)
                            last = gated_mult(dve, gf[j], y[j], 4 + 2 * j)
                            last.then_inc(g_f, 1)
                        dve.wait_ge(g_f, t0 + 2 * i + 2)
                        dve.nop().then_inc(banks_free[1], 1)
                        dve_chain.end()

        st_out_sem, st_t, st_ev = sem("state_out"), sem("state_t"), sem("state_ev")

        new_states = []
        def ffn(l, stages_l, gain):
            reg = Region(R)
            hhi, hlo = reg.take("h_hi", [128, KT, T], F32R), reg.take("h_lo", [128, KT, T], F32R)
            ghi, glo = reg.take("g_hi", [128, 12, T], F32R), reg.take("g_lo", [128, 12, T], F32R)
            for up, down, f0, nf in stages_l:
                r2 = Region(reg.at)
                scratch = r2.at + 4 * (4 * EW + 2 * T) + 192
                ffn_up(l, up, f0, hhi, hlo, ghi, glo, r2, norm(gain, hhi, hlo, scratch) if f0 == 0 else None)
                residual(down, ghi, glo, sum_squares=(f0 > 0 and l == 0))
            groups = [(flat(newffn[:, l, 0, :, :]), 44, [(0, 44, o["ffn_p"][0, l].rearrange("k (c p) -> (k c) p", p=128))])]
            for n in range(4):
                groups.append((flat(newffn[:, l, 1 + 2 * n:3 + 2 * n, :, :]), 88,
                               [(44 * h, 44 * h + 44, o["ffn_s"][2 * n + h, l].rearrange("k (c p) -> (k c) p", p=128)) for h in range(2)]))
            new_states.extend(groups)

        def conv_mixer():
            reg = Region(R)
            hhi, hlo = reg.take("h_hi", [128, KT, T], F32R), reg.take("h_lo", [128, KT, T], F32R)
            mhi, mlo = reg.take("m_hi", [128, KT, T], F32R), reg.take("m_lo", [128, KT, T], F32R)
            nrm = norm(V_MIX + 8, hhi, hlo, reg.at + 4 * (4 * T + 4 * EW) + 256)
            cg = [reg.take("cg", [128, T]) for _ in range(2)]
            ext = [reg.take("ext", [128, EW]) for _ in range(2)]
            y = [reg.take("y", [128, EW]) for _ in range(2)]
            gf = [reg.take("gf", [128, T]) for _ in range(2)]
            st, G, t0 = st_odd, st_odd["base"], tiles_done[0]
            tiles_done[0] += 8
            zero_count[0] += 2
            zc = zero_count[0]
            cg_ready, u_done = sem("cg_ready"), sem("u_done")
            def tile(i, h, j):
                return 4 * i + 2 * h + j
            with nc.Block() as block:
                @block.sync
                def _(sp):
                    for q in range(2, 6):
                        load_slab(sp, st, 0, q, 6)
                    for q in range(6):
                        load_slab(sp, st, 1, q, 6)
                    loads_after(sp, G + 12)

                @block.gpsimd
                def _(pool):
                    nrm["pool"](pool)

                    def trip(i, last):
                        for h in range(2):
                            for q in range(3):
                                qq = 3 * h + q + 1
                                split_lo(pool, *(last if qq == 6 else (st, i, qq, 6)))
                            for j in range(2):
                                tt = tile(i, h, j)
                                pool.wait_ge(g_hi_ready, t0 + tt + 1)
                                pool.tensor_tensor(mlo[:, tt, :], gf[j][:, :], mhi[:, tt, :].bitcast(F32),
                                                   ALU.subtract).then_inc(g_lo_ready, 1)
                    trip(0, (st, 1, 0, 6))
                    trip(1, follow(G + 12))

                @block.scalar
                def _(act):
                    nrm["act"](act)

                    def trip(i, last):
                        for h in range(2):
                            qb = 6 * i + 3 * h
                            bank = [4 * ((3 * h + q) % 2) for q in range(3)]
                            split_hi(act, st, i, 3 * h + 1, 6)
                            act.wait_ge(slab_done, G + qb + 1)
                            if t0 + tile(i, h, 0) > t0:
                                act.wait_ge(u_done, tile(i, h, 0))
                            for j in range(2):
                                act.copy(cg[j][:, :].rearrange("p (a t) -> p a t", a=2),
                                         ps[:, bank[0] + 2 * j:bank[0] + 2 * j + 2, 0:HT]).then_inc(cg_ready, 1)
                            act.wait_ge(cg_ready, tile(i, h, 0) + 2)
                            act.nop().then_inc(banks_free[(3 * h) % 2], 1)
                            split_hi(act, st, i, 3 * h + 2, 6)
                            split_hi(act, *(last if h == 1 else (st, i, 3, 6)))
                            for j in range(2):
                                tt = tile(i, h, j)
                                act.wait_ge(g_f, t0 + tt + 1)
                                act.copy(mhi[:, tt, :], gf[j][:, :]).then_inc(g_hi_ready, 1)
                    trip(0, (st, 1, 0, 6))
                    trip(1, follow(G + 12))

                @block.tensor
                def _(pe):
                    nrm["pe"](pe)
                    for i in range(2):
                        for q in range(6):
                            products(pe, st, i, q, 6, 4 * (q % 2), 0, hhi, hlo, nrm["ready"] if i == q == 0 else None)

                @block.vector
                def _(dve):
                    nrm["dve"](dve)
                    for e in ext:
                        dve.memset(e[:, 0:2], 0.0).then_inc(zeroed, 1)
                    dve.wait_ge(zeroed, zc)
                    for i in range(2):
                        for h in range(2):
                            b = [4 * ((3 * h + q) % 2) for q in range(3)]
                            dve.wait_ge(cg_ready, tile(i, h, 0) + 2)
                            dve.wait_ge(slab_done, G + 6 * i + 3 * h + 2)
                            for j in range(2):
                                f = tile(i, h, j)
                                e, bk = ext[j], b[1] + 2 * j
                                dve.tensor_tensor(e[:, 2:2 + HT], cg[j][:, 0:HT], ps[:, bk, 0:HT], ALU.mult)
                                dve.tensor_tensor(e[:, 2 + HT:2 + TP], cg[j][:, HT:TP], ps[:, bk + 1, 0:H1], ALU.mult)
                                dve.tensor_copy(sample_of(e)[:, :, 0:2], convst[:, :, :, f])
                                dve.tensor_tensor(sample_of(e)[:, :, 2:2 + TS], cg[j][:, TP:T].rearrange("p (b t) -> p b t", b=NB),
                                                  ps[:, bk + 1, H1:HT].rearrange("p (b t) -> p b t", b=NB), ALU.mult).then_inc(u_done, 1)
                            dve.wait_ge(u_done, tile(i, h, 0) + 2)
                            dve.nop().then_inc(banks_free[(3 * h + 1) % 2], 1)
                            for j in range(2):
                                f = tile(i, h, j)
                                keep_last(dve, newconv, f, ext[j])
                                convolve(dve, y[j], ext[j], lambda kk: vec[:, V_CONV + 8 * kk + f:V_CONV + 8 * kk + f + 1]).then_inc(conv_done, 1)
                            dve.wait_ge(conv_done, t0 + tile(i, h, 0) + 2)
                            dve.wait_ge(slab_done, G + 6 * i + 3 * h + 3)
                            for j in range(2):
                                f = tile(i, h, j)
                                dve.wait_ge(g_lo_ready, t0 + f - 1)
                                gated_mult(dve, gf[j], y[j], b[2] + 2 * j).then_inc(g_f, 1)
                            dve.wait_ge(g_f, t0 + tile(i, h, 0) + 2)
                            dve.nop().then_inc(banks_free[(3 * h + 2) % 2], 1)
            residual(st_oout, mhi, mlo)
            groups = [(flat(newconv[:, 0, :, :]), 16, [(0, 16, o["conv_p"][0, 0].rearrange("k (c p) -> (k c) p", p=128))]),
                      (flat(newconv[:, 1:9, :, :]), 128, [(0, 128, o["conv_s"][:, 0].rearrange("b k (c p) -> (b k c) p", p=128))])]
            new_states.extend(groups)

        def store_all():
            reg = Region(R)
            yt = reg.take("yt", [128, 5, D])
            bufs = [reg.take("rows", [128, 128]) for _ in new_states]
            yt_t, yt_ev, y_out = sem("yt_t"), sem("yt_ev"), sem("y_out")
            stores = [0]
            with nc.Block() as block:
                @block.tensor
                def _(pe):
                    for n, (src, r, _) in enumerate(new_states):
                        if n >= 4:
                            pe.wait_ge(st_ev, n - 3)
                        pe.transpose(ps[0:r, n % 4, 0:128], src, ident[:, :]).then_inc(st_t, 1)
                    for n in range(10):
                        t, c = n // 2, n % 2
                        w = 128 if t < 4 else NS
                        if n >= 4:
                            pe.wait_ge(yt_ev, n - 3)
                        for q in range(4):
                            last = pe.transpose(ps[0:w, 4 + n % 4, 128 * q:128 * q + 128],
                                                xT[:, 4 * c + q, 128 * t:128 * t + w], ident[:, :])
                        last.then_inc(yt_t, 1)

                @block.scalar
                def _(act):
                    for n, (src, r, _) in enumerate(new_states):
                        act.wait_ge(st_t, n + 1)
                        act.copy(bufs[n][0:r, :], ps[0:r, n % 4, 0:128]).then_inc(st_ev, 1)

                @block.vector
                def _(dve):
                    for n in range(10):
                        t, c = n // 2, n % 2
                        w = 128 if t < 4 else NS
                        dve.wait_ge(yt_t, n + 1)
                        dve.tensor_copy(yt[0:w, t, 512 * c:512 * c + 512], ps[0:w, 4 + n % 4, :]).then_inc(yt_ev, 1)

                @block.sync
                def _(sp):
                    def states(lo, hi):
                        for n in range(lo, min(hi, len(new_states))):
                            sp.wait_ge(st_ev, n + 1)
                            for a0, a1, dst in new_states[n][2]:
                                sp.dma_start(dst, bufs[n][a0:a1, :]).then_inc(st_out_sem, 16)
                                stores[0] += 16
                    states(0, 4)
                    for t in range(4):
                        sp.wait_ge(yt_ev, 2 * t + 2)
                        sp.dma_start(o["y_prompt"][0, 128 * t:128 * t + 128, :], yt[:, t, :]).then_inc(y_out, 16)
                        states(4 + 2 * t, 6 + 2 * t)
                    sp.wait_ge(yt_ev, 10)
                    sp.dma_start(o["y_sample"].rearrange("b t d -> (b t) d"), yt[0:NS, 4, :]).then_inc(y_out, 16)
                    states(12, len(new_states))
                    sp.wait_ge(y_out, 80)
                    sp.wait_ge(st_out_sem, stores[0])

        def even_mixer():
            reg = Region(R)
            hhi, hlo = reg.take("h_hi", [128, KT, TPAD], F32R), reg.take("h_lo", [128, KT, TPAD], F32R)
            MIX = reg.at
            mixf = reg.take("mixf", [128, KT, T])
            zq = reg.take("zq", [128, 5, W_NSA])
            E0 = reg.at
            pad_zero = sem("pad_zero")
            with nc.Block() as block:
                @block.vector
                def _(dve):
                    dve.memset(hhi[:, :, T:TPAD].bitcast(F32), 0.0).then_inc(pad_zero, 1)
                    dve.memset(hlo[:, :, T:TPAD].bitcast(F32), 0.0).then_inc(pad_zero, 1)

            def products_tok(pe, st, p, q, m, ready=None):
                g = st["base"] + p * m + q
                slot = (st["base"] + q) % 2
                wait_banks(pe, st, p, q, m)
                pe.wait_ge(w_lo_ready, g + 1)
                W = st["width"]
                for tok in range(5):
                    out = ps[:, 4 * (q % 2) + tok // 2, 256 * (tok % 2):256 * (tok % 2) + W]
                    for t in range(KT):
                        if ready is not None and tok == 0:
                            ready(pe, t)
                        for n, (w, x) in enumerate(((whi, hhi), (whi, hlo), (wlo, hhi))):
                            last = pe.matmul(out, x[:, t, 128 * tok:128 * tok + 128], w[slot][:, t * W:t * W + W],
                                             start=(t == 0 and n == 0), stop=(t == KT - 1 and n == 2))
                last.then_inc(slab_done, 1)

            def take_tok(dve, st, p, q, m, c0):
                g = st["base"] + p * m + q
                W, b = st["width"], 4 * (q % 2)
                dve.wait_ge(slab_done, g + 1)
                dve.tensor_copy(zq[:, 0:4, bass.ds(c0, W)].rearrange("p (b u) c -> p b u c", u=2),
                                ps[:, b:b + 2, :].rearrange("p b (u c) -> p b u c", u=2)[:, :, :, 0:W])
                dve.tensor_copy(zq[:, 4, bass.ds(c0, W)], ps[:, b + 2, 0:W]).then_inc(banks_free[q % 2], 1)

            r = Region(E0)
            kcT = r.take("kcT", [128, 288])
            vc = r.take("vc", [128, 3, 128])
            E1 = r.at
            seg = [r.take("seg", [128, 16, 128]) for _ in range(2)]
            segr = at("seg_by_group", [128, 2, 16, HD], F32, MIX)
            KTc = r.take("segT", [128, 2, 8, 290])
            rm = Region(MIX + 4 * 2 * 16 * HD)
            w1 = r.take("phi_w1", [128, 16, 128])
            w2 = r.take("phi_w2", [128, 2, HD])
            hid = rm.take("hid", [128, 2, 288])
            pe_rows = r.take("pe_rows", [16, 2, 128])
            peT = r.take("peT", [128, 2, 16])
            pe_bias = r.take("pe_bias", [128, 2])
            kcn = rm.take("kcn", [128, 3, 128])
            kcs = r.take("kcs", [128, 3, 2])
            gain_c = r.take("gain_c", [128, HD])
            pt = r.take("pt", [1, 32], I32)
            c_in, seg_in, seg_t, seg_ev, w1_in = sem("c_in"), [sem("seg_in0"), sem("seg_in1")], sem("seg_t"), sem("seg_ev"), sem("w1_in")
            hid_done, hid_ready, c_done, peb_ps, peb_ready, kc_ready, kc_t = (sem(x) for x in (
                "hid_done", "hid_ready", "c_done", "peb_ps", "peb_ready", "kc_ready", "kc_t"))
            n_pool = a["cache_cmp_kv"].shape[0]
            seg_a, seg_d, kc_copied = sem("seg_act"), sem("seg_dve"), sem("kc_copied")
            pt_in = sem("pt_in")
            kc_taken, vc_done, kc_sq, kc_ms = sem("kc_taken"), sem("vc_done"), sem("kc_sq"), sem("kc_ms")
            rows_of = (128, 128, 32)

            def load_pages(sp, n, lo, hi):
                kv, st = n // 3, n % 3
                for b in range(lo, hi):
                    page = sp.value_load(pt[0:1, 16 * st + b:16 * st + b + 1], min_val=0, max_val=n_pool - 1)
                    src = a["cache_cmp_kv"][bass.ds(page, 1), 0, :, kv].rearrange("o (m j) g d -> (o m) j (g d)", j=16)
                    sp.dma_start(seg[n % 2][8 * b:8 * b + 8, :, :], src).then_inc(seg_in[n % 2], 16)

            def regroup(copy, eng, n, g, done):
                rws, loads = rows_of[n % 3], (16, 16, 1, 16, 16, 1)
                eng.wait_ge(seg_in[n % 2], 16 * sum(loads[n % 2:n + 1:2]))
                if n >= 1:
                    eng.wait_ge(seg_t, 4 * n)
                copy(segr[0:rws, g, :, :], seg[n % 2][0:rws, :, 64 * g:64 * g + 64]).then_inc(done, 1)

            def load_w1(sp, kv):
                sp.dma_start(w1[:, :, :], a["phi_w1"][0, kv].rearrange("(i j) d e -> (j d) i e", j=2)).then_inc(w1_in, 16)

            raw_out = sem("raw_out")
            nrm = norm(V_MIX, hhi, hlo, MIX, summed=False)
            with nc.Block() as block:
                @block.sync
                def _(sp):
                    sp.dma_start(pt[:, :], a["page_table"].rearrange("(o b) n -> o (b n)", o=1)).then_inc(pt_in, 16)
                    for q in range(2, 5):
                        load_slab(sp, st_nsa, 0, q, 2)
                        sp.wait_ge(pt_in, 16)
                        load_pages(sp, (q - 2) // 2, 8 * ((q - 2) % 2), 8 * ((q - 2) % 2) + 8)
                    load_slab(sp, st_gate, 0, 0, 2)
                    load_pages(sp, 1, 8, 16)
                    for kv in range(2):
                        sp.dma_start(w2[:, kv, :], a["phi_w2"][0, kv]).then_inc(c_in, 16)
                        sp.dma_start(pe_rows[:, kv, :], a["phi_pe"][0, kv].rearrange("(i j) d -> i (j d)", j=2)).then_inc(c_in, 16)
                    sp.dma_start(gain_c[:, :], bass.AP(a["k_norm"].tensor, a["k_norm"].offset, [[0, 128], [1, HD]])).then_inc(c_in, 16)
                    load_w1(sp, 0)
                    loads_after(sp, 6)

                @block.scalar
                def _(act):
                    nrm["act"](act)
                    for g in range(1, 7):
                        split_hi(act, *follow(g))

                @block.gpsimd
                def _(pool):
                    nrm["pool"](pool)
                    for g in range(1, 7):
                        split_lo(pool, *follow(g))

                @block.tensor
                def _(pe):
                    nrm["pe"](pe)
                    for i in range(2):
                        for q in range(2):
                            products_tok(pe, st_nsa, i, q, 2, nrm["ready"] if i == q == 0 else None)
                    products_tok(pe, st_nsa, 2, 0, 2)
                    products_tok(pe, st_gate, 0, 0, 2)

                @block.vector
                def _(dve):
                    nrm["dve"](dve)
                    with dve.Fori(0, 2) as i:
                        for q in range(2):
                            take_tok(dve, st_nsa, i, q, 2, 512 * i + 256 * q)
                    take_tok(dve, st_nsa, 2, 0, 2, 1024)
                    take_tok(dve, st_gate, 0, 0, 2, 1280)

            def kv_out(sp, c0, dst_p, dst_s, s):
                sp.dma_start(dst_p.rearrange("(t p) k g d -> p t (k g d)", p=128), zq[:, 0:4, c0:c0 + 256]).then_inc(s, 16)
                for b in range(NB):
                    sp.dma_start(dst_s[b], zq[TS * b:TS * b + TS, 4, c0:c0 + 256]).then_inc(s, 16)

            with nc.Block() as block:
                @block.sync
                def _(sp):
                    kv_out(sp, 512, o["cmp_p"][0, 0], o["cmp_s"][:, 0].rearrange("b t k g d -> b t (k g d)"), raw_out)
                    for n in range(2, 6):
                        if n == 5:
                            sp.wait_ge(hid_done, 2)
                            load_w1(sp, 1)
                        sp.wait_ge(seg_a, n - 1)
                        sp.wait_ge(seg_d, n - 1)
                        if n % 3 == 2:
                            sp.wait_ge(raw_out, 16 * 9)
                            src = o["cmp_p"][0, 0, :, n // 3].rearrange("(m j) g d -> m j (g d)", j=16)
                            sp.dma_start(seg[n % 2][0:32, :, :], src).then_inc(seg_in[n % 2], 16)
                        else:
                            load_pages(sp, n, 0, 16)

                @block.tensor
                def _(pe):
                    pe.wait_ge(c_in, 80)
                    for kv in range(2):
                        pe.transpose(ps[:, 7, 16 * kv:16 * kv + 16], pe_rows[:, kv, :], ident[0:16, 0:16]).then_inc(peb_ps, 1)
                    for kv in range(2):
                        pe.wait_ge(w1_in, 16 * (kv + 1))
                        pe.wait_ge(peb_ready, 1)
                        if kv == 1:
                            pe.wait_ge(kc_copied, 1)
                        for i in range(16):
                            last = pe.matmul(ps[:, 7, 64 + kv:65 + kv], w1[:, i, :], peT[:, kv, i:i + 1], start=(i == 0), stop=(i == 15))
                        last.then_inc(peb_ps, 1)
                        for st in range(3):
                            n, rws = 3 * kv + st, rows_of[st]
                            pe.wait_ge(seg_a, n + 1)
                            pe.wait_ge(seg_d, n + 1)
                            for u in range(4):
                                e = 4 * n + u
                                if e >= 4:
                                    pe.wait_ge(seg_ev, e - 3)
                                gg, j0 = u // 2, 4 * (u % 2)
                                for jj in range(4):
                                    src = segr[0:rws, gg, 2 * (j0 + jj):2 * (j0 + jj) + 2, :].rearrange("p j d -> p (j d)")
                                    last = pe.transpose(ps[:, e % 4, 128 * jj:128 * jj + rws], src, ident[0:rws, 0:rws])
                                last.then_inc(seg_t, 1)
                        pe.wait_ge(seg_ev, 12 * (kv + 1))
                        for gg in range(2):
                            if kv == 1:
                                pe.wait_ge(hid_ready, gg + 1)
                            for i in range(16):
                                last = pe.matmul(ps[:, 4 + gg, 0:288], w1[:, i, :], KTc[:, gg, i % 8, i // 8:i // 8 + 288],
                                                 start=(i == 0), stop=(i == 15))
                            last.then_inc(hid_done, 1)
                        pe.wait_ge(hid_ready, 2 * (kv + 1))
                        if kv == 1:
                            pe.wait_ge(kc_taken, 1)
                        for nt in range(3):
                            for gg in range(2):
                                rws = rows_of[nt]
                                last = pe.matmul(ps[0:rws, 6, 128 * nt + 64 * gg:128 * nt + 64 * gg + 64],
                                                 hid[:, gg, 128 * nt:128 * nt + rws], w2[:, kv, :], start=True, stop=True)
                        last.then_inc(c_done, 1)
                        if kv == 0:
                            pe.wait_ge(kc_ready, 2)
                            for nt in range(3):
                                rws = rows_of[nt]
                                last = pe.transpose(ps[:, 7, 128 + 128 * nt:128 + 128 * nt + rws], kcn[0:rws, nt, :], ident[0:rws, 0:rws])
                            last.then_inc(kc_t, 1)

                @block.scalar
                def _(act):
                    act.wait_ge(peb_ps, 2)
                    act.copy(peT[:, :, :], ps[:, 7, 0:32].rearrange("p (a b) -> p a b", a=2)).then_inc(peb_ready, 1)
                    for kv in range(2):
                        for st in range(3):
                            regroup(act.copy, act, 3 * kv + st, 0, seg_a)
                        act.wait_ge(peb_ps, 3 + kv)
                        act.copy(pe_bias[:, kv:kv + 1], ps[:, 7, 64 + kv:65 + kv]).then_inc(act_chain.sem, 1)
                        act_chain.n += 1
                        act.wait_ge(act_chain.sem, act_chain.n)
                        for gg in range(2):
                            act.wait_ge(hid_done, 2 * kv + gg + 1)
                            if kv == 1:
                                act.wait_ge(c_done, 1)
                            act.activation(hid[:, gg, :], ps[:, 4 + gg, 0:288], ACT.Gelu_apprx_tanh, bias=pe_bias[:, kv:kv + 1]).then_inc(hid_ready, 1)
                        if kv == 0:
                            act.wait_ge(c_done, 1)
                            act.activation(kcn[:, 0:2, :], ps[:, 6, 0:256].rearrange("p (a b) -> p a b", a=2), ACT.Square)
                            act.activation(kcn[0:32, 2, :], ps[0:32, 6, 256:384], ACT.Square).then_inc(kc_sq, 1)
                            act.wait_ge(kc_ms, 1)
                            act.activation(kcs[:, 0:2, :], kcs[:, 0:2, :], ACT.Sqrt)
                            act.activation(kcs[0:32, 2, :], kcs[0:32, 2, :], ACT.Sqrt).then_inc(kc_sq, 1)

                @block.vector
                def _(dve):
                    dve.memset(KTc[:, :, :, 288:290], 0.0)
                    for kv in range(2):
                        for st in range(3):
                            rws = rows_of[st]
                            regroup(dve.tensor_copy, dve, 3 * kv + st, 1, seg_d)
                            for u in range(4):
                                e = 12 * kv + 4 * st + u
                                dve.wait_ge(seg_t, e + 1)
                                if kv == 1 and st == 0 and u == 0:
                                    dve.wait_ge(hid_done, 2)
                                gg, j0 = u // 2, 4 * (u % 2)
                                dve.tensor_copy(KTc[:, gg, j0:j0 + 4, 128 * st:128 * st + rws],
                                                ps[:, e % 4, :].rearrange("p (j n) -> p j n", j=4)[:, :, 0:rws]).then_inc(seg_ev, 1)
                        dve.wait_ge(c_done, kv + 1)
                        if kv == 0:
                            dve.wait_ge(kc_sq, 1)
                            dve.tensor_reduce(kcs[:, 0:2, :], kcn[:, 0:2, :].rearrange("p n (g d) -> p n g d", g=2), AX.X, ALU.add)
                            dve_chain(dve, dve.tensor_reduce(kcs[0:32, 2, :], kcn[0:32, 2, :].rearrange("p (g d) -> p g d", g=2), AX.X, ALU.add))
                            dve.tensor_scalar(kcs[:, 0:2, :], kcs[:, 0:2, :], 1.0 / HD, EPS, ALU.mult, ALU.add)
                            dve.tensor_scalar(kcs[0:32, 2, :], kcs[0:32, 2, :], 1.0 / HD, EPS, ALU.mult, ALU.add).then_inc(kc_ms, 1)
                            dve.wait_ge(kc_sq, 2)
                            dve.reciprocal(kcs[:, 0:2, :], kcs[:, 0:2, :])
                            dve_chain(dve, dve.reciprocal(kcs[0:32, 2, :], kcs[0:32, 2, :]))
                            def scaled(rr, lo, hi):
                                nn = hi - lo
                                out = kcn[0:rr, lo:hi, :].rearrange("p n (g d) -> p (n g) d", g=2)
                                src = ps[0:rr, 6, 128 * lo:128 * hi].rearrange("p (n d) -> p n d", d=HD)
                                fac = kcs[0:rr, lo:hi, :].rearrange("p n (g o) -> p (n g) o", o=1).to_broadcast([rr, 2 * nn, HD])
                                dve_chain(dve, dve.tensor_tensor(out, src, fac, ALU.mult))
                                gn = gain_c[0:rr, :].rearrange("p (o d) -> p o d", o=1).to_broadcast([rr, 2 * nn, HD])
                                return dve.tensor_tensor(out, out, gn, ALU.mult)
                            scaled(128, 0, 2).then_inc(kc_ready, 1)
                            scaled(32, 2, 3).then_inc(kc_ready, 1)
                            dve.wait_ge(kc_ready, 2)
                            dve.nop().then_inc(kc_taken, 1)
                            dve.wait_ge(kc_t, 1)
                            dve.tensor_copy(kcT[:, :], ps[:, 7, 128:128 + 288]).then_inc(kc_copied, 1)
                        else:
                            dve.tensor_copy(vc[:, 0:2, :], ps[:, 6, 0:256].rearrange("p (a b) -> p a b", a=2))
                            dve.tensor_copy(vc[0:32, 2, :], ps[0:32, 6, 256:384]).then_inc(vc_done, 1)

            r = Region(E1)
            gs = r.take("gate_s", [128, 4, 3])
            gp = r.take("gate_p", [128, 5, 24])
            gpr = r.take("gate_prompt_rev", [128, 4, 24])
            flip = r.take("flip", [128, 128])
            qbd = r.take("qbd", [128, NB, 64])
            kNew = [r.take("k_new", [128, NS]) for _ in range(2)]
            EQ = r.at
            assert st_gate["base"] % 2 == 1
            w_hi_at = nc.sbuf_base + (-nc.sbuf_base) % 64 + 3 * 4 * SLAB
            w_lo_at = w_hi_at + 2 * 4 * SLAB
            q_st = [r.take("q_st", [128, 4, TP], F32R), at("q_st", [128, 4, TP], F32R, w_hi_at)]
            k_mv = [[[at("k_mv", [128, TP], F32R, place + 4 * TP * (2 * part + g)) for g in range(2)] for part in range(2)]
                    for place in (w_lo_at, MIX + 4 * 4 * T)]
            kc_mv = [[r.take("kc_mv", [128, 32], F32R) for g in range(2)] for part in range(2)]
            E2 = r.at
            sqs = r.take("sqs", [128, 5, 12, HD])
            qn = sqs[:, :, 0:8, :].rearrange("p t (h g) d -> p t h g d", g=2)
            rs = r.take("rs", [128, 5, 12])
            gains = r.take("gains", [128, 3, HD])
            n_in, n_sq, n_ms, n_std, n_done, g_sig, q_t, q_ev = (sem(x) for x in ("n_in", "n_sq", "n_ms", "n_std", "n_done", "g_sig", "q_t", "q_ev"))
            gpr_ps = sem("gpr_ps")
            gate_out, gate_in, slc_out, rel_in = sem("gate_out"), sem("gate_in"), sem("slc_out"), sem("rel_in")
            onehot = r.take("onehot", [NBK, RVL])
            masked = r.take("masked", [NH, RVL])
            relb = r.take("rel_bias", [NBK, NH])
            rv = r.take("rv_sb", [NH, RVL])
            rv_ps, rv_sb, rv_out = sem("rv_ps"), sem("rv_ready"), sem("rv_out")
            RC = RVL // 4
            heads = ((0, 8, 0, 0), (768, 2, 8, 1), (1024, 2, 10, 2))
            with nc.Block() as block:
                @block.sync
                def _(sp):
                    def bcast(dst, src, off, n):
                        sp.dma_start(dst, bass.AP(src.tensor, off, [[0, 128], [1, n]])).then_inc(n_in, 16)
                    bcast(gains[:, 0, :], a["q_norm"], 0, HD)
                    bcast(gains[:, 1, :], a["k_norm"], HD, HD)
                    bcast(gains[:, 2, :], a["k_norm"], 2 * HD, HD)
                    sp.dma_start(flip[:, :], k["flip"]).then_inc(n_in, 16)
                    sp.dma_start(onehot[:, :], k["onehot"]).then_inc(rel_in, 16)
                    sp.dma_start(masked[:, :], k["masked"]).then_inc(rel_in, 16)
                    sp.dma_start(relb[:, :], a["rel_bias"]).then_inc(rel_in, 16)
                    sp.wait_ge(rv_sb, 4)
                    sp.dma_start(rv_dram, rv[:, :]).then_inc(rv_out, 16)
                    sp.wait_ge(g_sig, 1)
                    sp.dma_start(gate_dram, gp[0:NS, 4, :]).then_inc(gate_out, 16)
                    sp.wait_ge(gate_out, 16)
                    for grp in range(4):
                        for s2 in range(2):
                            src = bass.AP(gate_dram.tensor, (2 * grp + s2) * TS * 24, [[3, NH], [24, TS], [1, 3]])
                            sp.dma_start(gs[64 * s2:64 * s2 + 64, grp, :], src).then_inc(gate_in, 16)
                    sp.wait_ge(raw_out, 16 * 9)
                    sp.wait_ge(gate_in, 128)
                    sp.wait_ge(rv_out, 16)

                @block.scalar
                def _(act):
                    for c0, nh, s0, _ in heads:
                        act.activation(sqs[:, :, s0:s0 + nh, :], zq[:, :, c0:c0 + 64 * nh].rearrange("p t (h d) -> p t h d", d=HD), ACT.Square).then_inc(n_sq, 1)
                    act.activation(gp[:, :, :], zq[:, :, 1280:1304], ACT.Sigmoid).then_inc(g_sig, 1)
                    act.wait_ge(n_ms, 1)
                    act.activation(rs[:, :, :], rs[:, :, :], ACT.Sqrt).then_inc(n_std, 1)
                    for n in range(4):
                        act.wait_ge(q_t, n + 1)
                        for g in range(2):
                            last = act.copy(q_st[g][0:64, n, :], ps[64 * g:64 * g + 64, n, :])
                        last.then_inc(q_ev, 1)
                    for n in range(2):
                        act.wait_ge(q_t, 6 + n)
                        for g in range(2):
                            for half in range(2):
                                last = act.copy(k_mv[n][0][g][64 * half:64 * half + 64, :], ps[64 * g:64 * g + 64, 5 + n, :])
                        last.then_inc(q_ev, 1)

                @block.vector
                def _(dve):
                    dve.memset(qbd[:, :, :], 0.0)
                    dve.wait_ge(n_sq, 3)
                    dve_chain(dve, dve.tensor_reduce(rs[:, :, :], sqs[:, :, :, :], AX.X, ALU.add))
                    dve.tensor_scalar(rs[:, :, :], rs[:, :, :], 1.0 / HD, EPS, ALU.mult, ALU.add).then_inc(n_ms, 1)
                    dve.wait_ge(n_std, 1)
                    dve_chain(dve, dve.reciprocal(rs[:, :, :], rs[:, :, :]))
                    dve_chain(dve, dve.tensor_scalar(rs[:, :, 0:8], rs[:, :, 0:8], HD ** -0.5, None, ALU.mult))
                    dve.wait_ge(n_in, 64)
                    for c0, nh, s0, gi in heads:
                        z = zq[:, :, c0:c0 + 64 * nh].rearrange("p t (h d) -> p t h d", d=HD)
                        dve_chain(dve, dve.tensor_tensor(z, z, rs[:, :, s0:s0 + nh].rearrange("p t (h o) -> p t h o", o=1).to_broadcast([128, 5, nh, HD]), ALU.mult))
                        gb = gains[:, gi, :].rearrange("p (a b d) -> p a b d", a=1, b=1).to_broadcast([128, 5, nh, HD])
                        if gi == 0:
                            for g in range(2):
                                last = dve.tensor_tensor(qn[:, :, :, g, :], z[:, :, 4 * g:4 * g + 4, :], gb[:, :, 0:4, :], ALU.mult)
                            last.then_inc(n_done, 1)
                        else:
                            dve.tensor_tensor(z, z, gb, ALU.mult).then_inc(n_done, 1)
                    dve.wait_ge(rel_in, 48)
                    for n in range(4):
                        dve.wait_ge(rv_ps, n + 1)
                        dve.tensor_tensor(rv[:, RC * n:RC * n + RC], ps[0:NH, 7, 0:RC], masked[:, RC * n:RC * n + RC], ALU.add).then_inc(rv_sb, 1)
                    dve.wait_ge(gpr_ps, 1)
                    dve.tensor_copy(flat(gpr[:, :, :]), ps[:, 7, 0:96])
                    dve.wait_ge(q_t, 5)
                    for g in range(2):
                        dve.tensor_copy(qbd[64 * g:64 * g + 64, :, 32 * g:32 * g + 32].rearrange("p s (h t) -> p s h t", h=4),
                                        ps[64 * g:64 * g + 64, 4, 0:256].rearrange("p (h s t) -> p s h t", h=4, s=NB))
                    for n in range(4):
                        dve.wait_ge(q_ev, n + 1)
                        for g in range(2):
                            dve.tensor_tensor(q_st[g][64:128, n, :], ps[64 * g:64 * g + 64, n, :], q_st[g][0:64, n, :].bitcast(F32), ALU.subtract)
                    for g in range(2):
                        src = kcT[64 * g:64 * g + 64, 256:288]
                        dve.tensor_copy(kc_mv[0][g][0:64, :], src)
                        dve_chain(dve, dve.tensor_copy(kc_mv[0][g][64:128, :], src))
                        for half in range(2):
                            dve.tensor_tensor(kc_mv[1][g][64 * half:64 * half + 64, :], src, kc_mv[0][g][64 * g:64 * g + 64, :].bitcast(F32), ALU.subtract)
                    for n in range(2):
                        dve.tensor_copy(kNew[n][:, :], ps[:, 4, 256 + 64 * n:320 + 64 * n])
                        dve.wait_ge(q_ev, 5 + n)
                        for g in range(2):
                            for half in range(2):
                                rows = slice(64 * half, 64 * half + 64)
                                dve.tensor_tensor(k_mv[n][1][g][rows, :], ps[64 * g:64 * g + 64, 5 + n, :], k_mv[n][0][g][rows, :].bitcast(F32), ALU.subtract)

                @block.tensor
                def _(pe):
                    pe.wait_ge(rel_in, 48)
                    for n in range(4):
                        if n >= 1:
                            pe.wait_ge(rv_sb, n)
                        pe.matmul(ps[0:NH, 7, 0:RC], relb[:, :], onehot[:, RC * n:RC * n + RC], start=True, stop=True).then_inc(rv_ps, 1)
                    pe.wait_ge(g_sig, 1)
                    pe.wait_ge(n_in, 64)
                    pe.wait_ge(rv_sb, 4)
                    pe.matmul(ps[:, 7, 0:96], flip[:, :], gp[:, 0:4, :].rearrange("p t n -> p (t n)"), start=True, stop=True).then_inc(gpr_ps, 1)
                    pe.wait_ge(n_done, 3)

                    def q_of(tok, hh, rws):
                        return qn[0:rws, tok, hh].rearrange("p g d -> p (g d)")
                    for hh in range(4):
                        for tok in range(4):
                            last = pe.matmul(ps[:, hh, 128 * tok:128 * tok + 128], q_of(tok, hh, 128), flip[:, :], start=True, stop=True)
                        last.then_inc(q_t, 1)
                    for hh in range(4):
                        last = pe.transpose(ps[:, 4, 64 * hh:64 * hh + 64], q_of(4, hh, NS), ident[0:NS, 0:NS])
                    for n, c0 in enumerate((768, 1024)):
                        last = pe.transpose(ps[:, 4, 256 + 64 * n:320 + 64 * n], zq[0:NS, 4, c0:c0 + 128], ident[0:NS, 0:NS])
                    last.then_inc(q_t, 1)
                    for n, c0 in enumerate((768, 1024)):
                        for tok in range(4):
                            last = pe.transpose(ps[:, 5 + n, 128 * tok:128 * tok + 128], zq[:, tok, c0:c0 + 128], ident[:, :])
                        last.then_inc(q_t, 1)

            r = Region(E2)
            onat = r.take("onat", [128, 4, 512])
            BT = [r.take("BT", [128, BTW]) for _ in range(2)]
            sS = [r.take("s_slc", [128, TP]) for _ in range(2)]
            sW = [r.take("s_win", [128, TP]) for _ in range(2)]
            sC = [r.take("s_cmp", [128, 32]) for _ in range(2)]
            PTs = r.take("PTs", [128, 4, 128])
            PTw = r.take("PTw", [128, 4, 128])
            PTc = r.take("PTc", [32, 128])
            mx = r.take("mx", [128, 2, 3])
            den = r.take("den", [128, 2, 3])
            bt_in, s_ready, s_taken, p_ready, pt_ready, pt_act, pt_dve, o_ready, o_taken, m_ready = (sem(x) for x in (
                "bt_in", "s_ready", "s_taken", "p_ready", "pt_ready", "pt_act", "pt_dve", "o_ready", "o_taken", "m_ready"))
            on_t, on_ev = sem("on_t"), sem("on_ev")
            U = 4 * NH
            with nc.Block() as block:
                @block.sync
                def _(sp):
                    for h in range(NH):
                        if h >= 2:
                            sp.wait_ge(s_taken, 4 * (h - 1))
                        src = bass.AP(rv_dram.tensor, h * RVL, [[1, 128], [1, BTW]])
                        sp.dma_start(BT[h % 2][:, :], src).then_inc(bt_in, 16)
                        sp.wait_ge(bt_in, 16 * (h + 1))
                        if h == 1:
                            kv_out(sp, 768, o["slc_p"][0, 0], o["slc_s"][:, 0].rearrange("b t k g d -> b t (k g d)"), slc_out)
                            kv_out(sp, 1024, o["win_p"][0, 0], o["win_s"][:, 0, 504:512].rearrange("b t k g d -> b t (k g d)"), slc_out)
                            for b in range(NB):
                                sp.dma_start(o["win_s"][b, 0, 0:504].rearrange("t k g d -> t (k g d)"),
                                             a["cache_win_kv"][b, 0, 8:512].rearrange("t k g d -> t (k g d)")).then_inc(slc_out, 16)
                    sp.wait_ge(slc_out, 16 * 26)

                @block.tensor
                def _(pe):
                    def scores(u):
                        h, qt, s = u // 4, u % 4, u % 2
                        g, hh = h // 4, h % 4
                        if u >= 1:
                            pe.wait_ge(s_taken, u)
                        q = q_st[g][:, hh, 128 * qt:128 * qt + 128]
                        nk = 128 * (qt + 1)
                        for out, keys in ((ps[:, s, 0:nk], [k_mv[0][part][g][:, 0:nk] for part in range(2)]),
                                          (ps[:, 2 + s, 0:nk], [k_mv[1][part][g][:, 0:nk] for part in range(2)]),
                                          (ps[:, 4, 0:32], [kc_mv[part][g][:, :] for part in range(2)])):
                            pe.matmul(out, q, keys[0], start=True, stop=False)
                            last = pe.matmul(out, q, keys[1], start=False, stop=True)
                        last.then_inc(s_ready, 1)
                    scores(0)
                    scores(1)
                    for u in range(U):
                        h, qt, s = u // 4, u % 4, u % 2
                        g = h // 4
                        pe.wait_ge(p_ready, u + 1)
                        if u >= 1:
                            pe.wait_ge(pt_act, u)
                            pe.wait_ge(pt_dve, u)
                        for kt in range(qt + 1):
                            pe.transpose(ps[:, 5, 128 * kt:128 * kt + 128], sS[s][:, 128 * kt:128 * kt + 128], ident[:, :])
                            pe.transpose(ps[:, 6, 128 * kt:128 * kt + 128], sW[s][:, 128 * kt:128 * kt + 128], ident[:, :])
                        if u >= 1:
                            pe.wait_ge(o_taken, u)
                        pe.transpose(ps[0:32, 7, 256:384], sC[s][:, :], ident[:, :]).then_inc(pt_ready, 1)
                        if u + 2 < U:
                            scores(u + 2)
                        pe.wait_ge(pt_act, u + 1)
                        pe.wait_ge(pt_dve, u + 1)
                        O = ps[:, 7, 0:192]
                        pe.matmul(O[:, 0:64], PTc[:, :], vc[0:32, 2, 64 * g:64 * g + 64], start=True, stop=True)
                        for n, (PT, c0) in enumerate(((PTs, 896), (PTw, 1152))):
                            for kt in range(qt + 1):
                                last = pe.matmul(O[:, 64 * (n + 1):64 * (n + 2)], PT[:, kt, :], zq[:, kt, c0 + 64 * g:c0 + 64 * g + 64],
                                                 start=(kt == 0), stop=(kt == qt))
                        last.then_inc(o_ready, 1)
                    for qt in range(4):
                        pe.wait_ge(o_taken, U)
                        for c in range(4):
                            last = pe.matmul(ps[:, qt, 128 * c:128 * c + 128], onat[:, qt, 128 * c:128 * c + 128], flip[:, :], start=True, stop=True)
                        last.then_inc(on_t, 1)

                @block.vector
                def _(dve):
                    def masked_max(u):
                        h, qt, s = u // 4, u % 4, u % 2
                        nk = 128 * (qt + 1)
                        dve.wait_ge(s_ready, u + 1)
                        dve.wait_ge(bt_in, 16 * (h + 1))
                        if u >= 2:
                            dve.wait_ge(pt_ready, u - 1)
                        y0 = 511 - 128 * qt
                        B = BT[h % 2]
                        dve.tensor_tensor_reduce(sC[s][:, :], ps[:, 4, 0:32], B[:, y0 + 31:y0 + 31 + 16 * 31 + 1:16], 1.0, FLOOR,
                                                 ALU.add, ALU.max, mx[:, s, 0:1])
                        dve.tensor_tensor_reduce(sS[s][:, 0:nk], ps[:, s, 0:nk], B[:, y0:y0 + nk], 1.0, FLOOR, ALU.add, ALU.max, mx[:, s, 1:2])
                        dve.tensor_tensor_reduce(sW[s][:, 0:nk], ps[:, 2 + s, 0:nk], B[:, y0:y0 + nk], 1.0, FLOOR, ALU.add, ALU.max,
                                                 mx[:, s, 2:3]).then_inc(s_taken, 1)
                        dve.wait_ge(s_taken, u + 1)
                        dve.tensor_scalar(mx[:, s, :], mx[:, s, :], -1.0, None, ALU.mult).then_inc(m_ready, 1)
                    masked_max(0)
                    masked_max(1)
                    for u in range(U):
                        h, qt, s = u // 4, u % 4, u % 2
                        dve.wait_ge(pt_ready, u + 1)
                        if u >= 1:
                            dve.wait_ge(o_ready, u)
                        dve.tensor_copy(PTw[:, 0:qt + 1, :], ps[:, 6, 0:128 * (qt + 1)].rearrange("p (a b) -> p a b", b=128)).then_inc(pt_dve, 1)
                        dve.wait_ge(p_ready, u + 1)
                        dve_chain(dve, dve.tensor_scalar(den[:, s, :], den[:, s, :], 1e-30, None, ALU.max))
                        dve_chain(dve, dve.reciprocal(den[:, s, :], den[:, s, :]))
                        dve_chain(dve, dve.tensor_tensor(den[:, s, :], den[:, s, :], gpr[:, qt, 3 * h:3 * h + 3], ALU.mult))
                        if u + 2 < U:
                            masked_max(u + 2)
                        dve.wait_ge(o_ready, u + 1)
                        O, out = ps[:, 7, 0:192], onat[:, qt, 64 * h:64 * h + 64]
                        dve_chain(dve, dve.tensor_scalar(out, O[:, 0:64], den[:, s, 0:1], None, ALU.mult))
                        dve_chain(dve, dve.scalar_tensor_tensor(out, O[:, 64:128], den[:, s, 1:2], out, ALU.mult, ALU.add))
                        dve.scalar_tensor_tensor(out, O[:, 128:192], den[:, s, 2:3], out, ALU.mult, ALU.add).then_inc(o_taken, 1)

                @block.scalar
                def _(act):
                    def exps(u):
                        qt, s = u % 4, u % 2
                        nk = 128 * (qt + 1)
                        act.wait_ge(m_ready, u + 1)
                        if u >= 2:
                            act.wait_ge(o_taken, u - 1)
                        act.activation(sC[s][:, :], sC[s][:, :], ACT.Exp, bias=mx[:, s, 0:1], accum_out=den[:, s, 0:1])
                        act.activation(sS[s][:, 0:nk], sS[s][:, 0:nk], ACT.Exp, bias=mx[:, s, 1:2], accum_out=den[:, s, 1:2])
                        act.activation(sW[s][:, 0:nk], sW[s][:, 0:nk], ACT.Exp, bias=mx[:, s, 2:3], accum_out=den[:, s, 2:3]).then_inc(p_ready, 1)
                    exps(0)
                    for u in range(U):
                        qt = u % 4
                        act.wait_ge(pt_ready, u + 1)
                        if u >= 1:
                            act.wait_ge(o_ready, u)
                        act.copy(PTc[:, :], ps[0:32, 7, 256:384])
                        act.copy(PTs[:, 0:qt + 1, :], ps[:, 5, 0:128 * (qt + 1)].rearrange("p (a b) -> p a b", b=128)).then_inc(pt_act, 1)
                        if u + 1 < U:
                            exps(u + 1)
                    for qt in range(4):
                        act.wait_ge(on_t, qt + 1)
                        act.copy(mixf[:, 0:4, 128 * qt:128 * qt + 128], ps[:, qt, :].rearrange("p (c t) -> p c t", c=4)).then_inc(on_ev, 1)

            r = Region(EQ)
            assert st_gate["base"] % 2 == 1
            w_at = nc.sbuf_base + (-nc.sbuf_base) % 64 + 4 * 4 * SLAB - 4 * SLAB
            KV = [[[r.take("kv_rows", [128, 4, 256]) for _ in range(2)] for _ in range(2)],
                  [[at("kv_rows", [128, 4, 256], F32, w_at + 4096 * n + 2 * 4 * SLAB * br) for n in range(2)] for br in range(2)]]
            SBs = r.take("bias_past", [128, TP])
            SBw = r.take("bias_win", [128, TP])
            SBn = r.take("bias_new", [128, 4, NS])
            SBc = r.take("bias_cmp", [128, 2, 128])
            wm = r.take("wmask", [128, TS])
            S2 = [r.take("s_past", [128, TP + NS]) for _ in range(2)]
            Sc = r.take("s_cmps", [128, 128])
            kT = [r.take("kT", [128, TP]) for _ in range(2)]
            PT2 = [r.take("PT2", [128, 4, 128]) for _ in range(2)]
            PTn = r.take("PTn", [64, 2, 128])
            PTcs = r.take("PTcs", [128, 128])
            mx2 = r.take("mx2", [128, 3])
            den2 = r.take("den2", [128, 3])
            acc = r.take("acc", [128, HD])
            tab_zero, tab_in = sem("tab_zero"), sem("tab_in")
            kvp_in = [[sem(f"kvp_in{g}{s2}") for s2 in range(2)] for g in range(2)]
            kvw_in = [[sem(f"kvw_in{g}{s2}") for s2 in range(2)] for g in range(2)]
            kS_done = sem("kS_done")
            kT_ps, kT_sb, ss_taken, sm_ready, sp_ready = (sem(x) for x in ("kT_ps", "kT_sb", "ss_taken", "sm_ready", "sp_ready"))
            spt_ready, spt_a, spt_d, so_ready, so_acc, so_t, so_ev = (sem(x) for x in (
                "spt_ready", "spt_act", "spt_dve", "so_ready", "so_acc", "so_t", "so_ev"))
            pt2 = r.take("pt2", [1, 32], I32)

            def load_rows(sp, grp):
                for s2 in range(2):
                    b, K = 2 * grp + s2, KV[grp % 2]
                    for pg in range(4):
                        page = sp.value_load(pt2[0:1, 4 * b + pg:4 * b + pg + 1], min_val=0, max_val=n_pool - 1)
                        src = a["cache_slc_kv"][bass.ds(page, 1), 0].rearrange("o t k g d -> (o t) (k g d)")
                        sp.dma_start(K[0][s2][:, pg, :], src).then_inc(kvp_in[grp % 2][s2], 16)
                    sp.dma_start(K[1][s2][:, :, :], a["cache_win_kv"][b, 0].rearrange("(t p) k g d -> p t (k g d)", p=128)).then_inc(kvw_in[grp % 2][s2], 16)

            with nc.Block() as block:
                @block.sync
                def _(sp):
                    sp.dma_start(pt2[:, :], a["page_table"].rearrange("(o b) n -> o (b n)", o=1)).then_inc(tab_in, 16)
                    sp.dma_start(wm[:, :], k["wmask"]).then_inc(tab_in, 16)
                    sp.wait_ge(tab_in, 32)
                    load_rows(sp, 0)
                    for s2 in range(2):
                        sp.dma_start(SBs[64 * s2:64 * s2 + 64, :],
                                     bass.AP(rv_dram.tensor, RV0 - TP, [[RVL, NH], [-1, TS], [1, TP]])).then_inc(tab_in, 16)
                    sp.wait_ge(tab_zero, 1)
                    for s2 in range(2):
                        for grp in range(4):
                            c0 = TS * (2 * grp + s2)
                            sp.dma_start(SBn[64 * s2:64 * s2 + 64, grp, c0:c0 + TS],
                                         bass.AP(rv_dram.tensor, RV0, [[RVL, NH], [-1, TS], [1, TS]])).then_inc(tab_in, 16)
                    load_rows(sp, 1)
                    for grp in range(2, 4):
                        sp.wait_ge(so_ready, grp - 1)
                        load_rows(sp, grp)

                @block.tensor
                def _(pe):
                    pe.wait_ge(tab_in, 32)

                    def keys(n):
                        grp, s2, br = n // 4, (n // 2) % 2, n % 2
                        if br == 0:
                            pe.wait_ge(kvp_in[grp % 2][s2], 64 * (grp // 2 + 1))
                            pe.wait_ge(kvw_in[grp % 2][s2], 16 * (grp // 2 + 1))
                        if n >= 2:
                            pe.wait_ge(kT_sb, n - 1)
                        for pg in range(4):
                            last = pe.transpose(ps[:, br, 128 * pg:128 * pg + 128], KV[grp % 2][br][s2][:, pg, 0:128], ident[:, :])
                        last.then_inc(kT_ps, 1)

                    def scores(n):
                        grp, s2, br = n // 4, (n // 2) % 2, n % 2
                        b, rows = 2 * grp + s2, slice(64 * s2, 64 * s2 + 64)
                        pe.wait_ge(kT_sb, n + 1)
                        if n % 4 == 0 and grp >= 1:
                            pe.wait_ge(ss_taken, grp)
                        pe.matmul(ps[rows, 2 + br, :], qbd[:, b, :], kT[br][:, :], start=True, stop=True)
                        last = pe.matmul(ps[rows, 4, 64 * br:64 * br + 64], qbd[:, b, :], kNew[br][:, :], start=True, stop=True)
                        if br == 1:
                            last = pe.matmul(ps[rows, 4, 128:256], qbd[:, b, :], kcT[:, 128 * (b // 4):128 * (b // 4) + 128], start=True, stop=True)
                        last.then_inc(kS_done, 1)

                    def group_scores(grp):
                        keys(4 * grp)
                        for n in range(4 * grp, 4 * grp + 4):
                            if n % 4 < 3:
                                keys(n + 1)
                            scores(n)

                    def outputs_back(grp):
                        pe.wait_ge(so_acc, grp + 1)
                        pe.transpose(ps[0:64, 7, 384:512], acc[:, :], ident[:, :]).then_inc(so_t, 1)

                    group_scores(0)
                    for grp in range(4):
                        if grp >= 1:
                            outputs_back(grp - 1)
                            pe.wait_ge(so_ev, grp)
                        pe.wait_ge(sp_ready, grp + 1)
                        for br in range(2):
                            for kt in range(4):
                                pe.transpose(ps[:, 5 + br, 128 * kt:128 * kt + 128], S2[br][:, 128 * kt:128 * kt + 128], ident[:, :])
                            pe.transpose(ps[0:64, 7, 128 * br:128 * br + 128], S2[br][:, TP:TP + NS], ident[:, :])
                        pe.transpose(ps[:, 7, 256:384], Sc[:, :], ident[:, :]).then_inc(spt_ready, 1)
                        if grp < 3:
                            group_scores(grp + 1)
                        pe.wait_ge(spt_a, grp + 1)
                        pe.wait_ge(spt_d, grp + 1)
                        K = KV[grp % 2]
                        for s2 in range(2):
                            rows = slice(64 * s2, 64 * s2 + 64)
                            b = 2 * grp + s2
                            for br, c0 in ((0, 896), (1, 1152)):
                                out = ps[rows, 7, 128 * (br + 1):128 * (br + 2)]
                                for kt in range(4):
                                    pe.matmul(out, PT2[br][:, kt, rows], K[br][s2][:, kt, 128:256], start=(kt == 0), stop=False)
                                pe.matmul(out, PTn[:, br, rows], zq[0:64, 4, c0:c0 + 128], start=False, stop=True)
                            last = pe.matmul(ps[rows, 7, 0:128], PTcs[:, rows], vc[:, b // 4, :], start=True, stop=True)
                        last.then_inc(so_ready, 1)
                    outputs_back(3)

                @block.scalar
                def _(act):
                    def keys(grp):
                        for n in range(4 * grp, 4 * grp + 4):
                            act.wait_ge(kT_ps, n + 1)
                            if n >= 2:
                                act.wait_ge(kS_done, n - 1)
                            act.copy(kT[n % 2][:, :], ps[:, n % 2, :]).then_inc(kT_sb, 1)

                    def outputs_back(grp):
                        act.wait_ge(so_t, grp + 1)
                        for par in range(2):
                            src = ps[0:64, 7, 384:512].rearrange("p (s c r t) -> p s c r t", s=2, c=4, r=2)[:, :, :, par, :]
                            dst = mixf[64 * par:64 * par + 64, 0:4, TP + 16 * grp:TP + 16 * grp + 16].rearrange("p c (s t) -> p s c t", s=2)
                            for s2 in range(2):
                                last = act.copy(dst[:, s2], src[:, s2])
                        last.then_inc(so_ev, 1)

                    keys(0)
                    for grp in range(4):
                        act.wait_ge(sm_ready, grp + 1)
                        if grp >= 1:
                            act.wait_ge(so_acc, grp)
                        act.activation(S2[0][:, :], S2[0][:, :], ACT.Exp, bias=mx2[:, 0:1], accum_out=den2[:, 0:1])
                        act.activation(S2[1][:, :], S2[1][:, :], ACT.Exp, bias=mx2[:, 1:2], accum_out=den2[:, 1:2])
                        act.activation(Sc[:, :], Sc[:, :], ACT.Exp, bias=mx2[:, 2:3], accum_out=den2[:, 2:3]).then_inc(sp_ready, 1)
                        if grp >= 1:
                            outputs_back(grp - 1)
                        act.wait_ge(spt_ready, grp + 1)
                        act.copy(PT2[0][:, :, :], ps[:, 5, :].rearrange("p (a b) -> p a b", a=4)).then_inc(spt_a, 1)
                        if grp < 3:
                            keys(grp + 1)
                    outputs_back(3)

                @block.vector
                def _(dve):
                    dve.memset(SBn[:, :, :], NEG)
                    dve.memset(SBc[:, :, :], NEG).then_inc(tab_zero, 1)
                    dve.wait_ge(tab_in, 16 * 12)
                    dve.wait_ge(tab_zero, 1)
                    for par in range(2):
                        for s2 in range(2):
                            c0 = 64 * par + 32 * s2
                            dve.tensor_copy(SBc[64 * s2:64 * s2 + 64, par, c0:c0 + 31], SBs[64 * s2:64 * s2 + 64, 31:31 + 16 * 30 + 1:16])
                    dve.tensor_copy(SBw[:, TS:TP], SBs[:, TS:TP])
                    dve_chain(dve, dve.tensor_tensor(SBw[:, 0:TS], SBs[:, 0:TS], wm[:, :], ALU.add))
                    def take_scores(grp):
                        dve.wait_ge(kS_done, 4 * grp + 4)
                        if grp >= 1:
                            dve.wait_ge(spt_ready, grp)
                        for br in range(2):
                            dve.tensor_tensor(S2[br][:, 0:TP], ps[:, 2 + br, :], (SBs, SBw)[br][:, :], ALU.add)
                            dve.tensor_tensor(S2[br][:, TP:TP + NS], ps[:, 4, 64 * br:64 * br + 64], SBn[:, grp, :], ALU.add)
                        dve.tensor_tensor(Sc[:, :], ps[:, 4, 128:256], SBc[:, grp % 2, :], ALU.add).then_inc(ss_taken, 1)
                        dve.wait_ge(ss_taken, grp + 1)
                        for n, S in enumerate((S2[0], S2[1], Sc)):
                            last = dve.tensor_reduce(mx2[:, n:n + 1], S[:, :], AX.X, ALU.max)
                        dve_chain(dve, last)
                        dve.tensor_scalar(mx2[:, :], mx2[:, :], FLOOR, -1.0, ALU.max, ALU.mult).then_inc(sm_ready, 1)

                    take_scores(0)
                    for grp in range(4):
                        dve.wait_ge(spt_ready, grp + 1)
                        dve.tensor_copy(PT2[1][:, :, :], ps[:, 6, :].rearrange("p (a b) -> p a b", a=4))
                        dve.tensor_copy(PTcs[:, :], ps[:, 7, 256:384])
                        dve.tensor_copy(PTn[:, :, :], ps[0:64, 7, 0:256].rearrange("p (a b) -> p a b", a=2)).then_inc(spt_d, 1)
                        dve.wait_ge(sp_ready, grp + 1)
                        dve_chain(dve, dve.tensor_scalar(den2[:, :], den2[:, :], 1e-30, None, ALU.max))
                        dve_chain(dve, dve.reciprocal(den2[:, :], den2[:, :]))
                        dve.tensor_tensor(den2[:, 0:2], den2[:, 0:2], gs[:, grp, 1:3], ALU.mult)
                        dve_chain(dve, dve.tensor_tensor(den2[:, 2:3], den2[:, 2:3], gs[:, grp, 0:1], ALU.mult))
                        if grp < 3:
                            take_scores(grp + 1)
                        dve.wait_ge(so_ready, grp + 1)
                        for n, (cc, slot) in enumerate(((2, 0), (0, 1), (1, 2))):
                            for blk in range(4):
                                rr = slice(32 * blk, 32 * blk + 32)
                                g = blk % 2
                                O = ps[rr, 7, 128 * slot + 64 * g:128 * slot + 64 * g + 64]
                                if n == 0:
                                    last = dve.tensor_scalar(acc[rr, :], O, den2[rr, cc:cc + 1], None, ALU.mult)
                                else:
                                    last = dve.scalar_tensor_tensor(acc[rr, :], O, den2[rr, cc:cc + 1], acc[rr, :], ALU.mult, ALU.add)
                            if n < 2:
                                dve_chain(dve, last)
                        last.then_inc(so_acc, 1)

            retire_semaphores()
            RZ = MIX + 4 * KT * T
            r = Region(RZ)
            zz = r.take("zz", [128, RT, T])
            AB = r.take("ab_hat", [128, 2, 4, T])
            pc = r.take("p_end", [64, NH, 16])
            bonus = r.take("bonus", [128, 5, NH])
            lnw = r.take("ln_w", [128, 512])
            lnb = r.take("ln_b", [128, 512])
            w2 = r.take("rwkv_w2", [128, 512])
            g2 = r.take("rwkv_g2", [128, 512])
            R2 = r.at
            shT = r.take("shiftT", [128, NB, RT])
            ext = [r.take("z_ext", [128, 1 + TP + NB * (TS + 1)]) for _ in range(2)]
            df = [r.take("z_diff", [128, TP + NB * (TS + 1)]) for _ in range(2)]
            sh_rows = r.take("sh_rows", [NB * RT, 128])
            rw_in, sh_in, sh_t, sh_ev, rx_ready, rx_used = (sem(x) for x in ("rw_in", "sh_in", "sh_t", "sh_ev", "rx_ready", "rx_used"))
            def z_sample(e):
                return e[:, 1 + TP:].rearrange("p (b t) -> p b t", b=NB)

            with nc.Block() as block:
                @block.sync
                def _(sp):
                    sp.dma_start(sh_rows[:, :], a["state_rwkv_shift"].rearrange("b o (c p) -> (b o c) p", p=128)).then_inc(sh_in, 16)
                    with sp.Fori(0, 2) as i:
                        for q in (2, 3):
                            load_slab(sp, st_rw, i, q, 2)
                    for dst, name in ((lnw, "rwkv_ln_w"), (lnb, "rwkv_ln_b")):
                        sp.dma_start(dst[:, :], bass.AP(a[name].tensor, 0, [[0, 128], [1, 512]])).then_inc(rw_in, 16)
                    sp.dma_start(w2[0:64, :], a["rwkv_w2"][0]).then_inc(rw_in, 16)
                    sp.dma_start(w2[64:128, :], a["rwkv_a2"][0]).then_inc(rw_in, 16)
                    sp.dma_start(g2[:, :], a["rwkv_g2"][0]).then_inc(rw_in, 16)
                    load_slab(sp, st_rw, 3, 0, 2)
                    loads_after(sp, st_rw["base"] + 7)
                    sp.wait_ge(rw_in, 80)

                @block.scalar
                def _(act):
                    def slab(i, q, nxt):
                        split_hi(act, *nxt)
                        act.wait_ge(slab_done, st_rw["base"] + 2 * i + q + 1)
                        for j in range(2):
                            kk = 4 * i + 2 * q + j
                            act.wait_ge(rx_used, kk + 1)
                            e, b = ext[j], 4 * q + 2 * j
                            act.copy(e[:, 1:1 + HT], ps[:, b, 0:HT])
                            act.copy(e[:, 1 + HT:1 + TP], ps[:, b + 1, 0:H1])
                            act.copy(z_sample(e)[:, :, 0:1], shT[:, :, bass.ds(kk, 1)])
                            act.copy(z_sample(e)[:, :, 1:1 + TS], ps[:, b + 1, H1:HT].rearrange("p (b t) -> p b t", b=NB)).then_inc(rx_ready, 1)
                        act.wait_ge(rx_ready, 4 * i + 2 * q + 2)
                        act.nop().then_inc(banks_free[q], 1)
                    act.wait_ge(sh_t, 1)
                    act.copy(flat(shT[:, :, :]), ps[:, 4, 0:NB * RT]).then_inc(sh_ev, 1)
                    act.wait_ge(sh_ev, 1)
                    with act.Fori(0, 3) as i:
                        slab(i, 0, (st_rw, i, 1, 2))
                        slab(i, 1, (st_rw, i, 2, 2))
                    slab(3, 0, follow(st_rw["base"] + 7))

                @block.gpsimd
                def _(pool):
                    with pool.Fori(0, 3) as i:
                        split_lo(pool, st_rw, i, 1, 2)
                        split_lo(pool, st_rw, i, 2, 2)
                    split_lo(pool, *follow(st_rw["base"] + 7))

                @block.tensor
                def _(pe):
                    pe.wait_ge(sh_in, 16)
                    pe.transpose(ps[:, 4, 0:NB * RT], sh_rows[:, :], ident[0:NB * RT, 0:NB * RT]).then_inc(sh_t, 1)
                    for i in range(3):
                        for q in range(2):
                            if i == 0 and q == 1:
                                pe.wait_ge(sh_ev, 1)
                            products(pe, st_rw, i, q, 2, 4 * q, 0, hhi, hlo)
                    products(pe, st_rw, 3, 0, 2, 0, 0, hhi, hlo)

                @block.vector
                def _(dve):
                    for e in ext:
                        dve.memset(e[:, 0:1], 0.0).then_inc(rx_used, 1)

                    def tile(kk, j):
                        e, d = ext[j], df[j]
                        dve.wait_ge(rx_ready, kk + 1)
                        dve.tensor_copy(zlast[:, 0:1, bass.ds(kk, 1)], e[:, TP:TP + 1].rearrange("p (a b) -> p a b", a=1))
                        dve.tensor_copy(zlast[:, 1:9, bass.ds(kk, 1)], z_sample(e)[:, :, TS:TS + 1])
                        n = TP + NB * (TS + 1)
                        dve_chain(dve, dve.tensor_tensor(d[:, :], e[:, 0:n], e[:, 1:1 + n], ALU.subtract))
                        mu = vec[:, bass.ds(V_MU + kk, 1)]
                        dve.scalar_tensor_tensor(zz[:, bass.ds(kk, 1), 0:TP].rearrange("p o t -> p (o t)"), d[:, 0:TP], mu, e[:, 1:1 + TP], ALU.mult, ALU.add)
                        dd = d[:, TP:TP + NB * (TS + 1)].rearrange("p (b t) -> p b t", b=NB)[:, :, 1:1 + TS]
                        dve.scalar_tensor_tensor(zz[:, bass.ds(kk, 1), TP:T].rearrange("p o (b t) -> p (o b) t", b=NB), dd, mu,
                                                 z_sample(e)[:, :, 1:1 + TS], ALU.mult, ALU.add).then_inc(rx_used, 1)

                    with dve.Fori(0, 3) as i:
                        dve_chain.begin(i, 4, 3)
                        for q in range(2):
                            for j in range(2):
                                tile(4 * i + 2 * q + j, j)
                        dve_chain.end()
                    for j in range(2):
                        tile(12 + j, j)

            r = Region(R)
            sg, aa, kk_ = ([r.take(x, [128, T]) for _ in range(4)] for x in ("log_decay", "rate", "removal"))
            tt_ = [r.take("norm_decay", [128, T]) for _ in range(4)]
            keep = r.take("keep", [128, T])
            hones = r.take("headones", [128, 128])
            omka = r.take("omka", [128, 4])
            assert r.at <= MIX
            r = Region(R2)
            PI, km, BO = ([r.take(x, [128, T]) for _ in range(2)] for x in ("decay_inv", "km", "bonus_in"))
            k_in, act_lora, wa_ps, sig_ready, cm_ready, exp_ready, kk_ready, sq2_ready, ss_ps, ss_m, ss_std, rk_ready, bo_ps, c_free = (
                sem(x) for x in ("k_in", "act_lora", "wa_ps", "sig_ready", "cm_ready", "exp_ready", "kk_ready", "sq2_ready",
                                 "ss_ps", "ss_m", "ss_std", "rk_ready", "bo_ps", "c_free"))
            halves = lambda t: t.rearrange("p (a t) -> p a t", a=2)
            ss_bank = lambda c: 4 + 2 * (c % 2)
            with nc.Block() as block:
                @block.sync
                def _(sp):
                    sp.dma_start(keep[:, :], k["keep"]).then_inc(k_in, 16)
                    sp.dma_start(hones[:, :], k["headones"]).then_inc(k_in, 16)
                    sp.wait_ge(k_in, 32)

                @block.scalar
                def _(act):
                    act.activation(zz[0:64, 12, :], zz[0:64, 12, :], ACT.Tanh)
                    act.activation(zz[:, 13, :], zz[:, 13, :], ACT.Sigmoid).then_inc(act_lora, 1)
                    for c in range(4):
                        act.wait_ge(kk_ready, c + 1)
                        act.activation(tt_[c][:, :], kk_[c][:, :], ACT.Square).then_inc(sq2_ready, 1)
                    for c in range(4):
                        act.wait_ge(ss_m, c + 1)
                        act.activation(tt_[c][:, :], tt_[c][:, :], ACT.Sqrt).then_inc(ss_std, 1)
                    for c in range(4):
                        act.wait_ge(wa_ps, c + 1)
                        act.activation(halves(sg[c][:, :]), ps[:, 0:2, 0:HT], ACT.Sigmoid, bias=vec[:, V_W0 + c:V_W0 + c + 1])
                        act.activation(halves(aa[c][:, :]), ps[:, 2:4, 0:HT], ACT.Sigmoid, bias=vec[:, V_A0 + c:V_A0 + c + 1]).then_inc(sig_ready, 1)
                    for c in range(4):
                        act.wait_ge(cm_ready, c + 1)
                        if c >= 2:
                            act.wait_ge(c_free, c - 1)
                        act.activation(PI[c % 2][:, :], tt_[c][:, :], ACT.Exp, scale=-1.0).then_inc(act_chain.sem, 1)
                        act_chain.n += 1
                        act.wait_ge(act_chain.sem, act_chain.n)
                        act.activation(tt_[c][:, :], tt_[c][:, :], ACT.Exp)
                        act.activation(sg[c][:, :], sg[c][:, :], ACT.Exp).then_inc(exp_ready, 1)

                @block.tensor
                def _(pe):
                    pe.wait_ge(k_in, 32)
                    for c in range(4):
                        pe.wait_ge(sq2_ready, c + 1)
                        if c >= 2:
                            pe.wait_ge(ss_m, c - 1)
                        for half in range(2):
                            last = pe.matmul(ps[:, ss_bank(c) + half, 0:HT], hones[:, :], tt_[c][:, half * HT:(half + 1) * HT], start=True, stop=True)
                        last.then_inc(ss_ps, 1)
                    pe.wait_ge(act_lora, 1)
                    for c in range(4):
                        if c >= 1:
                            pe.wait_ge(sig_ready, c)
                        for half in range(2):
                            cols_ = slice(half * HT, (half + 1) * HT)
                            pe.matmul(ps[:, half, 0:HT], w2[0:64, 128 * c:128 * c + 128], zz[0:64, 12, cols_], start=True, stop=True)
                            last = pe.matmul(ps[:, 2 + half, 0:HT], w2[64:128, 128 * c:128 * c + 128], zz[64:128, 12, cols_], start=True, stop=True)
                        last.then_inc(wa_ps, 1)
                    pe.wait_ge(ss_m, 4)
                    for c in range(4):
                        pe.wait_ge(rk_ready, c + 1)
                        for tok in range(5):
                            w = 128 if tok < 4 else NS
                            last = pe.matmul(ps[0:w, 6, 8 * tok + 2 * c:8 * tok + 2 * c + 2], BO[c % 2][:, 128 * tok:128 * tok + w], hones[:, 0:128:64],
                                             start=True, stop=True)
                        last.then_inc(bo_ps, 1)

                @block.vector
                def _(dve):
                    L = lambda ins: dve_chain(dve, ins)
                    ka = vec[:, V_KA:V_KA + 4]
                    col = lambda v, c: vec[:, v + c:v + c + 1]
                    for c in range(4):
                        dve.tensor_scalar(kk_[c][:, :], zz[:, 4 + c, :], col(V_KK, c), None, ALU.mult).then_inc(kk_ready, 1)
                    L(dve.tensor_scalar(omka[:, :], ka, -1.0, 1.0, ALU.mult, ALU.add))
                    dve.wait_ge(k_in, 32)
                    for c in range(4):
                        dve.wait_ge(ss_ps, c + 1)
                        dve.tensor_scalar(halves(tt_[c][:, :]), ps[:, ss_bank(c):ss_bank(c) + 2, 0:HT], 1e-24, None, ALU.max).then_inc(ss_m, 1)
                    for c in range(4):
                        dve.wait_ge(ss_std, c + 1)
                        L(dve.reciprocal(tt_[c][:, :], tt_[c][:, :]))
                        L(dve.tensor_tensor(kk_[c][:, :], kk_[c][:, :], tt_[c][:, :], ALU.mult))

                    def sums(c):
                        dve.wait_ge(sig_ready, c + 1)
                        if c >= 2:
                            dve.wait_ge(c_free, c - 1)
                        L(dve.tensor_scalar(sg[c][:, :], sg[c][:, :], -math.exp(-0.5), None, ALU.mult))
                        L(dve.tensor_tensor_scan(tt_[c][:, :], keep[:, :], sg[c][:, :], 0.0, ALU.mult, ALU.add))
                        dve.tensor_tensor(sg[c][:, :], tt_[c][:, :], sg[c][:, :], ALU.subtract).then_inc(cm_ready, 1)
                        L(dve.tensor_scalar(km[c % 2][:, :], aa[c][:, :], col(V_KA, c), omka[:, c:c + 1], ALU.mult, ALU.add))
                        L(dve.tensor_tensor(km[c % 2][:, :], km[c % 2][:, :], zz[:, 4 + c, :], ALU.mult))

                    def scaled(c):
                        if c >= 2:
                            dve.wait_ge(bo_ps, c - 1)
                        dve.scalar_tensor_tensor(BO[c % 2][:, :], zz[:, c, :], col(V_RK, c), km[c % 2][:, :], ALU.mult, ALU.mult).then_inc(rk_ready, 1)
                        dve.tensor_tensor(aa[c][:, :], kk_[c][:, :], aa[c][:, :], ALU.mult).then_inc(dve_chain.sem, 1)
                        dve_chain.n += 1
                        dve.wait_ge(exp_ready, c + 1)
                        dve.scalar_tensor_tensor(AB[:, 0, c, :], kk_[c][:, :], -1.0, sg[c][:, :], ALU.mult, ALU.mult)
                        dve.wait_ge(dve_chain.sem, dve_chain.n)
                        dve.tensor_tensor(AB[:, 1, c, :], aa[c][:, :], PI[c % 2][:, :], ALU.mult)
                        dve.tensor_tensor(zz[:, 4 + c, :], km[c % 2][:, :], PI[c % 2][:, :], ALU.mult)
                        dve.wait_ge(rk_ready, c + 1)
                        dve.tensor_tensor(zz[:, c, :], zz[:, c, :], tt_[c][:, :], ALU.mult)
                        for hb in range(2):
                            rows_ = slice(64 * hb, 64 * hb + 64)
                            dve.tensor_copy(pc[:, 2 * c + hb, 0:8], tt_[c][rows_, CH - 1:TP:CH])
                            last = dve.tensor_copy(pc[:, 2 * c + hb, 8:16], tt_[c][rows_, TP + TS - 1:T:TS])
                        last.then_inc(c_free, 1)

                    for c in range(5):
                        if c < 4:
                            sums(c)
                        if c >= 1:
                            scaled(c - 1)
                    dve.wait_ge(bo_ps, 4)
                    dve.tensor_copy(bonus[:, 0:4, :], ps[:, 6, 0:32].rearrange("p (a b) -> p a b", a=4))
                    dve.tensor_copy(bonus[0:NS, 4, :], ps[0:NS, 6, 32:40])

            r = Region(R)
            G1 = r.take("state_in", [128, 2, NH, 128])
            G2 = r.take("state_out", [128, 2, NH, 128])
            BK = r.take("b_k", [64, 2, NH, 2, CH])
            Sv = [r.take("sv", [128, 512]) for _ in range(2)]
            Uv = [r.take("uv", [128, 512]) for _ in range(2)]
            Zs = r.take("zs", [128, 512])
            yb = r.take("yb", [128, 512])
            gmask = r.take("gmask", [128, 2, 128])
            imask = r.take("imask", [128, 2, 4, CH])
            smask = r.take("smask", [128, NB])
            assert r.at <= MIX, r.at - MIX
            AR = G1[0:64]
            r = Region(R2)
            MV = r.take("moving", [128, NH, 3, CH])
            mE = r.take("moving_e", [128, 512])
            assert st_out["base"] % 2 == 1
            w_at = nc.sbuf_base + (-nc.sbuf_base) % 64 + 2 * 4 * SLAB
            DIA = [at("diagonal", [128, NH, 128], F32, w_at + 4096 * n) for n in range(2)]
            SpO = r.take("sp", [128, 4, CH])
            st8 = r.take("stats", [128, 2, NH])
            ysq_v = mE
            mA, mY, mC = range(3)
            STEPS = [(0, mA, mA, mC, False),
                     (mC, 1),
                     (1, mY, mC, mA, True),
                     (mA, 0),
                     (0, mA, mY, mC, True),
                     (mC, 1),
                     (1, mY, mY, None, True),
                     (mY, 0),
                     (0, None, None, mC, False),
                     (mC, 1),
                     (1, mY, mC, mA, True),
                     (mA, 0),
                     (0, mY, mY, None, True)]
            NSTEP = len(STEPS)
            ADDS = [s for s in range(NSTEP) if STEPS[s][-1] is True]
            MOVES = [s for s in range(NSTEP) if s not in ADDS]
            TILES = 5
            chunks_of = lambda t: 2 if t < 4 else 1
            ntok = lambda t: 128 if t < 4 else NS
            chunk_no = lambda t, ch: 2 * t + ch
            slot1 = lambda t, ch: ch if t < 4 else 1
            chunks_to = lambda t: 2 * t + chunks_of(t)
            m_in, cp_a, cp_d, gg_ps, dd_sb, gg_sb, y_set, bkt_ps, bkt_sb, v_ps, v_sb, g_zero = (sem(x) for x in (
                "m_in", "cp_ar", "cp_bk", "gg_ps", "dd_sb", "gg_sb", "y_set", "bkt_ps", "bkt_sb", "v_ps", "v_sb", "g_zero"))
            inv_ps = [sem("inv_ps0"), sem("inv_ps1")]
            inv_0, inv_m1, inv_y1 = sem("inv_taken0"), sem("inv_moved1"), sem("inv_added1")
            z_ps, z_sb, u_ps, u_sb, n_ps, n_sb, yc_sb, gate_ps, yn_a, yn_b, yn_c, yo, yt_ps2, yt_sb2 = (sem(x) for x in (
                "z_ps", "z_sb", "u_ps", "u_sb", "n_ps", "n_sb", "yc_sb", "gate_ps", "yn_mean", "yn_sq", "yn_std", "y_out_ready", "ymix_ps", "ymix_sb"))
            sT_ps, sT_sb, zsT_ps, zsT_sb, um_ready, sn_ps, sn_sb, so_ps, so_sb, st_in, wkv_out, pT_ps, pT_sb = (sem(x) for x in (
                "sT_ps", "sT_sb", "zsT_ps", "zsT_sb", "um_ready", "sn_ps", "sn_sb", "sO_ps", "sO_sb", "st_in", "wkv_out", "pT_ps", "pT_sb"))
            q = Region(RZ)
            S0T = q.take("s0T", [64, NB, 512])
            assert q.at <= RZ + 4 * 8 * T
            q = Region(RZ + 4 * RT * T)
            S0n = q.take("s0", [128, NB, 4, CH])
            Um = [q.take("um", [128, NB, CH]) for _ in range(2)]
            Sn = [q.take("sn", [64, NB, CH]) for _ in range(2)]
            assert q.at <= RZ + 4 * RT * T + 4 * 8 * T
            So = at("so", [128, NH, 4, CH], F32, R)

            def take_out(eng, copy, t, s, half):
                C, P = chunks_of(t), 64 * chunks_of(t)
                hs = slice(4 * half, 4 * half + 4)
                st, bank = STEPS[s], ps[:, half, :]
                if len(st) == 2:
                    for ch in range(C):
                        src = bank[0:64].rearrange("p (h x t) -> p h x t", h=4, x=2)[:, :, ch, :]
                        last = copy(DIA[st[1]][64 * ch:64 * ch + 64, hs, 64 * ch:64 * ch + 64], src)
                    return last
                first, dst, add = st[1], st[3], st[4]
                out = bank[0:P].rearrange("p (h x t) -> p h x t", h=4, x=2)
                if dst is not None:
                    last = copy(MV[0:P, hs, dst, :], out[:, :, 1 if first == mY else 0, :])
                if add:
                    Y = MV[0:P, hs, mY, :]
                    last = eng.tensor_tensor(Y, out[:, :, 0 if first == mY else 1, :], Y, ALU.add)
                return last

            with nc.Block() as block:
                @block.sync
                def _(sp):
                    sp.dma_start(gmask[:, :, :], k["gmask"]).then_inc(m_in, 16)
                    sp.dma_start(imask[:, :, :, :], k["invmask"]).then_inc(m_in, 16)
                    sp.dma_start(smask[:, :], k["seqmask"]).then_inc(m_in, 16)
                    sp.wait_ge(cp_a, TILES)
                    sp.wait_ge(cp_d, TILES)
                    for b in range(NB):
                        for h2 in range(2):
                            sp.dma_start(S0n[64 * h2:64 * h2 + 64, b, :, :],
                                         a["state_rwkv_wkv"][b, 0].rearrange("(c h) i j -> h i c j", h=2)[h2]).then_inc(st_in, 16)
                    sp.wait_ge(pT_sb, 1)
                    for h2 in range(2):
                        sp.dma_start(o["wkv_p"][0, 0].rearrange("(c h) i j -> h i c j", h=2)[h2], SpO[64 * h2:64 * h2 + 64, :, :]).then_inc(wkv_out, 16)
                    sp.wait_ge(so_sb, NH)
                    for qq in range(4):
                        for b2 in range(2):
                            sp.dma_start(o["wkv_s"][2 * qq + b2, 0].rearrange("h i j -> i h j"), So[64 * b2:64 * b2 + 64, :, qq, :]).then_inc(wkv_out, 16)
                    sp.wait_ge(wkv_out, 160)

                @block.tensor
                def _(pe):
                    def token_products(t):
                        C = chunks_of(t)
                        pe.wait_ge(cp_a, t + 1)
                        pe.wait_ge(cp_d, t + 1)
                        if t >= 1:
                            pe.wait_ge(yc_sb, 2 * chunks_to(t - 1))
                        for ch in range(C):
                            for h in range(NH):
                                pe.matmul(ps[:, 2 * ch + h // 4, 128 * (h % 4):128 * (h % 4) + 128],
                                          BK[:, ch, h].rearrange("p x t -> p (x t)"), AR[:, ch, h, :], start=True, stop=True)
                                last = pe.matmul(ps[64 * ch:64 * ch + 64, 4, 64 * h:64 * h + 64], AR[:, ch, h, 0:64], BK[:, ch, h, 0, :], start=True, stop=True)
                        last.then_inc(gg_ps, 1)

                    def inverse_taken(half, t, s):
                        if half == 0:
                            pe.wait_ge(inv_0, NSTEP * t + s)
                        elif s - 1 in ADDS:
                            pe.wait_ge(inv_y1, len(ADDS) * t + ADDS.index(s - 1) + 1)
                        else:
                            pe.wait_ge(inv_m1, len(MOVES) * t + MOVES.index(s - 1) + 1)

                    def out_transposed(t):
                        w = ntok(t)
                        pe.wait_ge(yo, t + 1)
                        for c in range(4):
                            last = pe.transpose(ps[:, 6, 128 * c:128 * c + w], yb[0:w, 128 * c:128 * c + 128], ident[0:w, 0:w])
                        last.then_inc(yt_ps2, 1)

                    for t in range(TILES):
                        C, P, w = chunks_of(t), 64 * chunks_of(t), ntok(t)
                        token_products(t)
                        if t >= 1:
                            out_transposed(t - 1)
                            pe.wait_ge(yt_sb2, t)
                        for ch in range(C):
                            for h in range(NH):
                                last = pe.transpose(ps[:, 5 + ch, 64 * h:64 * h + 64], BK[:, ch, h].rearrange("p x t -> p (x t)"), ident[0:64, 0:64])
                        last.then_inc(bkt_ps, 1)
                        for c in range(4):
                            last = pe.transpose(ps[0:w, 7, 128 * c:128 * c + 128], zz[:, 8 + c, 128 * t:128 * t + w], ident[:, :])
                        last.then_inc(v_ps, 1)
                        if t == 4:
                            pe.wait_ge(st_in, 256)
                            for b in range(NB):
                                if b >= 1:
                                    pe.wait_ge(sT_sb, b)
                                for c in range(4):
                                    last = pe.transpose(ps[0:64, 6, 128 * c:128 * c + 128], S0n[:, b, c, :], ident[:, :])
                                last.then_inc(sT_ps, 1)
                            pe.wait_ge(sT_sb, NB)
                            for h in range(NH):
                                for b in range(NB):
                                    last = pe.matmul(ps[0:64, 2 + h // 4, 128 * (h % 4):128 * (h % 4) + 128].rearrange("p (x t) -> p x t", x=2)[:, :, 8 * b:8 * b + 8],
                                                     S0T[:, b, 64 * h:64 * h + 64], AR[:, 0, h, :].rearrange("p (x t) -> p x t", x=2)[:, :, 8 * b:8 * b + 8],
                                                     start=True, stop=True)
                            last.then_inc(zsT_ps, 1)
                            pe.wait_ge(zsT_sb, 1)
                        pe.wait_ge(gg_sb, t + 1)
                        for s, st in enumerate(STEPS):
                            if s == ADDS[0]:
                                pe.wait_ge(y_set, t + 1)
                            for half in range(2):
                                if s >= 1:
                                    inverse_taken(half, t, s)
                                for h4 in range(4):
                                    h = 4 * half + h4
                                    if len(st) == 2:
                                        last = pe.transpose(ps[0:64, half, 128 * h4:128 * h4 + P], MV[0:P, h, st[0], :], ident[0:P, 0:P])
                                    else:
                                        mov = mE[0:P, 64 * h:64 * h + 64] if st[1] is None else MV[0:P, h, st[1]:st[2] + 1, :].rearrange("p x t -> p (x t)")
                                        width = 64 if st[1] == st[2] else 128
                                        last = pe.matmul(ps[0:P, half, 128 * h4:128 * h4 + width], DIA[st[0]][0:P, h, 0:P], mov, start=True, stop=True)
                                last.then_inc(inv_ps[half], 1)
                        for half in range(2):
                            inverse_taken(half, t, NSTEP)
                        pe.wait_ge(bkt_sb, t + 1)
                        for ch in range(C):
                            n = chunk_no(t, ch)
                            S, Un = Sv[n % 2], Uv[n % 2]
                            pe.wait_ge(v_sb, n + 1)
                            pe.wait_ge(n_sb, n + 1)
                            for h in range(NH):
                                hs = slice(64 * h, 64 * h + 64)
                                last = pe.matmul(ps[:, 4 - ch, hs], G1[:, slot1(t, ch), h, :], S[:, hs], start=True, stop=True)
                            last.then_inc(z_ps, 1)
                            pe.wait_ge(z_sb, n + 1)
                            rows = slice(64 * ch, 64 * ch + 64)
                            for h in range(NH):
                                hs = slice(64 * h, 64 * h + 64)
                                last = pe.matmul(ps[0:64, 5, hs], MV[rows, h, mY, :], Zs[rows, hs], start=True, stop=True)
                            last.then_inc(u_ps, 1)
                            pe.wait_ge(u_sb, n + 1)
                            for h in range(NH):
                                hs = slice(64 * h, 64 * h + 64)
                                last = pe.matmul(ps[:, 6 - 4 * ch, hs], G2[:, ch, h, :], Un[:, hs], start=True, stop=True)
                            last.then_inc(n_ps, 1)
                        pe.matmul(ps[0:w, 5, :], zz[:, 13, 128 * t:128 * t + w], g2[:, :], start=True, stop=True).then_inc(gate_ps, 1)
                        if t == 3:
                            pe.wait_ge(n_sb, 9)
                            pe.wait_ge(yc_sb, 2 * chunks_to(t))
                            for c in range(4):
                                last = pe.transpose(ps[:, 6, 64 * c:64 * c + 64], Sv[0][0:64, 128 * c:128 * c + 128], ident[0:64, 0:64])
                            last.then_inc(pT_ps, 1)
                            pe.wait_ge(pT_sb, 1)
                    out_transposed(TILES - 1)
                    for h in range(NH):
                        pe.wait_ge(um_ready, h + 1)
                        if h >= 2:
                            pe.wait_ge(sn_sb, h - 1)
                        if h == 0:
                            pe.wait_ge(yt_sb2, TILES)
                        pe.matmul(ps[0:64, h % 2, :], G2[:, 0, h, 0:64], Um[h % 2][:, :, :].rearrange("p b i -> p (b i)"), start=True, stop=True).then_inc(sn_ps, 1)
                        pe.wait_ge(sn_sb, h + 1)
                        if h >= 2:
                            pe.wait_ge(so_sb, h - 1)
                        for qq in range(4):
                            last = pe.transpose(ps[:, 2 + h % 2, 64 * qq:64 * qq + 64], Sn[h % 2][:, 2 * qq:2 * qq + 2, :].rearrange("p b i -> p (b i)"), ident[0:64, 0:64])
                        last.then_inc(so_ps, 1)

                @block.gpsimd
                def _(pool):
                    for n in range(2):
                        pool.memset(DIA[n][:, :, :], 0.0).then_inc(g_zero, 1)
                    for t in range(TILES):
                        pool.wait_ge(dd_sb, t + 1)
                        for ch in range(chunks_of(t)):
                            rows = slice(64 * ch, 64 * ch + 64)
                            idb = ident[rows, rows].rearrange("p (o t) -> p o t", o=1).to_broadcast([64, NH, CH])
                            last = pool.tensor_tensor(MV[rows, :, mY, :], MV[rows, :, mA, :], idb, ALU.add)
                        last.then_inc(y_set, 1)

                @block.scalar
                def _(act):

                    def take_ar(t):
                        C, w = chunks_of(t), ntok(t)
                        if t >= 1:
                            act.wait_ge(z_ps, chunks_to(t - 1))
                        for x, src in ((0, AB[:, 0]), (1, zz[:, 0:4])):
                            for hb in range(2):
                                last = act.copy(AR[:, 0:C, hb::2, 64 * x:64 * x + 64].rearrange("p n c t -> p c n t"),
                                                src[64 * hb:64 * hb + 64, :, 128 * t:128 * t + w].rearrange("p c (n t) -> p c n t", n=C))
                        last.then_inc(cp_a, 1)

                    take_ar(0)
                    for t in range(TILES):
                        C, P, w = chunks_of(t), 64 * chunks_of(t), ntok(t)
                        act.wait_ge(bkt_ps, t + 1)
                        act.copy(G2[:, 0:C, :, 0:64], ps[:, 5:5 + C, :].rearrange("p c (h j) -> p c h j", h=NH)).then_inc(bkt_sb, 1)
                        act.wait_ge(v_ps, t + 1)
                        for ch in range(C):
                            n = chunk_no(t, ch)
                            rows = slice(64 * ch, 64 * ch + 64)
                            act.copy(Sv[n % 2][64:128, :], ps[rows, 7, :])
                            act.copy(Uv[n % 2][64:128, :], ps[rows, 7, :]).then_inc(v_sb, 1)
                        if t == 4:
                            for b in range(NB):
                                act.wait_ge(sT_ps, b + 1)
                                act.copy(S0T[:, b, :], ps[0:64, 6, :]).then_inc(sT_sb, 1)
                            act.wait_ge(zsT_ps, 1)
                            act.copy(G1[0:64, 1].rearrange("p (b h) w -> p b (h w)", b=2), ps[0:64, 2:4, :]).then_inc(zsT_sb, 1)
                        for s in MOVES:
                            act.wait_ge(inv_ps[1], NSTEP * t + s + 1)
                            take_out(act, act.copy, t, s, 1).then_inc(inv_m1, 1)
                        if t + 1 < TILES:
                            take_ar(t + 1)
                        if t == 3:
                            act.wait_ge(pT_ps, 1)
                            act.copy(SpO[:, :, :], ps[:, 6, 0:256].rearrange("p (c j) -> p c j", c=4)).then_inc(pT_sb, 1)
                        act.wait_ge(yn_a, t + 1)
                        act.activation(ysq_v[0:w, :], yb[0:w, :], ACT.Square).then_inc(yn_b, 1)
                        act.wait_ge(yn_c, 2 * t + 1)
                        act.activation(st8[0:w, 1, :], st8[0:w, 1, :], ACT.Sqrt).then_inc(yn_b, 1)
                        act.wait_ge(yt_ps2, t + 1)
                        act.copy(mixf[:, 4:8, 128 * t:128 * t + w], ps[:, 6, :].rearrange("p (c t) -> p c t", c=4)[:, :, 0:w]).then_inc(yt_sb2, 1)
                    for h in range(NH):
                        act.wait_ge(so_ps, h + 1)
                        act.copy(So[:, h, :, :], ps[:, 2 + h % 2, 0:256].rearrange("p (q j) -> p q j", q=4)).then_inc(so_sb, 1)

                @block.vector
                def _(dve):
                    L = lambda ins: dve_chain(dve, ins)
                    dve.memset(G1[64:128, :, :, 64:128], 0.0)
                    dve.memset(Sv[0][0:64, :], 0.0).then_inc(n_sb, 1)
                    dve.wait_ge(m_in, 48)

                    def take_bk(t):
                        C, w = chunks_of(t), ntok(t)
                        if t >= 1:
                            dve.wait_ge(bkt_ps, t)
                        for x, src in ((0, AB[:, 1]), (1, zz[:, 4:8])):
                            for hb in range(2):
                                last = dve.tensor_copy(BK[:, 0:C, hb::2, x, :].rearrange("p n c t -> p c n t"),
                                                       src[64 * hb:64 * hb + 64, :, 128 * t:128 * t + w].rearrange("p c (n t) -> p c n t", n=C))
                        last.then_inc(cp_d, 1)

                    take_bk(0)
                    dve.wait_ge(g_zero, 2)
                    for t in range(TILES):
                        C, P, w, ms = chunks_of(t), 64 * chunks_of(t), ntok(t), int(t == 4)
                        dve.wait_ge(gg_ps, t + 1)
                        hv = lambda x: x.rearrange("p (h t) -> p h t", h=NH)
                        bm = lambda rows, m_, x: imask[rows, m_, 2 * ms + x:2 * ms + x + 1, :].to_broadcast([rows.stop - rows.start, NH, CH])
                        prod = lambda rows, ch, x: ps[rows, 2 * ch:2 * ch + 2, :].rearrange("p b (h x t) -> p (b h) x t", h=4, x=2)[:, :, x, :]
                        low = slice(0, 64)
                        for ch in range(C):
                            rows = slice(64 * ch, 64 * ch + 64)
                            dve.tensor_tensor(MV[rows, :, mA, :], prod(low, ch, 0), bm(low, 0, 0), ALU.mult)
                            last = dve.tensor_tensor(DIA[0][rows, :, rows], hv(ps[rows, 4, :]), bm(rows, 1, 0), ALU.mult)
                        last.then_inc(dd_sb, 1)
                        for ch in range(C):
                            dve.tensor_tensor(hv(mE[64 * ch:64 * ch + 64]), prod(low, ch, 0), bm(low, 0, 1), ALU.mult)
                            mk = lambda rows, x: gmask[rows, ms:ms + 1, 64 * x:64 * x + 64].to_broadcast([rows.stop - rows.start, NH, CH])
                            dve.tensor_tensor(G1[64:128, slot1(t, ch), :, 0:64], prod(slice(64, 128), ch, 0), mk(slice(64, 128), 0), ALU.mult)
                            last = dve.tensor_tensor(G2[:, ch, :, 64:128], prod(slice(0, 128), ch, 1), mk(slice(0, 128), 1), ALU.mult)
                        last.then_inc(gg_sb, 1)
                        if t == 4:
                            dve.tensor_copy(hv(Sv[0][0:64, :]), ident[0:64, 0:64].rearrange("p (o t) -> p o t", o=1).to_broadcast([64, NH, CH]))
                        for s in range(NSTEP):
                            dve.wait_ge(inv_ps[0], NSTEP * t + s + 1)
                            take_out(dve, dve.tensor_copy, t, s, 0).then_inc(inv_0, 1)
                            if s in ADDS:
                                dve.wait_ge(inv_ps[1], NSTEP * t + s + 1)
                                take_out(dve, dve.tensor_copy, t, s, 1).then_inc(inv_y1, 1)
                        for ch in range(C):
                            n = chunk_no(t, ch)
                            S, Nx, Un = Sv[n % 2], Sv[(n + 1) % 2], Uv[n % 2]
                            rows = slice(64 * ch, 64 * ch + 64)
                            dve.wait_ge(z_ps, n + 1)
                            dve.tensor_copy(Zs[rows, :], ps[0:64, 4 - ch, :]).then_inc(z_sb, 1)
                            dve.wait_ge(u_ps, n + 1)
                            dve.tensor_copy(Un[0:64, :], ps[0:64, 5, :]).then_inc(u_sb, 1)
                            dve.wait_ge(n_ps, n + 1)
                            if t < 4:
                                L(dve.tensor_tensor(Nx[0:64, :], ps[0:64, 6 - 4 * ch, :], S[0:64, :], ALU.add))
                                nx = Nx[0:64, :].rearrange("p (h i) -> p h i", h=NH)
                                dve.tensor_tensor(nx, nx, pc[:, :, n:n + 1].to_broadcast([64, NH, CH]), ALU.mult).then_inc(n_sb, 1)
                            if t >= 1:
                                dve.wait_ge(yt_ps2, t)
                            dve.tensor_copy(yb[rows, :], ps[64:128, 4 - ch, :]).then_inc(yc_sb, 1)
                            dve.wait_ge(yc_sb, 2 * n + 1)
                            dve.tensor_tensor(yb[rows, :], yb[rows, :], ps[64:128, 6 - 4 * ch, :], ALU.add).then_inc(yc_sb, 1)
                        if t + 1 < TILES:
                            take_bk(t + 1)
                        dve.wait_ge(yc_sb, 2 * chunks_to(t))
                        per = lambda x: x.rearrange("p (h o) -> p h o", o=1).to_broadcast([w, NH, CH])
                        L(dve.tensor_reduce(st8[0:w, 0, :], hv(yb[0:w, :]), AX.X, ALU.add))
                        L(dve.tensor_scalar(st8[0:w, 0, :], st8[0:w, 0, :], 1.0 / HD, None, ALU.mult))
                        dve.tensor_tensor(hv(yb[0:w, :]), hv(yb[0:w, :]), per(st8[0:w, 0, :]), ALU.subtract).then_inc(yn_a, 1)
                        dve.wait_ge(yn_b, 2 * t + 1)
                        L(dve.tensor_reduce(st8[0:w, 1, :], hv(ysq_v[0:w, :]), AX.X, ALU.add))
                        dve.tensor_scalar(st8[0:w, 1, :], st8[0:w, 1, :], 1.0 / HD, GN_EPS, ALU.mult, ALU.add).then_inc(yn_c, 1)
                        dve.wait_ge(yn_b, 2 * t + 2)
                        dve.nop().then_inc(yn_c, 1)
                        L(dve.reciprocal(st8[0:w, 1, :], st8[0:w, 1, :]))
                        L(dve.tensor_tensor(hv(yb[0:w, :]), hv(yb[0:w, :]), per(st8[0:w, 1, :]), ALU.mult))
                        L(dve.tensor_tensor(yb[0:w, :], yb[0:w, :], lnw[0:w, :], ALU.mult))
                        L(dve.tensor_tensor(yb[0:w, :], yb[0:w, :], lnb[0:w, :], ALU.add))
                        L(dve.tensor_tensor(hv(ysq_v[0:w, :]), hv(ps[0:w, 7, :]), per(bonus[0:w, t, :]), ALU.mult))
                        L(dve.tensor_tensor(yb[0:w, :], yb[0:w, :], ysq_v[0:w, :], ALU.add))
                        dve.wait_ge(gate_ps, t + 1)
                        dve.tensor_tensor(yb[0:w, :], yb[0:w, :], ps[0:w, 5, :], ALU.mult).then_inc(yo, 1)
                    dve.wait_ge(yt_ps2, TILES)
                    for h in range(NH):
                        if h >= 2:
                            dve.wait_ge(sn_ps, h - 1)
                        hs = slice(64 * h, 64 * h + 64)
                        dve.tensor_tensor(Um[h % 2][:, :, :], Uv[0][:, hs].rearrange("p (o i) -> p o i", o=1).to_broadcast([128, NB, CH]),
                                          smask[:, :].rearrange("p (b o) -> p b o", o=1).to_broadcast([128, NB, CH]), ALU.mult).then_inc(um_ready, 1)
                        dve.wait_ge(sn_ps, h + 1)
                        if h >= 2:
                            dve.wait_ge(so_ps, h - 1)
                        L(dve.tensor_tensor(Sn[h % 2][:, :, :], ps[0:64, h % 2, :].rearrange("p (b i) -> p b i", b=NB), S0T[:, :, hs], ALU.add))
                        dve.tensor_tensor(Sn[h % 2][:, :, :], Sn[h % 2][:, :, :],
                                          pc[:, h, 8:16].rearrange("p (b o) -> p b o", o=1).to_broadcast([64, NB, CH]), ALU.mult).then_inc(sn_sb, 1)

            new_states.append((flat(zlast[:, :, :]), 9 * RT, [(0, RT, o["shift_p"].rearrange("b o (c p) -> (b o c) p", p=128)),
                                                              (RT, 9 * RT, o["shift_s"].rearrange("b o (c p) -> (b o c) p", p=128))]))
            mix_out(mixf)

        def mix_out(mixf):
            reg = Region(R + 8 * T * 4 + 2 * KT * TPAD * 4)
            mhi, mlo = reg.take("mix_hi", [128, KT, T], F32R), reg.take("mix_lo", [128, KT, T], F32R)
            mix_hi_ready, mix_lo_ready = sem("mix_hi_ready"), sem("mix_lo_ready")

            def hi(act):
                for c in range(KT):
                    act.copy(mhi[:, c, :], mixf[:, c, :]).then_inc(mix_hi_ready, 1)

            def lo(dve):
                for c in range(KT):
                    dve.wait_ge(mix_hi_ready, c + 1)
                    dve.tensor_tensor(mlo[:, c, :], mixf[:, c, :], mhi[:, c, :].bitcast(F32), ALU.subtract).then_inc(mix_lo_ready, 1)
            residual(st_out, mhi, mlo, first=dict(act=hi, dve=lo, ready=lambda pe, c: pe.wait_ge(mix_lo_ready, c + 1)))


        keep_semaphores()
        even_mixer()
        retire_semaphores()
        ffn(0, ffn0, V_FFN)
        conv_mixer()
        ffn(1, ffn1, V_FFN + 8)
        store_all()


_INS = ["x_prompt", "x_sample", "cache_cmp_kv", "cache_slc_kv", "cache_win_kv", "state_rwkv_wkv",
        "state_rwkv_shift", "state_conv", "state_ffn_conv", "page_table", "norm_mix", "norm_ffn",
        "rel_bias", "w_in_even", "w_out_even", "q_norm", "k_norm", "phi_pe", "phi_w1", "phi_w2",
        "rwkv_mu", "rwkv_w0", "rwkv_w2", "rwkv_a0", "rwkv_a2", "rwkv_g2", "rwkv_kk", "rwkv_ka", "rwkv_rk",
        "rwkv_ln_w", "rwkv_ln_b", "w_in_odd", "conv_w", "w_out_odd", "ffn_up", "ffn_conv", "ffn_down"]
_OUTS = [("y_prompt", (1, TP, D)), ("y_sample", (NB, TS, D)),
         ("cmp_p", (1, 1, TP, 2, 2, HD)), ("cmp_s", (NB, 1, TS, 2, 2, HD)),
         ("slc_p", (1, 1, TP, 2, 2, HD)), ("slc_s", (NB, 1, TS, 2, 2, HD)),
         ("win_p", (1, 1, TP, 2, 2, HD)), ("win_s", (NB, 1, 512, 2, 2, HD)),
         ("wkv_p", (1, 1, NH, HD, HD)), ("wkv_s", (NB, 1, NH, HD, HD)),
         ("shift_p", (1, 1, W_RW)), ("shift_s", (NB, 1, W_RW)),
         ("conv_p", (1, 1, 2, D)), ("conv_s", (NB, 1, 2, D)),
         ("ffn_p", (1, 2, 2, DFF)), ("ffn_s", (NB, 2, 2, DFF))]


def kernel(**inputs):
    import concourse.bacc as bacc
    from concourse.bass_utils import run_bass_kernel_spmd

    nc = bacc.Bacc("TRN2", target_bir_lowering=False, num_devices=1)
    arrays, ins, outs, consts = {}, {}, {}, {}
    for name in _INS:
        a = np.ascontiguousarray(inputs[name])
        arrays[f"in_{name}"] = a
        ins[name] = nc.dram_tensor(f"in_{name}", a.shape, mybir.dt.from_np(a.dtype), kind="ExternalInput").ap()
    for name, a in tables().items():
        arrays[f"const_{name}"] = a
        consts[name] = nc.dram_tensor(f"const_{name}", a.shape, F32, kind="ExternalInput").ap()
    for name, shape in _OUTS:
        outs[name] = nc.dram_tensor(f"out_{name}", shape, F32, kind="ExternalOutput").ap()
    build(nc, ins, outs, consts)
    r = run_bass_kernel_spmd(nc, [arrays], core_ids=[0])
    return tuple(r.results[0][f"out_{name}"] for name, _ in _OUTS)
```
